# Optimizing a Trainium2 kernel written in Bass

```python
import math
import jax
import jax.numpy as jnp
from jax import lax
import numpy as np

D_MODEL = 1024
BATCH = 1
SEQ = 512
DEPTH = 2

GRID_W = 64
CTX_LEN = 256
HEAD_DIM = 64
BRANCH_W = D_MODEL // 2
MIX_W = 2 * BRANCH_W
NA_HEADS = BRANCH_W // HEAD_DIM
NA_WIN_ROWS = 8
NA_WIN_COLS = 16
GQA_HEADS = BRANCH_W // HEAD_DIM
GQA_KV_HEADS = 2
GQA_GROUP = GQA_HEADS // GQA_KV_HEADS
GQA_KV_W = GQA_KV_HEADS * HEAD_DIM
ROPE_THETA = 10000.0
ROPE_FREQS = HEAD_DIM // 4
Q_BLOCK = 128
RWKV_HEADS = BRANCH_W // HEAD_DIM
DECAY_LORA = 32
ICLR_LORA = 32
HY_WIDTH = BRANCH_W
HY_ORDER = 2
HY_POS_BANDS = 16
HY_POS_DIM = 1 + 2 * HY_POS_BANDS
HY_FILTER_HIDDEN = 64
HY_DECAY_TARGET = 1e-2
HY_FAST_DECAY_PCT = 0.3
HY_SLOW_DECAY_PCT = 1.5
NORM_EPS = 1e-6
RWKV_GN_EPS = 64e-5
N_ATTN_LAYERS = (DEPTH + 1) // 2
N_REC_LAYERS = DEPTH // 2
ATTN_SPLITS = (BRANCH_W, BRANCH_W, BRANCH_W, BRANCH_W, BRANCH_W, GQA_KV_W, GQA_KV_W, BRANCH_W)
ATTN_IN = 6 * BRANCH_W + 2 * GQA_KV_W
RWKV_SPLITS = (BRANCH_W, BRANCH_W, BRANCH_W, DECAY_LORA, DECAY_LORA, ICLR_LORA, ICLR_LORA)
RWKV_SHIFT_W = 3 * BRANCH_W + 2 * DECAY_LORA + 2 * ICLR_LORA
HY_IN_W = (HY_ORDER + 1) * HY_WIDTH
REC_SPLITS = (RWKV_SHIFT_W, BRANCH_W, HY_IN_W, HY_WIDTH)
REC_IN = RWKV_SHIFT_W + BRANCH_W + HY_IN_W + HY_WIDTH


def split_cols(u, sizes):
    parts, start = [], 0
    for s in sizes:
        parts.append(u[..., start:start + s])
        start += s
    return parts

def to_heads(t, n_heads):
    return t.reshape(t.shape[:-1] + (n_heads, HEAD_DIM))

def rms_norm(x, gain):
    xf = x.astype(jnp.float32)
    y = xf * lax.rsqrt(jnp.mean(xf * xf, axis=-1, keepdims=True) + NORM_EPS)
    return (y * gain.astype(jnp.float32)).astype(x.dtype)

def adaln(cond, ada_w, ada_b):
    m = jax.nn.silu(cond) @ ada_w + ada_b
    return jnp.split(m, 3, axis=-1)

def modulate(x, gain, shift, scale):
    return rms_norm(x, gain) * (1 + scale) + shift

def centred_pad(u):
    return jnp.pad(u, ((0, 0), (1, 1), (0, 0)))

def centred_conv3(u, taps):
    up = centred_pad(u)
    return up[:, :-2] * taps[0] + up[:, 1:-1] * taps[1] + up[:, 2:] * taps[2]

def centred_token_shift(u, mu):
    up = centred_pad(u)
    return u + (0.5 * (up[:, :-2] + up[:, 2:]) - u) * mu

def axial_rope_tables(n):
    t = jnp.arange(n, dtype=jnp.int32)
    pos = jnp.stack([t // GRID_W, t % GRID_W], axis=-1).astype(jnp.float32)
    inv_freq = ROPE_THETA ** (-jnp.arange(ROPE_FREQS, dtype=jnp.float32) / ROPE_FREQS)
    ang = pos[:, :, None] * inv_freq
    return jnp.cos(ang), jnp.sin(ang)

def apply_axial_rope(x, cos, sin):
    xs = x.astype(jnp.float32).reshape(x.shape[:-1] + (2, 2, ROPE_FREQS))
    x1, x2 = xs[..., 0, :], xs[..., 1, :]
    c, s = cos[None, :, None], sin[None, :, None]
    y = jnp.stack([x1 * c - x2 * s, x2 * c + x1 * s], axis=-2)
    return y.reshape(x.shape).astype(x.dtype)

def softmax_f32(s):
    return jax.nn.softmax(s.astype(jnp.float32), axis=-1)

def dense_gqa(q, k, v):
    s = jnp.einsum('bqhgd,bkhd->bhgqk', q, k) * (q.shape[-1] ** -0.5)
    p = softmax_f32(s).astype(v.dtype)
    return jnp.einsum('bhgqk,bkhd->bqhgd', p, v)

def blockwise_gqa(q, k, v, k_ctx, v_ctx):
    b, n, hk, g, dh = q.shape
    scale = dh ** -0.5

    def block(q_blk):
        s = jnp.concatenate([jnp.einsum('bqhgd,bkhd->bhgqk', q_blk, k),
                             jnp.einsum('bqhgd,bkhd->bhgqk', q_blk, k_ctx)], axis=-1) * scale
        p = softmax_f32(s).astype(v.dtype)
        return (jnp.einsum('bhgqk,bkhd->bqhgd', p[..., :n], v)
                + jnp.einsum('bhgqk,bkhd->bqhgd', p[..., n:], v_ctx))

    q_blocks = jnp.moveaxis(q.reshape(b, n // Q_BLOCK, Q_BLOCK, hk, g, dh), 1, 0)
    out = lax.map(block, q_blocks)
    return jnp.moveaxis(out, 0, 1).reshape(b, n, hk, g, dh)

def neighbourhood_layout(n, rows):
    kh, kw = min(NA_WIN_ROWS, rows), NA_WIN_COLS
    t = jnp.arange(n, dtype=jnp.int32)
    q_row, q_col = t // GRID_W, t % GRID_W
    row0 = jnp.clip(q_row - kh // 2, 0, rows - kh)
    col0 = jnp.clip(q_col - kw // 2, 0, GRID_W - kw)
    k_row = row0[:, None, None] + jnp.arange(kh, dtype=jnp.int32)[None, :, None]
    k_col = col0[:, None, None] + jnp.arange(kw, dtype=jnp.int32)[None, None, :]
    shape = (n, kh, kw)
    idx = jnp.broadcast_to(k_row * GRID_W + k_col, shape).reshape(n, kh * kw)
    rel_r = jnp.broadcast_to(k_row - q_row[:, None, None] + NA_WIN_ROWS - 1, shape).reshape(n, kh * kw)
    rel_c = jnp.broadcast_to(k_col - q_col[:, None, None] + NA_WIN_COLS - 1, shape).reshape(n, kh * kw)
    return idx, rel_r, rel_c

def neighbourhood_attention(q, k, v, k_ctx, v_ctx, rpb, rows):
    b, n, h, dh = q.shape
    idx, rel_r, rel_c = neighbourhood_layout(n, rows)
    n_win = idx.shape[-1]
    nblk = n // Q_BLOCK
    scale = dh ** -0.5

    def block(args):
        q_blk, idx_blk, rr_blk, rc_blk = args
        k_win = jnp.take(k, idx_blk, axis=1)
        v_win = jnp.take(v, idx_blk, axis=1)
        s_win = jnp.einsum('bqhd,bqkhd->bhqk', q_blk, k_win) * scale + rpb[:, rr_blk, rc_blk][None]
        s_ctx = jnp.einsum('bqhd,bkhd->bhqk', q_blk, k_ctx) * scale
        p = softmax_f32(jnp.concatenate([s_win, s_ctx], axis=-1)).astype(v.dtype)
        return (jnp.einsum('bhqk,bqkhd->bqhd', p[..., :n_win], v_win)
                + jnp.einsum('bhqk,bkhd->bqhd', p[..., n_win:], v_ctx))

    xs = (jnp.moveaxis(q.reshape(b, nblk, Q_BLOCK, h, dh), 1, 0),
          idx.reshape(nblk, Q_BLOCK, n_win),
          rel_r.reshape(nblk, Q_BLOCK, n_win),
          rel_c.reshape(nblk, Q_BLOCK, n_win))
    out = lax.map(block, xs)
    return jnp.moveaxis(out, 0, 1).reshape(b, n, h, dh)

def rwkv_features(u, w0, w_up, a0, a_up, k_k, k_a):
    r, k, v, dw_f, dw_b, da_f, da_b = split_cols(u, RWKV_SPLITS)
    kk = to_heads(k * k_k, RWKV_HEADS).astype(jnp.float32)
    kk = kk * lax.rsqrt(jnp.sum(kk * kk, axis=-1, keepdims=True) + 1e-12)
    dirs = []
    for d, (dw, da) in enumerate(((dw_f, da_f), (dw_b, da_b))):
        w_log = -jax.nn.softplus(-(w0[d] + jnp.tanh(dw) @ w_up[d])) - 0.5
        decay = jnp.exp(-jnp.exp(w_log.astype(jnp.float32)))
        a = jax.nn.sigmoid(a0[d] + da @ a_up[d])
        k_d = k * (1 + (a - 1) * k_a)
        dirs.append((to_heads(decay, RWKV_HEADS), to_heads(k_d, RWKV_HEADS), kk * to_heads(a, RWKV_HEADS)))
    return to_heads(r, RWKV_HEADS), to_heads(v, RWKV_HEADS), kk, dirs

def wkv_scan(s0, r, decay, k, v, kk, b, reverse, emit):
    xs = tuple(jnp.moveaxis(t, 1, 0) for t in (r, decay, k, v, kk, b))

    def step(s, inp):
        r_t, w_t, k_t, v_t, kk_t, b_t = inp
        sa = jnp.einsum('bhij,bhj->bhi', s, kk_t)
        s = s * w_t[:, :, None, :] - sa[..., None] * b_t[:, :, None, :] + v_t[..., None] * k_t[:, :, None, :]
        y = jnp.einsum('bhij,bhj->bhi', s, r_t) if emit else None
        return s, y

    s_final, ys = lax.scan(step, s0, xs, reverse=reverse)
    return s_final, (jnp.moveaxis(ys, 0, 1) if emit else None)

def rwkv_readout(y, r, k_bonus, v, r_k, gn_w, gn_b):
    yf = y.astype(jnp.float32)
    mean = jnp.mean(yf, axis=-1, keepdims=True)
    var = jnp.mean(jnp.square(yf - mean), axis=-1, keepdims=True)
    yn = ((yf - mean) * lax.rsqrt(var + RWKV_GN_EPS)).reshape(y.shape[:2] + (BRANCH_W,))
    yn = (yn * gn_w + gn_b).astype(v.dtype)
    bonus = jnp.sum(r * k_bonus * r_k, axis=-1, keepdims=True) * v
    return yn + bonus.reshape(yn.shape)

def rwkv_branch(u_lat, u_ctx, mu, w0, w_up, a0, a_up, k_k, k_a, r_k, gn_w, gn_b, ctx_out):
    r, v, kk, dirs = rwkv_features(centred_token_shift(u_lat, mu), w0, w_up, a0, a_up, k_k, k_a)
    rc, vc, kkc, dirs_c = rwkv_features(centred_token_shift(u_ctx, mu), w0, w_up, a0, a_up, k_k, k_a)
    s0 = jnp.zeros((u_lat.shape[0], RWKV_HEADS, HEAD_DIM, HEAD_DIM), jnp.float32)
    y_lat, y_ctx = [], []
    for d in range(2):
        reverse = d == 1
        decay_c, k_c, b_c = dirs_c[d]
        s_ctx, yc = wkv_scan(s0, rc, decay_c, k_c, vc, kkc, b_c, reverse, ctx_out)
        decay_l, k_l, b_l = dirs[d]
        _, yl = wkv_scan(s_ctx, r, decay_l, k_l, v, kk, b_l, reverse, True)
        y_lat.append(yl)
        y_ctx.append(yc)
    out_lat = rwkv_readout(y_lat[0] + y_lat[1], r, 0.5 * (dirs[0][1] + dirs[1][1]), v, r_k, gn_w, gn_b)
    out_ctx = None
    if ctx_out:
        out_ctx = rwkv_readout(y_ctx[0] + y_ctx[1], rc, 0.5 * (dirs_c[0][1] + dirs_c[1][1]), vc, r_k, gn_w, gn_b)
    return out_lat, out_ctx

def hyena_filters(L, w1, b1, w2, b2, w3, b3):
    t_idx = jnp.arange(L, dtype=jnp.float32)
    t = t_idx / max(L - 1, 1)
    bands = jnp.linspace(1e-4, HY_POS_BANDS - 1, HY_POS_BANDS, dtype=jnp.float32)
    ang = 2.0 * math.pi * bands[None, :] * t_idx[:, None] / L
    feats = jnp.concatenate([t[:, None], jnp.cos(ang), -jnp.sin(ang)], axis=-1)
    hid = jnp.sin(feats @ w1 + b1)
    hid = jnp.sin(hid @ w2 + b2)
    taps = (hid @ w3 + b3).reshape(L, 2, HY_ORDER, HY_WIDTH)
    deltas = jnp.linspace(math.log(HY_DECAY_TARGET) / HY_FAST_DECAY_PCT,
                          math.log(HY_DECAY_TARGET) / HY_SLOW_DECAY_PCT, HY_WIDTH, dtype=jnp.float32)
    window = jnp.exp(-t[:, None] * jnp.abs(deltas))
    taps = taps * window[:, None, None, :]
    fwd, bwd = taps[:, 0], taps[:, 1]
    kern = jnp.concatenate([fwd[:1] + bwd[:1], fwd[1:], jnp.zeros_like(fwd[:1]), bwd[:0:-1]], axis=0)
    kern = kern.astype(jnp.float32)
    return kern * lax.rsqrt(jnp.sum(kern * kern, axis=0, keepdims=True))

def fft_long_conv(z, kern, skip):
    L = z.shape[1]
    zf = jnp.fft.rfft(z.astype(jnp.float32), n=2 * L, axis=1)
    kf = jnp.fft.rfft(kern, n=2 * L, axis=0)
    y = jnp.fft.irfft(zf * kf[None], n=2 * L, axis=1)[:, :L]
    return (y + z * skip).astype(z.dtype)

def hyena_operator(u, short_taps, kern, skip):
    v, x1, x2 = split_cols(centred_conv3(u, short_taps), (HY_WIDTH, HY_WIDTH, HY_WIDTH))
    z = v
    for o, gate in enumerate((x1, x2)):
        z = gate * fft_long_conv(z, kern[:, o], skip[o])
    return z

def attn_layer(x, ctx, c, c_ctx, norm_g, ada_w, ada_b, w_in, rpb, q_gain, k_gain, w_out, cos, sin, rows, ctx_out):
    b, n, _ = x.shape
    lc = ctx.shape[1]
    shift, scale, gate = adaln(c, ada_w, ada_b)
    shift_c, scale_c, gate_c = adaln(c_ctx, ada_w, ada_b)
    u = modulate(x, norm_g, shift[:, None], scale[:, None]) @ w_in
    uc = modulate(ctx, norm_g, shift_c, scale_c) @ w_in
    qa, ka, va, ga, qb, kb, vb, gb = split_cols(u, ATTN_SPLITS)
    qa_c, ka_c, va_c, ga_c, qb_c, kb_c, vb_c, gb_c = split_cols(uc, ATTN_SPLITS)
    ka_c, va_c = to_heads(ka_c, NA_HEADS), to_heads(va_c, NA_HEADS)
    o_a = neighbourhood_attention(to_heads(qa, NA_HEADS), to_heads(ka, NA_HEADS), to_heads(va, NA_HEADS),
                                  ka_c, va_c, rpb, rows)
    kb_c = rms_norm(to_heads(kb_c, GQA_KV_HEADS), k_gain)
    vb_c = to_heads(vb_c, GQA_KV_HEADS)
    q_lat = apply_axial_rope(rms_norm(to_heads(qb, GQA_HEADS), q_gain), cos, sin)
    q_lat = q_lat.reshape(b, n, GQA_KV_HEADS, GQA_GROUP, HEAD_DIM)
    k_lat = apply_axial_rope(rms_norm(to_heads(kb, GQA_KV_HEADS), k_gain), cos, sin)
    o_b = blockwise_gqa(q_lat, k_lat, to_heads(vb, GQA_KV_HEADS), kb_c, vb_c)
    y = jnp.concatenate([o_a.reshape(b, n, BRANCH_W) * jax.nn.silu(ga),
                         o_b.reshape(b, n, BRANCH_W) * jax.nn.silu(gb)], axis=-1) @ w_out
    x = x + gate[:, None] * y
    if ctx_out:
        oa_c = dense_gqa(to_heads(qa_c, NA_HEADS)[:, :, :, None], ka_c, va_c)
        qb_c = rms_norm(to_heads(qb_c, GQA_HEADS), q_gain).reshape(b, lc, GQA_KV_HEADS, GQA_GROUP, HEAD_DIM)
        ob_c = dense_gqa(qb_c, kb_c, vb_c)
        yc = jnp.concatenate([oa_c.reshape(b, lc, BRANCH_W) * jax.nn.silu(ga_c),
                              ob_c.reshape(b, lc, BRANCH_W) * jax.nn.silu(gb_c)], axis=-1) @ w_out
        ctx = ctx + gate_c * yc
    return x, ctx

def rec_layer(x, ctx, c, c_ctx, norm_g, ada_w, ada_b, w_in, mu, w0, w_up, a0, a_up, k_k, k_a, r_k, gn_w, gn_b,
              hy_short, hy_w1, hy_b1, hy_w2, hy_b2, hy_w3, hy_b3, hy_skip, w_out, ctx_out):
    shift, scale, gate = adaln(c, ada_w, ada_b)
    shift_c, scale_c, gate_c = adaln(c_ctx, ada_w, ada_b)
    u = modulate(x, norm_g, shift[:, None], scale[:, None]) @ w_in
    uc = modulate(ctx, norm_g, shift_c, scale_c) @ w_in
    u_rw, g_rw, u_hy, g_hy = split_cols(u, REC_SPLITS)
    uc_rw, gc_rw, uc_hy, gc_hy = split_cols(uc, REC_SPLITS)
    y_rw, yc_rw = rwkv_branch(u_rw, uc_rw, mu, w0, w_up, a0, a_up, k_k, k_a, r_k, gn_w, gn_b, ctx_out)
    y_hy = hyena_operator(u_hy, hy_short, hyena_filters(x.shape[1], hy_w1, hy_b1, hy_w2, hy_b2, hy_w3, hy_b3), hy_skip)
    y = jnp.concatenate([y_rw * jax.nn.silu(g_rw), y_hy * jax.nn.silu(g_hy)], axis=-1) @ w_out
    x = x + gate[:, None] * y
    if ctx_out:
        kern_c = hyena_filters(ctx.shape[1], hy_w1, hy_b1, hy_w2, hy_b2, hy_w3, hy_b3)
        yc_hy = hyena_operator(uc_hy, hy_short, kern_c, hy_skip)
        yc = jnp.concatenate([yc_rw * jax.nn.silu(gc_rw), yc_hy * jax.nn.silu(gc_hy)], axis=-1) @ w_out
        ctx = ctx + gate_c * yc
    return x, ctx

def first_inputs(seed: int = 0) -> dict:
    key = jax.random.key(seed)
    keys = iter(jax.random.split(key, 48))

    def normal(shape, scale=1.0):
        return scale * jax.random.normal(next(keys), shape, jnp.float32)

    na, nr, d = N_ATTN_LAYERS, N_REC_LAYERS, D_MODEL
    return {
        "x": normal((BATCH, SEQ, d)),
        "c": normal((BATCH, d)),
        "ctx": normal((BATCH, CTX_LEN, d)),
        "c_ctx": normal((d,)),
        "attn_norm": 1.0 + normal((na, d), 0.1),
        "attn_ada_w": normal((na, d, 3 * d), d ** -0.5),
        "attn_ada_b": normal((na, 3 * d), 0.1),
        "attn_w_in": normal((na, d, ATTN_IN), d ** -0.5),
        "na_rpb": normal((na, NA_HEADS, 2 * NA_WIN_ROWS - 1, 2 * NA_WIN_COLS - 1), 0.5),
        "gqa_q_gain": 1.0 + normal((na, HEAD_DIM), 0.1),
        "gqa_k_gain": 1.0 + normal((na, HEAD_DIM), 0.1),
        "attn_w_out": normal((na, MIX_W, d), MIX_W ** -0.5),
        "rec_norm": 1.0 + normal((nr, d), 0.1),
        "rec_ada_w": normal((nr, d, 3 * d), d ** -0.5),
        "rec_ada_b": normal((nr, 3 * d), 0.1),
        "rec_w_in": normal((nr, d, REC_IN), d ** -0.5),
        "rwkv_mu": jax.random.uniform(next(keys), (nr, RWKV_SHIFT_W), jnp.float32),
        "rwkv_w0": jnp.linspace(-6.0, -0.5, BRANCH_W, dtype=jnp.float32) + normal((nr, 2, BRANCH_W), 0.1),
        "rwkv_w_up": normal((nr, 2, DECAY_LORA, BRANCH_W), 0.1),
        "rwkv_a0": normal((nr, 2, BRANCH_W), 0.5),
        "rwkv_a_up": normal((nr, 2, ICLR_LORA, BRANCH_W), ICLR_LORA ** -0.5),
        "rwkv_k_k": 0.85 + normal((nr, BRANCH_W), 0.05),
        "rwkv_k_a": 1.0 + normal((nr, BRANCH_W), 0.05),
        "rwkv_r_k": normal((nr, RWKV_HEADS, HEAD_DIM), 0.1),
        "rwkv_gn_w": 1.0 + normal((nr, BRANCH_W), 0.1),
        "rwkv_gn_b": normal((nr, BRANCH_W), 0.1),
        "hy_short": normal((nr, 3, HY_IN_W), 3 ** -0.5),
        "hy_w1": normal((nr, HY_POS_DIM, HY_FILTER_HIDDEN), HY_POS_DIM ** -0.5),
        "hy_b1": normal((nr, HY_FILTER_HIDDEN), 0.1),
        "hy_w2": normal((nr, HY_FILTER_HIDDEN, HY_FILTER_HIDDEN), HY_FILTER_HIDDEN ** -0.5),
        "hy_b2": normal((nr, HY_FILTER_HIDDEN), 0.1),
        "hy_w3": normal((nr, HY_FILTER_HIDDEN, 2 * HY_ORDER * HY_WIDTH), HY_FILTER_HIDDEN ** -0.5),
        "hy_b3": normal((nr, 2 * HY_ORDER * HY_WIDTH), 0.1),
        "hy_skip": normal((nr, HY_ORDER, HY_WIDTH), 0.5),
        "rec_w_out": normal((nr, MIX_W, d), MIX_W ** -0.5),
        "final_norm": 1.0 + normal((d,), 0.1),
    }

def first_block(x, c, ctx, c_ctx, attn_norm, attn_ada_w, attn_ada_b, attn_w_in, na_rpb, gqa_q_gain, gqa_k_gain,
              attn_w_out, rec_norm, rec_ada_w, rec_ada_b, rec_w_in, rwkv_mu, rwkv_w0, rwkv_w_up, rwkv_a0, rwkv_a_up,
              rwkv_k_k, rwkv_k_a, rwkv_r_k, rwkv_gn_w, rwkv_gn_b, hy_short, hy_w1, hy_b1, hy_w2, hy_b2, hy_w3, hy_b3,
              hy_skip, rec_w_out, final_norm):
    n = x.shape[1]
    rows = n // GRID_W
    cos, sin = axial_rope_tables(n)
    for layer in range(DEPTH):
        i = layer // 2
        ctx_out = layer < DEPTH - 1
        if layer % 2 == 0:
            x, ctx = attn_layer(x, ctx, c, c_ctx, attn_norm[i], attn_ada_w[i], attn_ada_b[i], attn_w_in[i],
                                na_rpb[i], gqa_q_gain[i], gqa_k_gain[i], attn_w_out[i], cos, sin, rows, ctx_out)
        else:
            x, ctx = rec_layer(x, ctx, c, c_ctx, rec_norm[i], rec_ada_w[i], rec_ada_b[i], rec_w_in[i],
                               rwkv_mu[i], rwkv_w0[i], rwkv_w_up[i], rwkv_a0[i], rwkv_a_up[i], rwkv_k_k[i],
                               rwkv_k_a[i], rwkv_r_k[i], rwkv_gn_w[i], rwkv_gn_b[i], hy_short[i], hy_w1[i],
                               hy_b1[i], hy_w2[i], hy_b2[i], hy_w3[i], hy_b3[i], hy_skip[i], rec_w_out[i], ctx_out)
    return rms_norm(x, final_norm)


DEPTH_2 = 1

N_MEM = 256
D_FF = 2816
NEG_INF = -1e30
FORCE_SCORE = 1e4

NSA_HEADS = 8
NSA_GROUPS = 2
NSA_HPG = NSA_HEADS // NSA_GROUPS
NSA_HEAD_DIM = 64
CMP_BLOCK = 32
CMP_STRIDE = 16
CMP_HIDDEN = 256
SEL_BLOCK = 64
SEL_TOPK = 16
WINDOW = 512
WIN_QBLOCK = 128
SEL_QCHUNK = 16

REL_BUCKETS = 32
REL_MAX_DIST = 128

DN_HEADS = 4
DN_HEAD_DIM = 128
DN_CONV = 4
DN_CHUNK = 64

X_HEADS = 4
X_HEAD_DIM = 128

N_BRANCH = 3
NSA_Q = NSA_HEADS * NSA_HEAD_DIM
NSA_KV = NSA_GROUPS * NSA_HEAD_DIM
DN_W = DN_HEADS * DN_HEAD_DIM
X_W = X_HEADS * X_HEAD_DIM
IN_SPLITS = (NSA_Q, 6 * NSA_KV, 3 * NSA_HEADS, 3 * DN_W, DN_HEADS, DN_HEADS, DN_W, X_W)
IN_WIDTH = NSA_Q + 6 * NSA_KV + 3 * NSA_HEADS + 3 * DN_W + 2 * DN_HEADS + DN_W + X_W


def rms_norm_2(x, gain):
    xf = x.astype(jnp.float32)
    y = xf * lax.rsqrt(jnp.mean(xf * xf, axis=-1, keepdims=True) + NORM_EPS)
    return (y * gain.astype(jnp.float32)).astype(x.dtype)

def l2_norm(x):
    xf = x.astype(jnp.float32)
    return xf * lax.rsqrt(jnp.sum(xf * xf, axis=-1, keepdims=True) + NORM_EPS)

def swiglu(x, w_gate, w_up, w_down):
    return (jax.nn.silu(x @ w_gate) * (x @ w_up)) @ w_down

def split_cols_2(a, sizes):
    out, start = [], 0
    for n in sizes:
        out.append(a[..., start:start + n])
        start += n
    return out

def rel_bucket(dist):
    exact = REL_BUCKETS // 2
    d = jnp.maximum(dist, 1).astype(jnp.float32)
    log_bucket = exact + (jnp.log(d / exact) / math.log(REL_MAX_DIST / exact)
                          * (REL_BUCKETS - exact)).astype(jnp.int32)
    return jnp.where(dist < exact, dist, jnp.minimum(log_bucket, REL_BUCKETS - 1))

def masked_softmax(logits, mask):
    return jax.nn.softmax(jnp.where(mask, logits.astype(jnp.float32), NEG_INF), axis=-1)

def compress_blocks(kv, pos_emb, w1, w2):
    b, s, g, dh = kv.shape
    r = CMP_BLOCK // CMP_STRIDE
    n_chunk = s // CMP_STRIDE
    n_cmp = n_chunk - r + 1
    ch = kv.reshape(b, n_chunk, CMP_STRIDE, g, dh)
    blocks = jnp.concatenate([ch[:, j:j + n_cmp] for j in range(r)], axis=2)
    blocks = blocks + pos_emb[:, None, :]
    flat = blocks.transpose(0, 1, 3, 2, 4).reshape(b, n_cmp, g, CMP_BLOCK * dh)
    return jax.nn.silu(flat @ w1) @ w2

def nsa_compressed(q, k_c, v_c, rel_bias):
    seq, n_cmp = q.shape[1], k_c.shape[1]
    t = jnp.arange(seq)
    block_end = jnp.arange(n_cmp) * CMP_STRIDE + CMP_BLOCK - 1
    dist = t[:, None] - block_end[None, :]
    bias = rel_bias[rel_bucket(jnp.maximum(dist, 0))]
    bias = bias.reshape(seq, n_cmp, NSA_GROUPS, NSA_HPG).transpose(2, 3, 0, 1)
    logits = jnp.einsum('bsgjd,bcgd->bgjsc', q, k_c) * NSA_HEAD_DIM ** -0.5 + bias
    has_block = (t >= CMP_BLOCK - 1).astype(jnp.float32)[:, None]
    p = masked_softmax(logits, dist >= 0) * has_block
    out = jnp.einsum('bgjsc,bcgd->bsgjd', p.astype(v_c.dtype), v_c)
    return out, p

def select_blocks(p_cmp, seq):
    n_cmp = p_cmp.shape[-1]
    n_blk = seq // SEL_BLOCK
    n_sel = min(SEL_TOPK, n_blk)
    c0 = jnp.arange(n_cmp) * CMP_STRIDE
    s0 = jnp.arange(n_blk) * SEL_BLOCK
    overlap = jnp.maximum(jnp.minimum(c0[:, None] + CMP_BLOCK, s0[None, :] + SEL_BLOCK)
                          - jnp.maximum(c0[:, None], s0[None, :]), 0)
    to_sel = overlap.astype(jnp.float32) / CMP_BLOCK
    importance = jnp.einsum('bgjsc,cn->bgsn', p_cmp, to_sel)
    cur = jnp.arange(seq) // SEL_BLOCK
    blk = jnp.arange(n_blk)
    forced = (blk[None] == 0) | (blk[None] == cur[:, None]) | (blk[None] == cur[:, None] - 1)
    causal = blk[None] <= cur[:, None]
    score = jnp.where(forced, FORCE_SCORE, jnp.where(causal, importance, -FORCE_SCORE))
    vals, idx = lax.top_k(score, n_sel)
    return idx, vals > -1.0

def nsa_selected(q, k_s, v_s, idx, ok, rel_bias):
    b, s, g, j, dh = q.shape
    n_blk = s // SEL_BLOCK
    n_sel = idx.shape[-1]
    kb = k_s.reshape(b, n_blk, SEL_BLOCK, g, dh).transpose(0, 3, 1, 2, 4)
    vb = v_s.reshape(b, n_blk, SEL_BLOCK, g, dh).transpose(0, 3, 1, 2, 4)
    table_g = rel_bias.reshape(REL_BUCKETS, NSA_GROUPS, NSA_HPG)
    offs = jnp.arange(SEL_BLOCK)

    def one(qg, kg, vg, ix, okg, t, tab):
        ks = kg[ix]
        vs = vg[ix]
        dist = t[:, None, None] - (ix[..., None] * SEL_BLOCK + offs)
        mask = okg[..., None] & (dist >= 0)
        bias = tab[rel_bucket(jnp.maximum(dist, 0))].transpose(0, 3, 1, 2)
        logits = jnp.einsum('qjd,qknd->qjkn', qg, ks) * NSA_HEAD_DIM ** -0.5 + bias
        nq = logits.shape[0]
        p = masked_softmax(logits.reshape(nq, j, n_sel * SEL_BLOCK),
                           mask.reshape(nq, 1, n_sel * SEL_BLOCK)).reshape(nq, j, n_sel, SEL_BLOCK)
        return jnp.einsum('qjkn,qknd->qjd', p.astype(vs.dtype), vs)

    per_g = jax.vmap(one, in_axes=(1, 0, 0, 0, 0, None, 1), out_axes=1)
    per_bg = jax.vmap(per_g, in_axes=(0, 0, 0, 0, 0, None, None), out_axes=0)
    n_chunk = s // SEL_QCHUNK
    qs = q.reshape(b, n_chunk, SEL_QCHUNK, g, j, dh).transpose(1, 0, 2, 3, 4, 5)
    ixs = idx.reshape(b, g, n_chunk, SEL_QCHUNK, n_sel).transpose(2, 0, 1, 3, 4)
    oks = ok.reshape(b, g, n_chunk, SEL_QCHUNK, n_sel).transpose(2, 0, 1, 3, 4)
    ts = jnp.arange(s).reshape(n_chunk, SEL_QCHUNK)

    def chunk(args):
        qc, ixc, okc, tc = args
        return per_bg(qc, kb, vb, ixc, okc, tc, table_g)

    out = lax.map(chunk, (qs, ixs, oks, ts))
    return out.transpose(1, 0, 2, 3, 4, 5).reshape(b, s, g, j, dh)

def nsa_window(q, k_w, v_w, rel_bias):
    b, s, g, j, dh = q.shape
    n_qb = s // WIN_QBLOCK
    span = WINDOW + WIN_QBLOCK
    pad = ((0, 0), (WINDOW, 0), (0, 0), (0, 0))
    kp = jnp.pad(k_w, pad)
    vp = jnp.pad(v_w, pad)
    qi = jnp.arange(WIN_QBLOCK)
    kj = jnp.arange(span)
    rel = qi[:, None] + WINDOW - kj[None, :]
    bias = rel_bias[rel_bucket(jnp.maximum(rel, 0))]
    bias = bias.reshape(WIN_QBLOCK, span, g, j).transpose(2, 3, 0, 1)
    band = (rel >= 0) & (rel < WINDOW)

    def block(i):
        start = i * WIN_QBLOCK
        qb = lax.dynamic_slice_in_dim(q, start, WIN_QBLOCK, axis=1)
        kb = lax.dynamic_slice_in_dim(kp, start, span, axis=1)
        vb = lax.dynamic_slice_in_dim(vp, start, span, axis=1)
        mask = band & ((start - WINDOW + kj) >= 0)[None, :]
        logits = jnp.einsum('bqgjd,bkgd->bgjqk', qb, kb) * NSA_HEAD_DIM ** -0.5 + bias
        p = masked_softmax(logits, mask)
        return jnp.einsum('bgjqk,bkgd->bqgjd', p.astype(vb.dtype), vb)

    out = lax.map(block, jnp.arange(n_qb))
    return out.transpose(1, 0, 2, 3, 4, 5).reshape(b, s, g, j, dh)

def causal_depthwise_conv(x, w):
    return lax.conv_general_dilated(
        x, w[:, None, :].astype(x.dtype), window_strides=(1,), padding=[(w.shape[0] - 1, 0)],
        dimension_numbers=('NWC', 'WIO', 'NWC'), feature_group_count=x.shape[-1])

def gated_delta_rule(q, k, v, log_decay, beta):
    f32 = jnp.float32
    b, s, h, dk = q.shape
    dv = v.shape[-1]
    c = DN_CHUNK
    n = s // c

    def chunks(a):
        a = a.astype(f32).reshape((b, n, c, h) + a.shape[3:])
        return jnp.moveaxis(a, 3, 1)

    qc = chunks(q) * dk ** -0.5
    kc, vc = chunks(k), chunks(v)
    gc = jnp.cumsum(chunks(log_decay), axis=-1)
    bc = chunks(beta)
    causal = jnp.tril(jnp.ones((c, c), bool))
    strict = jnp.tril(jnp.ones((c, c), bool), -1)
    decay = jnp.exp(jnp.where(causal, gc[..., :, None] - gc[..., None, :], -jnp.inf))
    kk = jnp.einsum('bhnid,bhnjd->bhnij', kc, kc)
    a_mat = jnp.where(strict, bc[..., :, None] * kk * decay, 0.0) + jnp.eye(c, dtype=f32)
    rhs = jnp.concatenate([vc * bc[..., None], kc * (bc * jnp.exp(gc))[..., None]], axis=-1)
    sol = lax.linalg.triangular_solve(a_mat, rhs, left_side=True, lower=True, unit_diagonal=True)
    u, w = sol[..., :dv], sol[..., dv:]
    qk = jnp.einsum('bhnid,bhnjd->bhnij', qc, kc) * decay
    q_dec = qc * jnp.exp(gc)[..., None]
    k_dec = kc * jnp.exp(gc[..., -1:] - gc)[..., None]
    g_last = jnp.exp(gc[..., -1])

    def step(state, inp):
        qk_n, qd_n, kd_n, u_n, w_n, gl_n = inp
        v_new = u_n - jnp.einsum('bhck,bhkv->bhcv', w_n, state)
        o = jnp.einsum('bhck,bhkv->bhcv', qd_n, state) + jnp.einsum('bhcm,bhmv->bhcv', qk_n, v_new)
        state = state * gl_n[..., None, None] + jnp.einsum('bhck,bhcv->bhkv', kd_n, v_new)
        return state, o

    xs = tuple(jnp.moveaxis(a, 2, 0) for a in (qk, q_dec, k_dec, u, w, g_last))
    _, o = lax.scan(step, jnp.zeros((b, h, dk, dv), f32), xs)
    return o.transpose(1, 0, 3, 2, 4).reshape(b, s, h, dv)

def memory_cross_attention(q, mem_n, w_mem_kv):
    b, m, _ = mem_n.shape
    kv = (mem_n @ w_mem_kv).reshape(b, m, 2, X_HEADS, X_HEAD_DIM)
    k, v = kv[:, :, 0], kv[:, :, 1]
    logits = jnp.einsum('bshd,bmhd->bhsm', q, k) * X_HEAD_DIM ** -0.5
    p = jax.nn.softmax(logits.astype(jnp.float32), axis=-1).astype(v.dtype)
    return jnp.einsum('bhsm,bmhd->bshd', p, v)

def second_inputs(seed: int = 0) -> dict:
    key = jax.random.key(seed)
    keys = iter(jax.random.split(key, 48))
    f32 = jnp.float32
    L, D = DEPTH_2, D_MODEL

    def normal(shape, scale):
        return jax.random.normal(next(keys), shape, f32) * scale

    def gain(width):
        return 1.0 + 0.02 * jax.random.normal(next(keys), (L, width), f32)

    dt = jnp.exp(jax.random.uniform(next(keys), (L, DN_HEADS), f32, math.log(1e-3), math.log(1e-1)))
    a_log = jnp.log(jax.random.uniform(next(keys), (L, DN_HEADS), f32, 1.0, 16.0))
    return {
        "x": normal((BATCH, SEQ, D), 1.0),
        "mem": normal((BATCH, N_MEM, D), 1.0),
        "ffn1_pre_norm": gain(D),
        "ffn1_w_gate": normal((L, D, D_FF), D ** -0.5),
        "ffn1_w_up": normal((L, D, D_FF), D ** -0.5),
        "ffn1_w_down": normal((L, D_FF, D), D_FF ** -0.5),
        "ffn1_post_norm": gain(D),
        "mix_pre_norm": gain(D),
        "w_in": normal((L, D, IN_WIDTH), D ** -0.5),
        "cmp_pos_k": normal((L, CMP_BLOCK, NSA_HEAD_DIM), 0.1),
        "cmp_pos_v": normal((L, CMP_BLOCK, NSA_HEAD_DIM), 0.1),
        "cmp_k_w1": normal((L, CMP_BLOCK * NSA_HEAD_DIM, CMP_HIDDEN), (CMP_BLOCK * NSA_HEAD_DIM) ** -0.5),
        "cmp_k_w2": normal((L, CMP_HIDDEN, NSA_HEAD_DIM), CMP_HIDDEN ** -0.5),
        "cmp_v_w1": normal((L, CMP_BLOCK * NSA_HEAD_DIM, CMP_HIDDEN), (CMP_BLOCK * NSA_HEAD_DIM) ** -0.5),
        "cmp_v_w2": normal((L, CMP_HIDDEN, NSA_HEAD_DIM), CMP_HIDDEN ** -0.5),
        "rel_bias": normal((REL_BUCKETS, NSA_HEADS), 0.5),
        "dn_conv_w": normal((L, DN_CONV, 3 * DN_W), DN_CONV ** -0.5),
        "dn_a_log": a_log,
        "dn_dt_bias": dt + jnp.log(-jnp.expm1(-dt)),
        "dn_out_norm": gain(DN_HEAD_DIM),
        "mem_norm": gain(D),
        "w_mem_kv": normal((L, D, 2 * X_W), D ** -0.5),
        "w_branch_nsa": normal((L, NSA_Q, D), NSA_Q ** -0.5),
        "w_branch_dn": normal((L, DN_W, D), DN_W ** -0.5),
        "w_branch_mem": normal((L, X_W, D), X_W ** -0.5),
        "w_branch_gate": normal((L, D, N_BRANCH * D), D ** -0.5),
        "w_out": normal((L, D, D), D ** -0.5),
        "mix_post_norm": gain(D),
        "ffn2_pre_norm": gain(D),
        "ffn2_w_gate": normal((L, D, D_FF), D ** -0.5),
        "ffn2_w_up": normal((L, D, D_FF), D ** -0.5),
        "ffn2_w_down": normal((L, D_FF, D), D_FF ** -0.5),
        "ffn2_post_norm": gain(D),
    }

def second_block(x, mem, ffn1_pre_norm, ffn1_w_gate, ffn1_w_up, ffn1_w_down, ffn1_post_norm,
              mix_pre_norm, w_in, cmp_pos_k, cmp_pos_v, cmp_k_w1, cmp_k_w2, cmp_v_w1, cmp_v_w2,
              rel_bias, dn_conv_w, dn_a_log, dn_dt_bias, dn_out_norm, mem_norm, w_mem_kv,
              w_branch_nsa, w_branch_dn, w_branch_mem, w_branch_gate, w_out, mix_post_norm,
              ffn2_pre_norm, ffn2_w_gate, ffn2_w_up, ffn2_w_down, ffn2_post_norm):
    b, s, d = x.shape
    f32 = jnp.float32
    for l in range(DEPTH_2):
        h = swiglu(rms_norm_2(x, ffn1_pre_norm[l]), ffn1_w_gate[l], ffn1_w_up[l], ffn1_w_down[l])
        x = x + 0.5 * rms_norm_2(h, ffn1_post_norm[l])

        u = rms_norm_2(x, mix_pre_norm[l])
        nsa_q, nsa_kv, nsa_g, dn_qkv, dn_a, dn_b, dn_z, mem_q = split_cols_2(u @ w_in[l], IN_SPLITS)

        q = nsa_q.reshape(b, s, NSA_GROUPS, NSA_HPG, NSA_HEAD_DIM)
        kv = nsa_kv.reshape(b, s, 6, NSA_GROUPS, NSA_HEAD_DIM)
        k_cmp = compress_blocks(kv[:, :, 0], cmp_pos_k[l], cmp_k_w1[l], cmp_k_w2[l])
        v_cmp = compress_blocks(kv[:, :, 1], cmp_pos_v[l], cmp_v_w1[l], cmp_v_w2[l])
        o_cmp, p_cmp = nsa_compressed(q, k_cmp, v_cmp, rel_bias)
        sel_idx, sel_ok = select_blocks(p_cmp, s)
        o_sel = nsa_selected(q, kv[:, :, 2], kv[:, :, 3], sel_idx, sel_ok, rel_bias)
        o_win = nsa_window(q, kv[:, :, 4], kv[:, :, 5], rel_bias)
        g = jax.nn.sigmoid(nsa_g).reshape(b, s, 3, NSA_GROUPS, NSA_HPG, 1)
        o_nsa = (g[:, :, 0] * o_cmp + g[:, :, 1] * o_sel + g[:, :, 2] * o_win).reshape(b, s, NSA_Q)

        qkv = jax.nn.silu(causal_depthwise_conv(dn_qkv, dn_conv_w[l]))
        dq, dk, dv = split_cols_2(qkv, (DN_W, DN_W, DN_W))
        dq = l2_norm(dq.reshape(b, s, DN_HEADS, DN_HEAD_DIM))
        dk = l2_norm(dk.reshape(b, s, DN_HEADS, DN_HEAD_DIM))
        dv = dv.reshape(b, s, DN_HEADS, DN_HEAD_DIM)
        log_decay = -jnp.exp(dn_a_log[l].astype(f32)) * jax.nn.softplus((dn_a + dn_dt_bias[l]).astype(f32))
        beta = jax.nn.sigmoid(dn_b.astype(f32))
        o_dn = gated_delta_rule(dq, dk, dv, log_decay, beta).astype(x.dtype)
        o_dn = rms_norm_2(o_dn, dn_out_norm[l]) * jax.nn.silu(dn_z.reshape(b, s, DN_HEADS, DN_HEAD_DIM))
        o_dn = o_dn.reshape(b, s, DN_W)

        o_mem = memory_cross_attention(mem_q.reshape(b, s, X_HEADS, X_HEAD_DIM),
                                       rms_norm_2(mem, mem_norm[l]), w_mem_kv[l]).reshape(b, s, X_W)

        gates = jax.nn.sigmoid(u @ w_branch_gate[l]).reshape(b, s, N_BRANCH, d)
        merged = (gates[:, :, 0] * (o_nsa @ w_branch_nsa[l])
                  + gates[:, :, 1] * (o_dn @ w_branch_dn[l])
                  + gates[:, :, 2] * (o_mem @ w_branch_mem[l]))
        x = x + rms_norm_2(merged @ w_out[l], mix_post_norm[l])

        h = swiglu(rms_norm_2(x, ffn2_pre_norm[l]), ffn2_w_gate[l], ffn2_w_up[l], ffn2_w_down[l])
        x = x + 0.5 * rms_norm_2(h, ffn2_post_norm[l])
    return x


def setup_inputs(seed=0):
    out = dict(first_inputs(seed))
    for name, value in second_inputs(seed + 1).items():
        if name != "x":
            out[name + "_2"] = value
    return out


def reference(
    x, c, ctx, c_ctx, attn_norm, attn_ada_w, attn_ada_b, attn_w_in, na_rpb, gqa_q_gain,
    gqa_k_gain, attn_w_out, rec_norm, rec_ada_w, rec_ada_b, rec_w_in, rwkv_mu, rwkv_w0,
    rwkv_w_up, rwkv_a0, rwkv_a_up, rwkv_k_k, rwkv_k_a, rwkv_r_k, rwkv_gn_w, rwkv_gn_b, hy_short,
    hy_w1, hy_b1, hy_w2, hy_b2, hy_w3, hy_b3, hy_skip, rec_w_out, final_norm, mem_2,
    ffn1_pre_norm_2, ffn1_w_gate_2, ffn1_w_up_2, ffn1_w_down_2, ffn1_post_norm_2,
    mix_pre_norm_2, w_in_2, cmp_pos_k_2, cmp_pos_v_2, cmp_k_w1_2, cmp_k_w2_2, cmp_v_w1_2,
    cmp_v_w2_2, rel_bias_2, dn_conv_w_2, dn_a_log_2, dn_dt_bias_2, dn_out_norm_2, mem_norm_2,
    w_mem_kv_2, w_branch_nsa_2, w_branch_dn_2, w_branch_mem_2, w_branch_gate_2, w_out_2,
    mix_post_norm_2, ffn2_pre_norm_2, ffn2_w_gate_2, ffn2_w_up_2, ffn2_w_down_2,
    ffn2_post_norm_2,
):
    x = first_block(
        x, c, ctx, c_ctx, attn_norm, attn_ada_w, attn_ada_b, attn_w_in, na_rpb, gqa_q_gain,
        gqa_k_gain, attn_w_out, rec_norm, rec_ada_w, rec_ada_b, rec_w_in, rwkv_mu, rwkv_w0,
        rwkv_w_up, rwkv_a0, rwkv_a_up, rwkv_k_k, rwkv_k_a, rwkv_r_k, rwkv_gn_w, rwkv_gn_b,
        hy_short, hy_w1, hy_b1, hy_w2, hy_b2, hy_w3, hy_b3, hy_skip, rec_w_out, final_norm,
    )
    return second_block(
        x, mem_2, ffn1_pre_norm_2, ffn1_w_gate_2, ffn1_w_up_2, ffn1_w_down_2, ffn1_post_norm_2,
        mix_pre_norm_2, w_in_2, cmp_pos_k_2, cmp_pos_v_2, cmp_k_w1_2, cmp_k_w2_2, cmp_v_w1_2,
        cmp_v_w2_2, rel_bias_2, dn_conv_w_2, dn_a_log_2, dn_dt_bias_2, dn_out_norm_2,
        mem_norm_2, w_mem_kv_2, w_branch_nsa_2, w_branch_dn_2, w_branch_mem_2, w_branch_gate_2,
        w_out_2, mix_post_norm_2, ffn2_pre_norm_2, ffn2_w_gate_2, ffn2_w_up_2, ffn2_w_down_2,
        ffn2_post_norm_2,
    )


_drawn_inputs = setup_inputs


def setup_inputs(seed=0):
    import zlib

    import numpy as np

    out = dict(_drawn_inputs(seed))
    spreads = {}
    factors = {'gqa_q_gain': 5.488,
     'gqa_k_gain': 5.287,
     'rwkv_gn_w': 3.266,
     'rwkv_gn_b': 2.762,
     'ffn1_pre_norm_2': 3.41,
     'ffn1_post_norm_2': 4.354,
     'cmp_pos_k_2': 64.0,
     'dn_out_norm_2': 35.923,
     'mem_norm_2': 8.0,
     'mix_post_norm_2': 10.984,
     'ffn2_pre_norm_2': 19.877,
     'ffn2_post_norm_2': 34.564,
     'cmp_pos_v_2': 8.0,
     'cmp_k_w1_2': 7.744,
     'cmp_k_w2_2': 7.523,
     'cmp_v_w1_2': 2.852,
     'rel_bias_2': 6.023}
    for name, (base, spread) in spreads.items():
        noise = np.random.default_rng([zlib.crc32(name.encode()), seed]).standard_normal(out[name].shape)
        drawn = base * np.exp(spread * noise) if base else spread * noise
        out[name] = jnp.asarray(drawn.astype(out[name].dtype))
    for name, factor in factors.items():
        out[name] = (out[name] * factor).astype(out[name].dtype)
    return out
```

```python
from contextlib import ExitStack

import numpy as np
import concourse.bass as bass
from concourse import mybir

F32 = mybir.dt.float32
ALU = mybir.AluOpType
ACT = mybir.ActivationFunctionType
AX = mybir.AxisListType
P = 128
BANK = 512
D = 1024
KD = D // P
S = 512
LC = 256
TT = S + LC
EPS = 1e-6
NEG = -1e30


class Stage:

    def __init__(self, nc, name):
        self.nc, self.name = nc, name

    used = 0

    def __enter__(self):
        self.stack = ExitStack()
        if Stage.used > 120:
            nc, free = self.nc, list(self.nc.free_semaphores)
            nc.gpsimd.sem_clear(range(min(free), max(free) + 1))
            nc.all_engine_barrier()
            Stage.used = 0
        return self

    def __exit__(self, *e):
        return self.stack.__exit__(*e)

    def sb(self, name, shape):
        return self.stack.enter_context(self.nc.sbuf_tensor(f"{self.name}_{name}", shape, F32))

    def ps(self, name, shape):
        return self.stack.enter_context(self.nc.psum_tensor(f"{self.name}_{name}", shape, F32))

    def sem(self, name):
        Stage.used += 1
        return self.stack.enter_context(self.nc.semaphore(f"{self.name}_{name}"))

    def block(self):
        return self.stack.enter_context(self.nc.Block())


class Chain:

    def __init__(self, engine, sem):
        self.engine, self.sem, self.n = engine, sem, 0

    def link(self, ins):
        self.n += 1
        ins.then_inc(self.sem, 1)
        self.engine.wait_ge(self.sem, self.n)


def spans(n, step):
    return [(a, min(step, n - a)) for a in range(0, n, step)]


def load(nc, name, pairs):
    with Stage(nc, name) as st:
        landed = st.sem("landed")
        block = st.block()

        @block.sync
        def _(sp):
            for dst, src in pairs[0::2]:
                sp.dma_start(dst, src).then_inc(landed, 16)
            sp.wait_ge(landed, 16 * len(pairs))

        @block.scalar
        def _(act):
            for dst, src in pairs[1::2]:
                act.dma_start(dst, src).then_inc(landed, 16)


def linear(nc, name, x, blocks, T, evict, kc=KD, bufs=3, width=512, engines="va"):
    tiles = [(b, i, w) for b, (_, ws) in enumerate(blocks) for i, w in enumerate(ws)]
    banks = -(-T // BANK)
    slots = 8 // banks if banks > 1 else 6
    last_of = [max(n for n, t in enumerate(tiles) if t[0] == b) for b in range(len(blocks))]
    with Stage(nc, name) as st:
        w = [st.sb(f"w{i}", [P, kc, width]) for i in range(bufs)]
        ps = [st.ps(f"acc{i}", [P, banks * BANK]) for i in range(slots)]
        w_landed = [st.sem(f"w_landed{i}") for i in range(bufs)]
        product_done = st.sem("product_done")
        stored = {"v": st.sem("stored_v"), "a": st.sem("stored_a")}
        block = st.block()
        landings, total = [], [0] * bufs
        for b, (loads, _) in enumerate(blocks):
            total[b % bufs] += 16 * len(loads)
            landings.append(total[b % bufs])

        @block.sync
        def _(sp):
            for b, (loads, _) in enumerate(blocks):
                if b >= bufs:
                    sp.wait_ge(product_done, last_of[b - bufs] + 1)
                for place, src in loads:
                    sp.dma_start(place(w[b % bufs]), src).then_inc(w_landed[b % bufs], 16)

        @block.tensor
        def _(pe):
            for n, (b, i, m) in enumerate(tiles):
                if i == 0:
                    pe.wait_ge(w_landed[b % bufs], landings[b])
                if n >= slots:
                    before = n - slots
                    pe.wait_ge(stored[engines[before % len(engines)]], before // len(engines) + 1)
                for t0, tn in spans(T, BANK):
                    for k in range(kc):
                        ins = pe.matmul(ps[n % slots][0:m, t0:t0 + tn], w[b % bufs][:, k, i * P:i * P + m],
                                        x(k)[:, t0:t0 + tn], start=(k == 0), stop=(k == kc - 1))
                ins.then_inc(product_done, 1)

        if "v" in engines:
            @block.vector
            def _(dve):
                for n in range(engines.index("v"), len(tiles), len(engines)):
                    dve.wait_ge(product_done, n + 1)
                    evict(dve, n, ps[n % slots]).then_inc(stored["v"], 1)

        if "a" in engines:
            @block.scalar
            def _(act):
                for n in range(engines.index("a"), len(tiles), len(engines)):
                    act.wait_ge(product_done, n + 1)
                    evict(act, n, ps[n % slots]).then_inc(stored["a"], 1)


def weight_blocks(W, start, n, kc=KD, width=512):
    src = W.rearrange("(k p) n -> p k n", p=P)
    return [([(lambda buf, m=m: buf[:, :, 0:m], src[:, :, start + a:start + a + m])],
             [c for _, c in spans(m, P)]) for a, m in spans(n, width)]


def linear_tokens(nc, name, x, blocks, tokens, evict, kc=KD):
    tiles = [(b, t) for b in range(len(blocks)) for t in range(tokens // P)]
    slots, bufs = 6, 2
    nt = tokens // P
    with Stage(nc, name) as st:
        w = [st.sb(f"w{i}", [P, kc, 512]) for i in range(bufs)]
        ps = [st.ps(f"acc{i}", [P, BANK]) for i in range(slots)]
        w_landed = [st.sem(f"w_landed{i}") for i in range(bufs)]
        product_done = st.sem("product_done")
        out_v, out_a = st.sem("out_v"), st.sem("out_a")
        block = st.block()

        @block.sync
        def _(sp):
            for b, (src, m) in enumerate(blocks):
                if b >= bufs:
                    sp.wait_ge(product_done, nt * (b - bufs + 1))
                sp.dma_start(w[b % bufs][:, :, 0:m],
                             src.rearrange("(k p) n -> p k n", p=P)).then_inc(w_landed[b % bufs], 16)

        @block.tensor
        def _(pe):
            for n, (b, t) in enumerate(tiles):
                m = blocks[b][1]
                if t == 0:
                    pe.wait_ge(w_landed[b % bufs], 16 * (b // bufs + 1))
                if n >= slots:
                    before = n - slots
                    pe.wait_ge((out_v, out_a)[before % 2], before // 2 + 1)
                for k in range(kc):
                    ins = pe.matmul(ps[n % slots][:, 0:m], x(k)[:, t * P:(t + 1) * P],
                                    w[b % bufs][:, k, 0:m], start=(k == 0), stop=(k == kc - 1))
                ins.then_inc(product_done, 1)

        @block.vector
        def _(dve):
            for n in range(0, len(tiles), 2):
                dve.wait_ge(product_done, n + 1)
                evict(dve, *tiles[n], ps[n % slots]).then_inc(out_v, 1)

        @block.scalar
        def _(act):
            for n in range(1, len(tiles), 2):
                act.wait_ge(product_done, n + 1)
                evict(act, *tiles[n], ps[n % slots]).then_inc(out_a, 1)


def copy_on(engine, nc, out, in_, scale=None):
    if engine is nc.vector or engine.engine == nc.vector.engine:
        if scale is None:
            return engine.tensor_copy(out, in_)
        return engine.tensor_scalar(out, in_, scale, None, ALU.mult)
    if scale is None:
        return engine.copy(out, in_)
    return engine.activation(out, in_, ACT.Copy, scale=scale)


def norm(nc, name, x, out, T, gain, ones, kc=KD, width=D, shift=None, residual=None, half=1.0):
    with Stage(nc, name) as st:
        rs = st.sb("rstd", [P, T])
        ps = st.ps("sum", [P, -(-T // BANK) * BANK])
        squared, summed, rooted = st.sem("squared"), st.sem("summed"), st.sem("rooted")
        with_eps = st.sem("with_eps")
        scaled, shifted, own = st.sem("scaled"), st.sem("shifted"), st.sem("own")
        block = st.block()

        @block.scalar
        def _(act):
            for k in range(kc):
                act.activation(out(k), x(k), ACT.Square, scale=float(width) ** -0.5).then_inc(squared, 1)
            act.wait_ge(with_eps, 1)
            act.activation(rs[:], rs[:], ACT.Sqrt).then_inc(rooted, 1)
            if shift is not None:
                for k in range(kc):
                    act.wait_ge(scaled, k + 1)
                    act.activation(out(k), out(k), ACT.Identity, bias=shift(k)).then_inc(shifted, 1)

        @block.tensor
        def _(pe):
            for t0, tn in spans(T, BANK):
                for k in range(kc):
                    if t0 == 0:
                        pe.wait_ge(squared, k + 1)
                    ins = pe.matmul(ps[:, t0:t0 + tn], ones, out(k)[:, t0:t0 + tn],
                                    start=(k == 0), stop=(k == kc - 1))
            ins.then_inc(summed, 1)

        @block.vector
        def _(dve):
            chain = Chain(dve, own)
            dve.wait_ge(summed, 1)
            dve.tensor_scalar(rs[:], ps[:, 0:T], EPS, None, ALU.add).then_inc(with_eps, 1)
            dve.wait_ge(rooted, 1)
            chain.link(dve.reciprocal(rs[:], rs[:]))
            for k in range(kc):
                ins = dve.scalar_tensor_tensor(out=out(k), in0=x(k), scalar=gain(k), in1=rs[:],
                                               op0=ALU.mult, op1=ALU.mult)
                if residual is None:
                    ins.then_inc(scaled, 1)
                else:
                    chain.link(ins)
                    dve.scalar_tensor_tensor(out=residual(k), in0=out(k), scalar=half, in1=residual(k),
                                             op0=ALU.mult, op1=ALU.add)
def adaln(nc, name, W, cond, bias, gain, mod, gs):
    src = W.rearrange("(k p) n -> p k n", p=P)
    n_blocks, bufs = 3 * D // 512, 3
    with Stage(nc, name) as st:
        w = [st.sb(f"w{i}", [P, KD, 512]) for i in range(bufs)]
        act_c = st.sb("silu", [P, KD, 2])
        ps = st.ps("m", [P, 24, 2])
        w_landed = [st.sem(f"w_landed{i}") for i in range(bufs)]
        silu_done, block_done, own = st.sem("silu_done"), st.sem("block_done"), st.sem("own")
        block = st.block()

        @block.sync
        def _(sp):
            for b in range(n_blocks):
                if b >= bufs:
                    sp.wait_ge(block_done, b - bufs + 1)
                sp.dma_start(w[b % bufs][:], src[:, :, b * 512:(b + 1) * 512]).then_inc(w_landed[b % bufs], 16)

        @block.scalar
        def _(act):
            act.activation(act_c[:], cond, ACT.Silu).then_inc(silu_done, 1)

        @block.tensor
        def _(pe):
            pe.wait_ge(silu_done, 1)
            for b in range(n_blocks):
                pe.wait_ge(w_landed[b % bufs], 16 * (b // bufs + 1))
                for i in range(4):
                    for k in range(KD):
                        ins = pe.matmul(ps[:, 4 * b + i, :], w[b % bufs][:, k, i * P:(i + 1) * P], act_c[:, k, :],
                                        start=(k == 0), stop=(k == KD - 1))
                ins.then_inc(block_done, 1)

        @block.vector
        def _(dve):
            chain = Chain(dve, own)
            dve.wait_ge(block_done, n_blocks)
            for j in range(2):
                chain.link(dve.tensor_tensor(mod[:, :, j], ps[:, :, j], bias, ALU.add))
                chain.link(dve.tensor_scalar(gs[:, :, j], mod[:, KD:2 * KD, j], 1.0, None, ALU.add))
                chain.link(dve.tensor_tensor(gs[:, :, j], gs[:, :, j], gain, ALU.mult))


def head_norm(nc, name, chunks, gains, group, rope=None):
    n, T = len(chunks), chunks[0].shape[1]
    with Stage(nc, name) as st:
        sq = [st.sb(f"sq{i}", [P, T]) for i in range(2)]
        rs = [st.sb(f"rs{i}", [P, T]) for i in range(2)]
        ps = [st.ps(f"sum{i}", [P, -(-T // BANK) * BANK]) for i in range(2)]
        turned = [st.ps(f"turned{i}", [P, BANK]) for i in range(2)]
        tmp = [st.sb(f"tmp{i}", [P, S]) for i in range(2)]
        squared, summed, with_eps, rooted = (st.sem(x) for x in ("squared", "summed", "with_eps", "rooted"))
        normed, swapped, done, own = (st.sem(x) for x in ("normed", "swapped", "done", "own"))
        block = st.block()

        @block.scalar
        def _(act):
            for i in range(n):
                if i >= 2:
                    act.wait_ge(summed, i - 1)
                act.activation(sq[i % 2][:], chunks[i], ACT.Square).then_inc(squared, 1)
                act.wait_ge(with_eps, i + 1)
                act.activation(rs[i % 2][:], rs[i % 2][:], ACT.Sqrt).then_inc(rooted, 1)

        @block.tensor
        def _(pe):
            for i in range(n):
                pe.wait_ge(squared, i + 1)
                if i >= 2:
                    pe.wait_ge(with_eps, i - 1)
                for t0, tn in spans(T, BANK):
                    ins = pe.matmul(ps[i % 2][:, t0:t0 + tn], group, sq[i % 2][:, t0:t0 + tn], start=True, stop=True)
                ins.then_inc(summed, 1)
                if rope is not None:
                    pe.wait_ge(normed, i + 1)
                    pe.matmul(turned[i % 2][:], rope[2], chunks[i][:, 0:S], start=True, stop=True).then_inc(swapped, 1)

        @block.vector
        def _(dve):
            chain = Chain(dve, own)
            for i in range(n):
                dve.wait_ge(summed, i + 1)
                dve.tensor_scalar(rs[i % 2][:], ps[i % 2][:, 0:T], EPS, None, ALU.add).then_inc(with_eps, 1)
                dve.wait_ge(rooted, i + 1)
                chain.link(dve.reciprocal(rs[i % 2][:], rs[i % 2][:]))
                dve.scalar_tensor_tensor(out=chunks[i], in0=chunks[i], scalar=gains[i], in1=rs[i % 2][:],
                                         op0=ALU.mult, op1=ALU.mult).then_inc(normed, 1)
                if rope is not None:
                    dve.wait_ge(swapped, i + 1)
                    chain.link(dve.tensor_tensor(tmp[i % 2][:], turned[i % 2][:], rope[1], ALU.mult))
                    chain.link(dve.tensor_tensor(chunks[i][:, 0:S], chunks[i][:, 0:S], rope[0], ALU.mult))
                    chain.link(dve.tensor_tensor(chunks[i][:, 0:S], chunks[i][:, 0:S], tmp[i % 2][:], ALU.add))


def attention(nc, name, units, ident):
    n_units = len(units)
    with Stage(nc, name) as st:
        prob = [st.sb(f"prob{i}", [P, 1024]) for i in range(2)]
        prob_t = [st.sb(f"prob_t{i}", [P, 6, P]) for i in range(2)]
        stat = st.sb("stat", [P, 3, 8])
        score = [st.ps(f"score{i}", [P, 1024]) for i in range(2)]
        turned = st.ps("turned", [P, 1024])
        out_ps = [st.ps(f"out{i}", [P, BANK]) for i in range(2)]
        scored, maxed, exped, transposed, copied, weighed, stored, own = (
            st.sem(x) for x in ("scored", "maxed", "exped", "transposed", "copied", "weighed", "stored", "own"))
        block = st.block()

        def widths(u):
            return [k.shape[1] for k in u["keys"]]

        def tiles(u):
            return spans(sum(widths(u)), P)

        @block.tensor
        def _(pe):
            def scores(i):
                u = units[i]
                if i >= 2:
                    pe.wait_ge(exped, i - 1)
                at = 0
                for k in u["keys"]:
                    ins = pe.matmul(score[i % 2][:, at:at + k.shape[1]], u["q"], k, start=True, stop=True)
                    at += BANK if at + k.shape[1] < sum(widths(u)) else 0
                ins.then_inc(scored, 1)

            def transposes(i):
                pe.wait_ge(exped, i + 1)
                if i >= 1:
                    pe.wait_ge(copied, i)
                for j, (a, m) in enumerate(tiles(units[i])):
                    ins = pe.transpose(turned[0:m, j * P:(j + 1) * P], prob[i % 2][:, a:a + m], ident)
                ins.then_inc(transposed, 1)

            def weigh(i):
                pe.wait_ge(copied, i + 1)
                if i >= 2:
                    pe.wait_ge(stored, i - 1)
                u = units[i]
                last = len(tiles(u)) - 1
                for j, (a, m) in enumerate(tiles(u)):
                    ins = pe.matmul(out_ps[i % 2][:, 0:u["out"].shape[1]], prob_t[i % 2][0:m, j, :],
                                    u["values"][j], start=(j == 0), stop=(j == last))
                ins.then_inc(weighed, 1)

            for i in range(n_units + 2):
                if i < n_units:
                    scores(i)
                if 1 <= i <= n_units:
                    transposes(i - 1)
                if i >= 2:
                    weigh(i - 2)

        @block.vector
        def _(dve):
            chain = Chain(dve, own)

            def maxima(i):
                u, s = units[i], stat[:, i % 3, :]
                dve.wait_ge(scored, i + 1)
                if u["bias"] is None:
                    n = sum(widths(u))
                    dve.tensor_reduce(s[:, 0:1], score[i % 2][:, 0:n], AX.X, ALU.max, negate=True).then_inc(maxed, 1)
                    return
                if i >= 2:
                    dve.wait_ge(transposed, i - 1)
                n = widths(u)[0]
                chain.link(dve.tensor_tensor_reduce(out=prob[i % 2][:, 0:n], in0=score[i % 2][:, 0:n], in1=u["bias"],
                                                    scale=1.0, scalar=-3e38, op0=ALU.add, op1=ALU.max,
                                                    accum_out=s[:, 1:2]))
                if len(u["keys"]) == 2:
                    m = widths(u)[1]
                    chain.link(dve.tensor_reduce(s[:, 2:3], score[i % 2][:, BANK:BANK + m], AX.X, ALU.max))
                    dve.tensor_scalar(s[:, 0:1], s[:, 1:2], s[:, 2:3], -1.0, ALU.max, ALU.mult).then_inc(maxed, 1)
                else:
                    dve.tensor_scalar(s[:, 0:1], s[:, 1:2], -1.0, None, ALU.mult).then_inc(maxed, 1)

            def store(i):
                u, s = units[i], stat[:, i % 3, :]
                dve.wait_ge(weighed, i + 1)
                total = s[:, 3:4]
                if u["bias"] is not None and len(u["keys"]) == 2:
                    chain.link(dve.tensor_tensor(s[:, 5:6], s[:, 3:4], s[:, 4:5], ALU.add))
                    total = s[:, 5:6]
                chain.link(dve.reciprocal(s[:, 6:7], total))
                if u.get("rows") is None:
                    dve.tensor_scalar(u["out"], out_ps[i % 2][:, 0:u["out"].shape[1]], s[:, 6:7], None,
                                      ALU.mult).then_inc(stored, 1)
                else:
                    dve.tensor_scalar(u["out"], out_ps[i % 2][:, 0:u["out"].shape[1]], s[:, 6:7], u["rows"],
                                      ALU.mult, ALU.mult).then_inc(stored, 1)

            for i in range(n_units + 2):
                if i < n_units:
                    if i >= 3:
                        dve.wait_ge(stored, i - 2)
                    maxima(i)
                if i >= 2:
                    store(i - 2)

        @block.scalar
        def _(act):
            def exponentials(i):
                u, s = units[i], stat[:, i % 3, :]
                act.wait_ge(maxed, i + 1)
                if u["bias"] is None:
                    if i >= 2:
                        act.wait_ge(transposed, i - 1)
                    n = sum(widths(u))
                    act.activation(prob[i % 2][:, 0:n], score[i % 2][:, 0:n], ACT.Exp, bias=s[:, 0:1],
                                   accum_out=s[:, 3:4]).then_inc(exped, 1)
                    return
                n = widths(u)[0]
                ins = act.activation(prob[i % 2][:, 0:n], prob[i % 2][:, 0:n], ACT.Exp, bias=s[:, 0:1],
                                     accum_out=s[:, 3:4])
                if len(u["keys"]) == 2:
                    m = widths(u)[1]
                    ins = act.activation(prob[i % 2][:, n:n + m], score[i % 2][:, BANK:BANK + m], ACT.Exp,
                                         bias=s[:, 0:1], accum_out=s[:, 4:5])
                ins.then_inc(exped, 1)

            def copies(i):
                act.wait_ge(transposed, i + 1)
                if i >= 2:
                    act.wait_ge(weighed, i - 1)
                ts = tiles(units[i])
                full = len([m for _, m in ts if m == P])
                if full:
                    ins = act.copy(prob_t[i % 2][:, 0:full, :].rearrange("p j q -> p (j q)"), turned[:, 0:full * P])
                if full < len(ts):
                    m = ts[-1][1]
                    ins = act.copy(prob_t[i % 2][0:m, full, :], turned[0:m, full * P:(full + 1) * P])
                ins.then_inc(copied, 1)

            for i in range(n_units + 1):
                if i < n_units:
                    exponentials(i)
                if i >= 1:
                    copies(i - 1)


def to_features(nc, name, jobs, ident):
    n = len(jobs)
    with Stage(nc, name) as st:
        ps = [st.ps(f"turned{i}", [P, 1024]) for i in range(3)]
        turned, stored = st.sem("turned"), st.sem("stored")
        block = st.block()

        @block.tensor
        def _(pe):
            for i, (pieces, _, _) in enumerate(jobs):
                if i >= 3:
                    pe.wait_ge(stored, i - 2)
                for j, piece in enumerate(pieces):
                    ins = pe.transpose(ps[i % 3][:, j * P:(j + 1) * P], piece, ident)
                ins.then_inc(turned, 1)

        @block.vector
        def _(dve):
            for i, (pieces, factor, out) in enumerate(jobs):
                dve.wait_ge(turned, i + 1)
                src = ps[i % 3][:, 0:len(pieces) * P]
                if factor is None:
                    dve.tensor_copy(out, src).then_inc(stored, 1)
                else:
                    dve.tensor_tensor(out, src, factor, ALU.mult).then_inc(stored, 1)


def in_place(nc, name, parts, func):
    with Stage(nc, name) as st:
        block = st.block()

        @block.scalar
        def _(act):
            for part in parts:
                out, src = part if isinstance(part, tuple) else (part, part)
                act.activation(out, src, func)


def na_bias(nc, name, rpb, table, mask, pad_dram, tiles=14):
    heads, rows, cols = 8, 15, 31
    wide = 127
    with Stage(nc, name) as st:
        padded = st.sb("padded", [heads * rows, wide])
        cleared, landed, stored = st.sem("cleared"), st.sem("landed"), st.sem("stored")
        own = st.sem("own")
        block = st.block()

        @block.vector
        def _(dve):
            dve.memset(padded[:], 0.0).then_inc(cleared, 1)
            dve.wait_ge(stored, 16 * (1 + 2 * heads))
            for h in range(heads):
                dve.tensor_tensor(table[:, h], table[:, h],
                                  mask.rearrange("p (a c) -> p a c", a=1).broadcast_to([P, tiles, 64]), ALU.add)

        @block.sync
        def _(sp):
            sp.wait_ge(cleared, 1)
            sp.dma_start(padded[:, 48:79], rpb.rearrange("h r c -> (h r) c")).then_inc(landed, 16)
            sp.wait_ge(landed, 16)
            sp.dma_start(pad_dram.rearrange("c r w -> r c w"),
                         padded[:].rearrange("r (a w) -> r a w", a=1).broadcast_to([heads * rows, 64, wide])
                         ).then_inc(stored, 16)
            sp.wait_ge(stored, 16)
            for h in range(heads):
                for half in range(2):
                    src = bass.AP(tensor=pad_dram.tensor, offset=(h * rows + 1 - half) * wide + 63,
                                  ap=[[heads * rows * wide - 1, 64], [wide, tiles], [1, 64]])
                    sp.dma_start(table[64 * half:64 * half + 64, h], src).then_inc(stored, 16)


def attn_layer(nc, d, c, x, ctx, mod, gs):
    W = d["attn_w_in"]
    wv = W.rearrange("(k p) n -> p k n", p=P)
    with ExitStack() as keep:
        def sb(name, shape):
            return keep.enter_context(nc.sbuf_tensor("attn_" + name, shape, F32))

        qa, ka, ga, qb, gb = (sb(n, [P, 4, TT]) for n in ("qa", "ka", "ga", "qb", "gb"))
        kb = sb("kb", [P, TT])
        va, vb = sb("va", [P, 6, 512]), sb("vb", [P, 6, P])
        with ExitStack() as inner:
            h = inner.enter_context(nc.sbuf_tensor("attn_h", [P, KD, TT], F32))
            norm(nc, "attn_norm_x", lambda k: x[:, k, :], lambda k: h[:, k, 0:S], S,
                 lambda k: gs[:, k, 0:1], c["ones"], shift=lambda k: mod[:, k, 0:1])
            norm(nc, "attn_norm_ctx", lambda k: ctx[:, k, :], lambda k: h[:, k, S:TT], LC,
                 lambda k: gs[:, k, 1:2], c["ones"], shift=lambda k: mod[:, k, 1:2])
            qb_loads = [(lambda buf, s=s: buf[:, :, 0:512].rearrange("p k (i s d) -> p k i s d", i=4, s=2)[:, :, :, s, :],
                         wv[:, :, 2048 + 256 * s:2304 + 256 * s].rearrange("p k (i d) -> p k i d", i=4))
                        for s in range(2)]
            qb_loads = [(lambda buf, s=s, i=i: buf[:, :, P * i + 64 * s:P * i + 64 * s + 64],
                         wv[:, :, 2048 + 256 * s + 64 * i:2048 + 256 * s + 64 * i + 64])
                        for s in range(2) for i in range(4)]
            blocks = (weight_blocks(W, 0, 512) + weight_blocks(W, 512, 512) + weight_blocks(W, 1536, 512)
                      + [(qb_loads, [P] * 4)] + weight_blocks(W, 2816, 512) + weight_blocks(W, 2560, 128))
            outs = [(t[:, i, :], 0.125 if t is qa else None) for t in (qa, ka, ga, qb, gb) for i in range(4)]
            outs.append((kb[:], None))
            linear(nc, "attn_in", lambda k: h[:, k, :], blocks, TT,
                   lambda e, n, ps: copy_on(e, nc, outs[n][0], ps[:, 0:TT], outs[n][1]), bufs=2)
            linear_tokens(nc, "attn_v", lambda k: h[:, k, :], [(W[:, 1024:1536], 512), (W[:, 2688:2816], 128)], TT,
                          lambda e, b, t, ps: copy_on(e, nc, va[:, t, :] if b == 0 else vb[:, t, :],
                                                      ps[:, 0:512] if b == 0 else ps[:, 0:P]))
        with ExitStack() as inner:
            rope = inner.enter_context(nc.sbuf_tensor("attn_rope", [P, 2, S], F32))
            load(nc, "rope_load", [(rope[:, 0, :], d["c_cos"]), (rope[:, 1, :], d["c_sin"])])
            head_norm(nc, "attn_head_norm", [qb[:, i, :] for i in range(4)] + [kb[:]],
                      [c["q_gain"]] * 4 + [c["k_gain"]], c["group64"], (rope[:, 0, :], rope[:, 1, :], c["swap"]))
        with ExitStack() as inner:
            oa = inner.enter_context(nc.sbuf_tensor("attn_oa", [P, 6, 512], F32))
            ob = inner.enter_context(nc.sbuf_tensor("attn_ob", [P, 6, 512], F32))
            with ExitStack() as tabled:
                table = tabled.enter_context(nc.sbuf_tensor("attn_table", [P, 8, 14, 64], F32))
                na_bias(nc, "attn_bias", d["na_rpb"], table, c["window"], d["s_rpb"])
                units = []
                for t in range(6):
                    q_at = slice(t * P, (t + 1) * P)
                    for h in range(8):
                        a, b = 64 * (h % 2), 64 * (h // 4)
                        first = 4 if t >= 4 else 0
                        local = [] if t >= 4 else [ka[a:a + 64, h // 2, 0:S]]
                        units.append(dict(
                            q=qa[a:a + 64, h // 2, q_at], keys=local + [ka[a:a + 64, h // 2, S:TT]],
                            bias=None if t >= 4 else
                            table[:, h, 6 - 2 * t:14 - 2 * t, :].rearrange("p r c -> p (r c)"),
                            values=[va[:, j, 64 * h:64 * h + 64] for j in range(first, 6)],
                            out=oa[:, t, 64 * h:64 * h + 64]))
                        grouped = [] if t >= 4 else [kb[b:b + 64, 0:S]]
                        units.append(dict(
                            q=qb[b:b + 64, h % 4, q_at], keys=grouped + [kb[b:b + 64, S:TT]], bias=None,
                            values=[vb[:, j, b:b + 64] for j in range(first, 6)],
                            out=ob[:, t, 64 * h:64 * h + 64]))
                attention(nc, "attn", units, c["ident"])
            y = inner.enter_context(nc.sbuf_tensor("attn_y", [P, KD, TT], F32))
            in_place(nc, "attn_gates", [g[:, i, :] for g in (ga, gb) for i in range(4)], ACT.Silu)
            to_features(nc, "attn_turn", [([o[:, t, i * P:(i + 1) * P] for t in range(6)], g[:, i, :], y[:, 4 * n + i, :])
                                          for n, (o, g) in enumerate(((oa, ga), (ob, gb))) for i in range(4)], c["ident"])

            gated_out(nc, "attn_out", d["attn_w_out"], y, x, ctx, mod)


def gated_out(nc, name, W, y, x, ctx, mod):
    T = TT if ctx is not None else S
    with Stage(nc, name) as st:
        w = [st.sb(f"w{i}", [P, KD, 256]) for i in range(2)]
        ps = [st.ps(f"acc{i}", [P, 1024]) for i in range(4)]
        w_landed = [st.sem(f"w_landed{i}") for i in range(2)]
        product_done, stored = st.sem("product_done"), st.sem("stored")
        src = W.rearrange("(k p) n -> p k n", p=P)
        block = st.block()

        @block.sync
        def _(sp):
            for b in range(4):
                if b >= 2:
                    sp.wait_ge(product_done, 2 * (b - 1))
                sp.dma_start(w[b % 2][:], src[:, :, 256 * b:256 * b + 256]).then_inc(w_landed[b % 2], 16)

        @block.tensor
        def _(pe):
            for n in range(KD):
                if n % 2 == 0:
                    pe.wait_ge(w_landed[(n // 2) % 2], 16 * (n // 4 + 1))
                if n >= 4:
                    pe.wait_ge(stored, n - 3)
                for t0, tn in spans(T, BANK):
                    for k in range(KD):
                        ins = pe.matmul(ps[n % 4][:, t0:t0 + tn], w[(n // 2) % 2][:, k, (n % 2) * P:(n % 2) * P + P],
                                        y[:, k, t0:t0 + tn], start=(k == 0), stop=(k == KD - 1))
                ins.then_inc(product_done, 1)

        @block.vector
        def _(dve):
            for n in range(KD):
                dve.wait_ge(product_done, n + 1)
                ins = dve.scalar_tensor_tensor(out=x[:, n, :], in0=ps[n % 4][:, 0:S], scalar=mod[:, 16 + n, 0:1],
                                               in1=x[:, n, :], op0=ALU.mult, op1=ALU.add)
                if ctx is not None:
                    ins = dve.scalar_tensor_tensor(out=ctx[:, n, :], in0=ps[n % 4][:, S:TT],
                                                   scalar=mod[:, 16 + n, 1:2], in1=ctx[:, n, :],
                                                   op0=ALU.mult, op1=ALU.add)
                ins.then_inc(stored, 1)
CH = 64
PAIRS = 4
PADDED = TT + 4


def token_shift(nc, name, up, out, mu):
    n = len(up)
    with Stage(nc, name) as st:
        tmp = [[st.sb(f"tmp{e}{i}", [P, TT]) for i in range(2)] for e in range(1)]
        own = st.sem("own")
        block = st.block()

        @block.vector
        def _(dve):
            chain = Chain(dve, own)
            for i in range(n):
                t, (dst, u) = tmp[0][i % 2], (out[i], up[i])
                last = None
                for a, b, m in ((0, 1, S), (S, S + 3, LC)):
                    chain.link(dve.tensor_tensor(t[:, a:a + m], u[:, b - 1:b - 1 + m], u[:, b + 1:b + 1 + m], ALU.add))
                    chain.link(dve.scalar_tensor_tensor(out=t[:, a:a + m], in0=t[:, a:a + m], scalar=0.5,
                                                        in1=u[:, b:b + m], op0=ALU.mult, op1=ALU.subtract))
                    chain.link(dve.scalar_tensor_tensor(out=dst[:, a:a + m], in0=t[:, a:a + m], scalar=mu[:, i:i + 1],
                                                        in1=u[:, b:b + m], op0=ALU.mult, op1=ALU.add))


def rwkv_features(nc, name, d, c, v, us, bonus, ends):
    with Stage(nc, name) as st:
        up = st.sb("up", [P, 4, 512])
        kk = st.sb("kk", [P, 4, TT])
        restart = st.sb("restart", [P, TT])
        sq, rs = st.sb("sq", [P, TT]), st.sb("rs", [P, TT])
        not_ka = st.sb("not_ka", [P, 4])
        gate_ps = [st.ps(f"gate{i}", [P, 1024]) for i in range(4)]
        sw, sa = ([st.sb(f"{x}{i}", [P, TT]) for i in range(2)] for x in ("sw", "sa"))
        lsum = st.sb("lsum", [P, TT])
        before, upto, inverse = st.sb("before", [P, TT]), st.sb("upto", [P, TT]), st.sb("inverse", [P, TT])
        kd = st.sb("kd", [P, TT])
        out = [[st.sb(f"out{j}_{i}", [P, TT]) for j in range(4)] for i in range(2)]
        (cleared, landed, squared, summed, with_eps, rooted, tanhed, gates_done, sigmoids, summed_log,
         exps, features, own, kk_done) = (st.sem(x) for x in (
             "cleared", "landed", "squared", "summed", "with_eps", "rooted", "tanhed", "gates_done", "sigmoids",
             "summed_log", "exps", "features", "own", "kk_done"))
        saved = [st.sem(f"saved{i}") for i in range(2)]
        block = st.block()
        lora = us[12]

        @block.gpsimd
        def _(pool):
            pool.memset(up[:], 0.0).then_inc(cleared, 1)
            pool.memset(restart[:], 1.0).then_inc(cleared, 1)
            pool.wait_ge(cleared, 2)
            pool.memset(restart[:].rearrange("p (c t) -> p c t", t=CH)[:, :, 0:1], 0.0).then_inc(cleared, 1)

        @block.sync
        def _(sp):
            sp.wait_ge(cleared, 1)
            for i, w in enumerate((d["rwkv_w_up"][0], d["rwkv_w_up"][1], d["rwkv_a_up"][0], d["rwkv_a_up"][1])):
                sp.dma_start(up[32 * i:32 * i + 32, i, :], w).then_inc(landed, 16)
            for n in range(8):
                sp.wait_ge(features, n + 1)
                for j in range(4):
                    sp.dma_start(d["s_feat"][n // 4, j, (n % 4) * P:(n % 4) * P + P, :],
                                 out[n % 2][j][:]).then_inc(saved[n % 2], 16)
            for s in saved:
                sp.wait_ge(s, 16 * 16)

        @block.tensor
        def _(pe):
            pe.wait_ge(landed, 64)
            for i in range(4):
                pe.wait_ge(squared, i + 1)
                for t0, tn in spans(TT, BANK):
                    ins = pe.matmul(gate_ps[3][:, t0:t0 + tn], c["heads2"], sq[:, t0:t0 + tn], start=True, stop=True)
                ins.then_inc(summed, 1)
            pe.wait_ge(tanhed, 1)
            pe.wait_ge(with_eps, 4)
            for n in range(8):
                dr, i = n // 4, n % 4
                if n >= 2:
                    pe.wait_ge(sigmoids, 2 * (n - 1))
                for g in range(2):
                    for t0, tn in spans(TT, BANK):
                        ins = pe.matmul(gate_ps[2 * (n % 2) + g][:, t0:t0 + tn], up[:, 2 * g + dr, i * P:(i + 1) * P],
                                        lora[:, t0:t0 + tn], start=True, stop=True)
                ins.then_inc(gates_done, 1)

        @block.scalar
        def _(act):
            for i in range(4):
                if i:
                    act.wait_ge(summed, i)
                act.activation(sq[:], us[4 + i], ACT.Square, scale=v("rwkv_k_k", i, 1)).then_inc(squared, 1)
                act.wait_ge(with_eps, i + 1)
                act.activation(rs[:], rs[:], ACT.Sqrt).then_inc(rooted, 1)
            act.activation(lora[0:64, :], lora[0:64, :], ACT.Tanh).then_inc(tanhed, 1)
            for n in range(8):
                dr, i = n // 4, n % 4
                act.wait_ge(gates_done, n + 1)
                if n >= 2:
                    act.wait_ge(features, n - 1)
                act.activation(sw[n % 2][:], gate_ps[2 * (n % 2)][:, 0:TT], ACT.Sigmoid,
                               bias=v("w0", 4 * dr + i, 1)).then_inc(sigmoids, 1)
                act.activation(sa[n % 2][:], gate_ps[2 * (n % 2) + 1][:, 0:TT], ACT.Sigmoid,
                               bias=v("a0", 4 * dr + i, 1)).then_inc(sigmoids, 1)
                act.wait_ge(summed_log, n + 1)
                act.activation(upto[:], lsum[:], ACT.Exp)
                act.activation(inverse[:], lsum[:], ACT.Exp, scale=-1.0)
                act.activation(before[:], before[:], ACT.Exp).then_inc(exps, 1)

        @block.vector
        def _(dve):
            chain = Chain(dve, own)
            chain.link(dve.tensor_scalar(not_ka[:], v("rwkv_k_a"), -1.0, 1.0, ALU.mult, ALU.add))
            for i in range(4):
                dve.wait_ge(summed, i + 1)
                if i:
                    dve.wait_ge(kk_done, i)
                dve.tensor_scalar(rs[:], gate_ps[3][:, 0:TT], 1e-12, None, ALU.add).then_inc(with_eps, 1)
                dve.wait_ge(rooted, i + 1)
                chain.link(dve.reciprocal(rs[:], rs[:]))
                dve.scalar_tensor_tensor(out=kk[:, i, :], in0=us[4 + i], scalar=v("rwkv_k_k", i, 1), in1=rs[:],
                                         op0=ALU.mult, op1=ALU.mult).then_inc(kk_done, 1)
            dve.wait_ge(cleared, 3)
            dve.wait_ge(kk_done, 4)
            for n in range(8):
                dr, i = n // 4, n % 4
                a, o = sa[n % 2], out[n % 2]
                dve.wait_ge(sigmoids, 2 * (n + 1))
                chain.link(dve.tensor_scalar(sw[n % 2][:], sw[n % 2][:], -float(np.exp(-0.5)), None, ALU.mult))
                chain.link(dve.tensor_tensor_scan(lsum[:], restart[:], sw[n % 2][:], 0.0, ALU.mult, ALU.add))
                if dr == 0:
                    dve.tensor_tensor(before[:], lsum[:], sw[n % 2][:], ALU.subtract).then_inc(summed_log, 1)
                else:
                    chunks = lsum[:].rearrange("p (c t) -> p c t", t=CH)
                    chain.link(dve.tensor_tensor(before[:].rearrange("p (c t) -> p c t", t=CH),
                                                 chunks[:, :, CH - 1:CH].broadcast_to([P, TT // CH, CH]), chunks,
                                                 ALU.subtract))
                    dve.tensor_tensor(lsum[:], before[:], sw[n % 2][:], ALU.add).then_inc(summed_log, 1)
                chain.link(dve.tensor_scalar(kd[:], a[:], v("rwkv_k_a", i, 1), not_ka[:, i:i + 1], ALU.mult, ALU.add))
                chain.link(dve.tensor_tensor(kd[:], kd[:], us[4 + i], ALU.mult))
                if dr == 0:
                    chain.link(dve.tensor_copy(bonus[:, i, :], kd[:, 0:S]))
                else:
                    chain.link(dve.tensor_tensor(bonus[:, i, :], bonus[:, i, :], kd[:, 0:S], ALU.add))
                    chain.link(dve.scalar_tensor_tensor(out=bonus[:, i, :], in0=bonus[:, i, :], scalar=0.5,
                                                        in1=us[i][:, 0:S], op0=ALU.mult, op1=ALU.mult))
                    chain.link(dve.tensor_scalar(bonus[:, i, :], bonus[:, i, :], v("r_k", i, 1), None, ALU.mult))
                chain.link(dve.tensor_tensor(a[:], a[:], kk[:, i, :], ALU.mult))
                if n >= 2:
                    dve.wait_ge(saved[n % 2], 64 * (n // 2))
                dve.wait_ge(exps, n + 1)
                chain.link(dve.tensor_tensor(o[0][:], kk[:, i, :], before[:], ALU.mult))
                chain.link(dve.tensor_tensor(o[1][:], us[i], upto[:], ALU.mult))
                chain.link(dve.tensor_tensor(o[2][:], a[:], inverse[:], ALU.mult))
                at = CH - 1 if dr == 0 else 0
                chain.link(dve.tensor_copy(ends[:, dr, i, :], upto[:].rearrange("p (c t) -> p c t", t=CH)[:, :, at]))
                dve.tensor_tensor(o[3][:], kd[:], inverse[:], ALU.mult).then_inc(features, 1)
                dve.wait_ge(features, n + 1)


HEADS_T = 8
TURN, GRAM, FLIP, POW2, POW4, POW8, TDIAG, OFF, Z1, Z2, Z3, LAY = range(12)
DVE_STEPS = (GRAM, FLIP, POW4, POW8, TDIAG, OFF, Z1, Z2, Z3)
ACT_STEPS = (TURN, FLIP, POW2, POW4, POW8, OFF, LAY)


def upto_step(steps, step, i, per=HEADS_T):
    return per * steps.index(step) + i + 1


def last_step(steps, step):
    return max(s for s in steps if s < step) if any(s < step for s in steps) else None


def rwkv_group(nc, name, d, c, state, value, ends, y, dr, tile):
    lat = tile < 4
    strict, incl = (c["strict_fwd"], c["incl_fwd"]) if dr == 0 else (c["strict_rev"], c["incl_rev"])
    with Stage(nc, name) as st:
        feat = st.sb("feat", [P, 4, PAIRS, P])
        tok = st.sb("tok", [P, PAIRS, 3, P])
        mask = st.sb("mask", [P, 2, P])
        off16 = st.sb("off16", [P, P])
        gram = st.sb("gram", [P, HEADS_T, 4, P])
        dn, en = st.sb("diag", [P, HEADS_T, P]), st.sb("off", [P, HEADS_T, P])
        dt, m = st.sb("diag_t", [P, HEADS_T, P]), st.sb("inv_t", [P, HEADS_T, P])
        p2, p4 = st.sb("pow2", [P, HEADS_T, 2, P]), st.sb("pow4", [P, HEADS_T, 2, P])
        p8, ft = st.sb("pow8", [P, HEADS_T, P]), st.sb("off_t", [P, HEADS_T, P])
        xs = st.sb("rhs", [P, 2, HEADS_T, CH])
        y1, z = (st.sb(n, [P, HEADS_T, 2, CH]) for n in ("y1", "z"))
        wt = st.sb("w_t", [P, PAIRS, P])
        san = st.sb("minus_sa", [P, PAIRS, P])
        ps = [st.ps(f"ps{i}", [P, BANK]) for i in range(8)]
        banks = 8
        (landed, made, pe_done, dve_done, act_done, pool_done, scan_pe, scan_dve, own) = (
            st.sem(x) for x in ("landed", "made", "pe_done", "dve_done", "act_done", "pool_done", "scan_pe",
                                "scan_dve", "own"))
        block = st.block()
        halves = (0, 1) if dr == 0 else (1, 0)
        at = tile * P

        @block.sync
        def _(sp):
            for j in range(4):
                sp.dma_start(feat[:, j], d["s_feat"][dr, j].rearrange("(i p) t -> p i t", p=P)[:, :, at:at + P]
                             ).then_inc(landed, 16)

        @block.tensor
        def _(pe):
            def order(step, i):
                n = step * HEADS_T + i
                for steps, sem in ((DVE_STEPS, dve_done), (ACT_STEPS, act_done)):
                    s = last_step(steps, step)
                    if s is not None:
                        pe.wait_ge(sem, upto_step(steps, s, i))
                return ps[n % banks]

            pe.wait_ge(landed, 64)
            for i in range(HEADS_T):
                b = order(TURN, i)
                pair = i // 2
                srcs = (0, 2) if i % 2 == 0 else (3,)
                for j, s in enumerate(srcs):
                    ins = pe.transpose(b[:, j * P:(j + 1) * P], feat[:, s, pair, :], c["ident"])
                ins.then_inc(pe_done, 1)
            for i in range(HEADS_T):
                b = order(GRAM, i)
                pair, r = i // 2, slice(CH * (i % 2), CH * (i % 2) + CH)
                for j in range(2):
                    ins = pe.matmul(b[:, 2 * j * P:(2 * j + 2) * P], feat[r, 2 + j, pair, :],
                                    feat[r, 0:2, pair, :], start=True, stop=True)
                ins.then_inc(pe_done, 1)
            for i in range(HEADS_T):
                b = order(FLIP, i)
                pe.transpose(b[:, 0:P], gram[:, i, 0, :], c["ident"])
                pe.matmul(b[:, P:P + CH], gram[:, i, 2, :], value[:, tile, CH * i:CH * i + CH],
                          start=True, stop=True).then_inc(pe_done, 1)
            for i in range(HEADS_T):
                b = order(POW2, i)
                pe.wait_ge(pool_done, i + 1)
                pe.matmul(b[:, 0:P], dt[:, i, :], dn[:, i, :], start=True, stop=True)
                pe.matmul(b[:, P:2 * P], dn[:, i, :], dt[:, i, :], start=True, stop=True).then_inc(pe_done, 1)
            for i in range(HEADS_T):
                b = order(POW4, i)
                pe.matmul(b[:, 0:P], p2[:, i, 1, :], p2[:, i, 0, :], start=True, stop=True)
                pe.matmul(b[:, P:2 * P], p2[:, i, 0, :], p2[:, i, 1, :], start=True, stop=True)
                pe.matmul(b[:, 2 * P:3 * P], p2[:, i, 0, :], m[:, i, :], start=True, stop=True).then_inc(pe_done, 1)
            for i in range(HEADS_T):
                b = order(POW8, i)
                pe.matmul(b[:, 0:P], p4[:, i, 1, :], p4[:, i, 0, :], start=True, stop=True)
                pe.matmul(b[:, P:2 * P], p4[:, i, 0, :], m[:, i, :], start=True, stop=True).then_inc(pe_done, 1)
            for i in range(HEADS_T):
                b = order(TDIAG, i)
                pe.matmul(b[:, 0:P], p8[:, i, :], m[:, i, :], start=True, stop=True).then_inc(pe_done, 1)
            for i in range(HEADS_T):
                b = order(OFF, i)
                pe.matmul(b[:, 0:P], en[:, i, :], m[:, i, :], start=True, stop=True)
                pe.matmul(b[:, P:2 * P], m[:, i, :], xs[:, :, i, :],
                          start=True, stop=True).then_inc(pe_done, 1)
            for step in (Z1, Z2, Z3):
                for i in range(HEADS_T):
                    b = order(step, i)
                    src = y1 if step == Z1 else z
                    pe.matmul(b[:, 0:P], ft[:, i, :], src[:, i].rearrange("p a b -> p (a b)"),
                              start=True, stop=True).then_inc(pe_done, 1)
            for i in range(PAIRS):
                b = order(LAY, 2 * i + 1)
                pe.transpose(b[:, 0:P], xs[:, 1, 2 * i:2 * i + 2, :].rearrange("p a b -> p (a b)"),
                             c["ident"]).then_inc(pe_done, 1)
            pe.wait_ge(act_done, upto_step(ACT_STEPS, LAY, PAIRS - 1))
            pe.wait_ge(dve_done, upto_step(DVE_STEPS, Z3, HEADS_T - 1))
            for k, hf in enumerate(halves):
                r = slice(CH * hf, CH * hf + CH)
                if k:
                    pe.wait_ge(scan_dve, 2)
                for i in range(PAIRS):
                    ins = pe.matmul(ps[0][r, i * P:(i + 1) * P], wt[:, i, r], state[:, i, :], start=True, stop=True)
                ins.then_inc(scan_pe, 1)
                if lat:
                    for i in range(PAIRS):
                        pe.matmul(ps[2 + hf][:, i * CH:(i + 1) * CH], state[:, i, :], feat[:, 1, i, r],
                                  start=True, stop=True)
                pe.wait_ge(scan_dve, 2 * k + 1)
                for i in range(PAIRS):
                    pe.matmul(ps[1][:, i * P:(i + 1) * P], tok[r, i, 2, :], value[r, tile, i * P:(i + 1) * P],
                              start=True, stop=False)
                    ins = pe.matmul(ps[1][:, i * P:(i + 1) * P], tok[r, i, 1, :], san[r, i, :], start=False, stop=True)
                ins.then_inc(scan_pe, 1)
            if lat:
                for i in range(HEADS_T):
                    r = slice(CH * (i % 2), CH * (i % 2) + CH)
                    cols = slice((i // 2) * P, (i // 2) * P + P)
                    pe.matmul(ps[4 + i % 2][r, cols], value[:, tile, CH * i:CH * i + CH], gram[:, i, 3, :],
                              start=True, stop=False)
                    ins = pe.matmul(ps[4 + i % 2][r, cols], san[:, i // 2, r], gram[:, i, 1, :],
                                    start=False, stop=True)
                ins.then_inc(scan_pe, 1)

        @block.gpsimd
        def _(pool):
            for j, mk in enumerate((strict, incl)):
                pool.tensor_copy(mask[:, j, :], mk)
            pool.tensor_scalar(off16[:], c["same16"], -1.0, 1.0, ALU.mult, ALU.add).then_inc(made, 1)
            pool.wait_ge(made, 1)
            for i in range(HEADS_T):
                pool.wait_ge(dve_done, upto_step(DVE_STEPS, GRAM, i))
                pool.wait_ge(act_done, upto_step(ACT_STEPS, TURN, i - i % 2 + 1))
                pool.tensor_tensor(dt[:, i, :], gram[:, i, 0, :], c["same16"], ALU.mult).then_inc(made, 1)
                pool.tensor_scalar(xs[:, 1, i, :], tok[:, i // 2, 0, CH * (i % 2):CH * (i % 2) + CH], -1.0, None,
                                   ALU.mult)
                pool.wait_ge(made, i + 2)
                pool.tensor_tensor(m[:, i, :], c["ident"], dt[:, i, :], ALU.subtract).then_inc(pool_done, 1)

        @block.vector
        def _(dve):
            def ready(step, i):
                dve.wait_ge(pe_done, step * HEADS_T + i + 1)
                return ps[(step * HEADS_T + i) % banks]

            dve.wait_ge(made, 1)
            for i in range(HEADS_T):
                b = ready(GRAM, i)
                dve.tensor_tensor(gram[:, i].rearrange("p (a b) t -> p a b t", a=2),
                                  b[:].rearrange("p (a b t) -> p a b t", a=2, b=2),
                                  bass.AP(tensor=mask[:].tensor, offset=mask[:].offset,
                                          ap=[list(mask[:].ap[0]), [0, 2], [P, 2], [1, P]]),
                                  ALU.mult).then_inc(dve_done, 1)
            for i in range(HEADS_T):
                b = ready(FLIP, i)
                dve.tensor_tensor(dn[:, i, :], b[:, 0:P], c["same16"], ALU.mult)
                dve.tensor_tensor(en[:, i, :], b[:, 0:P], off16[:], ALU.mult).then_inc(dve_done, 1)
            for step, col in ((POW4, 2), (POW8, 1), (TDIAG, 0)):
                for i in range(HEADS_T):
                    b = ready(step, i)
                    dve.tensor_tensor(m[:, i, :], m[:, i, :], b[:, col * P:(col + 1) * P], ALU.add).then_inc(dve_done, 1)
            for i in range(HEADS_T):
                b = ready(OFF, i)
                dve.tensor_copy(y1[:, i].rearrange("p a b -> p (a b)"), b[:, P:2 * P]).then_inc(dve_done, 1)
            for step in (Z1, Z2, Z3):
                for i in range(HEADS_T):
                    b = ready(step, i)
                    dst = xs[:, :, i, :] if step == Z3 else z[:, i]
                    dve.tensor_tensor(dst, y1[:, i], b[:, 0:P].rearrange("p (a b) -> p a b", a=2),
                                      ALU.subtract).then_inc(dve_done, 1)
            dve.wait_ge(dve_done, upto_step(DVE_STEPS, Z3, HEADS_T - 1))
            chain = Chain(dve, own)
            for k, hf in enumerate(halves):
                r = slice(CH * hf, CH * hf + CH)
                n_chunk = 2 * tile + hf
                dve.wait_ge(scan_pe, 2 * k + 1)
                dve.tensor_tensor(san[r].rearrange("p i (h j) -> p i h j", h=2),
                                  xs[r, 0].rearrange("p (i h) j -> p i h j", h=2),
                                  ps[0][r, :].rearrange("p (i h j) -> p i h j", h=2, j=CH), ALU.add).then_inc(scan_dve, 1)
                dve.wait_ge(scan_pe, 2 * k + 2)
                for i in range(PAIRS):
                    end = ends[:, dr, i, n_chunk:n_chunk + 1]
                    new = y1[:, i].rearrange("p a b -> p (a b)")
                    chain.link(dve.scalar_tensor_tensor(out=new, in0=ps[1][:, i * P:(i + 1) * P], scalar=end,
                                                        in1=c["heads2"], op0=ALU.mult, op1=ALU.mult))
                    ins = dve.scalar_tensor_tensor(out=state[:, i, :], in0=state[:, i, :], scalar=end, in1=new,
                                                   op0=ALU.mult, op1=ALU.add)
                ins.then_inc(scan_dve, 1)
            if lat:
                dve.wait_ge(scan_pe, 5)
                yt = y[:, :, at:at + P]
                for hf in range(2):
                    a = yt[:, :, CH * hf:CH * hf + CH]
                    chain.link(dve.tensor_tensor(a, a, ps[2 + hf][:, 0:PAIRS * CH].rearrange("p (i t) -> p i t", t=CH),
                                                 ALU.add))
                for h in range(2):
                    r = slice(CH * h, CH * h + CH)
                    chain.link(dve.tensor_tensor(yt[r], yt[r], ps[4 + h][r, :].rearrange("p (i t) -> p i t", t=P),
                                                 ALU.add))

        @block.scalar
        def _(act):
            def ready(step, i):
                act.wait_ge(pe_done, step * HEADS_T + i + 1)
                if step in DVE_STEPS:
                    act.wait_ge(dve_done, upto_step(DVE_STEPS, step, i))
                return ps[(step * HEADS_T + i) % banks]

            for i in range(HEADS_T):
                b = ready(TURN, i)
                if i % 2 == 0:
                    act.copy(tok[:, i // 2, 0:2, :].rearrange("p a b -> p (a b)"), b[:, 0:2 * P]).then_inc(act_done, 1)
                else:
                    act.copy(tok[:, i // 2, 2, :], b[:, 0:P]).then_inc(act_done, 1)
            for i in range(HEADS_T):
                b = ready(FLIP, i)
                act.mul(xs[:, 0, i, :], b[:, P:P + CH], -1.0).then_inc(act_done, 1)
            for i in range(HEADS_T):
                b = ready(POW2, i)
                act.copy(p2[:, i].rearrange("p a b -> p (a b)"), b[:, 0:2 * P]).then_inc(act_done, 1)
            for i in range(HEADS_T):
                b = ready(POW4, i)
                act.copy(p4[:, i].rearrange("p a b -> p (a b)"), b[:, 0:2 * P]).then_inc(act_done, 1)
            for i in range(HEADS_T):
                b = ready(POW8, i)
                act.copy(p8[:, i, :], b[:, 0:P]).then_inc(act_done, 1)
            for i in range(HEADS_T):
                b = ready(OFF, i)
                act.copy(ft[:, i, :], b[:, 0:P]).then_inc(act_done, 1)
            for i in range(PAIRS):
                act.wait_ge(pe_done, LAY * HEADS_T + i + 1)
                act.copy(wt[:, i, :], ps[2 * i + 1][:, 0:P]).then_inc(act_done, 1)


def group_norm_out(nc, name, c, v, y, bonus, value, gate, out):
    with Stage(nc, name) as st:
        mean_ps, var_ps, bonus_ps = (st.ps(x, [P, BANK]) for x in ("mean", "var", "bonus"))
        sq, rs, t = (st.sb(x, [P, S]) for x in ("sq", "rs", "t"))
        summed, centred, squared, varied, with_eps, rooted, done, own = (
            st.sem(x) for x in ("summed", "centred", "squared", "varied", "with_eps", "rooted", "done", "own"))
        block = st.block()

        @block.tensor
        def _(pe):
            for i in range(4):
                if i:
                    pe.wait_ge(done, i)
                pe.matmul(mean_ps[:], c["group64"], y[:, i, :], start=True, stop=True)
                pe.matmul(bonus_ps[:], c["heads2"], bonus[:, i, :], start=True, stop=True).then_inc(summed, 1)
                pe.wait_ge(squared, i + 1)
                pe.matmul(var_ps[:], c["group64"], sq[:], start=True, stop=True).then_inc(varied, 1)

        @block.scalar
        def _(act):
            for i in range(4):
                act.wait_ge(centred, i + 1)
                act.activation(sq[:], y[:, i, :], ACT.Square).then_inc(squared, 1)
                act.activation(gate[:, i, :], gate[:, i, :], ACT.Silu)
                act.wait_ge(with_eps, i + 1)
                act.activation(rs[:], rs[:], ACT.Sqrt).then_inc(rooted, 1)

        @block.vector
        def _(dve):
            chain = Chain(dve, own)
            for i in range(4):
                dve.wait_ge(summed, i + 1)
                dve.tensor_tensor(y[:, i, :], y[:, i, :], mean_ps[:], ALU.subtract).then_inc(centred, 1)
                chain.link(dve.tensor_tensor(t[:], bonus_ps[:], value[:, i, :], ALU.mult))
                dve.wait_ge(varied, i + 1)
                dve.tensor_scalar(rs[:], var_ps[:], 64e-5, None, ALU.add).then_inc(with_eps, 1)
                dve.wait_ge(rooted, i + 1)
                chain.link(dve.reciprocal(rs[:], rs[:]))
                chain.link(dve.scalar_tensor_tensor(out=rs[:], in0=y[:, i, :], scalar=v("rwkv_gn_w", i, 1), in1=rs[:],
                                                    op0=ALU.mult, op1=ALU.mult))
                chain.link(dve.scalar_tensor_tensor(out=rs[:], in0=rs[:], scalar=v("rwkv_gn_b", i, 1), in1=t[:],
                                                    op0=ALU.add, op1=ALU.add))
                dve.tensor_tensor(out[:, i, :], rs[:], gate[:, i, :], ALU.mult).then_inc(done, 1)
                dve.wait_ge(done, i + 1)


def rwkv_input(nc, d, v, h, us):
    with nc.sbuf_tensor("rwkv_padded", [P, 13, PADDED], F32) as up:
        with Stage(nc, "rwkv_pad") as st:
            block = st.block()

            @block.vector
            def _(dve):
                for at, n in ((0, 1), (S + 1, 2), (PADDED - 1, 1)):
                    dve.memset(up[:, :, at:at + n], 0.0)

        def evict(e, n, ps):
            copy_on(e, nc, up[:, n, 1:S + 1], ps[:, 0:S])
            return copy_on(e, nc, up[:, n, S + 3:S + 3 + LC], ps[:, S:TT])

        linear(nc, "rwkv_in", lambda k: h[:, k, :], weight_blocks(d["rec_w_in"], 0, 1664, width=256), TT,
               evict, bufs=2, width=256)
        token_shift(nc, "rwkv_shift", [up[:, i, :] for i in range(13)], [us[:, i, :] for i in range(13)], v("mu"))


def rwkv_scan(nc, d, c, vt, ends, y):
    with nc.sbuf_tensor("rwkv_state", [P, 2, PAIRS, P], F32) as state:
        with Stage(nc, "rwkv_zero") as st:
            block = st.block()

            @block.vector
            def _(dve):
                dve.memset(state[:], 0.0)
                dve.memset(y[:], 0.0)
        for step in range(6):
            for dr in range(2):
                tile = ((4, 5, 0, 1, 2, 3), (5, 4, 3, 2, 1, 0))[dr][step]
                rwkv_group(nc, f"rwkv{step}{dr}", d, c, state[:, dr], vt, ends, y, dr, tile)


def in_sbuf_copy(nc, name, out, in_):
    with Stage(nc, name) as st:
        block = st.block()

        @block.vector
        def _(dve):
            dve.tensor_copy(out, in_)
def products(nc, name, jobs, engines=2, slots=6):
    with Stage(nc, name) as st:
        ps = [st.ps(f"acc{i}", [P, BANK]) for i in range(slots)]
        product_done, out_v, out_a = st.sem("product_done"), st.sem("out_v"), st.sem("out_a")
        block = st.block()

        @block.tensor
        def _(pe):
            for n, (rows, cols, terms, _) in enumerate(jobs):
                if n >= slots:
                    before = n - slots
                    if engines == 1:
                        pe.wait_ge(out_v, before + 1)
                    else:
                        pe.wait_ge((out_v, out_a)[before % 2], before // 2 + 1)
                for j, (lhs, rhs) in enumerate(terms):
                    ins = pe.matmul(ps[n % slots][0:rows, 0:cols], lhs, rhs, start=(j == 0), stop=(j == len(terms) - 1))
                ins.then_inc(product_done, 1)

        @block.vector
        def _(dve):
            for n in range(0, len(jobs), engines):
                dve.wait_ge(product_done, n + 1)
                jobs[n][3](dve, ps[n % slots][0:jobs[n][0], 0:jobs[n][1]]).then_inc(out_v, 1)

        if engines == 2:
            @block.scalar
            def _(act):
                for n in range(1, len(jobs), 2):
                    act.wait_ge(product_done, n + 1)
                    jobs[n][3](act, ps[n % slots][0:jobs[n][0], 0:jobs[n][1]]).then_inc(out_a, 1)


def copy_to(nc, out, scale=None):
    return lambda e, ps: copy_on(e, nc, out, ps, scale)


def hyena_filters(nc, d, c, v, spectrum, root):
    two_pi = float(2 * np.pi)
    with ExitStack() as keep:
        def sb(name, shape, stack=keep):
            return stack.enter_context(nc.sbuf_tensor("filt_" + name, shape, F32))

        dft = sb("dft", [P, 2, 4, 512])
        ab = sb("sum_difference", [P, 2, 2, 4, 512])
        with ExitStack() as inner:
            hid = sb("hid", [65, S], inner)
            w3 = sb("w3", [65, 2048], inner)
            decay = sb("decay", [P, 4, 512], inner)
            taps = sb("taps", [P, 4, 2, 2, 512], inner)
            with Stage(nc, "filt_hidden") as st:
                w1, w2, feats = st.sb("w1", [33, 64]), st.sb("w2", [64, 64]), st.sb("feats", [33, S])
                arg, turns = st.sb("arg", [64, S]), st.sb("turns", [64, S])
                hid1 = st.sb("hid1", [64, S])
                ps = st.ps("hid", [64, BANK])
                landed, summed, reduced, sined, own = (st.sem(x) for x in ("landed", "summed", "reduced", "sined", "own"))
                block = st.block()

                @block.sync
                def _(sp):
                    for dst, src in ((w1[:], d["hy_w1"]), (w2[:], d["hy_w2"]), (feats[:], d["c_feats"]),
                                     (w3[0:64, :], d["hy_w3"]), (w3[64:65, :], d["hy_b3"]),
                                     (decay[:], d["c_decay"].rearrange("(a p) n -> p a n", p=P)),
                                     (dft[:, 0], d["c_dft"][0].rearrange("(a p) n -> p a n", p=P)),
                                     (dft[:, 1], d["c_dft"][1].rearrange("(a p) n -> p a n", p=P))):
                        sp.dma_start(dst, src).then_inc(landed, 16)
                    sp.wait_ge(landed, 128)

                @block.gpsimd
                def _(pool):
                    pool.memset(hid[64:65, :], 1.0)

                @block.tensor
                def _(pe):
                    pe.wait_ge(landed, 128)
                    pe.matmul(ps[:], w1[:], feats[:], start=True, stop=True).then_inc(summed, 1)
                    pe.wait_ge(sined, 1)
                    pe.matmul(ps[:], w2[:], hid1[:], start=True, stop=True).then_inc(summed, 1)

                @block.vector
                def _(dve):
                    chain = Chain(dve, own)
                    for n, b in enumerate(("hy_b1", "hy_b2")):
                        dve.wait_ge(summed, n + 1)
                        chain.link(dve.tensor_scalar(arg[:], ps[:], v(b)[0:64, :], None, ALU.add))
                        chain.link(dve.tensor_scalar(turns[:], arg[:], 1.0 / two_pi, 12582912.0, ALU.mult, ALU.add))
                        chain.link(dve.tensor_scalar(turns[:], turns[:], -12582912.0, None, ALU.add))
                        chain.link(dve.scalar_tensor_tensor(out=arg[:], in0=turns[:], scalar=-6.28125, in1=arg[:],
                                                            op0=ALU.mult, op1=ALU.add))
                        chain.link(dve.scalar_tensor_tensor(out=arg[:], in0=turns[:], scalar=-(two_pi - 6.28125),
                                                            in1=arg[:], op0=ALU.mult, op1=ALU.add))
                        dve.tensor_scalar(arg[:], arg[:], 3.1415925, -3.1415925, ALU.min, ALU.max).then_inc(reduced, 1)
                        dve.wait_ge(sined, n + 1)

                @block.scalar
                def _(act):
                    for n, out in enumerate((hid1[:], hid[0:64, :])):
                        act.wait_ge(reduced, n + 1)
                        act.activation(out, arg[:], ACT.Sin).then_inc(sined, 1)

            def windowed(t, j):
                return lambda e, ps: e.tensor_tensor(taps[:, t, j // 2, j % 2, :], ps, decay[:, t, :], ALU.mult)

            products(nc, "filt_taps", [(P, 512, [(hid[:, t * P:(t + 1) * P], w3[:, 512 * j:512 * j + 512])],
                                        windowed(t, j)) for t in range(4) for j in range(4)], engines=1)
            with Stage(nc, "filt_sum") as st:
                block = st.block()

                @block.vector
                def _(dve):
                    for o in range(2):
                        dve.tensor_tensor(ab[:, o, 0], taps[:, :, 0, o, :], taps[:, :, 1, o, :], ALU.add)

                @block.gpsimd
                def _(pool):
                    for o in range(2):
                        pool.tensor_tensor(ab[:, o, 1], taps[:, :, 0, o, :], taps[:, :, 1, o, :], ALU.subtract)
        with ExitStack() as inner:
            sq = sb("sq", [P, 2, 2, 4, 512], inner)
            in_place(nc, "filt_sq", [(sq[:, o, j], ab[:, o, j]) for o in range(2) for j in range(2)], ACT.Square)

            def weight(j, t):
                return c["half_col"] if t else (c["sum_col"], c["diff_col"])[j]

            products(nc, "filt_norm", [
                (P, 1, [(sq[:, o, j, t, i * P:(i + 1) * P], weight(j, t)) for j in range(2) for t in range(4)],
                 copy_to(nc, root[:, 4 * o + i:4 * o + i + 1])) for o in range(2) for i in range(4)])
        with Stage(nc, "filt_root") as st:
            rooted = st.sem("rooted")
            block = st.block()

            @block.scalar
            def _(act):
                act.activation(root[:], root[:], ACT.Sqrt).then_inc(rooted, 1)

            @block.vector
            def _(dve):
                dve.wait_ge(rooted, 1)
                dve.reciprocal(root[:], root[:])

        products(nc, "filt_spectrum", [
            (P, 512, [(dft[:, j, t, w * P:(w + 1) * P], ab[:, o, j, t, :]) for t in range(4)],
             copy_to(nc, spectrum[:, o, j, w, :])) for o in range(2) for j in range(2) for w in range(4)])


def hyena_input(nc, d, v, h, parts, gate):
    with ExitStack() as keep:
        def sb(name, shape):
            return keep.enter_context(nc.sbuf_tensor("hyin_" + name, shape, F32))

        up = sb("up", [P, 12, S + 2])
        with Stage(nc, "hy_pad") as st:
            block = st.block()

            @block.vector
            def _(dve):
                dve.memset(up[:, :, 0:1], 0.0)
                dve.memset(up[:, :, S + 1:S + 2], 0.0)
        linear(nc, "hy_in", lambda k: h[:, k, :], weight_blocks(d["rec_w_in"], 2176, 2048), S,
               lambda e, n, ps: copy_on(e, nc, up[:, n, 1:S + 1] if n < 12 else gate[:, n - 12, :], ps[:, 0:S]), bufs=2)
        with Stage(nc, "hy_conv") as st:
            convolved, gated, saved, own = st.sem("convolved"), st.sem("gated"), st.sem("saved"), st.sem("own")
            block = st.block()

            @block.scalar
            def _(act):
                for i in range(4):
                    act.activation(gate[:, i, :], gate[:, i, :], ACT.Silu).then_inc(gated, 1)

            @block.vector
            def _(dve):
                chain = Chain(dve, own)
                for i in range(12):
                    u = parts[i // 4][:, i % 4, :]
                    for tap in range(3):
                        w, src = v("hy_short", 12 * tap + i, 1), up[:, i, tap:tap + S]
                        if tap == 0:
                            chain.link(dve.tensor_scalar(u, src, w, None, ALU.mult))
                        else:
                            ins = dve.scalar_tensor_tensor(out=u, in0=src, scalar=w, in1=u,
                                                           op0=ALU.mult, op1=ALU.add)
                            if tap == 1:
                                chain.link(ins)
                    ins.then_inc(convolved, 1)

            @block.sync
            def _(sp):
                out = d["s_hy"].rearrange("(i p) t -> p i t", p=P)
                sp.wait_ge(gated, 4)
                sp.dma_start(out[:, 12:16], gate).then_inc(saved, 16)
                for i in range(3):
                    sp.wait_ge(convolved, 4 * (i + 1))
                    sp.dma_start(out[:, 4 * i:4 * i + 4], parts[i]).then_inc(saved, 16)
                sp.wait_ge(saved, 64)


def hyena_branch(nc, d, c, v, out):
    with ExitStack() as keep:
        def sb(name, shape, stack=keep):
            return stack.enter_context(nc.sbuf_tensor("hy_" + name, shape, F32))

        spectrum = sb("spectrum", [P, 2, 2, 4, 512])
        root = sb("root", [P, 8])
        hyena_filters(nc, d, c, v, spectrum, root)
        u, gate = sb("u", [P, 12, S]), sb("gate", [P, 4, S])
        dft, idft = sb("dft", [P, 2, 4, 512]), sb("idft", [P, 2, 4, 512])
        load(nc, "hy_tables", [(t[:, j], d[n][j].rearrange("(a p) n -> p a n", p=P))
                               for t, n in ((dft, "c_dft"), (idft, "c_idft")) for j in range(2)]
             + [(u[:], d["s_hy"].rearrange("(i p) t -> p i t", p=P)[:, 0:12]),
                (gate[:], d["s_hy"].rearrange("(i p) t -> p i t", p=P)[:, 12:16])])
        z = u[:, 0:4, :]
        zt = sb("z_tokens", [P, 4, 512])
        zw, yw = sb("z_spectrum", [P, 2, 4, 512]), sb("y_spectrum", [P, 2, 4, 512])
        tmp = sb("tmp", [P, 2, 4, 512])
        for o in range(2):
            to_features(nc, f"hy_turn{o}", [([z[:, i, t * P:(t + 1) * P] for i in range(4)], None, zt[:, t, :])
                                            for t in range(4)], c["ident"])
            products(nc, f"hy_dft{o}", [
                (P, 512, [(dft[:, j, t, w * P:(w + 1) * P], zt[:, t, :]) for t in range(4)],
                 copy_to(nc, zw[:, j, w, :])) for j in range(2) for w in range(4)])
            with Stage(nc, f"hy_mult{o}") as st:
                own, crossed = st.sem("own"), st.sem("crossed")
                block = st.block()

                @block.vector
                def _(dve):
                    chain = Chain(dve, own)
                    dve.tensor_tensor(yw[:, 0], zw[:, 0], spectrum[:, o, 0], ALU.mult)
                    chain.link(dve.tensor_tensor(tmp[:, 0], zw[:, 1], spectrum[:, o, 1], ALU.mult))
                    dve.tensor_tensor(yw[:, 0], yw[:, 0], tmp[:, 0], ALU.subtract)
                    dve.wait_ge(crossed, 2)
                    dve.tensor_tensor(yw[:, 1], yw[:, 1], tmp[:, 1], ALU.add)

                @block.gpsimd
                def _(pool):
                    pool.tensor_tensor(yw[:, 1], zw[:, 0], spectrum[:, o, 1], ALU.mult).then_inc(crossed, 1)
                    pool.tensor_tensor(tmp[:, 1], zw[:, 1], spectrum[:, o, 0], ALU.mult).then_inc(crossed, 1)
            products(nc, f"hy_idft{o}", [
                (P, 512, [(yw[:, j, w, i * P:(i + 1) * P], idft[:, j, w, :]) for j in range(2) for w in range(4)],
                 copy_to(nc, tmp[:, 0, i, :], root[:, 4 * o + i:4 * o + i + 1])) for i in range(4)])
            with Stage(nc, f"hy_gate{o}") as st:
                own = st.sem("own")
                block = st.block()

                @block.vector
                def _(dve):
                    chain = Chain(dve, own)
                    for i in range(4):
                        chain.link(dve.scalar_tensor_tensor(out=tmp[:, 1, i, :], in0=z[:, i, :],
                                                            scalar=v("hy_skip", 4 * o + i, 1), in1=tmp[:, 0, i, :],
                                                            op0=ALU.mult, op1=ALU.add))
                        chain.link(dve.tensor_tensor(z[:, i, :], tmp[:, 1, i, :], u[:, 4 + 4 * o + i, :], ALU.mult))
                        if o == 1:
                            dve.tensor_tensor(out[:, i, :], z[:, i, :], gate[:, i, :], ALU.mult)
FF = 2816
FFK = FF // P


def swiglu(nc, name, h, w_gate, w_up, w_down, mid, out):
    gate_src, up_src = (w.rearrange("(k p) n -> p k n", p=P) for w in (w_gate, w_up))
    bufs, slots, cols = 3, 4, 256
    n_blocks = FF // cols
    with Stage(nc, name + "_in") as st:
        w = [st.sb(f"w{i}", [P, 2, KD, cols]) for i in range(bufs)]
        silu = [st.sb(f"silu{i}", [P, S]) for i in range(2)]
        ps = [[st.ps(f"acc{i}{j}", [P, BANK]) for j in range(2)] for i in range(slots)]
        w_landed = [st.sem(f"w_landed{i}") for i in range(bufs)]
        product_done, silu_done, stored = st.sem("product_done"), st.sem("silu_done"), st.sem("stored")
        block = st.block()

        @block.sync
        def _(sp):
            for b in range(n_blocks):
                if b >= bufs:
                    sp.wait_ge(product_done, 2 * (b - bufs + 1))
                for j, src in enumerate((gate_src, up_src)):
                    sp.dma_start(w[b % bufs][:, j], src[:, :, b * cols:(b + 1) * cols]).then_inc(w_landed[b % bufs], 16)

        @block.tensor
        def _(pe):
            for n in range(FFK):
                b, i = n // 2, n % 2
                if i == 0:
                    pe.wait_ge(w_landed[b % bufs], 32 * (b // bufs + 1))
                if n >= slots:
                    pe.wait_ge(stored, n - slots + 1)
                for j in range(2):
                    for k in range(KD):
                        ins = pe.matmul(ps[n % slots][j][:], w[b % bufs][:, j, k, i * P:(i + 1) * P], h[:, k, :],
                                        start=(k == 0), stop=(k == KD - 1))
                ins.then_inc(product_done, 1)

        @block.scalar
        def _(act):
            for n in range(FFK):
                act.wait_ge(product_done, n + 1)
                if n >= 2:
                    act.wait_ge(stored, n - 1)
                act.activation(silu[n % 2][:], ps[n % slots][0][:], ACT.Silu).then_inc(silu_done, 1)

        @block.vector
        def _(dve):
            for n in range(FFK):
                dve.wait_ge(silu_done, n + 1)
                dve.tensor_tensor(mid[:, n, :], silu[n % 2][:], ps[n % slots][1][:], ALU.mult).then_inc(stored, 1)

    linear(nc, name + "_down", lambda k: mid[:, k, :], weight_blocks(w_down, 0, D, width=256), S,
           lambda e, n, ps: copy_on(e, nc, out[:, n, :], ps[:, 0:S]), kc=FFK, bufs=3, width=256)


def ffn(nc, name, d, c, v, x, n):
    with ExitStack() as keep:
        h = keep.enter_context(nc.sbuf_tensor(name + "_h", [P, KD, S], F32))
        out = keep.enter_context(nc.sbuf_tensor(name + "_out", [P, KD, S], F32))
        norm(nc, name + "_pre", lambda k: x[:, k, :], lambda k: h[:, k, :], S,
             lambda k: v(f"ffn{n}_pre_norm_2", k, 1), c["ones"])
        with ExitStack() as inner:
            mid = inner.enter_context(nc.sbuf_tensor(name + "_mid", [P, FFK, S], F32))
            swiglu(nc, name, h, d[f"ffn{n}_w_gate_2"], d[f"ffn{n}_w_up_2"], d[f"ffn{n}_w_down_2"], mid, out)
        norm(nc, name + "_post", lambda k: out[:, k, :], lambda k: h[:, k, :], S,
             lambda k: v(f"ffn{n}_post_norm_2", k, 1), c["ones"], residual=lambda k: x[:, k, :], half=0.5)


def rel_bias_table(nc, d, table):
    wide = 2 * S
    with Stage(nc, "rel_bias") as st:
        bucket, bias = st.sb("bucket", [32, wide]), st.sb("bias", [32, 8])
        causal, line = st.sb("causal", [8, wide]), st.sb("line", [8, wide])
        ps = st.ps("spread_line", [8, wide])
        landed, spread, masked, stored = (st.sem(x) for x in ("landed", "spread", "masked", "stored"))
        block = st.block()

        @block.sync
        def _(sp):
            for dst, src in ((bucket[:], d["c_bucket"]), (bias[:], d["rel_bias_2"]), (causal[:], d["c_causal"])):
                sp.dma_start(dst, src).then_inc(landed, 16)
            sp.wait_ge(masked, 1)
            sp.dma_start(d["s_rel"], line[:].rearrange("h (a m) -> h a m", a=1).broadcast_to([8, P, wide])
                         ).then_inc(stored, 16)
            sp.wait_ge(stored, 16)
            sp.dma_start(table[:], bass.AP(tensor=d["s_rel"].tensor, offset=P - 1, ap=[[wide - 1, P], [P * wide, 8], [1, 896]])
                         ).then_inc(stored, 16)
            sp.wait_ge(stored, 32)

        @block.tensor
        def _(pe):
            pe.wait_ge(landed, 48)
            for a in range(2):
                ins = pe.matmul(ps[:, a * BANK:(a + 1) * BANK], bias[:], bucket[:, a * BANK:(a + 1) * BANK],
                                start=True, stop=True)
            ins.then_inc(spread, 1)

        @block.vector
        def _(dve):
            dve.wait_ge(spread, 1)
            dve.tensor_tensor(line[:], ps[:], causal[:], ALU.add).then_inc(masked, 1)


N_CMP = 31


def compress(nc, name, kv, pos, w1, w2, keys=None, values=None):
    with Stage(nc, name) as st:
        w1_sb = st.sb("w1", [P, 32, 256])
        w2_sb = st.sb("w2", [P, 2, 64])
        blocks = st.sb("blocks", [P, 32, N_CMP])
        hid = st.sb("hid", [P, 2, 2, N_CMP])
        ps = [st.ps(f"hid{i}", [P, BANK]) for i in range(4)]
        out_ps = [st.ps(f"out{i}", [P, BANK]) for i in range(2)]
        landed, added, done, silu_done, out_done = (st.sem(x) for x in ("landed", "added", "done", "silu_done", "out_done"))
        block = st.block()

        @block.sync
        def _(sp):
            src = w1.rearrange("(t f) n -> f t n", f=64)
            sp.dma_start(w1_sb[0:64], src).then_inc(landed, 16)
            sp.dma_start(w1_sb[64:128], src).then_inc(landed, 16)
            sp.dma_start(w2_sb[:], w2.rearrange("(a p) n -> p a n", p=P)).then_inc(landed, 16)

        @block.vector
        def _(dve):
            src = bass.AP(tensor=kv.tensor, offset=kv.offset, ap=[list(kv.ap[0]), [1, 32], [16, N_CMP]])
            dve.tensor_tensor(blocks[:], src, pos.rearrange("p (t a) -> p t a", a=1).broadcast_to([P, 32, N_CMP]),
                              ALU.add).then_inc(added, 1)
            for g in range(2):
                dve.wait_ge(out_done, g + 1)
                if keys is not None:
                    dve.tensor_copy(keys[64 * g:64 * g + 64, :], out_ps[g][64 * g:64 * g + 64, 0:N_CMP])
                else:
                    dve.tensor_copy(values[:, 64 * g:64 * g + 64], out_ps[g][0:N_CMP, 0:64])

        @block.tensor
        def _(pe):
            pe.wait_ge(landed, 48)
            pe.wait_ge(added, 1)
            for g in range(2):
                r = slice(64 * g, 64 * g + 64)
                for a in range(2):
                    for t in range(32):
                        ins = pe.matmul(ps[2 * g + a][:, 0:N_CMP], w1_sb[r, t, a * P:(a + 1) * P], blocks[r, t, :],
                                        start=(t == 0), stop=(t == 31))
                    ins.then_inc(done, 1)
            for g in range(2):
                pe.wait_ge(silu_done, 2 * (g + 1))
                for a in range(2):
                    if keys is not None:
                        ins = pe.matmul(out_ps[g][64 * g:64 * g + 64, 0:N_CMP], w2_sb[:, a, :], hid[:, a, g, :],
                                        start=(a == 0), stop=(a == 1))
                    else:
                        ins = pe.matmul(out_ps[g][0:N_CMP, 0:64], hid[:, a, g, :], w2_sb[:, a, :],
                                        start=(a == 0), stop=(a == 1))
                ins.then_inc(out_done, 1)

        @block.scalar
        def _(act):
            for g in range(2):
                for a in range(2):
                    act.wait_ge(done, 2 * g + a + 1)
                    act.activation(hid[:, a, g, :], ps[2 * g + a][:, 0:N_CMP], ACT.Silu).then_inc(silu_done, 1)


def solve(nc, name, c, n_mat, rhs, out, n, width):
    steps = ("flip", "pow2", "pow4", "pow8", "tdiag", "off", "z1", "z2", "z3")
    with Stage(nc, name) as st:
        off16 = st.sb("off16", [P, P])
        dn, en, dt, m = (st.sb(x, [P, n, P]) for x in ("diag", "off", "diag_t", "inv_t"))
        p2, p4 = st.sb("pow2", [P, n, 2, P]), st.sb("pow4", [P, n, 2, P])
        p8, ft = st.sb("pow8", [P, n, P]), st.sb("off_t", [P, n, P])
        y1, z = st.sb("y1", [P, n, width]), st.sb("z", [P, n, width])
        ps = [st.ps(f"ps{i}", [P, BANK]) for i in range(8)]
        made, split = st.sem("made"), st.sem("split")
        pe_done, dve_done, act_done, pool_done = (st.sem(x) for x in ("pe_done", "dve_done", "act_done", "pool_done"))
        block = st.block()

        dve_steps = ("flip", "pow4", "pow8", "tdiag", "off", "z1", "z2", "z3")
        act_steps = ("pow2", "pow4", "pow8", "off")

        def counted(of, step, i):
            return n * of.index(step) + i + 1

        @block.tensor
        def _(pe):
            def order(step, i):
                earlier = steps[:steps.index(step)]
                for of, sem in ((dve_steps, dve_done), (act_steps, act_done)):
                    before = [s for s in earlier if s in of]
                    if before:
                        pe.wait_ge(sem, counted(of, before[-1], i))
                return ps[i % 8]

            for i in range(n):
                pe.transpose(order("flip", i)[:, 0:P], n_mat[:, i, :], c["ident"]).then_inc(pe_done, 1)
            for i in range(n):
                b = order("pow2", i)
                pe.wait_ge(pool_done, i + 1)
                pe.matmul(b[:, 0:P], dt[:, i, :], dn[:, i, :], start=True, stop=True)
                pe.matmul(b[:, P:2 * P], dn[:, i, :], dt[:, i, :], start=True, stop=True).then_inc(pe_done, 1)
            for i in range(n):
                b = order("pow4", i)
                pe.matmul(b[:, 0:P], p2[:, i, 1, :], p2[:, i, 0, :], start=True, stop=True)
                pe.matmul(b[:, P:2 * P], p2[:, i, 0, :], p2[:, i, 1, :], start=True, stop=True)
                pe.matmul(b[:, 2 * P:3 * P], p2[:, i, 0, :], m[:, i, :], start=True, stop=True).then_inc(pe_done, 1)
            for i in range(n):
                b = order("pow8", i)
                pe.matmul(b[:, 0:P], p4[:, i, 1, :], p4[:, i, 0, :], start=True, stop=True)
                pe.matmul(b[:, P:2 * P], p4[:, i, 0, :], m[:, i, :], start=True, stop=True).then_inc(pe_done, 1)
            for i in range(n):
                pe.matmul(order("tdiag", i)[:, 0:P], p8[:, i, :], m[:, i, :], start=True, stop=True).then_inc(pe_done, 1)
            for i in range(n):
                b = order("off", i)
                pe.matmul(b[:, 0:P], en[:, i, :], m[:, i, :], start=True, stop=True)
                pe.matmul(b[:, P:P + width], m[:, i, :], rhs[:, i, :], start=True, stop=True).then_inc(pe_done, 1)
            for step, src in (("z1", y1), ("z2", z), ("z3", z)):
                for i in range(n):
                    pe.matmul(order(step, i)[:, 0:width], ft[:, i, :], src[:, i, :],
                              start=True, stop=True).then_inc(pe_done, 1)

        @block.gpsimd
        def _(pool):
            pool.tensor_scalar(off16[:], c["same16"], -1.0, 1.0, ALU.mult, ALU.add).then_inc(made, 1)
            pool.wait_ge(made, 1)
            for i in range(n):
                pool.tensor_tensor(dn[:, i, :], n_mat[:, i, :], c["same16"], ALU.mult)
                pool.tensor_tensor(en[:, i, :], n_mat[:, i, :], off16[:], ALU.mult)
                pool.wait_ge(dve_done, i + 1)
                pool.tensor_tensor(m[:, i, :], c["ident"], dt[:, i, :], ALU.subtract).then_inc(pool_done, 1)

        @block.vector
        def _(dve):
            def ready(step, i):
                dve.wait_ge(pe_done, counted(steps, step, i))
                return ps[i % 8]

            for i in range(n):
                dve.tensor_tensor(dt[:, i, :], ready("flip", i)[:, 0:P], c["same16"], ALU.mult).then_inc(dve_done, 1)
            for step, col in (("pow4", 2), ("pow8", 1), ("tdiag", 0)):
                for i in range(n):
                    b = ready(step, i)
                    dve.tensor_tensor(m[:, i, :], m[:, i, :], b[:, col * P:(col + 1) * P], ALU.add).then_inc(dve_done, 1)
            for i in range(n):
                dve.tensor_copy(y1[:, i, :], ready("off", i)[:, P:P + width]).then_inc(dve_done, 1)
            for step in ("z1", "z2", "z3"):
                for i in range(n):
                    dve.tensor_tensor((out if step == "z3" else z)[:, i, :], y1[:, i, :],
                                      ready(step, i)[:, 0:width], ALU.subtract).then_inc(dve_done, 1)

        @block.scalar
        def _(act):
            for step, dst, cols in (("pow2", p2, 2 * P), ("pow4", p4, 2 * P), ("pow8", p8, P), ("off", ft, P)):
                for i in range(n):
                    act.wait_ge(pe_done, counted(steps, step, i))
                    if step in dve_steps:
                        act.wait_ge(dve_done, counted(dve_steps, step, i))
                    o = dst[:, i] if cols == P else dst[:, i].rearrange("p a b -> p (a b)")
                    act.copy(o, ps[i % 8][:, 0:cols]).then_inc(act_done, 1)


def delta_branch(nc, d, c, v, qkv, ab, out):
    with ExitStack() as keep:
        def sb(name, shape, stack=keep):
            return stack.enter_context(nc.sbuf_tensor("dn_" + name, shape, F32))

        q, k, val = qkv[:, 0:4], qkv[:, 4:8], qkv[:, 8:12]
        head_norm(nc, "dn_l2", [qkv[:, i, :] for i in range(8)], [c["root128"]] * 4 + [c["ones"][:, 0:1]] * 4, c["ones"])
        g, beta, sp_tmp = sb("g", [P, 4, 4]), sb("beta", [P, 4, 4]), sb("softplus", [P, 4, 4])
        gc, left, eg = sb("gc", [P, 4, 4]), sb("left", [P, 4, 4]), sb("exp_gc", [P, 4, 4])
        ktok, vtok = sb("k_tokens", [P, 4, 512]), sb("v_tokens", [P, 4, 512])
        to_features(nc, "dn_turn", [([src[:, i, t * P:(t + 1) * P] for i in range(4)], None, dst[:, t, :])
                                    for src, dst in ((k, ktok), (val, vtok)) for t in range(4)], c["ident"])
        with Stage(nc, "dn_gates") as st:
            a_log, dt_bias = st.sb("a_log", [P, 4]), st.sb("dt_bias", [P, 4])
            x, neg, e = st.sb("x", [P, 4, 4]), st.sb("neg", [P, 4, 4]), st.sb("e", [P, 4, 4])
            ps = [st.ps(f"sum{i}", [P, BANK]) for i in range(2)]
            landed, exped, prepared, logged, decays, summed, own = (
                st.sem(n) for n in ("landed", "exped", "prepared", "logged", "decays", "summed", "own"))
            block = st.block()

            @block.sync
            def _(sp):
                for dst, src in ((a_log, d["dn_a_log_2"]), (dt_bias, d["dn_dt_bias_2"])):
                    sp.dma_start(dst[:], bass.AP(tensor=src.tensor, offset=src.offset, ap=[[0, P], [1, 4]])
                                 ).then_inc(landed, 16)

            @block.scalar
            def _(act):
                act.wait_ge(landed, 32)
                act.activation(a_log[:], a_log[:], ACT.Exp).then_inc(exped, 1)
                act.activation(beta[:], ab[:, :, 4:8], ACT.Sigmoid).then_inc(exped, 1)
                act.wait_ge(prepared, 1)
                act.activation(e[:], neg[:], ACT.Exp).then_inc(logged, 1)
                act.wait_ge(prepared, 2)
                act.activation(e[:], e[:], ACT.Ln).then_inc(logged, 1)
                act.wait_ge(decays, 2)
                act.activation(left[:], left[:], ACT.Exp)
                act.activation(eg[:], gc[:], ACT.Exp)

            @block.vector
            def _(dve):
                chain = Chain(dve, own)

                def tiles(t):
                    return t[:].rearrange("p (a h) -> p a h", a=1).broadcast_to([P, 4, 4])

                dve.wait_ge(landed, 32)
                dve.wait_ge(exped, 2)
                chain.link(dve.tensor_tensor(x[:], ab[:, :, 0:4], tiles(dt_bias), ALU.add))
                chain.link(dve.tensor_scalar(neg[:], x[:], -1.0, None, ALU.mult))
                dve.tensor_tensor(neg[:], neg[:], x[:], ALU.min).then_inc(prepared, 1)
                dve.wait_ge(logged, 1)
                dve.tensor_scalar(e[:], e[:], 1.0, None, ALU.add).then_inc(prepared, 1)
                dve.wait_ge(logged, 2)
                chain.link(dve.scalar_tensor_tensor(out=g[:], in0=x[:], scalar=0.0, in1=e[:], op0=ALU.max, op1=ALU.add))
                chain.link(dve.tensor_tensor(g[:], g[:], tiles(a_log), ALU.mult))
                dve.tensor_scalar(g[:], g[:], -1.0, None, ALU.mult).then_inc(decays, 1)
                dve.wait_ge(summed, 1)
                chain.link(dve.tensor_copy(gc[:].rearrange("p a h -> p (a h)"), ps[0][:, 0:16]))
                dve.tensor_tensor(left[:].rearrange("p a h -> p (a h)"), ps[1][:, 0:16],
                                  gc[:].rearrange("p a h -> p (a h)"), ALU.subtract).then_inc(decays, 1)

            @block.tensor
            def _(pe):
                pe.wait_ge(decays, 1)
                gf = g[:].rearrange("p a h -> p (a h)")
                pe.matmul(ps[0][:, 0:16], c["incl_fwd"], gf, start=True, stop=True)
                pe.matmul(ps[1][:, 0:16], c["heads2"], gf, start=True, stop=True).then_inc(summed, 1)

        n_all = 16
        nmat, aqk = sb("n", [P, n_all, P]), sb("aqk_t", [P, n_all, P])
        rhs, sol = sb("rhs", [P, n_all, 256]), sb("sol", [P, n_all, 256])
        ends = sb("ends", [P, n_all, 2])
        with Stage(nc, "dn_matrices") as st:
            gb = [st.sb(f"g_spread{i}", [P, P]) for i in range(2)]
            arg = [st.sb(f"arg{i}", [P, 2, P]) for i in range(2)]
            row = [st.sb(f"row{i}", [P, P]) for i in range(2)]
            eb = st.sb("exp_beta", [P, 4, 4])
            ps_r = [st.ps(f"row_ps{i}", [P, BANK]) for i in range(2)]
            ps_k = [st.ps(f"gram{i}", [P, BANK]) for i in range(2)]
            spread, rowed, grammed, args, exped, rowed_exp, masked, own = (
                st.sem(n) for n in ("spread", "rowed", "grammed", "args", "exped", "rowed_exp", "masked", "own"))
            block = st.block()

            @block.gpsimd
            def _(pool):
                for i in range(n_all):
                    if i >= 2:
                        pool.wait_ge(rowed, i - 1)
                    pool.tensor_scalar(gb[i % 2][:], c["ones"], g[:, i // 4, i % 4:i % 4 + 1], None,
                                       ALU.mult).then_inc(spread, 1)

            @block.tensor
            def _(pe):
                for i in range(n_all):
                    t, h = i // 4, i % 4
                    at = slice(t * P, (t + 1) * P)
                    pe.wait_ge(spread, i + 1)
                    if i >= 2:
                        pe.wait_ge(exped, i - 1)
                        pe.wait_ge(masked, i - 1)
                    pe.matmul(ps_r[i % 2][:, 0:P], gb[i % 2][:], c["incl_fwd"], start=True, stop=True).then_inc(rowed, 1)
                    pe.matmul(ps_k[i % 2][:, 0:P], k[:, h, at], k[:, h, at], start=True, stop=True)
                    pe.matmul(ps_k[i % 2][:, P:2 * P], k[:, h, at], q[:, h, at], start=True, stop=True).then_inc(grammed, 1)

            @block.scalar
            def _(act):
                for i in range(n_all):
                    act.wait_ge(args, i + 1)
                    act.activation(row[i % 2][:], ps_r[i % 2][:, 0:P], ACT.Exp)
                    act.activation(arg[i % 2][:], arg[i % 2][:], ACT.Exp).then_inc(exped, 1)

            @block.vector
            def _(dve):
                chain = Chain(dve, own)
                chain.link(dve.tensor_tensor(eb[:], eg[:], beta[:], ALU.mult))
                chain.link(dve.tensor_scalar(eb[:], eb[:], -1.0, None, ALU.mult))
                for i in range(n_all):
                    t, h = i // 4, i % 4
                    at, hs = slice(t * P, (t + 1) * P), slice(h * P, (h + 1) * P)
                    dve.wait_ge(rowed, i + 1)
                    chain.link(dve.tensor_scalar(arg[i % 2][:, 0, :], ps_r[i % 2][:, 0:P], gc[:, t, h:h + 1], 0.0,
                                                 ALU.subtract, ALU.min))
                    chain.link(dve.tensor_scalar(arg[i % 2][:, 1, :], ps_r[i % 2][:, 0:P], gc[:, t, h:h + 1], 0.0,
                                                 ALU.subtract, ALU.max))
                    dve.tensor_scalar(arg[i % 2][:, 1, :], arg[i % 2][:, 1, :], -1.0, None, ALU.mult).then_inc(args, 1)
                    dve.tensor_scalar(rhs[:, i, 0:P], vtok[:, t, hs], beta[:, t, h:h + 1], None, ALU.mult)
                    dve.tensor_scalar(rhs[:, i, P:2 * P], ktok[:, t, hs], eb[:, t, h:h + 1], None, ALU.mult)
                    dve.wait_ge(exped, i + 1)
                    dve.wait_ge(grammed, i + 1)
                    chain.link(dve.tensor_tensor(arg[i % 2][:, 0, :], arg[i % 2][:, 0, :], c["incl_fwd"], ALU.mult))
                    chain.link(dve.tensor_tensor(arg[i % 2][:, 1, :], arg[i % 2][:, 1, :], c["strict_rev"], ALU.mult))
                    chain.link(dve.tensor_copy(ends[:, i, 0:1], row[i % 2][:, 63:64]))
                    chain.link(dve.tensor_copy(ends[:, i, 1:2], row[i % 2][:, 127:128]))
                    dve.tensor_tensor(aqk[:, i, :], ps_k[i % 2][:, P:2 * P], arg[i % 2][:, 0, :], ALU.mult)
                    dve.scalar_tensor_tensor(out=nmat[:, i, :], in0=ps_k[i % 2][:, 0:P], scalar=beta[:, t, h:h + 1],
                                             in1=arg[i % 2][:, 1, :], op0=ALU.mult, op1=ALU.mult).then_inc(masked, 1)
                    dve.wait_ge(masked, i + 1)
                    chain.link(dve.tensor_tensor(q[:, h, at], q[:, h, at], row[i % 2][:], ALU.mult))
                    chain.link(dve.tensor_scalar(ktok[:, t, hs], ktok[:, t, hs], left[:, t, h:h + 1], None, ALU.mult))
        for b in range(4):
            s = slice(4 * b, 4 * b + 4)
            solve(nc, f"dn_solve{b}", c, nmat[:, s], rhs[:, s], sol[:, s], 4, 256)
        turned = sb("w_t", [P, n_all, P])
        to_features(nc, "dn_w", [([sol[:, i + j, P:2 * P] for j in range(4)], None,
                                  turned[:, i:i + 4, :].rearrange("p a b -> p (a b)")) for i in range(0, n_all, 4)],
                    c["ident"])
        with Stage(nc, "dn_scan") as st:
            state, vnew = st.sb("state", [P, 4, P]), st.sb("v_new", [P, 4, P])
            ps_w, ps_s = st.ps("w_state", [P, BANK]), st.ps("new_state", [P, BANK])
            ps_o, ps_a = [st.ps(f"q_state{i}", [P, BANK]) for i in range(2)], [st.ps(f"qk_v{i}", [P, BANK]) for i in range(2)]
            cleared, pe_done, dve_done, tile_out, own = (st.sem(n) for n in ("cleared", "pe_done", "dve_done", "tile_out", "own"))
            block = st.block()

            @block.tensor
            def _(pe):
                pe.wait_ge(cleared, 1)
                for n in range(8):
                    t, hf = n // 2, n % 2
                    r = slice(CH * hf, CH * hf + CH)
                    at = slice(n * CH, n * CH + CH)
                    if n:
                        pe.wait_ge(dve_done, 2 * n)
                    if hf == 0 and t >= 2:
                        pe.wait_ge(tile_out, t - 1)
                    for h in range(4):
                        ins = pe.matmul(ps_w[r, h * P:(h + 1) * P], turned[:, 4 * t + h, r], state[:, h, :],
                                        start=True, stop=True)
                    ins.then_inc(pe_done, 1)
                    for h in range(4):
                        pe.matmul(ps_o[t % 2][:, h * P + CH * hf:h * P + CH * hf + CH], state[:, h, :], q[:, h, at],
                                  start=True, stop=True)
                    pe.wait_ge(dve_done, 2 * n + 1)
                    for h in range(4):
                        ins = pe.matmul(ps_s[:, h * P:(h + 1) * P], ktok[r, t, h * P:(h + 1) * P], vnew[r, h, :],
                                        start=True, stop=True)
                    ins.then_inc(pe_done, 1)
                    if hf == 1:
                        for h in range(4):
                            ins = pe.matmul(ps_a[t % 2][:, h * P:(h + 1) * P], vnew[:, h, :], aqk[:, 4 * t + h, :],
                                            start=True, stop=True)
                        ins.then_inc(pe_done, 1)

            @block.vector
            def _(dve):
                chain = Chain(dve, own)
                dve.memset(state[:], 0.0).then_inc(cleared, 1)
                dve.wait_ge(cleared, 1)
                for n in range(8):
                    t, hf = n // 2, n % 2
                    r = slice(CH * hf, CH * hf + CH)
                    done = 2 * n + n // 2
                    dve.wait_ge(pe_done, done + 1)
                    dve.tensor_tensor(vnew[r], sol[r, 4 * t:4 * t + 4, 0:P],
                                      ps_w[r, :].rearrange("p (h j) -> p h j", j=P), ALU.add).then_inc(dve_done, 1)
                    dve.wait_ge(pe_done, done + 2)
                    for h in range(4):
                        ins = dve.scalar_tensor_tensor(out=state[:, h, :], in0=state[:, h, :],
                                                       scalar=ends[:, 4 * t + h, hf:hf + 1],
                                                       in1=ps_s[:, h * P:(h + 1) * P], op0=ALU.mult, op1=ALU.add)
                    ins.then_inc(dve_done, 1)
                    if hf == 1:
                        dve.wait_ge(pe_done, done + 3)
                        o = out[:, :, t * P:(t + 1) * P]
                        chain.link(dve.tensor_copy(o, ps_o[t % 2][:].rearrange("p (h t) -> p h t", t=P)))
                        dve.tensor_tensor(o, o, ps_a[t % 2][:].rearrange("p (h t) -> p h t", t=P),
                                          ALU.add).then_inc(tile_out, 1)
                    dve.wait_ge(dve_done, 2 * n + 2)


def conv4(nc, qkv_padded, qkv, v):
    with Stage(nc, "dn_conv") as st:
        convolved, own = st.sem("convolved"), st.sem("own")
        block = st.block()

        @block.vector
        def _(dve):
            chain = Chain(dve, own)
            for i in range(12):
                for tap in range(4):
                    w, src = v("dn_conv", 12 * tap + i, 1), qkv_padded[:, i, tap:tap + S]
                    if tap == 0:
                        chain.link(dve.tensor_scalar(qkv[:, i, :], src, w, None, ALU.mult))
                    else:
                        ins = dve.scalar_tensor_tensor(out=qkv[:, i, :], in0=src, scalar=w, in1=qkv[:, i, :],
                                                       op0=ALU.mult, op1=ALU.add)
                        if tap < 3:
                            chain.link(ins)
                ins.then_inc(convolved, 1)

        @block.scalar
        def _(act):
            for i in range(12):
                act.wait_ge(convolved, i + 1)
                act.activation(qkv[:, i, :], qkv[:, i, :], ACT.Silu)


def mixer(nc, d, c, v, x):
    W = d["w_in_2"]
    wv = W.rearrange("(k p) n -> p k n", p=P)
    Q0, KV0, G0, DN0, AB0, Z0, MQ0 = 0, 512, 1280, 1304, 2840, 2848, 3360
    with ExitStack() as keep:
        def sb(name, shape, stack=keep):
            return stack.enter_context(nc.sbuf_tensor("mix_" + name, shape, F32))

        u = sb("u", [P, KD, S])
        branch = [sb(f"branch{i}", [P, 4, S]) for i in range(3)]
        norm(nc, "mix_pre", lambda k: x[:, k, :], lambda k: u[:, k, :], S, lambda k: v("mix_pre_norm_2", k, 1), c["ones"])

        with ExitStack() as inner:
            q = sb("q", [P, 4, S], inner)
            ks = sb("keys", [P, 4, S], inner)
            vs = sb("values", [P, 4, 256], inner)
            gates = sb("gates", [P, 4, 24], inner)
            q_loads = [(lambda buf, s=s, i=i: buf[:, :, P * i + 64 * s:P * i + 64 * s + 64],
                        wv[:, :, Q0 + 256 * s + 64 * i:Q0 + 256 * s + 64 * i + 64]) for s in range(2) for i in range(4)]
            blocks = ([(q_loads, [P] * 4)] + weight_blocks(W, KV0, 384) + weight_blocks(W, KV0 + 512, 128))
            outs = [(q[:, i, :], 0.125) for i in range(4)] + [(ks[:, i, :], None) for i in range(4)]
            linear(nc, "nsa_in", lambda k: u[:, k, :], blocks, S,
                   lambda e, n, ps: copy_on(e, nc, outs[n][0], ps[:, 0:S], outs[n][1]), bufs=3)

            def evict(e, b, t, ps):
                if b < 2:
                    return copy_on(e, nc, vs[:, t, P * b:P * b + P], ps[:, 0:P])
                return copy_on(e, nc, gates[:, t, :], ps[:, 0:24])

            linear_tokens(nc, "nsa_v", lambda k: u[:, k, :],
                          [(W[:, KV0 + 384:KV0 + 512], P), (W[:, KV0 + 640:KV0 + 768], P), (W[:, G0:G0 + 24], 24)], S, evict)
            kc, vc = sb("k_cmp", [P, N_CMP], inner), sb("v_cmp", [N_CMP, P], inner)
            compress(nc, "cmp_k", ks[:, 0, :], v("cmp_pos_k"), d["cmp_k_w1_2"], d["cmp_k_w2_2"], keys=kc)
            compress(nc, "cmp_v", ks[:, 1, :], v("cmp_pos_v"), d["cmp_v_w1_2"], d["cmp_v_w2_2"], values=vc)
            with Stage(nc, "nsa_gates") as st:
                opened = st.sem("opened")
                block = st.block()

                @block.scalar
                def _(act):
                    act.activation(gates[:], gates[:], ACT.Sigmoid).then_inc(opened, 1)

                @block.vector
                def _(dve):
                    dve.wait_ge(opened, 1)
                    dve.tensor_scalar(gates[:, 0, 0:8], gates[:, 0, 0:8], c["has_block"], None, ALU.mult)

            o = [sb(f"o{i}", [P, 4, 512], inner) for i in range(3)]
            table = sb("table", [P, 8, 896], inner)
            rel_bias_table(nc, d, table)
            units = []
            for t in range(4):
                for h in range(8):
                    b = 64 * (h // 4)
                    y0 = 384 - P * t
                    common = dict(q=q[b:b + 64, h % 4, t * P:(t + 1) * P])
                    ends = y0 + 31 + 16 * (N_CMP - 1) + 1
                    units.append(dict(common, keys=[kc[b:b + 64, :]], bias=table[:, h, y0 + 31:ends:16],
                                      values=[vc[:, b:b + 64]], out=o[0][:, t, 64 * h:64 * h + 64],
                                      rows=gates[:, t, h:h + 1]))
                    for n in range(2):
                        units.append(dict(common, keys=[ks[b:b + 64, 2 + n, 0:(t + 1) * P]],
                                          bias=table[:, h, y0:y0 + (t + 1) * P],
                                          values=[vs[:, j, P * n + b:P * n + b + 64] for j in range(t + 1)],
                                          out=o[1 + n][:, t, 64 * h:64 * h + 64],
                                          rows=gates[:, t, 8 * (n + 1) + h:8 * (n + 1) + h + 1]))
            attention(nc, "nsa", units, c["ident"])
            with Stage(nc, "nsa_sum") as st:
                own = st.sem("own")
                block = st.block()

                @block.vector
                def _(dve):
                    chain = Chain(dve, own)
                    chain.link(dve.tensor_tensor(o[1][:], o[1][:], o[0][:], ALU.add))
                    dve.tensor_tensor(o[2][:], o[2][:], o[1][:], ALU.add)
            to_features(nc, "nsa_turn", [([o[2][:, t, i * P:(i + 1) * P] for t in range(4)], None, branch[0][:, i, :])
                                         for i in range(4)], c["ident"])

        with ExitStack() as inner:
            zg = sb("dn_z", [P, 4, S], inner)
            qkv, ab = sb("qkv", [P, 12, S], inner), sb("ab", [P, 4, 8], inner)
            with ExitStack() as raw:
                padded = sb("qkv_padded", [P, 12, S + 3], raw)
                with Stage(nc, "dn_pad") as st:
                    block = st.block()

                    @block.vector
                    def _(dve):
                        dve.memset(padded[:, :, 0:3], 0.0)
                linear(nc, "dn_in", lambda k: u[:, k, :], weight_blocks(W, DN0, 1536) + weight_blocks(W, Z0, 512), S,
                       lambda e, n, ps: copy_on(e, nc, padded[:, n, 3:3 + S] if n < 12 else zg[:, n - 12, :], ps[:, 0:S]),
                       bufs=3)
                conv4(nc, padded, qkv, v)
            linear_tokens(nc, "dn_ab", lambda k: u[:, k, :], [(W[:, AB0:AB0 + 8], 8)], S,
                          lambda e, b, t, ps: copy_on(e, nc, ab[:, t, :], ps[:, 0:8]))
            delta_branch(nc, d, c, v, qkv, ab, branch[1])
            head_norm(nc, "dn_out_norm", [branch[1][:, i, :] for i in range(4)], [v("dn_out_norm")] * 4, c["group128"])
            in_place(nc, "dn_silu", [zg[:, i, :] for i in range(4)], ACT.Silu)
            with Stage(nc, "dn_gated") as st:
                block = st.block()

                @block.vector
                def _(dve):
                    dve.tensor_tensor(branch[1][:], branch[1][:], zg[:], ALU.mult)

        with ExitStack() as inner:
            mq, mk = sb("mem_q", [P, 4, S], inner), sb("mem_k", [P, 4, 256], inner)
            mv, mo = sb("mem_v", [P, 2, 512], inner), sb("mem_o", [P, 4, 512], inner)
            mem, mem_n = sb("mem", [P, KD, 256], inner), sb("mem_n", [P, KD, 256], inner)
            load(nc, "mem_load", [(mem[:], d["mem"].rearrange("(k p) t -> p k t", p=P))])
            norm(nc, "mem_norm", lambda k: mem[:, k, :], lambda k: mem_n[:, k, :], 256,
                 lambda k: v("mem_norm_2", k, 1), c["ones"])
            linear(nc, "mem_q", lambda k: u[:, k, :], weight_blocks(W, MQ0, 512), S,
                   lambda e, n, ps: copy_on(e, nc, mq[:, n, :], ps[:, 0:S], 128.0 ** -0.5), bufs=2)
            linear(nc, "mem_k", lambda k: mem_n[:, k, :], weight_blocks(d["w_mem_kv_2"], 0, 512), 256,
                   lambda e, n, ps: copy_on(e, nc, mk[:, n, :], ps[:, 0:256]), bufs=2)
            linear_tokens(nc, "mem_v", lambda k: mem_n[:, k, :], [(d["w_mem_kv_2"][:, 512:1024], 512)], 256,
                          lambda e, b, t, ps: copy_on(e, nc, mv[:, t, :], ps[:, 0:512]))
            attention(nc, "mem", [dict(q=mq[:, h, t * P:(t + 1) * P], keys=[mk[:, h, :]], bias=None,
                                       values=[mv[:, j, h * P:(h + 1) * P] for j in range(2)],
                                       out=mo[:, t, h * P:(h + 1) * P]) for t in range(4) for h in range(4)], c["ident"])
            to_features(nc, "mem_turn", [([mo[:, t, i * P:(i + 1) * P] for t in range(4)], None, branch[2][:, i, :])
                                         for i in range(4)], c["ident"])

        with ExitStack() as inner:
            gate = sb("branch_gates", [P, 24, S], inner)
            linear(nc, "merge_gates", lambda k: u[:, k, :], weight_blocks(d["w_branch_gate_2"], 0, 3 * D), S,
                   lambda e, n, ps: e.activation(gate[:, n, :], ps[:, 0:S], ACT.Sigmoid), bufs=3, engines="a")
            for b, wn in enumerate(("w_branch_nsa_2", "w_branch_dn_2", "w_branch_mem_2")):
                linear(nc, f"merge{b}", lambda k: branch[b][:, k, :], weight_blocks(d[wn], 0, D, kc=4), S,
                       lambda e, n, ps: e.tensor_tensor(gate[:, 8 * b + n, :], gate[:, 8 * b + n, :], ps[:, 0:S], ALU.mult),
                       kc=4, bufs=2, engines="v")
            with Stage(nc, "merge_sum") as st:
                own = st.sem("own")
                block = st.block()

                @block.vector
                def _(dve):
                    chain = Chain(dve, own)
                    chain.link(dve.tensor_tensor(gate[:, 0:8, :], gate[:, 0:8, :], gate[:, 8:16, :], ALU.add))
                    dve.tensor_tensor(gate[:, 0:8, :], gate[:, 0:8, :], gate[:, 16:24, :], ALU.add)
            linear(nc, "mix_out", lambda k: gate[:, k, :], weight_blocks(d["w_out_2"], 0, D), S,
                   lambda e, n, ps: copy_on(e, nc, gate[:, 8 + n, :], ps[:, 0:S]), bufs=2)
            norm(nc, "mix_post", lambda k: gate[:, 8 + k, :], lambda k: u[:, k, :], S,
                 lambda k: v("mix_post_norm_2", k, 1), c["ones"], residual=lambda k: x[:, k, :])


def second_block(nc, d, c, v, x):
    ffn(nc, "ffn1", d, c, v, x, 1)
    mixer(nc, d, c, v, x)
    ffn(nc, "ffn2", d, c, v, x, 2)
def constants():
    out = {}
    ident = np.eye(P, dtype=np.float32)
    ones = np.ones((P, P), np.float32)
    group64 = np.kron(np.eye(2), np.ones((64, 64)) / 64).astype(np.float32)
    swap = np.zeros((P, P), np.float32)
    for f in range(P):
        if f % 32 < 16:
            swap[f + 16, f] = -1.0
        else:
            swap[f - 16, f] = 1.0
    t = np.arange(S)
    pos = np.stack([t // 64, t % 64], 0).astype(np.float32)
    inv = (np.float32(10000.0) ** (-np.arange(16, dtype=np.float32) / np.float32(16))).astype(np.float32)
    f = np.arange(P) % 64
    ang = (pos[f // 32] * inv[f % 16][:, None]).astype(np.float32)
    out["cos"], out["sin"] = np.cos(ang).astype(np.float32), np.sin(ang).astype(np.float32)
    col = np.arange(64)
    start = np.clip(col - 8, 0, 48)
    window = np.where((col[None] >= start[:, None]) & (col[None] < start[:, None] + 16), 0.0, NEG)
    window = np.concatenate([window, window], 0).astype(np.float32)
    small = {"ident": ident, "ones": ones, "group64": group64, "swap": swap, "window": window}
    s_i, t_i = np.arange(P)[:, None], np.arange(P)[None, :]
    same64, same16 = s_i // 64 == t_i // 64, s_i // 16 == t_i // 16
    for name, before in (("fwd", s_i < t_i), ("rev", s_i > t_i)):
        small[f"strict_{name}"] = (before & same64).astype(np.float32)
        small[f"incl_{name}"] = ((before | (s_i == t_i)) & same64).astype(np.float32)
    small["same16"] = same16.astype(np.float32)
    small["heads2"] = np.kron(np.eye(2), np.ones((64, 64))).astype(np.float32)
    has = (np.arange(P) >= 31).astype(np.float32)[:, None]
    small["has_block"] = has
    small["group128"] = np.full((P, P), 1 / 128, np.float32)
    small["root128"] = np.full((P, 1), 128.0 ** -0.5, np.float32)
    first = (np.arange(P) == 0)[:, None]
    small["half_col"] = np.full((P, 1), 0.5, np.float32)
    small["sum_col"] = np.where(first, 1.0, 0.5).astype(np.float32)
    small["diff_col"] = np.where(first, 0.0, 0.5).astype(np.float32)
    out["small"] = np.concatenate(list(small.values()), 1)
    where, at = {}, 0
    for k, v in small.items():
        where[k] = (at, v.shape[1])
        at += v.shape[1]
    w = 2 * np.pi * (np.arange(S)[None, :] + 0.5) / (2 * S) * np.arange(S)[:, None]
    out["dft"] = np.stack([np.cos(w), np.sin(w)]).astype(np.float32)
    out["idft"] = (np.stack([np.cos(w).T, np.sin(w).T]) / S).astype(np.float32)
    ti = np.arange(S, dtype=np.float32)
    tt = ti / np.float32(S - 1)
    bands = np.linspace(1e-4, 15, 16, dtype=np.float32)
    ang = (np.float32(2.0 * np.pi) * bands[None, :] * ti[:, None] / np.float32(S)).astype(np.float32)
    out["feats"] = np.concatenate([tt[:, None], np.cos(ang), -np.sin(ang)], -1).T.astype(np.float32).copy()
    deltas = np.linspace(np.log(1e-2) / 0.3, np.log(1e-2) / 1.5, S, dtype=np.float32)
    out["decay"] = np.exp(-tt[:, None] * np.abs(deltas)).astype(np.float32)
    m = np.arange(2 * S)
    dist = (S - 1) - m
    dd = np.maximum(dist, 0)
    logb = 16 + (np.log(np.maximum(dd, 1).astype(np.float32) / 16) / np.log(128 / 16) * 16).astype(np.int32)
    bucket = np.where(dd < 16, dd, np.minimum(logb, 31))
    out["bucket"] = (np.arange(32)[:, None] == bucket[None]).astype(np.float32)
    out["causal"] = np.broadcast_to(np.where(dist >= 0, 0.0, NEG), (8, 2 * S)).astype(np.float32).copy()
    return out, where


def columns(v):
    return np.asarray(v).reshape(-1, P).T


def vectors(i):
    v = {
        "cond": np.stack([columns(i["c"][0]), columns(i["c_ctx"])], 2).reshape(P, -1),
        "attn_ada_b": columns(i["attn_ada_b"][0]), "rec_ada_b": columns(i["rec_ada_b"][0]),
        "q_gain": np.tile(i["gqa_q_gain"][0], 2)[:, None], "k_gain": np.tile(i["gqa_k_gain"][0], 2)[:, None],
        "mu": columns(i["rwkv_mu"][0]),
        "w0": columns(i["rwkv_w0"][0].reshape(-1)), "a0": columns(i["rwkv_a0"][0].reshape(-1)),
        "hy_short": columns(i["hy_short"][0].reshape(-1)), "hy_skip": columns(i["hy_skip"][0].reshape(-1)),
        "hy_b1": np.tile(i["hy_b1"][0], 2)[:, None], "hy_b2": np.tile(i["hy_b2"][0], 2)[:, None],
        "r_k": columns(i["rwkv_r_k"][0].reshape(-1)),
        "dn_conv": columns(i["dn_conv_w_2"][0].reshape(-1)),
        "dn_out_norm": columns(i["dn_out_norm_2"][0]),
        "cmp_pos_k": np.tile(i["cmp_pos_k_2"][0].T, (2, 1)), "cmp_pos_v": np.tile(i["cmp_pos_v_2"][0].T, (2, 1)),
    }
    for name in ("attn_norm", "rec_norm", "rwkv_k_k", "rwkv_k_a", "rwkv_gn_w", "rwkv_gn_b", "ffn1_pre_norm_2",
                 "ffn1_post_norm_2", "mix_pre_norm_2", "mem_norm_2", "mix_post_norm_2", "ffn2_pre_norm_2",
                 "ffn2_post_norm_2"):
        v[name] = columns(i[name][0])
    v["final_norm"] = columns(i["final_norm"])
    where, at = {}, 0
    for k, a in v.items():
        where[k] = (at, a.shape[1])
        at += a.shape[1]
    return np.ascontiguousarray(np.concatenate(list(v.values()), 1)), where
class Columns:

    def __init__(self, tile, where):
        self.tile, self.where = tile, where

    def __call__(self, name, first=0, count=None):
        at, n = self.where[name]
        n = n - first if count is None else count
        return self.tile[:, at + first:at + first + n]


def rec_layer(nc, d, c, v, x, ctx, mod, gs):
    with ExitStack() as keep:
        def sb(name, shape, stack=keep):
            return stack.enter_context(nc.sbuf_tensor("rec_" + name, shape, F32))

        y = sb("y", [P, KD, S])
        with ExitStack() as mid:
            gate, vt, ends = sb("gate", [P, 4, S], mid), sb("v_tokens", [P, 6, 512], mid), sb("ends", [P, 2, 4, TT // CH], mid)
            v_feat, bonus = sb("v_features", [P, 4, S], mid), sb("bonus", [P, 4, S], mid)
            with ExitStack() as shifted:
                us = sb("shifted", [P, 13, TT], shifted)
                with ExitStack() as inner:
                    h = sb("h", [P, KD, TT], inner)
                    norm(nc, "rec_norm_x", lambda k: x[:, k, :], lambda k: h[:, k, 0:S], S,
                         lambda k: gs[:, k, 0:1], c["ones"], shift=lambda k: mod[:, k, 0:1])
                    norm(nc, "rec_norm_ctx", lambda k: ctx[:, k, :], lambda k: h[:, k, S:TT], LC,
                         lambda k: gs[:, k, 1:2], c["ones"], shift=lambda k: mod[:, k, 1:2])
                    linear(nc, "rec_gate", lambda k: h[:, k, :], weight_blocks(d["rec_w_in"], 1664, 512), S,
                           lambda e, n, ps: copy_on(e, nc, gate[:, n, :], ps[:, 0:S]), bufs=1)
                    hyena_input(nc, d, v, h, [y[:, 0:4], y[:, 4:8], bonus[:]], v_feat[:])
                    rwkv_input(nc, d, v, h, us)
                to_features(nc, "rwkv_vt", [([us[:, 8 + i, t * P:(t + 1) * P] for i in range(4)], None, vt[:, t, :])
                                            for t in range(6)], c["ident"])
                in_sbuf_copy(nc, "rwkv_v", v_feat[:], us[:, 8:12, 0:S])
                rwkv_features(nc, "rwkv_feat", d, c, v, [us[:, i, :] for i in range(13)], bonus, ends)
            scanned = sb("scanned", [P, 4, S], mid)
            rwkv_scan(nc, d, c, vt, ends, scanned)
            group_norm_out(nc, "rwkv_out", c, v, scanned, bonus, v_feat, gate, y[:, 0:4, :])
        hyena_branch(nc, d, c, v, y[:, 4:8, :])
        gated_out(nc, "rec_out", d["rec_w_out"], y, x, None, mod)


def program(nc, d, vec_at, const_at):
    Stage.used = 0
    for name, shape in (("s_rpb", [64, 8 * 15, 127]), ("s_feat", [2, 4, 512, TT]), ("s_rel", [8, P, 2 * S]),
                        ("s_hy", [4 * 512, S])):
        d[name] = nc.dram_tensor(name, shape, F32, kind="Internal").ap()
    with ExitStack() as keep:
        def sb(name, shape, stack=keep):
            return stack.enter_context(nc.sbuf_tensor(name, shape, F32))

        out_stored = keep.enter_context(nc.semaphore("out_stored"))
        x = sb("x", [P, KD, S])
        vec, const = sb("vectors", list(d["vec"].shape)), sb("constants", list(d["c_small"].shape))
        v, constant = Columns(vec, vec_at), Columns(const, const_at)
        c = {n: constant(n) for n in const_at}
        with ExitStack() as first:
            ctx = sb("ctx", [P, KD, LC], first)
            mods = [(sb(f"mod{i}", [P, 24, 2], first), sb(f"gain_scale{i}", [P, KD, 2], first)) for i in range(2)]
            q_gain = sb("q_gain", [P, 1], first)
            load(nc, "inputs", [(x[:], d["x"].rearrange("(k p) t -> p k t", p=P)), (vec[:], d["vec"]),
                                (ctx[:], d["ctx"].rearrange("(k p) t -> p k t", p=P)), (const[:], d["c_small"])])
            cond = v("cond").rearrange("p (k j) -> p k j", j=2)
            for i, n in enumerate(("attn", "rec")):
                adaln(nc, n + "_adaln", d[n + "_ada_w"], cond, v(n + "_ada_b"), v(n + "_norm"), *mods[i])
            with Stage(nc, "gains") as st:
                block = st.block()

                @block.vector
                def _(dve):
                    dve.tensor_scalar(q_gain[:], v("q_gain"), 0.125, None, ALU.mult)
            c["q_gain"], c["k_gain"] = q_gain[:], v("k_gain")
            attn_layer(nc, d, c, x, ctx, *mods[0])
            rec_layer(nc, d, c, v, x, ctx, *mods[1])
            out = sb("first_out", [P, KD, S], first)
            norm(nc, "final_norm", lambda k: x[:, k, :], lambda k: out[:, k, :], S, lambda k: v("final_norm", k, 1),
                 c["ones"])
            in_sbuf_copy(nc, "first_to_second", x[:], out[:])
        second_block(nc, d, c, v, x)
        with Stage(nc, "store_out") as st:
            block = st.block()

            @block.sync
            def _(sp):
                sp.dma_start(d["out"].rearrange("(k p) t -> p k t", p=P), x[:]).then_inc(out_stored, 16)
                sp.wait_ge(out_stored, 16)


_WEIGHTS = ["attn_ada_w", "attn_w_in", "na_rpb", "attn_w_out", "rec_ada_w", "rec_w_in", "rwkv_w_up", "rwkv_a_up",
            "hy_w1", "hy_w2", "hy_w3", "rec_w_out", "ffn1_w_gate_2", "ffn1_w_up_2", "ffn1_w_down_2", "w_in_2",
            "cmp_k_w1_2", "cmp_k_w2_2", "cmp_v_w1_2", "cmp_v_w2_2", "dn_a_log_2", "dn_dt_bias_2", "w_mem_kv_2",
            "w_branch_nsa_2", "w_branch_dn_2", "w_branch_mem_2", "w_branch_gate_2", "w_out_2", "ffn2_w_gate_2",
            "ffn2_w_up_2", "ffn2_w_down_2"]


def kernel(**inputs):
    import concourse.bacc as _bacc
    from concourse.bass_utils import run_bass_kernel_spmd as _run

    i = {name: np.asarray(a) for name, a in inputs.items()}
    consts, const_at = constants()
    vec, vec_at = vectors(i)
    arrays = {name: i[name][0] for name in _WEIGHTS}
    arrays["rel_bias_2"], arrays["hy_b3"] = i["rel_bias_2"], i["hy_b3"]
    arrays["x"], arrays["ctx"], arrays["mem"] = i["x"][0].T, i["ctx"][0].T, i["mem_2"][0].T
    arrays["vec"] = vec
    arrays.update({"c_" + name: a for name, a in consts.items()})
    nc = _bacc.Bacc("TRN2", target_bir_lowering=False, num_devices=1)
    sent, d = {}, {}
    for name, a in arrays.items():
        sent[f"in_{name}"] = np.ascontiguousarray(a)
        d[name] = nc.dram_tensor(f"in_{name}", a.shape, F32, kind="ExternalInput").ap()
    d["out"] = nc.dram_tensor("out_0", [D, S], F32, kind="ExternalOutput").ap()
    program(nc, d, vec_at, const_at)
    r = _run(nc, [sent], core_ids=[0])
    return np.ascontiguousarray(r.results[0]["out_0"].T)[None]
```

```python
from contextlib import ExitStack

import numpy as np
import concourse.bass as bass
from concourse import mybir

F32 = mybir.dt.float32
F32R = mybir.dt.float32r
ALU = mybir.AluOpType
ACT = mybir.ActivationFunctionType
AX = mybir.AxisListType
P = 128
BANK = 512
D = 1024
KD = D // P
S = 512
LC = 256
TT = S + LC
EPS = 1e-6
NEG = -1e30


class Stage:

    def __init__(self, nc, name):
        self.nc, self.name = nc, name

    used = 0

    def __enter__(self):
        self.stack = ExitStack()
        if Stage.used > 120:
            nc, free = self.nc, sorted(self.nc.free_semaphores)
            starts = [s for s in free if s - 1 not in free]
            for s in starts:
                nc.gpsimd.sem_clear(range(s, next(e for e in range(s, free[-1] + 2) if e not in free)))
            nc.all_engine_barrier()
            Stage.used = 0
        return self

    def __exit__(self, *e):
        return self.stack.__exit__(*e)

    def sb(self, name, shape, dtype=F32):
        return self.stack.enter_context(self.nc.sbuf_tensor(f"{self.name}_{name}", shape, dtype))

    def ps(self, name, shape):
        return self.stack.enter_context(self.nc.psum_tensor(f"{self.name}_{name}", shape, F32))

    def sem(self, name):
        Stage.used += 1
        return self.stack.enter_context(self.nc.semaphore(f"{self.name}_{name}"))

    def block(self):
        return self.stack.enter_context(self.nc.Block())


class Chain:

    def __init__(self, engine, sem):
        self.engine, self.sem, self.n = engine, sem, 0

    def link(self, ins):
        self.n += 1
        ins.then_inc(self.sem, 1)
        self.engine.wait_ge(self.sem, self.n)


def spans(n, step):
    return [(a, min(step, n - a)) for a in range(0, n, step)]


def load(nc, name, pairs):
    with Stage(nc, name) as st:
        landed = st.sem("landed")
        block = st.block()

        @block.sync
        def _(sp):
            for dst, src in pairs[0::2]:
                sp.dma_start(dst, src).then_inc(landed, 16)
            sp.wait_ge(landed, 16 * len(pairs))

        @block.scalar
        def _(act):
            for dst, src in pairs[1::2]:
                act.dma_start(dst, src).then_inc(landed, 16)


class WeightStream:

    def __init__(self, nc, stack, name, blocks, bufs=4):
        def sb(n, dtype):
            return stack.enter_context(nc.sbuf_tensor(f"{name}_{n}", [P, 1024], dtype, side="right"))

        def sem(n):
            Stage.used += 1
            return stack.enter_context(nc.semaphore(f"{name}_{n}"))

        self.nc, self.bufs, self.loaded, self.blocks, self.ranges = nc, bufs, 0, [], {}
        for stage, of in blocks.items():
            self.ranges[stage] = (len(self.blocks), len(self.blocks) + len(of))
            self.blocks += of
        self.raw = [sb(f"raw{i}", F32) for i in range(bufs)]
        self.high, self.low = ([sb(f"{n}{i}", F32R) for i in range(2)] for n in ("high", "low"))
        self.landed = [sem(f"w_landed{i}") for i in range(bufs)]
        self.high_done, self.split_done = sem("w_high_done"), sem("w_split_done")
        self.landings, total = [], [0] * bufs
        for b, (loads, _, _) in enumerate(self.blocks):
            total[b % bufs] += 16 * len(loads)
            self.landings.append(total[b % bufs])

    def view(self, buf, b):
        _, widths, ks = self.blocks[b]
        return buf[:, 0:len(ks) * sum(widths)].rearrange("p (k n) -> p k n", k=len(ks))

    def load(self, queue, upto):
        for b in range(self.loaded, min(upto, len(self.blocks))):
            if b >= self.bufs:
                queue.wait_ge(self.split_done, b - self.bufs + 1)
            for place, src in self.blocks[b][0]:
                queue.dma_start(place(self.view(self.raw[b % self.bufs], b)), src
                                ).then_inc(self.landed[b % self.bufs], 16)
            self.loaded = b + 1

    def start(self):
        self.load(self.nc.sync, self.bufs)

    def load_stage(self, queue, name):
        self.load(queue, self.ranges[name][1] + self.bufs)

    def make_high(self, act, b, first, product_done, count):
        act.wait_ge(self.landed[b % self.bufs], self.landings[b])
        if b - 2 >= first:
            act.wait_ge(product_done, count(b - 2))
        act.copy(self.view(self.high[b % 2], b), self.view(self.raw[b % self.bufs], b)).then_inc(self.high_done, 1)

    def make_low(self, dve, b):
        dve.wait_ge(self.high_done, b + 1)
        dve.tensor_tensor(self.view(self.low[b % 2], b), self.view(self.raw[b % self.bufs], b),
                          self.view(self.high[b % 2], b).bitcast(F32), ALU.subtract).then_inc(self.split_done, 1)


def weight_blocks(W, start, n, kc=KD, width=256):
    src = W.rearrange("(k p) n -> p k n", p=P)
    blocks = []
    for a, m in spans(n, width):
        for k0, kn in spans(kc, min(KD, 1024 // m)):
            blocks.append(([(lambda buf: buf, src[:, k0:k0 + kn, start + a:start + a + m])],
                           [c for _, c in spans(m, P)], list(range(k0, k0 + kn))))
    return blocks


def split_products(pe, out, parts, first=True, last=True):
    for j, (sh, sl, mh, ml) in enumerate(parts):
        pe.matmul(out, sh, mh, start=(first and j == 0), stop=False)
        pe.matmul(out, sh, ml, start=False, stop=False)
        ins = pe.matmul(out, sl, mh, start=False, stop=(last and j == len(parts) - 1))
    return ins


def linear(nc, name, w, x, lo, T, evict, kc=KD, engines="va", raw=None, after=None, before=None):
    b0, b1 = w.ranges[name]
    steps, n0 = [], 0
    for b in range(b0, b1):
        _, widths, ks = w.blocks[b]
        steps += [(b, i, n0 + i) for i in range(len(widths))]
        if ks[-1] == kc - 1:
            n0 += len(widths)
    done = {n: s + 1 for s, (_, _, n) in enumerate(steps)}
    count = {b: s + 1 for s, (b, _, _) in enumerate(steps)}
    finishes = {b: sorted(n for n in done if steps[done[n] - 1][0] == b) for b in range(b0, b1)}

    def stored_by(n):
        letter = engines[n % len(engines)]
        return letter, sum(engines[m % len(engines)] == letter for m in range(n + 1))

    with Stage(nc, name) as st:
        banks = -(-T // BANK)
        slots = 8 // banks
        ps = [st.ps(f"acc{i}", [P, banks * BANK]) for i in range(slots)]
        product_done, x_high, x_split = st.sem("product_done"), st.sem("x_high"), st.sem("x_split")
        stored = {"v": st.sem("stored_v"), "a": st.sem("stored_a")}
        followed, own = st.sem("followed"), st.sem("own")
        block = st.block()

        @block.sync
        def _(sp):
            w.load_stage(sp, name)

        @block.tensor
        def _(pe):
            for b, i, n in steps:
                ks, m = w.blocks[b][2], w.blocks[b][1][i]
                if i == 0:
                    pe.wait_ge(w.split_done, b + 1)
                if b == b0 and i == 0 and raw is not None:
                    pe.wait_ge(x_split, kc)
                if n >= slots and ks[0] == 0:
                    letter, times = stored_by(n - slots)
                    pe.wait_ge(stored[letter], times)
                high, low = w.view(w.high[b % 2], b), w.view(w.low[b % 2], b)
                cols = slice(i * P, i * P + m)
                for t0, tn in spans(T, BANK):
                    ins = split_products(pe, ps[n % slots][0:m, t0:t0 + tn], [
                        (high[:, j, cols], low[:, j, cols], x(k)[:, t0:t0 + tn], lo(k)[:, t0:t0 + tn])
                        for j, k in enumerate(ks)], first=(ks[0] == 0), last=(ks[-1] == kc - 1))
                ins.then_inc(product_done, 1)

        def evictions(engine, letter, b):
            for n in finishes[b]:
                if engines[n % len(engines)] == letter:
                    engine.wait_ge(product_done, done[n])
                    if after is not None and 2 <= n < after[1] + 2:
                        engine.wait_ge(followed, n - 1)
                    if before is not None:
                        before(engine, n, stored)
                    evict(engine, n, ps[n % slots]).then_inc(stored[letter], 1)

        @block.vector
        def _(dve):
            chain = Chain(dve, own)
            for k in range(kc if raw is not None else 0):
                dve.wait_ge(x_high, k + 1)
                dve.tensor_tensor(lo(k), raw(k), x(k).bitcast(F32), ALU.subtract).then_inc(x_split, 1)
            w.make_low(dve, b0)
            for b in range(b0, b1):
                if b + 1 < b1:
                    w.make_low(dve, b + 1)
                evictions(dve, "v", b)
                for n in finishes[b]:
                    if after is not None and n < after[1]:
                        dve.wait_ge(stored["a"], n + 1)
                        after[0](dve, chain, n).then_inc(followed, 1)

        @block.scalar
        def _(act):
            for k in range(kc if raw is not None else 0):
                act.copy(x(k), raw(k)).then_inc(x_high, 1)
            w.make_high(act, b0, b0, product_done, None)
            for b in range(b0, b1):
                if b + 1 < b1:
                    w.make_high(act, b + 1, b0, product_done, lambda b: count[b])
                evictions(act, "a", b)


def linear_tokens(nc, name, w, x, lo, tokens, evict, kc=KD):
    pieces = spans(tokens, P)
    nt = len(pieces)
    b0, b1 = w.ranges[name]
    group, g = {}, 0
    for b in range(b0, b1):
        group[b] = g
        g += w.blocks[b][2][-1] == kc - 1
    with Stage(nc, name) as st:
        ps = [st.ps(f"acc{i}", [P, BANK]) for i in range(8)]
        product_done = st.sem("product_done")
        stored = (st.sem("stored_v"), st.sem("stored_a"))
        block = st.block()

        @block.sync
        def _(sp):
            w.load_stage(sp, name)

        @block.tensor
        def _(pe):
            for b in range(b0, b1):
                _, widths, ks = w.blocks[b]
                pe.wait_ge(w.split_done, b + 1)
                high, low = w.view(w.high[b % 2], b), w.view(w.low[b % 2], b)
                for t, (t0, rows) in enumerate(pieces):
                    n = group[b] * nt + t
                    if n >= 8 and ks[0] == 0:
                        pe.wait_ge(stored[n % 2], (n - 8) // 2 + 1)
                    at = slice(t0, t0 + rows)
                    split_products(pe, ps[n % 8][0:rows, 0:sum(widths)], [
                        (x(k)[:, at], lo(k)[:, at], high[:, j, :], low[:, j, :]) for j, k in enumerate(ks)],
                        first=(ks[0] == 0), last=(ks[-1] == kc - 1)).then_inc(product_done, 1)

        def evictions(engine, which, b):
            if w.blocks[b][2][-1] == kc - 1:
                for t in range(nt):
                    n = group[b] * nt + t
                    if n % 2 == which:
                        engine.wait_ge(product_done, nt * (b - b0) + t + 1)
                        evict(engine, group[b], t, ps[n % 8]).then_inc(stored[which], 1)

        @block.vector
        def _(dve):
            w.make_low(dve, b0)
            for b in range(b0, b1):
                if b + 1 < b1:
                    w.make_low(dve, b + 1)
                evictions(dve, 0, b)

        @block.scalar
        def _(act):
            w.make_high(act, b0, b0, product_done, None)
            for b in range(b0, b1):
                if b + 1 < b1:
                    w.make_high(act, b + 1, b0, product_done, lambda b: nt * (b - b0 + 1))
                evictions(act, 1, b)


def copy_on(engine, nc, out, in_, scale=None):
    if engine is nc.vector or engine.engine == nc.vector.engine:
        if scale is None:
            return engine.tensor_copy(out, in_)
        return engine.tensor_scalar(out, in_, scale, None, ALU.mult)
    if scale is None:
        return engine.copy(out, in_)
    return engine.activation(out, in_, ACT.Copy, scale=scale)


def norm(nc, name, x, T, gain, ones, out=None, split=None, kc=KD, width=D, shift=None, residual=None, half=1.0,
         scratch=None):
    with Stage(nc, name) as st:
        rs = st.sb("rstd", [P, T])
        sq = scratch or st.sb("squares", [P, kc, T])
        ps = st.ps("sum", [P, -(-T // BANK) * BANK])
        squared, summed, rooted = st.sem("squared"), st.sem("summed"), st.sem("rooted")
        with_eps = st.sem("with_eps")
        scaled, high_done, own = st.sem("scaled"), st.sem("high_done"), st.sem("own")
        block = st.block()

        @block.scalar
        def _(act):
            for k in range(kc):
                act.activation(sq[:, k, :], x(k), ACT.Square, scale=float(width) ** -0.5).then_inc(squared, 1)
            act.wait_ge(with_eps, 1)
            act.activation(rs[:], rs[:], ACT.Sqrt).then_inc(rooted, 1)
            if split is not None:
                for k in range(kc):
                    act.wait_ge(scaled, k + 1)
                    if shift is None:
                        act.copy(split[0](k), sq[:, k, :]).then_inc(high_done, 1)
                    else:
                        act.activation(split[0](k), sq[:, k, :], ACT.Identity, bias=shift(k)).then_inc(high_done, 1)

        @block.tensor
        def _(pe):
            for t0, tn in spans(T, BANK):
                for k in range(kc):
                    if t0 == 0:
                        pe.wait_ge(squared, k + 1)
                    ins = pe.matmul(ps[:, t0:t0 + tn], ones, sq[:, k, t0:t0 + tn],
                                    start=(k == 0), stop=(k == kc - 1))
            ins.then_inc(summed, 1)

        @block.vector
        def _(dve):
            chain = Chain(dve, own)
            dve.wait_ge(summed, 1)
            dve.tensor_scalar(rs[:], ps[:, 0:T], EPS, None, ALU.add).then_inc(with_eps, 1)
            dve.wait_ge(rooted, 1)
            chain.link(dve.reciprocal(rs[:], rs[:]))
            for k in range(kc):
                dst = sq[:, k, :] if out is None else out(k)
                ins = dve.scalar_tensor_tensor(out=dst, in0=x(k), scalar=gain(k), in1=rs[:],
                                               op0=ALU.mult, op1=ALU.mult)
                if residual is not None:
                    chain.link(ins)
                    dve.scalar_tensor_tensor(out=residual(k), in0=dst, scalar=half, in1=residual(k),
                                             op0=ALU.mult, op1=ALU.add)
                else:
                    ins.then_inc(scaled, 1)
            if split is not None:
                for k in range(kc):
                    dve.wait_ge(high_done, k + 1)
                    high = split[0](k).bitcast(F32)
                    if shift is None:
                        dve.tensor_tensor(split[1](k), sq[:, k, :], high, ALU.subtract)
                    else:
                        dve.scalar_tensor_tensor(out=split[1](k), in0=sq[:, k, :], scalar=shift(k), in1=high,
                                                 op0=ALU.add, op1=ALU.subtract)
def adaln(nc, w, cond, layers, ident):
    with ExitStack() as keep:
        rows = keep.enter_context(nc.sbuf_tensor("adaln_rows", [2, len(layers) * 3 * D], F32))
        high, low = (keep.enter_context(nc.sbuf_tensor("adaln_cond_" + n, [P, KD, 2], F32R)) for n in ("high", "low"))
        with Stage(nc, "adaln_silu") as st:
            silu = st.sb("silu", [P, KD, 2])
            silu_done, high_done = st.sem("silu_done"), st.sem("high_done")
            block = st.block()

            @block.scalar
            def _(act):
                act.activation(silu[:], cond, ACT.Silu).then_inc(silu_done, 1)
                act.wait_ge(silu_done, 1)
                act.copy(high[:], silu[:]).then_inc(high_done, 1)

            @block.vector
            def _(dve):
                dve.wait_ge(high_done, 1)
                dve.tensor_tensor(low[:], silu[:], high[:].bitcast(F32), ALU.subtract)

        linear_tokens(nc, "adaln", w, lambda k: high[:, k, :], lambda k: low[:, k, :], 2,
                      lambda e, g, t, ps: copy_on(e, nc, rows[:, BANK * g:BANK * g + BANK], ps[0:2, :]))
        with Stage(nc, "adaln_turn") as st:
            ps = st.ps("m", [P, len(layers), 24, 2])
            turned, own = st.sem("turned"), st.sem("own")
            block = st.block()

            @block.tensor
            def _(pe):
                for i in range(len(layers)):
                    for n in range(24):
                        at = 3 * D * i + P * n
                        ins = pe.transpose(ps[:, i, n, :], rows[:, at:at + P], ident[0:2, 0:2])
                ins.then_inc(turned, 1)

            @block.vector
            def _(dve):
                chain = Chain(dve, own)
                dve.wait_ge(turned, 1)
                for i, (bias, gain, mod, gs) in enumerate(layers):
                    for j in range(2):
                        chain.link(dve.tensor_tensor(mod[:, :, j], ps[:, i, :, j], bias, ALU.add))
                        chain.link(dve.tensor_scalar(gs[:, :, j], mod[:, KD:2 * KD, j], 1.0, None, ALU.add))
                        chain.link(dve.tensor_tensor(gs[:, :, j], gs[:, :, j], gain, ALU.mult))


def head_norm(nc, name, chunks, gains, group, rope=None):
    n, T = len(chunks), chunks[0].shape[1]
    with Stage(nc, name) as st:
        sq = [st.sb(f"sq{i}", [P, T]) for i in range(2)]
        rs = [st.sb(f"rs{i}", [P, T]) for i in range(2)]
        ps = [st.ps(f"sum{i}", [P, -(-T // BANK) * BANK]) for i in range(2)]
        turned = [st.ps(f"turned{i}", [P, BANK]) for i in range(2)]
        tmp = [st.sb(f"tmp{i}", [P, S]) for i in range(2)]
        squared, summed, with_eps, rooted = (st.sem(x) for x in ("squared", "summed", "with_eps", "rooted"))
        normed, swapped, done, own = (st.sem(x) for x in ("normed", "swapped", "done", "own"))
        block = st.block()

        @block.scalar
        def _(act):
            for i in range(n):
                if i >= 2:
                    act.wait_ge(summed, i - 1)
                act.activation(sq[i % 2][:], chunks[i], ACT.Square).then_inc(squared, 1)
                act.wait_ge(with_eps, i + 1)
                act.activation(rs[i % 2][:], rs[i % 2][:], ACT.Sqrt).then_inc(rooted, 1)

        @block.tensor
        def _(pe):
            for i in range(n):
                pe.wait_ge(squared, i + 1)
                if i >= 2:
                    pe.wait_ge(with_eps, i - 1)
                for t0, tn in spans(T, BANK):
                    ins = pe.matmul(ps[i % 2][:, t0:t0 + tn], group, sq[i % 2][:, t0:t0 + tn], start=True, stop=True)
                ins.then_inc(summed, 1)
                if rope is not None:
                    pe.wait_ge(normed, i + 1)
                    pe.matmul(turned[i % 2][:], rope[2], chunks[i][:, 0:S], start=True, stop=True).then_inc(swapped, 1)

        @block.vector
        def _(dve):
            chain = Chain(dve, own)
            for i in range(n):
                dve.wait_ge(summed, i + 1)
                dve.tensor_scalar(rs[i % 2][:], ps[i % 2][:, 0:T], EPS, None, ALU.add).then_inc(with_eps, 1)
                dve.wait_ge(rooted, i + 1)
                chain.link(dve.reciprocal(rs[i % 2][:], rs[i % 2][:]))
                dve.scalar_tensor_tensor(out=chunks[i], in0=chunks[i], scalar=gains[i], in1=rs[i % 2][:],
                                         op0=ALU.mult, op1=ALU.mult).then_inc(normed, 1)
                if rope is not None:
                    dve.wait_ge(swapped, i + 1)
                    chain.link(dve.tensor_tensor(tmp[i % 2][:], turned[i % 2][:], rope[1], ALU.mult))
                    chain.link(dve.tensor_tensor(chunks[i][:, 0:S], chunks[i][:, 0:S], rope[0], ALU.mult))
                    chain.link(dve.tensor_tensor(chunks[i][:, 0:S], chunks[i][:, 0:S], tmp[i % 2][:], ALU.add))


def attention(nc, name, units, ident):
    n_units = len(units)
    with Stage(nc, name) as st:
        prob = [st.sb(f"prob{i}", [P, 1024]) for i in range(2)]
        prob_t = [st.sb(f"prob_t{i}", [P, 6, P]) for i in range(2)]
        stat = st.sb("stat", [P, 3, 8])
        score = [st.ps(f"score{i}", [P, 1024]) for i in range(2)]
        turned = st.ps("turned", [P, 1024])
        out_ps = [st.ps(f"out{i}", [P, BANK]) for i in range(2)]
        scored, maxed, exped, transposed, copied, weighed, stored, own = (
            st.sem(x) for x in ("scored", "maxed", "exped", "transposed", "copied", "weighed", "stored", "own"))
        block = st.block()

        def widths(u):
            return [k.shape[1] for k in u["keys"]]

        def tiles(u):
            return spans(sum(widths(u)), P)

        @block.tensor
        def _(pe):
            def scores(i):
                u = units[i]
                if i >= 2:
                    pe.wait_ge(exped, i - 1)
                at = 0
                for k in u["keys"]:
                    ins = pe.matmul(score[i % 2][:, at:at + k.shape[1]], u["q"], k, start=True, stop=True)
                    at += BANK if at + k.shape[1] < sum(widths(u)) else 0
                ins.then_inc(scored, 1)

            def transposes(i):
                pe.wait_ge(exped, i + 1)
                if i >= 1:
                    pe.wait_ge(copied, i)
                for j, (a, m) in enumerate(tiles(units[i])):
                    ins = pe.transpose(turned[0:m, j * P:(j + 1) * P], prob[i % 2][:, a:a + m], ident)
                ins.then_inc(transposed, 1)

            def weigh(i):
                pe.wait_ge(copied, i + 1)
                if i >= 2:
                    pe.wait_ge(stored, i - 1)
                u = units[i]
                last = len(tiles(u)) - 1
                for j, (a, m) in enumerate(tiles(u)):
                    ins = pe.matmul(out_ps[i % 2][:, 0:u["out"].shape[1]], prob_t[i % 2][0:m, j, :],
                                    u["values"][j], start=(j == 0), stop=(j == last))
                ins.then_inc(weighed, 1)

            for i in range(n_units + 2):
                if i < n_units:
                    scores(i)
                if 1 <= i <= n_units:
                    transposes(i - 1)
                if i >= 2:
                    weigh(i - 2)

        @block.vector
        def _(dve):
            chain = Chain(dve, own)

            def maxima(i):
                u, s = units[i], stat[:, i % 3, :]
                dve.wait_ge(scored, i + 1)
                if u["bias"] is None:
                    n = sum(widths(u))
                    dve.tensor_reduce(s[:, 0:1], score[i % 2][:, 0:n], AX.X, ALU.max, negate=True).then_inc(maxed, 1)
                    return
                if i >= 2:
                    dve.wait_ge(transposed, i - 1)
                n = widths(u)[0]
                chain.link(dve.tensor_tensor_reduce(out=prob[i % 2][:, 0:n], in0=score[i % 2][:, 0:n], in1=u["bias"],
                                                    scale=1.0, scalar=-3e38, op0=ALU.add, op1=ALU.max,
                                                    accum_out=s[:, 1:2]))
                if len(u["keys"]) == 2:
                    m = widths(u)[1]
                    chain.link(dve.tensor_reduce(s[:, 2:3], score[i % 2][:, BANK:BANK + m], AX.X, ALU.max))
                    dve.tensor_scalar(s[:, 0:1], s[:, 1:2], s[:, 2:3], -1.0, ALU.max, ALU.mult).then_inc(maxed, 1)
                else:
                    dve.tensor_scalar(s[:, 0:1], s[:, 1:2], -1.0, None, ALU.mult).then_inc(maxed, 1)

            def store(i):
                u, s = units[i], stat[:, i % 3, :]
                dve.wait_ge(weighed, i + 1)
                total = s[:, 3:4]
                if u["bias"] is not None and len(u["keys"]) == 2:
                    chain.link(dve.tensor_tensor(s[:, 5:6], s[:, 3:4], s[:, 4:5], ALU.add))
                    total = s[:, 5:6]
                chain.link(dve.reciprocal(s[:, 6:7], total))
                if u.get("rows") is None:
                    dve.tensor_scalar(u["out"], out_ps[i % 2][:, 0:u["out"].shape[1]], s[:, 6:7], None,
                                      ALU.mult).then_inc(stored, 1)
                else:
                    dve.tensor_scalar(u["out"], out_ps[i % 2][:, 0:u["out"].shape[1]], s[:, 6:7], u["rows"],
                                      ALU.mult, ALU.mult).then_inc(stored, 1)

            for i in range(n_units + 2):
                if i < n_units:
                    if i >= 3:
                        dve.wait_ge(stored, i - 2)
                    maxima(i)
                if i >= 2:
                    store(i - 2)

        @block.scalar
        def _(act):
            def exponentials(i):
                u, s = units[i], stat[:, i % 3, :]
                act.wait_ge(maxed, i + 1)
                if u["bias"] is None:
                    if i >= 2:
                        act.wait_ge(transposed, i - 1)
                    n = sum(widths(u))
                    act.activation(prob[i % 2][:, 0:n], score[i % 2][:, 0:n], ACT.Exp, bias=s[:, 0:1],
                                   accum_out=s[:, 3:4]).then_inc(exped, 1)
                    return
                n = widths(u)[0]
                ins = act.activation(prob[i % 2][:, 0:n], prob[i % 2][:, 0:n], ACT.Exp, bias=s[:, 0:1],
                                     accum_out=s[:, 3:4])
                if len(u["keys"]) == 2:
                    m = widths(u)[1]
                    ins = act.activation(prob[i % 2][:, n:n + m], score[i % 2][:, BANK:BANK + m], ACT.Exp,
                                         bias=s[:, 0:1], accum_out=s[:, 4:5])
                ins.then_inc(exped, 1)

            def copies(i):
                act.wait_ge(transposed, i + 1)
                if i >= 2:
                    act.wait_ge(weighed, i - 1)
                ts = tiles(units[i])
                full = len([m for _, m in ts if m == P])
                if full:
                    ins = act.copy(prob_t[i % 2][:, 0:full, :].rearrange("p j q -> p (j q)"), turned[:, 0:full * P])
                if full < len(ts):
                    m = ts[-1][1]
                    ins = act.copy(prob_t[i % 2][0:m, full, :], turned[0:m, full * P:(full + 1) * P])
                ins.then_inc(copied, 1)

            for i in range(n_units + 1):
                if i < n_units:
                    exponentials(i)
                if i >= 1:
                    copies(i - 1)


def to_features(nc, name, jobs, ident):
    n = len(jobs)
    with Stage(nc, name) as st:
        ps = [st.ps(f"turned{i}", [P, 1024]) for i in range(3)]
        turned, stored = st.sem("turned"), st.sem("stored")
        block = st.block()

        @block.tensor
        def _(pe):
            for i, (pieces, _, _) in enumerate(jobs):
                if i >= 3:
                    pe.wait_ge(stored, i - 2)
                for j, piece in enumerate(pieces):
                    ins = pe.transpose(ps[i % 3][:, j * P:(j + 1) * P], piece, ident)
                ins.then_inc(turned, 1)

        @block.vector
        def _(dve):
            for i, (pieces, factor, out) in enumerate(jobs):
                dve.wait_ge(turned, i + 1)
                src = ps[i % 3][:, 0:len(pieces) * P]
                if factor is None:
                    dve.tensor_copy(out, src).then_inc(stored, 1)
                else:
                    dve.tensor_tensor(out, src, factor, ALU.mult).then_inc(stored, 1)


def in_place(nc, name, parts, func):
    with Stage(nc, name) as st:
        block = st.block()

        @block.scalar
        def _(act):
            for part in parts:
                out, src = part if isinstance(part, tuple) else (part, part)
                act.activation(out, src, func)


def na_bias(nc, name, rpb, table, mask, pad_dram, tiles=14):
    heads, rows, cols = 8, 15, 31
    wide = 127
    with Stage(nc, name) as st:
        padded = st.sb("padded", [heads * rows, wide])
        cleared, landed, stored = st.sem("cleared"), st.sem("landed"), st.sem("stored")
        own = st.sem("own")
        block = st.block()

        @block.vector
        def _(dve):
            dve.memset(padded[:], 0.0).then_inc(cleared, 1)
            dve.wait_ge(stored, 16 * (1 + 2 * heads))
            for h in range(heads):
                dve.tensor_tensor(table[:, h], table[:, h],
                                  mask.rearrange("p (a c) -> p a c", a=1).broadcast_to([P, tiles, 64]), ALU.add)

        @block.sync
        def _(sp):
            sp.wait_ge(cleared, 1)
            sp.dma_start(padded[:, 48:79], rpb.rearrange("h r c -> (h r) c")).then_inc(landed, 16)
            sp.wait_ge(landed, 16)
            sp.dma_start(pad_dram.rearrange("c r w -> r c w"),
                         padded[:].rearrange("r (a w) -> r a w", a=1).broadcast_to([heads * rows, 64, wide])
                         ).then_inc(stored, 16)
            sp.wait_ge(stored, 16)
            for h in range(heads):
                for half in range(2):
                    src = bass.AP(tensor=pad_dram.tensor, offset=(h * rows + 1 - half) * wide + 63,
                                  ap=[[heads * rows * wide - 1, 64], [wide, tiles], [1, 64]])
                    sp.dma_start(table[64 * half:64 * half + 64, h], src).then_inc(stored, 16)


def pair_blocks(wv, at, i0, kc=KD):
    def load(k0, i, s):
        c = P * (i - i0) + 64 * s
        return (lambda buf: buf[:, :, c:c + 64], wv[:, k0:k0 + 4, at + 256 * s + 64 * i:at + 256 * s + 64 * i + 64])

    return [([load(k0, i, s) for i in (i0, i0 + 1) for s in range(2)], [P, P], list(range(k0, k0 + 4)))
            for k0 in (0, 4)]


def attn_weights(d):
    W = d["attn_w_in"]
    wv = W.rearrange("(k p) n -> p k n", p=P)
    return {"attn_in": weight_blocks(W, 0, 1024) + weight_blocks(W, 1536, 512) + pair_blocks(wv, 2048, 0)
            + pair_blocks(wv, 2048, 2) + weight_blocks(W, 2816, 512) + weight_blocks(W, 2560, 128),
            "attn_v": weight_blocks(W, 1024, 512, width=512) + weight_blocks(W, 2688, 128),
            "attn_out": weight_blocks(d["attn_w_out"], 0, D)}


def attn_layer(nc, d, w, c, x, ctx, mod, gs):
    with ExitStack() as keep:
        def sb(name, shape):
            return keep.enter_context(nc.sbuf_tensor("attn_" + name, shape, F32))

        qa, ka, ga, qb, gb = (sb(n, [P, 4, TT]) for n in ("qa", "ka", "ga", "qb", "gb"))
        kb = sb("kb", [P, TT])
        va, vb = sb("va", [P, 6, 512]), sb("vb", [P, 6, P])
        with ExitStack() as inner:
            h = [inner.enter_context(nc.sbuf_tensor("attn_h_" + part, [P, KD, TT], F32R)) for part in ("high", "low")]
            norm(nc, "attn_norm_x", lambda k: x[:, k, :], S, lambda k: gs[:, k, 0:1], c["ones"],
                 split=[lambda k, t=t: t[:, k, 0:S] for t in h], shift=lambda k: mod[:, k, 0:1])
            norm(nc, "attn_norm_ctx", lambda k: ctx[:, k, :], LC, lambda k: gs[:, k, 1:2], c["ones"],
                 split=[lambda k, t=t: t[:, k, S:TT] for t in h], shift=lambda k: mod[:, k, 1:2])
            h = [lambda k, t=t: t[:, k, :] for t in h]
            outs = [(t[:, i, :], 0.125 if t is qa else None) for t in (qa, ka, ga, qb, gb) for i in range(4)]
            outs.append((kb[:], None))
            linear(nc, "attn_in", w, *h, TT, lambda e, n, ps: copy_on(e, nc, outs[n][0], ps[:, 0:TT], outs[n][1]))
            linear_tokens(nc, "attn_v", w, *h, TT,
                          lambda e, g, t, ps: copy_on(e, nc, vb[:, t, :] if g else va[:, t, :],
                                                      ps[:, 0:P] if g else ps[:, 0:512]))
        with ExitStack() as inner:
            rope = inner.enter_context(nc.sbuf_tensor("attn_rope", [P, 2, S], F32))
            load(nc, "rope_load", [(rope[:, 0, :], d["c_cos"]), (rope[:, 1, :], d["c_sin"])])
            head_norm(nc, "attn_head_norm", [qb[:, i, :] for i in range(4)] + [kb[:]],
                      [c["q_gain"]] * 4 + [c["k_gain"]], c["group64"], (rope[:, 0, :], rope[:, 1, :], c["swap"]))
        with ExitStack() as inner:
            oa = inner.enter_context(nc.sbuf_tensor("attn_oa", [P, 6, 512], F32))
            ob = inner.enter_context(nc.sbuf_tensor("attn_ob", [P, 6, 512], F32))
            with ExitStack() as tabled:
                table = tabled.enter_context(nc.sbuf_tensor("attn_table", [P, 8, 14, 64], F32))
                na_bias(nc, "attn_bias", d["na_rpb"], table, c["window"], d["s_rpb"])
                units = []
                for t in range(6):
                    q_at = slice(t * P, (t + 1) * P)
                    for h in range(8):
                        a, b = 64 * (h % 2), 64 * (h // 4)
                        first = 4 if t >= 4 else 0
                        local = [] if t >= 4 else [ka[a:a + 64, h // 2, 0:S]]
                        units.append(dict(
                            q=qa[a:a + 64, h // 2, q_at], keys=local + [ka[a:a + 64, h // 2, S:TT]],
                            bias=None if t >= 4 else
                            table[:, h, 6 - 2 * t:14 - 2 * t, :].rearrange("p r c -> p (r c)"),
                            values=[va[:, j, 64 * h:64 * h + 64] for j in range(first, 6)],
                            out=oa[:, t, 64 * h:64 * h + 64]))
                        grouped = [] if t >= 4 else [kb[b:b + 64, 0:S]]
                        units.append(dict(
                            q=qb[b:b + 64, h % 4, q_at], keys=grouped + [kb[b:b + 64, S:TT]], bias=None,
                            values=[vb[:, j, b:b + 64] for j in range(first, 6)],
                            out=ob[:, t, 64 * h:64 * h + 64]))
                attention(nc, "attn", units, c["ident"])
            in_place(nc, "attn_gates", [g[:, i, :] for g in (ga, gb) for i in range(4)], ACT.Silu)
            to_features(nc, "attn_turn", [([o[:, t, i * P:(i + 1) * P] for t in range(6)], g[:, i, :], (qa, qb)[n][:, i, :])
                                          for n, (o, g) in enumerate(((oa, ga), (ob, gb))) for i in range(4)], c["ident"])

        gated_out(nc, "attn_out", w, lambda k: (qa, qb)[k // 4][:, k % 4, :], x, ctx, mod)


def gated_out(nc, name, w, y, x, ctx, mod):
    T = TT if ctx is not None else S
    with ExitStack() as keep:
        y2 = [keep.enter_context(nc.sbuf_tensor(f"{name}_y_{part}", [P, KD, T], F32R)) for part in ("high", "low")]

        def evict(dve, n, ps):
            ins = dve.scalar_tensor_tensor(out=x[:, n, :], in0=ps[:, 0:S], scalar=mod[:, 16 + n, 0:1],
                                           in1=x[:, n, :], op0=ALU.mult, op1=ALU.add)
            if ctx is not None:
                ins = dve.scalar_tensor_tensor(out=ctx[:, n, :], in0=ps[:, S:TT], scalar=mod[:, 16 + n, 1:2],
                                               in1=ctx[:, n, :], op0=ALU.mult, op1=ALU.add)
            return ins

        linear(nc, name, w, *(lambda k, t=t: t[:, k, :] for t in y2), T, evict, engines="v", raw=y)
CH = 64
PAIRS = 4
PADDED = TT + 4


def rwkv_features(nc, name, d, c, v, us, bonus, ends):
    with Stage(nc, name) as st:
        up = st.sb("up", [P, 4, 512])
        kk = st.sb("kk", [P, 4, TT])
        restart = st.sb("restart", [P, TT])
        sq, rs = st.sb("sq", [P, TT]), st.sb("rs", [P, TT])
        not_ka = st.sb("not_ka", [P, 4])
        gate_ps = [st.ps(f"gate{i}", [P, 1024]) for i in range(4)]
        sw, sa = ([st.sb(f"{x}{i}", [P, TT]) for i in range(2)] for x in ("sw", "sa"))
        lsum = st.sb("lsum", [P, TT])
        before, upto, inverse = st.sb("before", [P, TT]), st.sb("upto", [P, TT]), st.sb("inverse", [P, TT])
        kd = st.sb("kd", [P, TT])
        out = [[st.sb(f"out{j}_{i}", [P, TT]) for j in range(4)] for i in range(2)]
        (cleared, landed, squared, summed, with_eps, rooted, tanhed, gates_done, sigmoids, summed_log,
         exps, features, own, kk_done) = (st.sem(x) for x in (
             "cleared", "landed", "squared", "summed", "with_eps", "rooted", "tanhed", "gates_done", "sigmoids",
             "summed_log", "exps", "features", "own", "kk_done"))
        saved = [st.sem(f"saved{i}") for i in range(2)]
        block = st.block()
        lora = us[12]

        @block.gpsimd
        def _(pool):
            pool.memset(up[:], 0.0).then_inc(cleared, 1)
            pool.memset(restart[:], 1.0).then_inc(cleared, 1)
            pool.wait_ge(cleared, 2)
            pool.memset(restart[:].rearrange("p (c t) -> p c t", t=CH)[:, :, 0:1], 0.0).then_inc(cleared, 1)

        @block.sync
        def _(sp):
            sp.wait_ge(cleared, 1)
            for i, w in enumerate((d["rwkv_w_up"][0], d["rwkv_w_up"][1], d["rwkv_a_up"][0], d["rwkv_a_up"][1])):
                sp.dma_start(up[32 * i:32 * i + 32, i, :], w).then_inc(landed, 16)
            for n in range(8):
                sp.wait_ge(features, n + 1)
                for j in range(4):
                    sp.dma_start(d["s_feat"][n // 4, j, (n % 4) * P:(n % 4) * P + P, :],
                                 out[n % 2][j][:]).then_inc(saved[n % 2], 16)
            for s in saved:
                sp.wait_ge(s, 16 * 16)

        @block.tensor
        def _(pe):
            pe.wait_ge(landed, 64)
            for i in range(4):
                pe.wait_ge(squared, i + 1)
                for t0, tn in spans(TT, BANK):
                    ins = pe.matmul(gate_ps[3][:, t0:t0 + tn], c["heads2"], sq[:, t0:t0 + tn], start=True, stop=True)
                ins.then_inc(summed, 1)
            pe.wait_ge(tanhed, 1)
            pe.wait_ge(with_eps, 4)
            for n in range(8):
                dr, i = n // 4, n % 4
                if n >= 2:
                    pe.wait_ge(sigmoids, 2 * (n - 1))
                for g in range(2):
                    for t0, tn in spans(TT, BANK):
                        ins = pe.matmul(gate_ps[2 * (n % 2) + g][:, t0:t0 + tn], up[:, 2 * g + dr, i * P:(i + 1) * P],
                                        lora[:, t0:t0 + tn], start=True, stop=True)
                ins.then_inc(gates_done, 1)

        @block.scalar
        def _(act):
            for i in range(4):
                if i:
                    act.wait_ge(summed, i)
                act.activation(sq[:], us[4 + i], ACT.Square, scale=v("rwkv_k_k", i, 1)).then_inc(squared, 1)
                act.wait_ge(with_eps, i + 1)
                act.activation(rs[:], rs[:], ACT.Sqrt).then_inc(rooted, 1)
            act.activation(lora[0:64, :], lora[0:64, :], ACT.Tanh).then_inc(tanhed, 1)
            for n in range(8):
                dr, i = n // 4, n % 4
                act.wait_ge(gates_done, n + 1)
                if n >= 2:
                    act.wait_ge(features, n - 1)
                act.activation(sw[n % 2][:], gate_ps[2 * (n % 2)][:, 0:TT], ACT.Sigmoid,
                               bias=v("w0", 4 * dr + i, 1)).then_inc(sigmoids, 1)
                act.activation(sa[n % 2][:], gate_ps[2 * (n % 2) + 1][:, 0:TT], ACT.Sigmoid,
                               bias=v("a0", 4 * dr + i, 1)).then_inc(sigmoids, 1)
                act.wait_ge(summed_log, n + 1)
                act.activation(upto[:], lsum[:], ACT.Exp)
                act.activation(inverse[:], lsum[:], ACT.Exp, scale=-1.0)
                act.activation(before[:], before[:], ACT.Exp).then_inc(exps, 1)

        @block.vector
        def _(dve):
            chain = Chain(dve, own)
            chain.link(dve.tensor_scalar(not_ka[:], v("rwkv_k_a"), -1.0, 1.0, ALU.mult, ALU.add))
            for i in range(4):
                dve.wait_ge(summed, i + 1)
                if i:
                    dve.wait_ge(kk_done, i)
                dve.tensor_scalar(rs[:], gate_ps[3][:, 0:TT], 1e-12, None, ALU.add).then_inc(with_eps, 1)
                dve.wait_ge(rooted, i + 1)
                chain.link(dve.reciprocal(rs[:], rs[:]))
                dve.scalar_tensor_tensor(out=kk[:, i, :], in0=us[4 + i], scalar=v("rwkv_k_k", i, 1), in1=rs[:],
                                         op0=ALU.mult, op1=ALU.mult).then_inc(kk_done, 1)
            dve.wait_ge(cleared, 3)
            dve.wait_ge(kk_done, 4)
            for n in range(8):
                dr, i = n // 4, n % 4
                a, o = sa[n % 2], out[n % 2]
                dve.wait_ge(sigmoids, 2 * (n + 1))
                chain.link(dve.tensor_scalar(sw[n % 2][:], sw[n % 2][:], -float(np.exp(-0.5)), None, ALU.mult))
                chain.link(dve.tensor_tensor_scan(lsum[:], restart[:], sw[n % 2][:], 0.0, ALU.mult, ALU.add))
                if dr == 0:
                    dve.tensor_tensor(before[:], lsum[:], sw[n % 2][:], ALU.subtract).then_inc(summed_log, 1)
                else:
                    chunks = lsum[:].rearrange("p (c t) -> p c t", t=CH)
                    chain.link(dve.tensor_tensor(before[:].rearrange("p (c t) -> p c t", t=CH),
                                                 chunks[:, :, CH - 1:CH].broadcast_to([P, TT // CH, CH]), chunks,
                                                 ALU.subtract))
                    dve.tensor_tensor(lsum[:], before[:], sw[n % 2][:], ALU.add).then_inc(summed_log, 1)
                chain.link(dve.tensor_scalar(kd[:], a[:], v("rwkv_k_a", i, 1), not_ka[:, i:i + 1], ALU.mult, ALU.add))
                chain.link(dve.tensor_tensor(kd[:], kd[:], us[4 + i], ALU.mult))
                if dr == 0:
                    chain.link(dve.tensor_copy(bonus[:, i, :], kd[:, 0:S]))
                else:
                    chain.link(dve.tensor_tensor(bonus[:, i, :], bonus[:, i, :], kd[:, 0:S], ALU.add))
                    chain.link(dve.scalar_tensor_tensor(out=bonus[:, i, :], in0=bonus[:, i, :], scalar=0.5,
                                                        in1=us[i][:, 0:S], op0=ALU.mult, op1=ALU.mult))
                    chain.link(dve.tensor_scalar(bonus[:, i, :], bonus[:, i, :], v("r_k", i, 1), None, ALU.mult))
                chain.link(dve.tensor_tensor(a[:], a[:], kk[:, i, :], ALU.mult))
                if n >= 2:
                    dve.wait_ge(saved[n % 2], 64 * (n // 2))
                dve.wait_ge(exps, n + 1)
                chain.link(dve.tensor_tensor(o[0][:], kk[:, i, :], before[:], ALU.mult))
                chain.link(dve.tensor_tensor(o[1][:], us[i], upto[:], ALU.mult))
                chain.link(dve.tensor_tensor(o[2][:], a[:], inverse[:], ALU.mult))
                at = CH - 1 if dr == 0 else 0
                chain.link(dve.tensor_copy(ends[:, dr, i, :], upto[:].rearrange("p (c t) -> p c t", t=CH)[:, :, at]))
                dve.tensor_tensor(o[3][:], kd[:], inverse[:], ALU.mult).then_inc(features, 1)
                dve.wait_ge(features, n + 1)


HEADS_T = 8
TURN, GRAM, FLIP, POW2, POW4, POW8, TDIAG, OFF, Z1, Z2, Z3, LAY = range(12)
DVE_STEPS = (GRAM, FLIP, POW4, POW8, TDIAG, OFF, Z1, Z2, Z3)
ACT_STEPS = (TURN, FLIP, POW2, POW4, POW8, OFF, LAY)


def upto_step(steps, step, i, per=HEADS_T):
    return per * steps.index(step) + i + 1


def last_step(steps, step):
    return max(s for s in steps if s < step) if any(s < step for s in steps) else None


def rwkv_group(nc, name, d, c, state, value, ends, y, dr, tile):
    lat = tile < 4
    strict, incl = (c["strict_fwd"], c["incl_fwd"]) if dr == 0 else (c["strict_rev"], c["incl_rev"])
    with Stage(nc, name) as st:
        feat = st.sb("feat", [P, 4, PAIRS, P])
        tok = st.sb("tok", [P, PAIRS, 3, P])
        mask = st.sb("mask", [P, 2, P])
        off16 = st.sb("off16", [P, P])
        gram = st.sb("gram", [P, HEADS_T, 4, P])
        dn, en = st.sb("diag", [P, HEADS_T, P]), st.sb("off", [P, HEADS_T, P])
        dt, m = st.sb("diag_t", [P, HEADS_T, P]), st.sb("inv_t", [P, HEADS_T, P])
        p2, p4 = st.sb("pow2", [P, HEADS_T, 2, P]), st.sb("pow4", [P, HEADS_T, 2, P])
        p8, ft = st.sb("pow8", [P, HEADS_T, P]), st.sb("off_t", [P, HEADS_T, P])
        xs = st.sb("rhs", [P, 2, HEADS_T, CH])
        y1, z = (st.sb(n, [P, HEADS_T, 2, CH]) for n in ("y1", "z"))
        wt = st.sb("w_t", [P, PAIRS, P])
        san = st.sb("minus_sa", [P, PAIRS, P])
        ps = [st.ps(f"ps{i}", [P, BANK]) for i in range(8)]
        banks = 8
        (landed, made, pe_done, dve_done, act_done, pool_done, scan_pe, scan_dve, own) = (
            st.sem(x) for x in ("landed", "made", "pe_done", "dve_done", "act_done", "pool_done", "scan_pe",
                                "scan_dve", "own"))
        block = st.block()
        halves = (0, 1) if dr == 0 else (1, 0)
        at = tile * P

        @block.sync
        def _(sp):
            for j in range(4):
                sp.dma_start(feat[:, j], d["s_feat"][dr, j].rearrange("(i p) t -> p i t", p=P)[:, :, at:at + P]
                             ).then_inc(landed, 16)

        @block.tensor
        def _(pe):
            def order(step, i):
                n = step * HEADS_T + i
                for steps, sem in ((DVE_STEPS, dve_done), (ACT_STEPS, act_done)):
                    s = last_step(steps, step)
                    if s is not None:
                        pe.wait_ge(sem, upto_step(steps, s, i))
                return ps[n % banks]

            pe.wait_ge(landed, 64)
            for i in range(HEADS_T):
                b = order(TURN, i)
                pair = i // 2
                srcs = (0, 2) if i % 2 == 0 else (3,)
                for j, s in enumerate(srcs):
                    ins = pe.transpose(b[:, j * P:(j + 1) * P], feat[:, s, pair, :], c["ident"])
                ins.then_inc(pe_done, 1)
            for i in range(HEADS_T):
                b = order(GRAM, i)
                pair, r = i // 2, slice(CH * (i % 2), CH * (i % 2) + CH)
                for j in range(2):
                    ins = pe.matmul(b[:, 2 * j * P:(2 * j + 2) * P], feat[r, 2 + j, pair, :],
                                    feat[r, 0:2, pair, :], start=True, stop=True)
                ins.then_inc(pe_done, 1)
            for i in range(HEADS_T):
                b = order(FLIP, i)
                pe.transpose(b[:, 0:P], gram[:, i, 0, :], c["ident"])
                pe.matmul(b[:, P:P + CH], gram[:, i, 2, :], value[:, tile, CH * i:CH * i + CH],
                          start=True, stop=True).then_inc(pe_done, 1)
            for i in range(HEADS_T):
                b = order(POW2, i)
                pe.wait_ge(pool_done, i + 1)
                pe.matmul(b[:, 0:P], dt[:, i, :], dn[:, i, :], start=True, stop=True)
                pe.matmul(b[:, P:2 * P], dn[:, i, :], dt[:, i, :], start=True, stop=True).then_inc(pe_done, 1)
            for i in range(HEADS_T):
                b = order(POW4, i)
                pe.matmul(b[:, 0:P], p2[:, i, 1, :], p2[:, i, 0, :], start=True, stop=True)
                pe.matmul(b[:, P:2 * P], p2[:, i, 0, :], p2[:, i, 1, :], start=True, stop=True)
                pe.matmul(b[:, 2 * P:3 * P], p2[:, i, 0, :], m[:, i, :], start=True, stop=True).then_inc(pe_done, 1)
            for i in range(HEADS_T):
                b = order(POW8, i)
                pe.matmul(b[:, 0:P], p4[:, i, 1, :], p4[:, i, 0, :], start=True, stop=True)
                pe.matmul(b[:, P:2 * P], p4[:, i, 0, :], m[:, i, :], start=True, stop=True).then_inc(pe_done, 1)
            for i in range(HEADS_T):
                b = order(TDIAG, i)
                pe.matmul(b[:, 0:P], p8[:, i, :], m[:, i, :], start=True, stop=True).then_inc(pe_done, 1)
            for i in range(HEADS_T):
                b = order(OFF, i)
                pe.matmul(b[:, 0:P], en[:, i, :], m[:, i, :], start=True, stop=True)
                pe.matmul(b[:, P:2 * P], m[:, i, :], xs[:, :, i, :],
                          start=True, stop=True).then_inc(pe_done, 1)
            for step in (Z1, Z2, Z3):
                for i in range(HEADS_T):
                    b = order(step, i)
                    src = y1 if step == Z1 else z
                    pe.matmul(b[:, 0:P], ft[:, i, :], src[:, i].rearrange("p a b -> p (a b)"),
                              start=True, stop=True).then_inc(pe_done, 1)
            for i in range(PAIRS):
                b = order(LAY, 2 * i + 1)
                pe.transpose(b[:, 0:P], xs[:, 1, 2 * i:2 * i + 2, :].rearrange("p a b -> p (a b)"),
                             c["ident"]).then_inc(pe_done, 1)
            pe.wait_ge(act_done, upto_step(ACT_STEPS, LAY, PAIRS - 1))
            pe.wait_ge(dve_done, upto_step(DVE_STEPS, Z3, HEADS_T - 1))
            for k, hf in enumerate(halves):
                r = slice(CH * hf, CH * hf + CH)
                if k:
                    pe.wait_ge(scan_dve, 2)
                for i in range(PAIRS):
                    ins = pe.matmul(ps[0][r, i * P:(i + 1) * P], wt[:, i, r], state[:, i, :], start=True, stop=True)
                ins.then_inc(scan_pe, 1)
                if lat:
                    for i in range(PAIRS):
                        pe.matmul(ps[2 + hf][:, i * CH:(i + 1) * CH], state[:, i, :], feat[:, 1, i, r],
                                  start=True, stop=True)
                pe.wait_ge(scan_dve, 2 * k + 1)
                for i in range(PAIRS):
                    pe.matmul(ps[1][:, i * P:(i + 1) * P], tok[r, i, 2, :], value[r, tile, i * P:(i + 1) * P],
                              start=True, stop=False)
                    ins = pe.matmul(ps[1][:, i * P:(i + 1) * P], tok[r, i, 1, :], san[r, i, :], start=False, stop=True)
                ins.then_inc(scan_pe, 1)
            if lat:
                for i in range(HEADS_T):
                    r = slice(CH * (i % 2), CH * (i % 2) + CH)
                    cols = slice((i // 2) * P, (i // 2) * P + P)
                    pe.matmul(ps[4 + i % 2][r, cols], value[:, tile, CH * i:CH * i + CH], gram[:, i, 3, :],
                              start=True, stop=False)
                    ins = pe.matmul(ps[4 + i % 2][r, cols], san[:, i // 2, r], gram[:, i, 1, :],
                                    start=False, stop=True)
                ins.then_inc(scan_pe, 1)

        @block.gpsimd
        def _(pool):
            for j, mk in enumerate((strict, incl)):
                pool.tensor_copy(mask[:, j, :], mk)
            pool.tensor_scalar(off16[:], c["same16"], -1.0, 1.0, ALU.mult, ALU.add).then_inc(made, 1)
            pool.wait_ge(made, 1)
            for i in range(HEADS_T):
                pool.wait_ge(dve_done, upto_step(DVE_STEPS, GRAM, i))
                pool.wait_ge(act_done, upto_step(ACT_STEPS, TURN, i - i % 2 + 1))
                pool.tensor_tensor(dt[:, i, :], gram[:, i, 0, :], c["same16"], ALU.mult).then_inc(made, 1)
                pool.tensor_scalar(xs[:, 1, i, :], tok[:, i // 2, 0, CH * (i % 2):CH * (i % 2) + CH], -1.0, None,
                                   ALU.mult)
                pool.wait_ge(made, i + 2)
                pool.tensor_tensor(m[:, i, :], c["ident"], dt[:, i, :], ALU.subtract).then_inc(pool_done, 1)

        @block.vector
        def _(dve):
            def ready(step, i):
                dve.wait_ge(pe_done, step * HEADS_T + i + 1)
                return ps[(step * HEADS_T + i) % banks]

            dve.wait_ge(made, 1)
            for i in range(HEADS_T):
                b = ready(GRAM, i)
                dve.tensor_tensor(gram[:, i].rearrange("p (a b) t -> p a b t", a=2),
                                  b[:].rearrange("p (a b t) -> p a b t", a=2, b=2),
                                  bass.AP(tensor=mask[:].tensor, offset=mask[:].offset,
                                          ap=[list(mask[:].ap[0]), [0, 2], [P, 2], [1, P]]),
                                  ALU.mult).then_inc(dve_done, 1)
            for i in range(HEADS_T):
                b = ready(FLIP, i)
                dve.tensor_tensor(dn[:, i, :], b[:, 0:P], c["same16"], ALU.mult)
                dve.tensor_tensor(en[:, i, :], b[:, 0:P], off16[:], ALU.mult).then_inc(dve_done, 1)
            for step, col in ((POW4, 2), (POW8, 1), (TDIAG, 0)):
                for i in range(HEADS_T):
                    b = ready(step, i)
                    dve.tensor_tensor(m[:, i, :], m[:, i, :], b[:, col * P:(col + 1) * P], ALU.add).then_inc(dve_done, 1)
            for i in range(HEADS_T):
                b = ready(OFF, i)
                dve.tensor_copy(y1[:, i].rearrange("p a b -> p (a b)"), b[:, P:2 * P]).then_inc(dve_done, 1)
            for step in (Z1, Z2, Z3):
                for i in range(HEADS_T):
                    b = ready(step, i)
                    dst = xs[:, :, i, :] if step == Z3 else z[:, i]
                    dve.tensor_tensor(dst, y1[:, i], b[:, 0:P].rearrange("p (a b) -> p a b", a=2),
                                      ALU.subtract).then_inc(dve_done, 1)
            dve.wait_ge(dve_done, upto_step(DVE_STEPS, Z3, HEADS_T - 1))
            chain = Chain(dve, own)
            for k, hf in enumerate(halves):
                r = slice(CH * hf, CH * hf + CH)
                n_chunk = 2 * tile + hf
                dve.wait_ge(scan_pe, 2 * k + 1)
                dve.tensor_tensor(san[r].rearrange("p i (h j) -> p i h j", h=2),
                                  xs[r, 0].rearrange("p (i h) j -> p i h j", h=2),
                                  ps[0][r, :].rearrange("p (i h j) -> p i h j", h=2, j=CH), ALU.add).then_inc(scan_dve, 1)
                dve.wait_ge(scan_pe, 2 * k + 2)
                for i in range(PAIRS):
                    end = ends[:, dr, i, n_chunk:n_chunk + 1]
                    new = y1[:, i].rearrange("p a b -> p (a b)")
                    chain.link(dve.scalar_tensor_tensor(out=new, in0=ps[1][:, i * P:(i + 1) * P], scalar=end,
                                                        in1=c["heads2"], op0=ALU.mult, op1=ALU.mult))
                    ins = dve.scalar_tensor_tensor(out=state[:, i, :], in0=state[:, i, :], scalar=end, in1=new,
                                                   op0=ALU.mult, op1=ALU.add)
                ins.then_inc(scan_dve, 1)
            if lat:
                dve.wait_ge(scan_pe, 5)
                yt = y[:, :, at:at + P]
                for hf in range(2):
                    a = yt[:, :, CH * hf:CH * hf + CH]
                    chain.link(dve.tensor_tensor(a, a, ps[2 + hf][:, 0:PAIRS * CH].rearrange("p (i t) -> p i t", t=CH),
                                                 ALU.add))
                for h in range(2):
                    r = slice(CH * h, CH * h + CH)
                    chain.link(dve.tensor_tensor(yt[r], yt[r], ps[4 + h][r, :].rearrange("p (i t) -> p i t", t=P),
                                                 ALU.add))

        @block.scalar
        def _(act):
            def ready(step, i):
                act.wait_ge(pe_done, step * HEADS_T + i + 1)
                if step in DVE_STEPS:
                    act.wait_ge(dve_done, upto_step(DVE_STEPS, step, i))
                return ps[(step * HEADS_T + i) % banks]

            for i in range(HEADS_T):
                b = ready(TURN, i)
                if i % 2 == 0:
                    act.copy(tok[:, i // 2, 0:2, :].rearrange("p a b -> p (a b)"), b[:, 0:2 * P]).then_inc(act_done, 1)
                else:
                    act.copy(tok[:, i // 2, 2, :], b[:, 0:P]).then_inc(act_done, 1)
            for i in range(HEADS_T):
                b = ready(FLIP, i)
                act.mul(xs[:, 0, i, :], b[:, P:P + CH], -1.0).then_inc(act_done, 1)
            for i in range(HEADS_T):
                b = ready(POW2, i)
                act.copy(p2[:, i].rearrange("p a b -> p (a b)"), b[:, 0:2 * P]).then_inc(act_done, 1)
            for i in range(HEADS_T):
                b = ready(POW4, i)
                act.copy(p4[:, i].rearrange("p a b -> p (a b)"), b[:, 0:2 * P]).then_inc(act_done, 1)
            for i in range(HEADS_T):
                b = ready(POW8, i)
                act.copy(p8[:, i, :], b[:, 0:P]).then_inc(act_done, 1)
            for i in range(HEADS_T):
                b = ready(OFF, i)
                act.copy(ft[:, i, :], b[:, 0:P]).then_inc(act_done, 1)
            for i in range(PAIRS):
                act.wait_ge(pe_done, LAY * HEADS_T + i + 1)
                act.copy(wt[:, i, :], ps[2 * i + 1][:, 0:P]).then_inc(act_done, 1)


def group_norm_out(nc, name, c, v, y, bonus, value, gate, out):
    with Stage(nc, name) as st:
        mean_ps, var_ps, bonus_ps = (st.ps(x, [P, BANK]) for x in ("mean", "var", "bonus"))
        sq, rs, t = (st.sb(x, [P, S]) for x in ("sq", "rs", "t"))
        summed, centred, squared, varied, with_eps, rooted, done, own = (
            st.sem(x) for x in ("summed", "centred", "squared", "varied", "with_eps", "rooted", "done", "own"))
        block = st.block()

        @block.tensor
        def _(pe):
            for i in range(4):
                if i:
                    pe.wait_ge(done, i)
                pe.matmul(mean_ps[:], c["group64"], y[:, i, :], start=True, stop=True)
                pe.matmul(bonus_ps[:], c["heads2"], bonus[:, i, :], start=True, stop=True).then_inc(summed, 1)
                pe.wait_ge(squared, i + 1)
                pe.matmul(var_ps[:], c["group64"], sq[:], start=True, stop=True).then_inc(varied, 1)

        @block.scalar
        def _(act):
            for i in range(4):
                act.wait_ge(centred, i + 1)
                act.activation(sq[:], y[:, i, :], ACT.Square).then_inc(squared, 1)
                act.activation(gate[:, i, :], gate[:, i, :], ACT.Silu)
                act.wait_ge(with_eps, i + 1)
                act.activation(rs[:], rs[:], ACT.Sqrt).then_inc(rooted, 1)

        @block.vector
        def _(dve):
            chain = Chain(dve, own)
            for i in range(4):
                dve.wait_ge(summed, i + 1)
                dve.tensor_tensor(y[:, i, :], y[:, i, :], mean_ps[:], ALU.subtract).then_inc(centred, 1)
                chain.link(dve.tensor_tensor(t[:], bonus_ps[:], value[:, i, :], ALU.mult))
                dve.wait_ge(varied, i + 1)
                dve.tensor_scalar(rs[:], var_ps[:], 64e-5, None, ALU.add).then_inc(with_eps, 1)
                dve.wait_ge(rooted, i + 1)
                chain.link(dve.reciprocal(rs[:], rs[:]))
                chain.link(dve.scalar_tensor_tensor(out=rs[:], in0=y[:, i, :], scalar=v("rwkv_gn_w", i, 1), in1=rs[:],
                                                    op0=ALU.mult, op1=ALU.mult))
                chain.link(dve.scalar_tensor_tensor(out=rs[:], in0=rs[:], scalar=v("rwkv_gn_b", i, 1), in1=t[:],
                                                    op0=ALU.add, op1=ALU.add))
                dve.tensor_tensor(out[:, i, :], rs[:], gate[:, i, :], ALU.mult).then_inc(done, 1)
                dve.wait_ge(done, i + 1)


def zero(nc, name, parts):
    with Stage(nc, name) as st:
        block = st.block()

        @block.vector
        def _(dve):
            for part in parts:
                dve.memset(part, 0.0)


def rwkv_input(nc, w, v, h, us, scratch):
    mu = v("mu")
    flat = scratch.rearrange("p k t -> p (k t)")
    padded = flat[:, 0:2 * PADDED].rearrange("p (i t) -> p i t", i=2)
    total = flat[:, 2 * PADDED:2 * PADDED + TT]
    zero(nc, "rwkv_pad", [padded])

    def evict(act, n, ps):
        act.copy(padded[:, n % 2, 1:S + 1], ps[:, 0:S])
        return act.copy(padded[:, n % 2, S + 3:S + 3 + LC], ps[:, S:TT])

    def shift(dve, chain, n):
        u = padded[:, n % 2, :]
        for a, b, m in ((0, 1, S), (S, S + 3, LC)):
            t = total[:, a:a + m]
            chain.link(dve.tensor_tensor(t, u[:, b - 1:b - 1 + m], u[:, b + 1:b + 1 + m], ALU.add))
            chain.link(dve.scalar_tensor_tensor(out=t, in0=t, scalar=0.5, in1=u[:, b:b + m],
                                                op0=ALU.mult, op1=ALU.subtract))
            ins = dve.scalar_tensor_tensor(out=us[:, n, a:a + m], in0=t, scalar=mu[:, n:n + 1],
                                           in1=u[:, b:b + m], op0=ALU.mult, op1=ALU.add)
        return ins

    linear(nc, "rwkv_in", w, *h, TT, evict, engines="a", after=(shift, 13))


def rwkv_scan(nc, d, c, vt, ends, y):
    with nc.sbuf_tensor("rwkv_state", [P, 2, PAIRS, P], F32) as state:
        with Stage(nc, "rwkv_zero") as st:
            block = st.block()

            @block.vector
            def _(dve):
                dve.memset(state[:], 0.0)
                dve.memset(y[:], 0.0)
        for step in range(6):
            for dr in range(2):
                tile = ((4, 5, 0, 1, 2, 3), (5, 4, 3, 2, 1, 0))[dr][step]
                rwkv_group(nc, f"rwkv{step}{dr}", d, c, state[:, dr], vt, ends, y, dr, tile)


def in_sbuf_copy(nc, name, out, in_):
    with Stage(nc, name) as st:
        block = st.block()

        @block.vector
        def _(dve):
            dve.tensor_copy(out, in_)
def products(nc, name, jobs, engines=2, slots=6):
    with Stage(nc, name) as st:
        ps = [st.ps(f"acc{i}", [P, BANK]) for i in range(slots)]
        product_done, out_v, out_a = st.sem("product_done"), st.sem("out_v"), st.sem("out_a")
        block = st.block()

        @block.tensor
        def _(pe):
            for n, (rows, cols, terms, _) in enumerate(jobs):
                if n >= slots:
                    before = n - slots
                    if engines == 1:
                        pe.wait_ge(out_v, before + 1)
                    else:
                        pe.wait_ge((out_v, out_a)[before % 2], before // 2 + 1)
                for j, (lhs, rhs) in enumerate(terms):
                    ins = pe.matmul(ps[n % slots][0:rows, 0:cols], lhs, rhs, start=(j == 0), stop=(j == len(terms) - 1))
                ins.then_inc(product_done, 1)

        @block.vector
        def _(dve):
            for n in range(0, len(jobs), engines):
                dve.wait_ge(product_done, n + 1)
                jobs[n][3](dve, ps[n % slots][0:jobs[n][0], 0:jobs[n][1]]).then_inc(out_v, 1)

        if engines == 2:
            @block.scalar
            def _(act):
                for n in range(1, len(jobs), 2):
                    act.wait_ge(product_done, n + 1)
                    jobs[n][3](act, ps[n % slots][0:jobs[n][0], 0:jobs[n][1]]).then_inc(out_a, 1)


def copy_to(nc, out, scale=None):
    return lambda e, ps: copy_on(e, nc, out, ps, scale)


def hyena_filters(nc, d, c, v, spectrum, root):
    two_pi = float(2 * np.pi)
    with ExitStack() as keep:
        def sb(name, shape, stack=keep):
            return stack.enter_context(nc.sbuf_tensor("filt_" + name, shape, F32))

        dft = sb("dft", [P, 2, 4, 512])
        ab = sb("sum_difference", [P, 2, 2, 4, 512])
        with ExitStack() as inner:
            hid = sb("hid", [65, S], inner)
            w3 = sb("w3", [65, 2048], inner)
            decay = sb("decay", [P, 4, 512], inner)
            taps = sb("taps", [P, 4, 2, 2, 512], inner)
            with Stage(nc, "filt_hidden") as st:
                w1, w2, feats = st.sb("w1", [33, 64]), st.sb("w2", [64, 64]), st.sb("feats", [33, S])
                arg, turns = st.sb("arg", [64, S]), st.sb("turns", [64, S])
                hid1 = st.sb("hid1", [64, S])
                ps = st.ps("hid", [64, BANK])
                landed, summed, reduced, sined, own = (st.sem(x) for x in ("landed", "summed", "reduced", "sined", "own"))
                block = st.block()

                @block.sync
                def _(sp):
                    for dst, src in ((w1[:], d["hy_w1"]), (w2[:], d["hy_w2"]), (feats[:], d["c_feats"]),
                                     (w3[0:64, :], d["hy_w3"]), (w3[64:65, :], d["hy_b3"]),
                                     (decay[:], d["c_decay"].rearrange("(a p) n -> p a n", p=P)),
                                     (dft[:, 0], d["c_dft"][0].rearrange("(a p) n -> p a n", p=P)),
                                     (dft[:, 1], d["c_dft"][1].rearrange("(a p) n -> p a n", p=P))):
                        sp.dma_start(dst, src).then_inc(landed, 16)
                    sp.wait_ge(landed, 128)

                @block.gpsimd
                def _(pool):
                    pool.memset(hid[64:65, :], 1.0)

                @block.tensor
                def _(pe):
                    pe.wait_ge(landed, 128)
                    pe.matmul(ps[:], w1[:], feats[:], start=True, stop=True).then_inc(summed, 1)
                    pe.wait_ge(sined, 1)
                    pe.matmul(ps[:], w2[:], hid1[:], start=True, stop=True).then_inc(summed, 1)

                @block.vector
                def _(dve):
                    chain = Chain(dve, own)
                    for n, b in enumerate(("hy_b1", "hy_b2")):
                        dve.wait_ge(summed, n + 1)
                        chain.link(dve.tensor_scalar(arg[:], ps[:], v(b)[0:64, :], None, ALU.add))
                        chain.link(dve.tensor_scalar(turns[:], arg[:], 1.0 / two_pi, 12582912.0, ALU.mult, ALU.add))
                        chain.link(dve.tensor_scalar(turns[:], turns[:], -12582912.0, None, ALU.add))
                        chain.link(dve.scalar_tensor_tensor(out=arg[:], in0=turns[:], scalar=-6.28125, in1=arg[:],
                                                            op0=ALU.mult, op1=ALU.add))
                        chain.link(dve.scalar_tensor_tensor(out=arg[:], in0=turns[:], scalar=-(two_pi - 6.28125),
                                                            in1=arg[:], op0=ALU.mult, op1=ALU.add))
                        dve.tensor_scalar(arg[:], arg[:], 3.1415925, -3.1415925, ALU.min, ALU.max).then_inc(reduced, 1)
                        dve.wait_ge(sined, n + 1)

                @block.scalar
                def _(act):
                    for n, out in enumerate((hid1[:], hid[0:64, :])):
                        act.wait_ge(reduced, n + 1)
                        act.activation(out, arg[:], ACT.Sin).then_inc(sined, 1)

            def windowed(t, j):
                return lambda e, ps: e.tensor_tensor(taps[:, t, j // 2, j % 2, :], ps, decay[:, t, :], ALU.mult)

            products(nc, "filt_taps", [(P, 512, [(hid[:, t * P:(t + 1) * P], w3[:, 512 * j:512 * j + 512])],
                                        windowed(t, j)) for t in range(4) for j in range(4)], engines=1)
            with Stage(nc, "filt_sum") as st:
                block = st.block()

                @block.vector
                def _(dve):
                    for o in range(2):
                        dve.tensor_tensor(ab[:, o, 0], taps[:, :, 0, o, :], taps[:, :, 1, o, :], ALU.add)

                @block.gpsimd
                def _(pool):
                    for o in range(2):
                        pool.tensor_tensor(ab[:, o, 1], taps[:, :, 0, o, :], taps[:, :, 1, o, :], ALU.subtract)
        with ExitStack() as inner:
            sq = sb("sq", [P, 2, 2, 4, 512], inner)
            with Stage(nc, "filt_sq") as st:
                squared, own = st.sem("squared"), st.sem("own")
                block = st.block()

                @block.scalar
                def _(act):
                    for o in range(2):
                        for j in range(2):
                            act.activation(sq[:, o, j, 0], ab[:, o, j, 0], ACT.Square, scale=(c["sum_root"], c["diff_root"])[j])
                            act.activation(sq[:, o, j, 1:4], ab[:, o, j, 1:4], ACT.Square,
                                           scale=c["half_root"]).then_inc(squared, 1)

                @block.vector
                def _(dve):
                    chain = Chain(dve, own)
                    for o in range(2):
                        dve.wait_ge(squared, 2 * o + 2)
                        chain.link(dve.tensor_tensor(sq[:, o, 0], sq[:, o, 0], sq[:, o, 1], ALU.add))
                        chain.link(dve.tensor_tensor(sq[:, o, 0, 0:2], sq[:, o, 0, 0:2], sq[:, o, 0, 2:4], ALU.add))
                        chain.link(dve.tensor_tensor(sq[:, o, 0, 0], sq[:, o, 0, 0], sq[:, o, 0, 1], ALU.add))

            products(nc, "filt_norm", [
                (P, 1, [(sq[:, o, 0, 0, i * P:(i + 1) * P], c["ones"][:, 0:1])],
                 copy_to(nc, root[:, 4 * o + i:4 * o + i + 1])) for o in range(2) for i in range(4)])
        with Stage(nc, "filt_root") as st:
            rooted = st.sem("rooted")
            block = st.block()

            @block.scalar
            def _(act):
                act.activation(root[:], root[:], ACT.Sqrt).then_inc(rooted, 1)

            @block.vector
            def _(dve):
                dve.wait_ge(rooted, 1)
                dve.reciprocal(root[:], root[:])

        products(nc, "filt_spectrum", [
            (P, 512, [(dft[:, j, t, w * P:(w + 1) * P], ab[:, o, j, t, :]) for t in range(4)],
             copy_to(nc, spectrum[:, o, j, w, :])) for o in range(2) for j in range(2) for w in range(4)])


def hyena_input(nc, d, w, v, h, parts, gate):
    with nc.sbuf_tensor("hyin_padded", [P, 2, S + 2], F32) as padded:
        zero(nc, "hy_pad", [padded[:]])

        def evict(act, n, ps):
            if n < 12:
                return act.copy(padded[:, n % 2, 1:S + 1], ps[:, 0:S])
            return act.activation(gate[:, n - 12, :], ps[:, 0:S], ACT.Silu)

        def convolve(dve, chain, n):
            u = parts[n // 4][:, n % 4, :]
            chain.link(dve.tensor_scalar(u, padded[:, n % 2, 0:S], v("hy_short", n, 1), None, ALU.mult))
            for tap in (1, 2):
                ins = dve.scalar_tensor_tensor(out=u, in0=padded[:, n % 2, tap:tap + S],
                                               scalar=v("hy_short", 12 * tap + n, 1), in1=u,
                                               op0=ALU.mult, op1=ALU.add)
                if tap == 1:
                    chain.link(ins)
            return ins

        linear(nc, "hy_in", w, *h, S, evict, engines="a", after=(convolve, 12))
    with Stage(nc, "hy_save") as st:
        saved = st.sem("saved")
        block = st.block()

        @block.sync
        def _(sp):
            out = d["s_hy"].rearrange("(i p) t -> p i t", p=P)
            for i, part in enumerate((*parts, gate)):
                sp.dma_start(out[:, 4 * i:4 * i + 4], part).then_inc(saved, 16)
            sp.wait_ge(saved, 64)


def hyena_branch(nc, d, c, v, out):
    with ExitStack() as keep:
        def sb(name, shape, stack=keep):
            return stack.enter_context(nc.sbuf_tensor("hy_" + name, shape, F32))

        spectrum = sb("spectrum", [P, 2, 2, 4, 512])
        root = sb("root", [P, 8])
        hyena_filters(nc, d, c, v, spectrum, root)
        u, gate = sb("u", [P, 12, S]), sb("gate", [P, 4, S])
        dft, idft = sb("dft", [P, 2, 4, 512]), sb("idft", [P, 2, 4, 512])
        load(nc, "hy_tables", [(t[:, j], d[n][j].rearrange("(a p) n -> p a n", p=P))
                               for t, n in ((dft, "c_dft"), (idft, "c_idft")) for j in range(2)]
             + [(u[:], d["s_hy"].rearrange("(i p) t -> p i t", p=P)[:, 0:12]),
                (gate[:], d["s_hy"].rearrange("(i p) t -> p i t", p=P)[:, 12:16])])
        z = u[:, 0:4, :]
        zt = sb("z_tokens", [P, 4, 512])
        zw, yw = sb("z_spectrum", [P, 2, 4, 512]), sb("y_spectrum", [P, 2, 4, 512])
        tmp = sb("tmp", [P, 2, 4, 512])
        for o in range(2):
            to_features(nc, f"hy_turn{o}", [([z[:, i, t * P:(t + 1) * P] for i in range(4)], None, zt[:, t, :])
                                            for t in range(4)], c["ident"])
            products(nc, f"hy_dft{o}", [
                (P, 512, [(dft[:, j, t, w * P:(w + 1) * P], zt[:, t, :]) for t in range(4)],
                 copy_to(nc, zw[:, j, w, :])) for j in range(2) for w in range(4)])
            with Stage(nc, f"hy_mult{o}") as st:
                own, crossed = st.sem("own"), st.sem("crossed")
                block = st.block()

                @block.vector
                def _(dve):
                    chain = Chain(dve, own)
                    dve.tensor_tensor(yw[:, 0], zw[:, 0], spectrum[:, o, 0], ALU.mult)
                    chain.link(dve.tensor_tensor(tmp[:, 0], zw[:, 1], spectrum[:, o, 1], ALU.mult))
                    dve.tensor_tensor(yw[:, 0], yw[:, 0], tmp[:, 0], ALU.subtract)
                    dve.wait_ge(crossed, 2)
                    dve.tensor_tensor(yw[:, 1], yw[:, 1], tmp[:, 1], ALU.add)

                @block.gpsimd
                def _(pool):
                    pool.tensor_tensor(yw[:, 1], zw[:, 0], spectrum[:, o, 1], ALU.mult).then_inc(crossed, 1)
                    pool.tensor_tensor(tmp[:, 1], zw[:, 1], spectrum[:, o, 0], ALU.mult).then_inc(crossed, 1)
            products(nc, f"hy_idft{o}", [
                (P, 512, [(yw[:, j, w, i * P:(i + 1) * P], idft[:, j, w, :]) for j in range(2) for w in range(4)],
                 copy_to(nc, tmp[:, 0, i, :], root[:, 4 * o + i:4 * o + i + 1])) for i in range(4)])
            with Stage(nc, f"hy_gate{o}") as st:
                own = st.sem("own")
                block = st.block()

                @block.vector
                def _(dve):
                    chain = Chain(dve, own)
                    for i in range(4):
                        chain.link(dve.scalar_tensor_tensor(out=tmp[:, 1, i, :], in0=z[:, i, :],
                                                            scalar=v("hy_skip", 4 * o + i, 1), in1=tmp[:, 0, i, :],
                                                            op0=ALU.mult, op1=ALU.add))
                        chain.link(dve.tensor_tensor(z[:, i, :], tmp[:, 1, i, :], u[:, 4 + 4 * o + i, :], ALU.mult))
                        if o == 1:
                            dve.tensor_tensor(out[:, i, :], z[:, i, :], gate[:, i, :], ALU.mult)
FF = 2816
FFK = FF // P


def ffn_weights(d, n):
    gate, up = d[f"ffn{n}_w_gate_2"], d[f"ffn{n}_w_up_2"]
    return {f"ffn{n}_in": [b for a in range(0, FF, 256) for W in (gate, up) for b in weight_blocks(W, a, 256)],
            f"ffn{n}_down": weight_blocks(d[f"ffn{n}_w_down_2"], 0, D, kc=FFK)}


def ffn(nc, name, d, w, c, v, x, n):
    with ExitStack() as keep:
        def sb(what, shape, dtype=F32, stack=keep):
            return stack.enter_context(nc.sbuf_tensor(f"{name}_{what}", shape, dtype))

        out = sb("out", [P, KD, S])
        with ExitStack() as inner:
            mid = [sb("mid_" + p, [P, FFK, S], F32R, inner) for p in ("high", "low")]
            with ExitStack() as first:
                h = [sb("h_" + p, [P, KD, S], F32R, first) for p in ("high", "low")]
                silu = sb("silu", [P, 4, S], stack=first)
                own = first.enter_context(nc.semaphore(f"{name}_own"))
                norm(nc, name + "_pre", lambda k: x[:, k, :], S, lambda k: v(f"ffn{n}_pre_norm_2", k, 1), c["ones"],
                     split=[lambda k, t=t: t[:, k, :] for t in h], scratch=out)
                chain = Chain(nc.vector, own)

                def before(engine, t, stored):
                    if t % 4 < 2:
                        if t >= 8:
                            engine.wait_ge(stored["v"], 2 * (t // 4 - 1))
                    else:
                        engine.wait_ge(stored["a"], 2 * (t // 4) + t % 4 - 1)

                def evict(engine, t, ps):
                    s = silu[:, 2 * (t // 4 % 2) + t % 2, :]
                    if t % 4 < 2:
                        return engine.activation(s, ps[:], ACT.Silu)
                    m = 2 * (t // 4) + t % 2
                    chain.link(engine.tensor_tensor(s, s, ps[:], ALU.mult))
                    chain.link(engine.tensor_copy(mid[0][:, m, :], s))
                    return engine.tensor_tensor(mid[1][:, m, :], s, mid[0][:, m, :].bitcast(F32), ALU.subtract)

                linear(nc, name + "_in", w, *(lambda k, t=t: t[:, k, :] for t in h), S, evict,
                       engines="aavv", before=before)
            linear(nc, name + "_down", w, *(lambda k, t=t: t[:, k, :] for t in mid), S,
                   lambda e, m, ps: copy_on(e, nc, out[:, m, :], ps[:, 0:S]), kc=FFK)
        norm(nc, name + "_post", lambda k: out[:, k, :], S, lambda k: v(f"ffn{n}_post_norm_2", k, 1), c["ones"],
             residual=lambda k: x[:, k, :], half=0.5)


def rel_bias_table(nc, d, table):
    wide = 2 * S
    with Stage(nc, "rel_bias") as st:
        bucket, bias = st.sb("bucket", [32, wide]), st.sb("bias", [32, 8])
        causal, line = st.sb("causal", [8, wide]), st.sb("line", [8, wide])
        ps = st.ps("spread_line", [8, wide])
        landed, spread, masked, stored = (st.sem(x) for x in ("landed", "spread", "masked", "stored"))
        block = st.block()

        @block.sync
        def _(sp):
            for dst, src in ((bucket[:], d["c_bucket"]), (bias[:], d["rel_bias_2"]), (causal[:], d["c_causal"])):
                sp.dma_start(dst, src).then_inc(landed, 16)
            sp.wait_ge(masked, 1)
            sp.dma_start(d["s_rel"], line[:].rearrange("h (a m) -> h a m", a=1).broadcast_to([8, P, wide])
                         ).then_inc(stored, 16)
            sp.wait_ge(stored, 16)
            sp.dma_start(table[:], bass.AP(tensor=d["s_rel"].tensor, offset=P - 1, ap=[[wide - 1, P], [P * wide, 8], [1, 896]])
                         ).then_inc(stored, 16)
            sp.wait_ge(stored, 32)

        @block.tensor
        def _(pe):
            pe.wait_ge(landed, 48)
            for a in range(2):
                ins = pe.matmul(ps[:, a * BANK:(a + 1) * BANK], bias[:], bucket[:, a * BANK:(a + 1) * BANK],
                                start=True, stop=True)
            ins.then_inc(spread, 1)

        @block.vector
        def _(dve):
            dve.wait_ge(spread, 1)
            dve.tensor_tensor(line[:], ps[:], causal[:], ALU.add).then_inc(masked, 1)


N_CMP = 31


def compress(nc, w, both, pos, w2, ident, keys, values):
    with ExitStack() as keep:
        def sb(name, shape, dtype=F32):
            return keep.enter_context(nc.sbuf_tensor("cmp_" + name, shape, dtype))

        n = 2 * N_CMP
        high, low = sb("high", [P, 2, 16, n], F32R), sb("low", [P, 2, 16, n], F32R)
        hid = sb("hid", [n, 2, 256])
        with Stage(nc, "cmp_blocks") as st:
            swapped = st.sb("swapped", [P, 2, S])
            blocks = st.sb("blocks", [P, 2, 16, n])
            moved, added, high_done = st.sem("moved"), st.sem("added"), st.sem("high_done")
            block = st.block()

            @block.sync
            def _(sp):
                sp.dma_start(swapped[0:64], both[64:128]).then_inc(moved, 16)
                sp.dma_start(swapped[64:128], both[0:64]).then_inc(moved, 16)

            @block.vector
            def _(dve):
                for moves in (False, True):
                    if moves:
                        dve.wait_ge(moved, 32)
                    for j in range(2):
                        for odd in range(2):
                            g, r = (1 - odd if moves else odd), slice(64 * odd, 64 * odd + 64)
                            kv = (swapped if moves else both)[r, j, :]
                            src = bass.AP(tensor=kv.tensor, offset=kv.offset + odd,
                                          ap=[list(kv.ap[0]), [2, 16], [16, N_CMP]])
                            at = pos[j][r, odd:32:2].rearrange("p (t a) -> p t a", a=1).broadcast_to([64, 16, N_CMP])
                            ins = dve.tensor_tensor(blocks[r, j, :, N_CMP * g:N_CMP * g + N_CMP], src, at, ALU.add)
                ins.then_inc(added, 1)
                dve.wait_ge(high_done, 1)
                dve.tensor_tensor(low[:], blocks[:], high[:].bitcast(F32), ALU.subtract)

            @block.scalar
            def _(act):
                act.wait_ge(added, 1)
                act.copy(high[:], blocks[:]).then_inc(high_done, 1)

        for j, name in enumerate(("cmp_k", "cmp_v")):
            linear_tokens(nc, name, w, *(lambda k, t=t: t[:, j, k, :] for t in (high, low)), n,
                          lambda e, g, t, ps: copy_on(e, nc, hid[:, j, :], ps[0:n, 0:256]), kc=16)
        with Stage(nc, "cmp_out") as st:
            w2_sb = st.sb("w2", [P, 2, 2, 64])
            hid_t = st.sb("hid_t", [P, 2, 2, n])
            turned = st.ps("turned", [P, 2, 2, n])
            out_ps = [st.ps(f"out{i}", [P, BANK]) for i in range(3)]
            landed, silu_done, turn_done, copied, out_done = (st.sem(x) for x in (
                "landed", "silu_done", "turn_done", "copied", "out_done"))
            block = st.block()

            @block.sync
            def _(sp):
                for j in range(2):
                    sp.dma_start(w2_sb[:, j], w2[j].rearrange("(a p) n -> p a n", p=P)).then_inc(landed, 16)

            @block.scalar
            def _(act):
                act.activation(hid[:], hid[:], ACT.Silu).then_inc(silu_done, 1)

            @block.tensor
            def _(pe):
                pe.wait_ge(silu_done, 1)
                for j in range(2):
                    for a in range(2):
                        ins = pe.transpose(turned[:, j, a, :], hid[:, j, a * P:(a + 1) * P], ident[0:n, 0:n])
                ins.then_inc(turn_done, 1)
                pe.wait_ge(landed, 32)
                pe.wait_ge(copied, 1)
                for g in range(2):
                    cols = slice(N_CMP * g, N_CMP * g + N_CMP)
                    for a in range(2):
                        pe.matmul(out_ps[g][64 * g:64 * g + 64, 0:N_CMP], w2_sb[:, 0, a, :], hid_t[:, 0, a, cols],
                                  start=(a == 0), stop=(a == 1))
                    for a in range(2):
                        ins = pe.matmul(out_ps[2][0:N_CMP, 64 * g:64 * g + 64], hid_t[:, 1, a, cols], w2_sb[:, 1, a, :],
                                        start=(a == 0), stop=(a == 1))
                ins.then_inc(out_done, 1)

            @block.vector
            def _(dve):
                dve.wait_ge(turn_done, 1)
                dve.tensor_copy(hid_t[:], turned[:]).then_inc(copied, 1)
                dve.wait_ge(out_done, 1)
                for g in range(2):
                    r = slice(64 * g, 64 * g + 64)
                    dve.tensor_copy(keys[r, :], out_ps[g][r, 0:N_CMP])
                dve.tensor_copy(values[:], out_ps[2][0:N_CMP, 0:P])


def solve(nc, name, c, n_mat, rhs, out, n, width):
    steps = ("flip", "pow2", "pow4", "pow8", "tdiag", "off", "z1", "z2", "z3")
    with Stage(nc, name) as st:
        off16 = st.sb("off16", [P, P])
        dn, en, dt, m = (st.sb(x, [P, n, P]) for x in ("diag", "off", "diag_t", "inv_t"))
        p2, p4 = st.sb("pow2", [P, n, 2, P]), st.sb("pow4", [P, n, 2, P])
        p8, ft = st.sb("pow8", [P, n, P]), st.sb("off_t", [P, n, P])
        y1, z = st.sb("y1", [P, n, width]), st.sb("z", [P, n, width])
        ps = [st.ps(f"ps{i}", [P, BANK]) for i in range(8)]
        made, split = st.sem("made"), st.sem("split")
        pe_done, dve_done, act_done, pool_done = (st.sem(x) for x in ("pe_done", "dve_done", "act_done", "pool_done"))
        block = st.block()

        dve_steps = ("flip", "pow4", "pow8", "tdiag", "off", "z1", "z2", "z3")
        act_steps = ("pow2", "pow4", "pow8", "off")

        def counted(of, step, i):
            return n * of.index(step) + i + 1

        @block.tensor
        def _(pe):
            def order(step, i):
                earlier = steps[:steps.index(step)]
                for of, sem in ((dve_steps, dve_done), (act_steps, act_done)):
                    before = [s for s in earlier if s in of]
                    if before:
                        pe.wait_ge(sem, counted(of, before[-1], i))
                return ps[i % 8]

            for i in range(n):
                pe.transpose(order("flip", i)[:, 0:P], n_mat[:, i, :], c["ident"]).then_inc(pe_done, 1)
            for i in range(n):
                b = order("pow2", i)
                pe.wait_ge(pool_done, i + 1)
                pe.matmul(b[:, 0:P], dt[:, i, :], dn[:, i, :], start=True, stop=True)
                pe.matmul(b[:, P:2 * P], dn[:, i, :], dt[:, i, :], start=True, stop=True).then_inc(pe_done, 1)
            for i in range(n):
                b = order("pow4", i)
                pe.matmul(b[:, 0:P], p2[:, i, 1, :], p2[:, i, 0, :], start=True, stop=True)
                pe.matmul(b[:, P:2 * P], p2[:, i, 0, :], p2[:, i, 1, :], start=True, stop=True)
                pe.matmul(b[:, 2 * P:3 * P], p2[:, i, 0, :], m[:, i, :], start=True, stop=True).then_inc(pe_done, 1)
            for i in range(n):
                b = order("pow8", i)
                pe.matmul(b[:, 0:P], p4[:, i, 1, :], p4[:, i, 0, :], start=True, stop=True)
                pe.matmul(b[:, P:2 * P], p4[:, i, 0, :], m[:, i, :], start=True, stop=True).then_inc(pe_done, 1)
            for i in range(n):
                pe.matmul(order("tdiag", i)[:, 0:P], p8[:, i, :], m[:, i, :], start=True, stop=True).then_inc(pe_done, 1)
            for i in range(n):
                b = order("off", i)
                pe.matmul(b[:, 0:P], en[:, i, :], m[:, i, :], start=True, stop=True)
                pe.matmul(b[:, P:P + width], m[:, i, :], rhs[:, i, :], start=True, stop=True).then_inc(pe_done, 1)
            for step, src in (("z1", y1), ("z2", z), ("z3", z)):
                for i in range(n):
                    pe.matmul(order(step, i)[:, 0:width], ft[:, i, :], src[:, i, :],
                              start=True, stop=True).then_inc(pe_done, 1)

        @block.gpsimd
        def _(pool):
            pool.tensor_scalar(off16[:], c["same16"], -1.0, 1.0, ALU.mult, ALU.add).then_inc(made, 1)
            pool.wait_ge(made, 1)
            for i in range(n):
                pool.tensor_tensor(dn[:, i, :], n_mat[:, i, :], c["same16"], ALU.mult)
                pool.tensor_tensor(en[:, i, :], n_mat[:, i, :], off16[:], ALU.mult)
                pool.wait_ge(dve_done, i + 1)
                pool.tensor_tensor(m[:, i, :], c["ident"], dt[:, i, :], ALU.subtract).then_inc(pool_done, 1)

        @block.vector
        def _(dve):
            def ready(step, i):
                dve.wait_ge(pe_done, counted(steps, step, i))
                return ps[i % 8]

            for i in range(n):
                dve.tensor_tensor(dt[:, i, :], ready("flip", i)[:, 0:P], c["same16"], ALU.mult).then_inc(dve_done, 1)
            for step, col in (("pow4", 2), ("pow8", 1), ("tdiag", 0)):
                for i in range(n):
                    b = ready(step, i)
                    dve.tensor_tensor(m[:, i, :], m[:, i, :], b[:, col * P:(col + 1) * P], ALU.add).then_inc(dve_done, 1)
            for i in range(n):
                dve.tensor_copy(y1[:, i, :], ready("off", i)[:, P:P + width]).then_inc(dve_done, 1)
            for step in ("z1", "z2", "z3"):
                for i in range(n):
                    dve.tensor_tensor((out if step == "z3" else z)[:, i, :], y1[:, i, :],
                                      ready(step, i)[:, 0:width], ALU.subtract).then_inc(dve_done, 1)

        @block.scalar
        def _(act):
            for step, dst, cols in (("pow2", p2, 2 * P), ("pow4", p4, 2 * P), ("pow8", p8, P), ("off", ft, P)):
                for i in range(n):
                    act.wait_ge(pe_done, counted(steps, step, i))
                    if step in dve_steps:
                        act.wait_ge(dve_done, counted(dve_steps, step, i))
                    o = dst[:, i] if cols == P else dst[:, i].rearrange("p a b -> p (a b)")
                    act.copy(o, ps[i % 8][:, 0:cols]).then_inc(act_done, 1)


def delta_branch(nc, d, c, v, qkv, ab, out, spare):
    with ExitStack() as keep:
        def sb(name, shape, stack=keep):
            return stack.enter_context(nc.sbuf_tensor("dn_" + name, shape, F32))

        q, k, val = qkv[:, 0:4], qkv[:, 4:8], qkv[:, 8:12]
        head_norm(nc, "dn_l2", [qkv[:, i, :] for i in range(8)], [c["root128"]] * 4 + [c["ones"][:, 0:1]] * 4, c["ones"])
        g, beta, sp_tmp = sb("g", [P, 4, 4]), sb("beta", [P, 4, 4]), sb("softplus", [P, 4, 4])
        gc, left, eg = sb("gc", [P, 4, 4]), sb("left", [P, 4, 4]), sb("exp_gc", [P, 4, 4])
        ktok, vtok = spare, out
        to_features(nc, "dn_turn", [([src[:, i, t * P:(t + 1) * P] for i in range(4)], None, dst[:, t, :])
                                    for src, dst in ((k, ktok), (val, vtok)) for t in range(4)], c["ident"])
        with Stage(nc, "dn_gates") as st:
            a_log, dt_bias = st.sb("a_log", [P, 4]), st.sb("dt_bias", [P, 4])
            x, neg, e = st.sb("x", [P, 4, 4]), st.sb("neg", [P, 4, 4]), st.sb("e", [P, 4, 4])
            ps = [st.ps(f"sum{i}", [P, BANK]) for i in range(2)]
            landed, exped, prepared, logged, decays, summed, own = (
                st.sem(n) for n in ("landed", "exped", "prepared", "logged", "decays", "summed", "own"))
            block = st.block()

            @block.sync
            def _(sp):
                for dst, src in ((a_log, d["dn_a_log_2"]), (dt_bias, d["dn_dt_bias_2"])):
                    sp.dma_start(dst[:], bass.AP(tensor=src.tensor, offset=src.offset, ap=[[0, P], [1, 4]])
                                 ).then_inc(landed, 16)

            @block.scalar
            def _(act):
                act.wait_ge(landed, 32)
                act.activation(a_log[:], a_log[:], ACT.Exp).then_inc(exped, 1)
                act.activation(beta[:], ab[:, :, 4:8], ACT.Sigmoid).then_inc(exped, 1)
                act.wait_ge(prepared, 1)
                act.activation(e[:], neg[:], ACT.Exp).then_inc(logged, 1)
                act.wait_ge(prepared, 2)
                act.activation(e[:], e[:], ACT.Ln).then_inc(logged, 1)
                act.wait_ge(decays, 2)
                act.activation(left[:], left[:], ACT.Exp)
                act.activation(eg[:], gc[:], ACT.Exp)

            @block.vector
            def _(dve):
                chain = Chain(dve, own)

                def tiles(t):
                    return t[:].rearrange("p (a h) -> p a h", a=1).broadcast_to([P, 4, 4])

                dve.wait_ge(landed, 32)
                dve.wait_ge(exped, 2)
                chain.link(dve.tensor_tensor(x[:], ab[:, :, 0:4], tiles(dt_bias), ALU.add))
                chain.link(dve.tensor_scalar(neg[:], x[:], -1.0, None, ALU.mult))
                dve.tensor_tensor(neg[:], neg[:], x[:], ALU.min).then_inc(prepared, 1)
                dve.wait_ge(logged, 1)
                dve.tensor_scalar(e[:], e[:], 1.0, None, ALU.add).then_inc(prepared, 1)
                dve.wait_ge(logged, 2)
                chain.link(dve.scalar_tensor_tensor(out=g[:], in0=x[:], scalar=0.0, in1=e[:], op0=ALU.max, op1=ALU.add))
                chain.link(dve.tensor_tensor(g[:], g[:], tiles(a_log), ALU.mult))
                dve.tensor_scalar(g[:], g[:], -1.0, None, ALU.mult).then_inc(decays, 1)
                dve.wait_ge(summed, 1)
                chain.link(dve.tensor_copy(gc[:].rearrange("p a h -> p (a h)"), ps[0][:, 0:16]))
                dve.tensor_tensor(left[:].rearrange("p a h -> p (a h)"), ps[1][:, 0:16],
                                  gc[:].rearrange("p a h -> p (a h)"), ALU.subtract).then_inc(decays, 1)

            @block.tensor
            def _(pe):
                pe.wait_ge(decays, 1)
                gf = g[:].rearrange("p a h -> p (a h)")
                pe.matmul(ps[0][:, 0:16], c["incl_fwd"], gf, start=True, stop=True)
                pe.matmul(ps[1][:, 0:16], c["heads2"], gf, start=True, stop=True).then_inc(summed, 1)

        n_all = 16
        nmat, aqk = sb("n", [P, n_all, P]), sb("aqk_t", [P, n_all, P])
        rhs = sb("rhs", [P, n_all, 256])
        sol = rhs
        ends = sb("ends", [P, n_all, 2])
        with Stage(nc, "dn_matrices") as st:
            gb = [st.sb(f"g_spread{i}", [P, P]) for i in range(2)]
            arg = [st.sb(f"arg{i}", [P, 2, P]) for i in range(2)]
            row = [st.sb(f"row{i}", [P, P]) for i in range(2)]
            eb = st.sb("exp_beta", [P, 4, 4])
            ps_r = [st.ps(f"row_ps{i}", [P, BANK]) for i in range(2)]
            ps_k = [st.ps(f"gram{i}", [P, BANK]) for i in range(2)]
            spread, rowed, grammed, args, exped, rowed_exp, masked, own = (
                st.sem(n) for n in ("spread", "rowed", "grammed", "args", "exped", "rowed_exp", "masked", "own"))
            block = st.block()

            @block.gpsimd
            def _(pool):
                for i in range(n_all):
                    if i >= 2:
                        pool.wait_ge(rowed, i - 1)
                    pool.tensor_scalar(gb[i % 2][:], c["ones"], g[:, i // 4, i % 4:i % 4 + 1], None,
                                       ALU.mult).then_inc(spread, 1)

            @block.tensor
            def _(pe):
                for i in range(n_all):
                    t, h = i // 4, i % 4
                    at = slice(t * P, (t + 1) * P)
                    pe.wait_ge(spread, i + 1)
                    if i >= 2:
                        pe.wait_ge(exped, i - 1)
                        pe.wait_ge(masked, i - 1)
                    pe.matmul(ps_r[i % 2][:, 0:P], gb[i % 2][:], c["incl_fwd"], start=True, stop=True).then_inc(rowed, 1)
                    pe.matmul(ps_k[i % 2][:, 0:P], k[:, h, at], k[:, h, at], start=True, stop=True)
                    pe.matmul(ps_k[i % 2][:, P:2 * P], k[:, h, at], q[:, h, at], start=True, stop=True).then_inc(grammed, 1)

            @block.scalar
            def _(act):
                for i in range(n_all):
                    act.wait_ge(args, i + 1)
                    act.activation(row[i % 2][:], ps_r[i % 2][:, 0:P], ACT.Exp)
                    act.activation(arg[i % 2][:], arg[i % 2][:], ACT.Exp).then_inc(exped, 1)

            @block.vector
            def _(dve):
                chain = Chain(dve, own)
                chain.link(dve.tensor_tensor(eb[:], eg[:], beta[:], ALU.mult))
                chain.link(dve.tensor_scalar(eb[:], eb[:], -1.0, None, ALU.mult))
                for i in range(n_all):
                    t, h = i // 4, i % 4
                    at, hs = slice(t * P, (t + 1) * P), slice(h * P, (h + 1) * P)
                    dve.wait_ge(rowed, i + 1)
                    chain.link(dve.tensor_scalar(arg[i % 2][:, 0, :], ps_r[i % 2][:, 0:P], gc[:, t, h:h + 1], 0.0,
                                                 ALU.subtract, ALU.min))
                    chain.link(dve.tensor_scalar(arg[i % 2][:, 1, :], ps_r[i % 2][:, 0:P], gc[:, t, h:h + 1], 0.0,
                                                 ALU.subtract, ALU.max))
                    dve.tensor_scalar(arg[i % 2][:, 1, :], arg[i % 2][:, 1, :], -1.0, None, ALU.mult).then_inc(args, 1)
                    dve.tensor_scalar(rhs[:, i, 0:P], vtok[:, t, hs], beta[:, t, h:h + 1], None, ALU.mult)
                    dve.tensor_scalar(rhs[:, i, P:2 * P], ktok[:, t, hs], eb[:, t, h:h + 1], None, ALU.mult)
                    dve.wait_ge(exped, i + 1)
                    dve.wait_ge(grammed, i + 1)
                    chain.link(dve.tensor_tensor(arg[i % 2][:, 0, :], arg[i % 2][:, 0, :], c["incl_fwd"], ALU.mult))
                    chain.link(dve.tensor_tensor(arg[i % 2][:, 1, :], arg[i % 2][:, 1, :], c["strict_rev"], ALU.mult))
                    chain.link(dve.tensor_copy(ends[:, i, 0:1], row[i % 2][:, 63:64]))
                    chain.link(dve.tensor_copy(ends[:, i, 1:2], row[i % 2][:, 127:128]))
                    dve.tensor_tensor(aqk[:, i, :], ps_k[i % 2][:, P:2 * P], arg[i % 2][:, 0, :], ALU.mult)
                    dve.scalar_tensor_tensor(out=nmat[:, i, :], in0=ps_k[i % 2][:, 0:P], scalar=beta[:, t, h:h + 1],
                                             in1=arg[i % 2][:, 1, :], op0=ALU.mult, op1=ALU.mult).then_inc(masked, 1)
                    dve.wait_ge(masked, i + 1)
                    chain.link(dve.tensor_tensor(q[:, h, at], q[:, h, at], row[i % 2][:], ALU.mult))
                    chain.link(dve.tensor_scalar(ktok[:, t, hs], ktok[:, t, hs], left[:, t, h:h + 1], None, ALU.mult))
        for b in range(4):
            s = slice(4 * b, 4 * b + 4)
            solve(nc, f"dn_solve{b}", c, nmat[:, s], rhs[:, s], sol[:, s], 4, 256)
        turned = sb("w_t", [P, n_all, P])
        to_features(nc, "dn_w", [([sol[:, i + j, P:2 * P] for j in range(4)], None,
                                  turned[:, i:i + 4, :].rearrange("p a b -> p (a b)")) for i in range(0, n_all, 4)],
                    c["ident"])
        with Stage(nc, "dn_scan") as st:
            state, vnew = st.sb("state", [P, 4, P]), st.sb("v_new", [P, 4, P])
            ps_w, ps_s = st.ps("w_state", [P, BANK]), st.ps("new_state", [P, BANK])
            ps_o, ps_a = [st.ps(f"q_state{i}", [P, BANK]) for i in range(2)], [st.ps(f"qk_v{i}", [P, BANK]) for i in range(2)]
            cleared, pe_done, dve_done, tile_out, own = (st.sem(n) for n in ("cleared", "pe_done", "dve_done", "tile_out", "own"))
            block = st.block()

            @block.tensor
            def _(pe):
                pe.wait_ge(cleared, 1)
                for n in range(8):
                    t, hf = n // 2, n % 2
                    r = slice(CH * hf, CH * hf + CH)
                    at = slice(n * CH, n * CH + CH)
                    if n:
                        pe.wait_ge(dve_done, 2 * n)
                    if hf == 0 and t >= 2:
                        pe.wait_ge(tile_out, t - 1)
                    for h in range(4):
                        ins = pe.matmul(ps_w[r, h * P:(h + 1) * P], turned[:, 4 * t + h, r], state[:, h, :],
                                        start=True, stop=True)
                    ins.then_inc(pe_done, 1)
                    for h in range(4):
                        pe.matmul(ps_o[t % 2][:, h * P + CH * hf:h * P + CH * hf + CH], state[:, h, :], q[:, h, at],
                                  start=True, stop=True)
                    pe.wait_ge(dve_done, 2 * n + 1)
                    for h in range(4):
                        ins = pe.matmul(ps_s[:, h * P:(h + 1) * P], ktok[r, t, h * P:(h + 1) * P], vnew[r, h, :],
                                        start=True, stop=True)
                    ins.then_inc(pe_done, 1)
                    if hf == 1:
                        for h in range(4):
                            ins = pe.matmul(ps_a[t % 2][:, h * P:(h + 1) * P], vnew[:, h, :], aqk[:, 4 * t + h, :],
                                            start=True, stop=True)
                        ins.then_inc(pe_done, 1)

            @block.vector
            def _(dve):
                chain = Chain(dve, own)
                dve.memset(state[:], 0.0).then_inc(cleared, 1)
                dve.wait_ge(cleared, 1)
                for n in range(8):
                    t, hf = n // 2, n % 2
                    r = slice(CH * hf, CH * hf + CH)
                    done = 2 * n + n // 2
                    dve.wait_ge(pe_done, done + 1)
                    dve.tensor_tensor(vnew[r], sol[r, 4 * t:4 * t + 4, 0:P],
                                      ps_w[r, :].rearrange("p (h j) -> p h j", j=P), ALU.add).then_inc(dve_done, 1)
                    dve.wait_ge(pe_done, done + 2)
                    for h in range(4):
                        ins = dve.scalar_tensor_tensor(out=state[:, h, :], in0=state[:, h, :],
                                                       scalar=ends[:, 4 * t + h, hf:hf + 1],
                                                       in1=ps_s[:, h * P:(h + 1) * P], op0=ALU.mult, op1=ALU.add)
                    ins.then_inc(dve_done, 1)
                    if hf == 1:
                        dve.wait_ge(pe_done, done + 3)
                        o = out[:, :, t * P:(t + 1) * P]
                        chain.link(dve.tensor_copy(o, ps_o[t % 2][:].rearrange("p (h t) -> p h t", t=P)))
                        dve.tensor_tensor(o, o, ps_a[t % 2][:].rearrange("p (h t) -> p h t", t=P),
                                          ALU.add).then_inc(tile_out, 1)
                    dve.wait_ge(dve_done, 2 * n + 2)


def rows_to_tokens(nc, name, rows, out, ident):
    m = rows.shape[0]
    with Stage(nc, name) as st:
        ps = st.ps("turned", [P, 4, m])
        turned = st.sem("turned")
        block = st.block()

        @block.tensor
        def _(pe):
            for t in range(4):
                ins = pe.transpose(ps[:, t, :], rows[:, t * P:(t + 1) * P], ident[0:m, 0:m])
            ins.then_inc(turned, 1)

        @block.vector
        def _(dve):
            dve.wait_ge(turned, 1)
            dve.tensor_copy(out[:], ps[:])


Q0, KV0, G0, DN0, AB0, Z0, MQ0 = 0, 512, 1280, 1304, 2840, 2848, 3360


def mixer_weights(d):
    W, kv = d["w_in_2"], d["w_mem_kv_2"]
    wv = W.rearrange("(k p) n -> p k n", p=P)
    v_blocks = [([(lambda buf, i=i: buf[:, :, P * i:P * i + P],
                   wv[:, k0:k0 + 4, KV0 + 384 + 256 * i:KV0 + 512 + 256 * i]) for i in range(2)],
                 [P, P], list(range(k0, k0 + 4))) for k0 in (0, 4)]
    return {"nsa_in": pair_blocks(wv, Q0, 0) + pair_blocks(wv, Q0, 2) + weight_blocks(W, KV0, 256)
            + weight_blocks(W, KV0 + 256, 128) + weight_blocks(W, KV0 + 512, 128) + weight_blocks(W, G0, 24),
            "nsa_v": v_blocks,
            "cmp_k": weight_blocks(d["cmp_k_w1_2"], 0, 256, kc=16), "cmp_v": weight_blocks(d["cmp_v_w1_2"], 0, 256, kc=16),
            "dn_in": weight_blocks(W, DN0, 1536) + weight_blocks(W, Z0, 512) + weight_blocks(W, AB0, 8),
            "mem_q": weight_blocks(W, MQ0, 512), "mem_k": weight_blocks(kv, 0, 512),
            "mem_v": weight_blocks(kv, 512, 512, width=512),
            "merge_gates": weight_blocks(d["w_branch_gate_2"], 0, 3 * D),
            **{f"merge{b}": weight_blocks(d[n], 0, D, kc=4)
               for b, n in enumerate(("w_branch_nsa_2", "w_branch_dn_2", "w_branch_mem_2"))},
            "mix_out": weight_blocks(d["w_out_2"], 0, D)}


def mixer(nc, d, w, c, v, x):
    with ExitStack() as keep:
        def sb(name, shape, stack=keep, dtype=F32):
            return stack.enter_context(nc.sbuf_tensor("mix_" + name, shape, dtype))

        def pair(name, shape, stack):
            return [sb(f"{name}_{part}", shape, stack, F32R) for part in ("high", "low")]

        def parts(tiles):
            return [lambda k, t=t: t[:, k, :] for t in tiles]

        u2 = pair("u", [P, KD, S], keep)
        u = parts(u2)
        branch = [sb(f"branch{i}", [P, 4, S]) for i in range(3)]
        norm(nc, "mix_pre", lambda k: x[:, k, :], S, lambda k: v("mix_pre_norm_2", k, 1), c["ones"], split=u)

        with ExitStack() as inner:
            q = sb("q", [P, 4, S], inner)
            ks = sb("keys", [P, 4, S], inner)
            vs = sb("values", [P, 4, 256], inner)
            gates, gate_rows = sb("gates", [P, 4, 24], inner), sb("gate_rows", [24, S], inner)
            outs = ([(q[:, i, :], 0.125) for i in range(4)] + [(ks[:, i, :], None) for i in range(4)]
                    + [(gate_rows[:], None)])
            linear(nc, "nsa_in", w, *u, S,
                   lambda e, n, ps: copy_on(e, nc, outs[n][0], ps[0:outs[n][0].shape[0], 0:S], outs[n][1]))

            linear_tokens(nc, "nsa_v", w, *u, S, lambda e, b, t, ps: copy_on(e, nc, vs[:, t, :], ps[:, 0:256]))
            rows_to_tokens(nc, "nsa_gate_turn", gate_rows[:], gates, c["ident"])
            kc, vc = sb("k_cmp", [P, N_CMP], inner), sb("v_cmp", [N_CMP, P], inner)
            compress(nc, w, ks[:, 0:2, :], (v("cmp_pos_k"), v("cmp_pos_v")), (d["cmp_k_w2_2"], d["cmp_v_w2_2"]),
                     c["ident"], kc, vc)
            with Stage(nc, "nsa_gates") as st:
                opened = st.sem("opened")
                block = st.block()

                @block.scalar
                def _(act):
                    act.activation(gates[:], gates[:], ACT.Sigmoid).then_inc(opened, 1)

                @block.vector
                def _(dve):
                    dve.wait_ge(opened, 1)
                    dve.tensor_scalar(gates[:, 0, 0:8], gates[:, 0, 0:8], c["has_block"], None, ALU.mult)

            o = [sb(f"o{i}", [P, 4, 512], inner) for i in range(3)]
            table = sb("table", [P, 8, 896], inner)
            rel_bias_table(nc, d, table)
            units = []
            for t in range(4):
                for h in range(8):
                    b = 64 * (h // 4)
                    y0 = 384 - P * t
                    common = dict(q=q[b:b + 64, h % 4, t * P:(t + 1) * P])
                    ends = y0 + 31 + 16 * (N_CMP - 1) + 1
                    units.append(dict(common, keys=[kc[b:b + 64, :]], bias=table[:, h, y0 + 31:ends:16],
                                      values=[vc[:, b:b + 64]], out=o[0][:, t, 64 * h:64 * h + 64],
                                      rows=gates[:, t, h:h + 1]))
                    for n in range(2):
                        units.append(dict(common, keys=[ks[b:b + 64, 2 + n, 0:(t + 1) * P]],
                                          bias=table[:, h, y0:y0 + (t + 1) * P],
                                          values=[vs[:, j, P * n + b:P * n + b + 64] for j in range(t + 1)],
                                          out=o[1 + n][:, t, 64 * h:64 * h + 64],
                                          rows=gates[:, t, 8 * (n + 1) + h:8 * (n + 1) + h + 1]))
            attention(nc, "nsa", units, c["ident"])
            with Stage(nc, "nsa_sum") as st:
                own = st.sem("own")
                block = st.block()

                @block.vector
                def _(dve):
                    chain = Chain(dve, own)
                    chain.link(dve.tensor_tensor(o[1][:], o[1][:], o[0][:], ALU.add))
                    dve.tensor_tensor(o[2][:], o[2][:], o[1][:], ALU.add)
            to_features(nc, "nsa_turn", [([o[2][:, t, i * P:(i + 1) * P] for t in range(4)], None, branch[0][:, i, :])
                                         for i in range(4)], c["ident"])

        with ExitStack() as inner:
            zg = sb("dn_z", [P, 4, S], inner)
            qkv, ab = sb("qkv", [P, 12, S], inner), sb("ab", [P, 4, 8], inner)
            ab_rows = sb("ab_rows", [8, S], inner)
            with nc.sbuf_tensor("dn_padded", [P, 2, S + 3], F32) as padded:
                zero(nc, "dn_pad", [padded[:]])

                def evict(act, n, ps):
                    if n < 12:
                        return act.copy(padded[:, n % 2, 3:3 + S], ps[:, 0:S])
                    if n < 16:
                        return act.activation(zg[:, n - 12, :], ps[:, 0:S], ACT.Silu)
                    return act.copy(ab_rows[:], ps[0:8, 0:S])

                def convolve(dve, chain, n):
                    o = qkv[:, n, :]
                    chain.link(dve.tensor_scalar(o, padded[:, n % 2, 0:S], v("dn_conv", n, 1), None, ALU.mult))
                    for tap in (1, 2, 3):
                        ins = dve.scalar_tensor_tensor(out=o, in0=padded[:, n % 2, tap:tap + S],
                                                       scalar=v("dn_conv", 12 * tap + n, 1), in1=o,
                                                       op0=ALU.mult, op1=ALU.add)
                        if tap < 3:
                            chain.link(ins)
                    return ins

                linear(nc, "dn_in", w, *u, S, evict, engines="a", after=(convolve, 12))
            in_place(nc, "dn_conv_silu", [qkv[:, i, :] for i in range(12)], ACT.Silu)
            rows_to_tokens(nc, "dn_ab_turn", ab_rows[:], ab, c["ident"])
            delta_branch(nc, d, c, v, qkv, ab, branch[1], branch[2])
            head_norm(nc, "dn_out_norm", [branch[1][:, i, :] for i in range(4)], [v("dn_out_norm")] * 4, c["group128"])
            with Stage(nc, "dn_gated") as st:
                block = st.block()

                @block.vector
                def _(dve):
                    dve.tensor_tensor(branch[1][:], branch[1][:], zg[:], ALU.mult)

        with ExitStack() as inner:
            mq, mk = sb("mem_q", [P, 4, S], inner), sb("mem_k", [P, 4, 256], inner)
            mv, mo = sb("mem_v", [P, 2, 512], inner), sb("mem_o", [P, 4, 512], inner)
            mem, mem_n2 = sb("mem", [P, KD, 256], inner), pair("mem_n", [P, KD, 256], inner)
            mem_n = parts(mem_n2)
            load(nc, "mem_load", [(mem[:], d["mem"].rearrange("(k p) t -> p k t", p=P))])
            norm(nc, "mem_norm", lambda k: mem[:, k, :], 256,
                 lambda k: v("mem_norm_2", k, 1), c["ones"], split=mem_n)
            linear(nc, "mem_q", w, *u, S,
                   lambda e, n, ps: copy_on(e, nc, mq[:, n, :], ps[:, 0:S], 128.0 ** -0.5))
            linear(nc, "mem_k", w, *mem_n, 256,
                   lambda e, n, ps: copy_on(e, nc, mk[:, n, :], ps[:, 0:256]))
            linear_tokens(nc, "mem_v", w, *mem_n, 256,
                          lambda e, b, t, ps: copy_on(e, nc, mv[:, t, :], ps[:]))
            attention(nc, "mem", [dict(q=mq[:, h, t * P:(t + 1) * P], keys=[mk[:, h, :]], bias=None,
                                       values=[mv[:, j, h * P:(h + 1) * P] for j in range(2)],
                                       out=mo[:, t, h * P:(h + 1) * P]) for t in range(4) for h in range(4)], c["ident"])
            to_features(nc, "mem_turn", [([mo[:, t, i * P:(i + 1) * P] for t in range(4)], None, branch[2][:, i, :])
                                         for i in range(4)], c["ident"])

        with ExitStack() as inner:
            gate = sb("branch_gates", [P, 24, S], inner)
            linear(nc, "merge_gates", w, *u, S,
                   lambda e, n, ps: e.activation(gate[:, n, :], ps[:, 0:S], ACT.Sigmoid), engines="a")
            branch2 = parts(pair("branch_now", [P, 4, S], inner))
            for b in range(3):
                linear(nc, f"merge{b}", w, *branch2, S,
                       lambda e, n, ps: e.tensor_tensor(gate[:, 8 * b + n, :], gate[:, 8 * b + n, :], ps[:, 0:S], ALU.mult),
                       kc=4, engines="v", raw=lambda k: branch[b][:, k, :])
            with Stage(nc, "merge_sum") as st:
                own = st.sem("own")
                block = st.block()

                @block.vector
                def _(dve):
                    chain = Chain(dve, own)
                    chain.link(dve.tensor_tensor(gate[:, 0:8, :], gate[:, 0:8, :], gate[:, 8:16, :], ALU.add))
                    dve.tensor_tensor(gate[:, 0:8, :], gate[:, 0:8, :], gate[:, 16:24, :], ALU.add)
            linear(nc, "mix_out", w, *u, S,
                   lambda e, n, ps: copy_on(e, nc, gate[:, 8 + n, :], ps[:, 0:S]),
                   raw=lambda k: gate[:, k, :])
            norm(nc, "mix_post", lambda k: gate[:, 8 + k, :], S,
                 lambda k: v("mix_post_norm_2", k, 1), c["ones"], residual=lambda k: x[:, k, :])


def constants():
    out = {}
    ident = np.eye(P, dtype=np.float32)
    ones = np.ones((P, P), np.float32)
    group64 = np.kron(np.eye(2), np.ones((64, 64)) / 64).astype(np.float32)
    swap = np.zeros((P, P), np.float32)
    for f in range(P):
        if f % 32 < 16:
            swap[f + 16, f] = -1.0
        else:
            swap[f - 16, f] = 1.0
    t = np.arange(S)
    pos = np.stack([t // 64, t % 64], 0).astype(np.float32)
    inv = (np.float32(10000.0) ** (-np.arange(16, dtype=np.float32) / np.float32(16))).astype(np.float32)
    f = np.arange(P) % 64
    ang = (pos[f // 32] * inv[f % 16][:, None]).astype(np.float32)
    out["cos"], out["sin"] = np.cos(ang).astype(np.float32), np.sin(ang).astype(np.float32)
    col = np.arange(64)
    start = np.clip(col - 8, 0, 48)
    window = np.where((col[None] >= start[:, None]) & (col[None] < start[:, None] + 16), 0.0, NEG)
    window = np.concatenate([window, window], 0).astype(np.float32)
    small = {"ident": ident, "ones": ones, "group64": group64, "swap": swap, "window": window}
    s_i, t_i = np.arange(P)[:, None], np.arange(P)[None, :]
    same64, same16 = s_i // 64 == t_i // 64, s_i // 16 == t_i // 16
    for name, before in (("fwd", s_i < t_i), ("rev", s_i > t_i)):
        small[f"strict_{name}"] = (before & same64).astype(np.float32)
        small[f"incl_{name}"] = ((before | (s_i == t_i)) & same64).astype(np.float32)
    small["same16"] = same16.astype(np.float32)
    small["heads2"] = np.kron(np.eye(2), np.ones((64, 64))).astype(np.float32)
    has = (np.arange(P) >= 31).astype(np.float32)[:, None]
    small["has_block"] = has
    small["group128"] = np.full((P, P), 1 / 128, np.float32)
    small["root128"] = np.full((P, 1), 128.0 ** -0.5, np.float32)
    first = (np.arange(P) == 0)[:, None]
    small["half_root"] = np.full((P, 1), 0.5 ** 0.5, np.float32)
    small["sum_root"] = np.where(first, 1.0, 0.5 ** 0.5).astype(np.float32)
    small["diff_root"] = np.where(first, 0.0, 0.5 ** 0.5).astype(np.float32)
    out["small"] = np.concatenate(list(small.values()), 1)
    where, at = {}, 0
    for k, v in small.items():
        where[k] = (at, v.shape[1])
        at += v.shape[1]
    w = 2 * np.pi * (np.arange(S)[None, :] + 0.5) / (2 * S) * np.arange(S)[:, None]
    out["dft"] = np.stack([np.cos(w), np.sin(w)]).astype(np.float32)
    out["idft"] = (np.stack([np.cos(w).T, np.sin(w).T]) / S).astype(np.float32)
    ti = np.arange(S, dtype=np.float32)
    tt = ti / np.float32(S - 1)
    bands = np.linspace(1e-4, 15, 16, dtype=np.float32)
    ang = (np.float32(2.0 * np.pi) * bands[None, :] * ti[:, None] / np.float32(S)).astype(np.float32)
    out["feats"] = np.concatenate([tt[:, None], np.cos(ang), -np.sin(ang)], -1).T.astype(np.float32).copy()
    deltas = np.linspace(np.log(1e-2) / 0.3, np.log(1e-2) / 1.5, S, dtype=np.float32)
    out["decay"] = np.exp(-tt[:, None] * np.abs(deltas)).astype(np.float32)
    m = np.arange(2 * S)
    dist = (S - 1) - m
    dd = np.maximum(dist, 0)
    logb = 16 + (np.log(np.maximum(dd, 1).astype(np.float32) / 16) / np.log(128 / 16) * 16).astype(np.int32)
    bucket = np.where(dd < 16, dd, np.minimum(logb, 31))
    out["bucket"] = (np.arange(32)[:, None] == bucket[None]).astype(np.float32)
    out["causal"] = np.broadcast_to(np.where(dist >= 0, 0.0, NEG), (8, 2 * S)).astype(np.float32).copy()
    return out, where


def columns(v):
    return np.asarray(v).reshape(-1, P).T


def vectors(i):
    v = {
        "cond": np.stack([columns(i["c"][0]), columns(i["c_ctx"])], 2).reshape(P, -1),
        "attn_ada_b": columns(i["attn_ada_b"][0]), "rec_ada_b": columns(i["rec_ada_b"][0]),
        "q_gain": np.tile(i["gqa_q_gain"][0], 2)[:, None], "k_gain": np.tile(i["gqa_k_gain"][0], 2)[:, None],
        "mu": columns(i["rwkv_mu"][0]),
        "w0": columns(i["rwkv_w0"][0].reshape(-1)), "a0": columns(i["rwkv_a0"][0].reshape(-1)),
        "hy_short": columns(i["hy_short"][0].reshape(-1)), "hy_skip": columns(i["hy_skip"][0].reshape(-1)),
        "hy_b1": np.tile(i["hy_b1"][0], 2)[:, None], "hy_b2": np.tile(i["hy_b2"][0], 2)[:, None],
        "r_k": columns(i["rwkv_r_k"][0].reshape(-1)),
        "dn_conv": columns(i["dn_conv_w_2"][0].reshape(-1)),
        "dn_out_norm": columns(i["dn_out_norm_2"][0]),
        "cmp_pos_k": np.tile(i["cmp_pos_k_2"][0].T, (2, 1)), "cmp_pos_v": np.tile(i["cmp_pos_v_2"][0].T, (2, 1)),
    }
    for name in ("attn_norm", "rec_norm", "rwkv_k_k", "rwkv_k_a", "rwkv_gn_w", "rwkv_gn_b", "ffn1_pre_norm_2",
                 "ffn1_post_norm_2", "mix_pre_norm_2", "mem_norm_2", "mix_post_norm_2", "ffn2_pre_norm_2",
                 "ffn2_post_norm_2"):
        v[name] = columns(i[name][0])
    v["final_norm"] = columns(i["final_norm"])
    where, at = {}, 0
    for k, a in v.items():
        where[k] = (at, a.shape[1])
        at += a.shape[1]
    return np.ascontiguousarray(np.concatenate(list(v.values()), 1)), where
class Columns:

    def __init__(self, tile, where):
        self.tile, self.where = tile, where

    def __call__(self, name, first=0, count=None):
        at, n = self.where[name]
        n = n - first if count is None else count
        return self.tile[:, at + first:at + first + n]


def rec_weights(d):
    W = d["rec_w_in"]
    return {"rec_gate": weight_blocks(W, 1664, 512), "hy_in": weight_blocks(W, 2176, 2048),
            "rwkv_in": weight_blocks(W, 0, 1664)}


def rec_layer(nc, d, w, streams, c, v, x, ctx, mod, gs):
    with ExitStack() as keep:
        def sb(name, shape, stack=keep):
            return stack.enter_context(nc.sbuf_tensor("rec_" + name, shape, F32))

        y = sb("y", [P, KD, S])
        with ExitStack() as mid:
            gate, vt, ends = sb("gate", [P, 4, S], mid), sb("v_tokens", [P, 6, 512], mid), sb("ends", [P, 2, 4, TT // CH], mid)
            v_feat, bonus = sb("v_features", [P, 4, S], mid), sb("bonus", [P, 4, S], mid)
            with ExitStack() as shifted:
                us = sb("shifted", [P, 13, TT], shifted)
                with ExitStack() as inner:
                    h = [inner.enter_context(nc.sbuf_tensor("rec_h_" + part, [P, KD, TT], F32R))
                         for part in ("high", "low")]
                    norm(nc, "rec_norm_x", lambda k: x[:, k, :], S, lambda k: gs[:, k, 0:1], c["ones"],
                         split=[lambda k, t=t: t[:, k, 0:S] for t in h], shift=lambda k: mod[:, k, 0:1], scratch=y)
                    norm(nc, "rec_norm_ctx", lambda k: ctx[:, k, :], LC, lambda k: gs[:, k, 1:2], c["ones"],
                         split=[lambda k, t=t: t[:, k, S:TT] for t in h], shift=lambda k: mod[:, k, 1:2], scratch=y[:, :, 0:LC])
                    h = [lambda k, t=t: t[:, k, :] for t in h]
                    linear(nc, "rec_gate", w, *h, S, lambda e, n, ps: copy_on(e, nc, gate[:, n, :], ps[:, 0:S]))
                    hyena_input(nc, d, w, v, h, [y[:, 0:4], y[:, 4:8], bonus[:]], v_feat[:])
                    rwkv_input(nc, w, v, h, us, y[:])
                    streams.close()
                to_features(nc, "rwkv_vt", [([us[:, 8 + i, t * P:(t + 1) * P] for i in range(4)], None, vt[:, t, :])
                                            for t in range(6)], c["ident"])
                in_sbuf_copy(nc, "rwkv_v", v_feat[:], us[:, 8:12, 0:S])
                rwkv_features(nc, "rwkv_feat", d, c, v, [us[:, i, :] for i in range(13)], bonus, ends)
            scanned = sb("scanned", [P, 4, S], mid)
            rwkv_scan(nc, d, c, vt, ends, scanned)
            group_norm_out(nc, "rwkv_out", c, v, scanned, bonus, v_feat, gate, y[:, 0:4, :])
        hyena_branch(nc, d, c, v, y[:, 4:8, :])
        out_weights = WeightStream(nc, keep, "rec_out", {"rec_out": weight_blocks(d["rec_w_out"], 0, D)})
        gated_out(nc, "rec_out", out_weights, lambda k: y[:, k, :], x, None, mod)


def program(nc, d, vec_at, const_at):
    Stage.used = 0
    for name, shape in (("s_rpb", [64, 8 * 15, 127]), ("s_feat", [2, 4, 512, TT]), ("s_rel", [8, P, 2 * S]),
                        ("s_hy", [4 * 512, S])):
        d[name] = nc.dram_tensor(name, shape, F32, kind="Internal").ap()
    with ExitStack() as keep:
        def sb(name, shape, stack=keep):
            return stack.enter_context(nc.sbuf_tensor(name, shape, F32))

        out_stored = keep.enter_context(nc.semaphore("out_stored"))
        x = sb("x", [P, KD, S])
        vec, const = sb("vectors", list(d["vec"].shape)), sb("constants", list(d["c_small"].shape))
        v, constant = Columns(vec, vec_at), Columns(const, const_at)
        c = {n: constant(n) for n in const_at}
        with ExitStack() as first:
            ctx = sb("ctx", [P, KD, LC], first)
            mods = [(sb(f"mod{i}", [P, 24, 2], first), sb(f"gain_scale{i}", [P, KD, 2], first)) for i in range(2)]
            q_gain = sb("q_gain", [P, 1], first)
            streams = first.enter_context(ExitStack())
            w = WeightStream(nc, streams, "first_w", {
                "adaln": [b for n in ("attn", "rec") for b in weight_blocks(d[n + "_ada_w"], 0, 3 * D, width=512)],
                **attn_weights(d), **rec_weights(d)})
            w.start()
            load(nc, "inputs", [(x[:], d["x"].rearrange("(k p) t -> p k t", p=P)), (vec[:], d["vec"]),
                                (ctx[:], d["ctx"].rearrange("(k p) t -> p k t", p=P)), (const[:], d["c_small"])])
            cond = v("cond").rearrange("p (k j) -> p k j", j=2)
            adaln(nc, w, cond, [(v(n + "_ada_b"), v(n + "_norm"), *mods[i]) for i, n in enumerate(("attn", "rec"))],
                  c["ident"])
            with Stage(nc, "gains") as st:
                block = st.block()

                @block.vector
                def _(dve):
                    dve.tensor_scalar(q_gain[:], v("q_gain"), 0.125, None, ALU.mult)
            c["q_gain"], c["k_gain"] = q_gain[:], v("k_gain")
            attn_layer(nc, d, w, c, x, ctx, *mods[0])
            rec_layer(nc, d, w, streams, c, v, x, ctx, *mods[1])
            out = sb("first_out", [P, KD, S], first)
            norm(nc, "final_norm", lambda k: x[:, k, :], S, lambda k: v("final_norm", k, 1), c["ones"],
                 out=lambda k: out[:, k, :])
            in_sbuf_copy(nc, "first_to_second", x[:], out[:])
        with ExitStack() as streams:
            w = WeightStream(nc, streams, "second_w", {**ffn_weights(d, 1), **mixer_weights(d), **ffn_weights(d, 2)})
            w.start()
            ffn(nc, "ffn1", d, w, c, v, x, 1)
            mixer(nc, d, w, c, v, x)
            ffn(nc, "ffn2", d, w, c, v, x, 2)
        with Stage(nc, "store_out") as st:
            block = st.block()

            @block.sync
            def _(sp):
                sp.dma_start(d["out"].rearrange("(k p) t -> p k t", p=P), x[:]).then_inc(out_stored, 16)
                sp.wait_ge(out_stored, 16)


_WEIGHTS = ["attn_ada_w", "attn_w_in", "na_rpb", "attn_w_out", "rec_ada_w", "rec_w_in", "rwkv_w_up", "rwkv_a_up",
            "hy_w1", "hy_w2", "hy_w3", "rec_w_out", "ffn1_w_gate_2", "ffn1_w_up_2", "ffn1_w_down_2", "w_in_2",
            "cmp_k_w1_2", "cmp_k_w2_2", "cmp_v_w1_2", "cmp_v_w2_2", "dn_a_log_2", "dn_dt_bias_2", "w_mem_kv_2",
            "w_branch_nsa_2", "w_branch_dn_2", "w_branch_mem_2", "w_branch_gate_2", "w_out_2", "ffn2_w_gate_2",
            "ffn2_w_up_2", "ffn2_w_down_2"]


def kernel(**inputs):
    import concourse.bacc as _bacc
    from concourse.bass_utils import run_bass_kernel_spmd as _run

    i = {name: np.asarray(a) for name, a in inputs.items()}
    consts, const_at = constants()
    vec, vec_at = vectors(i)
    arrays = {name: i[name][0] for name in _WEIGHTS}
    arrays["rel_bias_2"], arrays["hy_b3"] = i["rel_bias_2"], i["hy_b3"]
    arrays["x"], arrays["ctx"], arrays["mem"] = i["x"][0].T, i["ctx"][0].T, i["mem_2"][0].T
    arrays["vec"] = vec
    arrays.update({"c_" + name: a for name, a in consts.items()})
    nc = _bacc.Bacc("TRN2", target_bir_lowering=False, num_devices=1)
    sent, d = {}, {}
    for name, a in arrays.items():
        sent[f"in_{name}"] = np.ascontiguousarray(a)
        d[name] = nc.dram_tensor(f"in_{name}", a.shape, F32, kind="ExternalInput").ap()
    d["out"] = nc.dram_tensor("out_0", [D, S], F32, kind="ExternalOutput").ap()
    program(nc, d, vec_at, const_at)
    r = _run(nc, [sent], core_ids=[0])
    return np.ascontiguousarray(r.results[0]["out_0"].T)[None]
```

```python
from contextlib import ExitStack

import numpy as np
import concourse.bass as bass
from concourse import mybir

F32 = mybir.dt.float32
F32R = mybir.dt.float32r
ALU = mybir.AluOpType
ACT = mybir.ActivationFunctionType
AX = mybir.AxisListType
P = 128
BANK = 512
D = 1024
KD = D // P
S = 512
LC = 256
TT = S + LC
NEG = -1e30


class Stage:

    def __init__(self, nc, name):
        self.nc, self.name = nc, name

    used = 0

    def __enter__(self):
        self.stack = ExitStack()
        if Stage.used > 120:
            nc, free = self.nc, sorted(self.nc.free_semaphores)
            starts = [s for s in free if s - 1 not in free]
            for s in starts:
                nc.gpsimd.sem_clear(range(s, next(e for e in range(s, free[-1] + 2) if e not in free)))
            nc.all_engine_barrier()
            Stage.used = 0
        return self

    def __exit__(self, *e):
        return self.stack.__exit__(*e)

    def sb(self, name, shape, dtype=F32):
        return self.stack.enter_context(self.nc.sbuf_tensor(f"{self.name}_{name}", shape, dtype))

    def ps(self, name, shape):
        return self.stack.enter_context(self.nc.psum_tensor(f"{self.name}_{name}", shape, F32))

    def sem(self, name):
        Stage.used += 1
        return self.stack.enter_context(self.nc.semaphore(f"{self.name}_{name}"))

    def block(self):
        return self.stack.enter_context(self.nc.Block())


class Chain:

    def __init__(self, engine, sem):
        self.engine, self.sem, self.n = engine, sem, 0

    def link(self, ins):
        self.n += 1
        ins.then_inc(self.sem, 1)
        self.engine.wait_ge(self.sem, self.n)


def spans(n, step):
    return [(a, min(step, n - a)) for a in range(0, n, step)]


def load(nc, name, pairs):
    with Stage(nc, name) as st:
        landed = st.sem("landed")
        block = st.block()

        @block.sync
        def _(sp):
            for dst, src in pairs[0::2]:
                sp.dma_start(dst, src).then_inc(landed, 16)
            sp.wait_ge(landed, 16 * len(pairs))

        @block.scalar
        def _(act):
            for dst, src in pairs[1::2]:
                act.dma_start(dst, src).then_inc(landed, 16)


class Ahead:

    def __init__(self, nc, stack, name):
        self.nc, self.stack, self.name, self.count, self.held = nc, stack, name, 0, 0
        Stage.used += 1
        self.landed = stack.enter_context(nc.semaphore(f"{name}_landed"))

    def sb(self, name, shape):
        return self.stack.enter_context(self.nc.sbuf_tensor(f"{self.name}_{name}", shape, F32, side="right"))

    def start(self, dst, src):
        self.nc.sync.dma_start(dst, src).then_inc(self.landed, 16)
        self.count += 16

    def wait(self, engine):
        engine.wait_ge(self.landed, self.count)

    def arrive(self):
        self.held += 1
        with Stage(self.nc, f"{self.name}_arrived{self.held}") as st:
            block = st.block()

            @block.sync
            def _(sp):
                self.wait(sp)


class WeightStream:

    def __init__(self, nc, stack, name, blocks, bufs=4, splits=3):
        def sb(n, dtype):
            return stack.enter_context(nc.sbuf_tensor(f"{name}_{n}", [P, 1024], dtype, side="right"))

        def sem(n):
            Stage.used += 1
            return stack.enter_context(nc.semaphore(f"{name}_{n}"))

        self.nc, self.bufs, self.loaded, self.blocks, self.ranges = nc, bufs, 0, [], {}
        for stage, of in blocks.items():
            self.ranges[stage] = (len(self.blocks), len(self.blocks) + len(of))
            self.blocks += of
        self.raw = [sb(f"raw{i}", F32) for i in range(bufs)]
        self.splits = splits
        self.high, self.low = ([sb(f"{n}{i}", F32R) for i in range(splits)] for n in ("high", "low"))
        self.landed = [sem(f"w_landed{i}") for i in range(bufs)]
        self.high_done, self.split_done = sem("w_high_done"), sem("w_split_done")
        self.landings, total = [], [0] * bufs
        for b, (loads, _, _) in enumerate(self.blocks):
            total[b % bufs] += 16 * len(loads)
            self.landings.append(total[b % bufs])

    def view(self, buf, b):
        _, widths, ks = self.blocks[b]
        return buf[:, 0:len(ks) * sum(widths)].rearrange("p (k n) -> p k n", k=len(ks))

    def load(self, queue, upto):
        for b in range(self.loaded, min(upto, len(self.blocks))):
            if b >= self.bufs:
                queue.wait_ge(self.split_done, b - self.bufs + 1)
            for place, src in self.blocks[b][0]:
                queue.dma_start(place(self.view(self.raw[b % self.bufs], b)), src
                                ).then_inc(self.landed[b % self.bufs], 16)
            self.loaded = b + 1

    def start(self):
        self.load(self.nc.sync, self.bufs)

    def load_stage(self, queue, name):
        self.load(queue, self.ranges[name][1] + self.bufs)

    def make_high(self, act, b, first, product_done, count):
        act.wait_ge(self.landed[b % self.bufs], self.landings[b])
        if b - self.splits >= first:
            act.wait_ge(product_done, count(b - self.splits))
        act.copy(self.view(self.high[b % self.splits], b), self.view(self.raw[b % self.bufs], b)).then_inc(self.high_done, 1)

    def make_low(self, dve, b):
        dve.wait_ge(self.high_done, b + 1)
        dve.tensor_tensor(self.view(self.low[b % self.splits], b), self.view(self.raw[b % self.bufs], b),
                          self.view(self.high[b % self.splits], b).bitcast(F32), ALU.subtract).then_inc(self.split_done, 1)


def weight_blocks(W, start, n, kc=KD, width=256):
    src = W.rearrange("(k p) n -> p k n", p=P)
    blocks = []
    for a, m in spans(n, width):
        for k0, kn in spans(kc, min(KD, 1024 // m)):
            blocks.append(([(lambda buf: buf, src[:, k0:k0 + kn, start + a:start + a + m])],
                           [c for _, c in spans(m, P)], list(range(k0, k0 + kn))))
    return blocks


def split_products(pe, out, parts, first=True, last=True):
    for j, (sh, sl, mh, ml) in enumerate(parts):
        pe.matmul(out, sh, mh, start=(first and j == 0), stop=False)
        pe.matmul(out, sh, ml, start=False, stop=False)
        ins = pe.matmul(out, sl, mh, start=False, stop=(last and j == len(parts) - 1))
    return ins


def linear(nc, name, w, x, lo, T, evict, kc=KD, engines="va", raw=None, after=None, before=None, save=None):
    b0, b1 = w.ranges[name]
    steps, n0 = [], 0
    for b in range(b0, b1):
        _, widths, ks = w.blocks[b]
        steps += [(b, i, n0 + i) for i in range(len(widths))]
        if ks[-1] == kc - 1:
            n0 += len(widths)
    done = {n: s + 1 for s, (_, _, n) in enumerate(steps)}
    count = {b: s + 1 for s, (b, _, _) in enumerate(steps)}
    finishes = {b: sorted(n for n in done if steps[done[n] - 1][0] == b) for b in range(b0, b1)}

    def stored_by(n):
        letter = engines[n % len(engines)]
        return letter, sum(engines[m % len(engines)] == letter for m in range(n + 1))

    with Stage(nc, name) as st:
        banks = -(-T // BANK)
        slots = 8 // banks
        ps = [st.ps(f"acc{i}", [P, banks * BANK]) for i in range(slots)]
        product_done, x_high, x_split = st.sem("product_done"), st.sem("x_high"), st.sem("x_split")
        stored = {"v": st.sem("stored_v"), "a": st.sem("stored_a")}
        followed, own = st.sem("followed"), st.sem("own")
        block = st.block()

        @block.sync
        def _(sp):
            w.load_stage(sp, name)
            if save is not None:
                save(sp, followed, stored)

        @block.tensor
        def _(pe):
            for b, i, n in steps:
                ks, m = w.blocks[b][2], w.blocks[b][1][i]
                if i == 0:
                    pe.wait_ge(w.split_done, b + 1)
                if b == b0 and i == 0 and raw is not None:
                    pe.wait_ge(x_split, kc)
                if n >= slots and ks[0] == 0:
                    letter, times = stored_by(n - slots)
                    pe.wait_ge(stored[letter], times)
                high, low = w.view(w.high[b % w.splits], b), w.view(w.low[b % w.splits], b)
                cols = slice(i * P, i * P + m)
                for t0, tn in spans(T, BANK):
                    ins = split_products(pe, ps[n % slots][0:m, t0:t0 + tn], [
                        (high[:, j, cols], low[:, j, cols], x(k)[:, t0:t0 + tn], lo(k)[:, t0:t0 + tn])
                        for j, k in enumerate(ks)], first=(ks[0] == 0), last=(ks[-1] == kc - 1))
                ins.then_inc(product_done, 1)

        def evictions(engine, letter, b):
            for n in finishes[b]:
                if engines[n % len(engines)] == letter:
                    engine.wait_ge(product_done, done[n])
                    if after is not None and 2 <= n < after[1] + 2:
                        engine.wait_ge(followed, n - 1)
                    if before is not None:
                        before(engine, n, stored)
                    evict(engine, n, ps[n % slots]).then_inc(stored[letter], 1)

        @block.vector
        def _(dve):
            chain = Chain(dve, own)
            for k in range(kc if raw is not None else 0):
                dve.wait_ge(x_high, k + 1)
                dve.tensor_tensor(lo(k), raw(k), x(k).bitcast(F32), ALU.subtract).then_inc(x_split, 1)
            for b in range(b0, min(b0 + w.splits - 1, b1)):
                w.make_low(dve, b)
            for b in range(b0, b1):
                if b + w.splits - 1 < b1:
                    w.make_low(dve, b + w.splits - 1)
                evictions(dve, "v", b)
                for n in finishes[b]:
                    if after is not None and n < after[1]:
                        dve.wait_ge(stored["a"], n + 1)
                        after[0](dve, chain, n).then_inc(followed, 1)

        @block.scalar
        def _(act):
            for k in range(kc if raw is not None else 0):
                act.copy(x(k), raw(k)).then_inc(x_high, 1)
            for b in range(b0, min(b0 + w.splits - 1, b1)):
                w.make_high(act, b, b0, product_done, None)
            for b in range(b0, b1):
                if b + w.splits - 1 < b1:
                    w.make_high(act, b + w.splits - 1, b0, product_done, lambda b: count[b])
                evictions(act, "a", b)


def linear_tokens(nc, name, w, x, lo, tokens, evict, kc=KD):
    pieces = spans(tokens, P)
    nt = len(pieces)
    b0, b1 = w.ranges[name]
    group, g = {}, 0
    for b in range(b0, b1):
        group[b] = g
        g += w.blocks[b][2][-1] == kc - 1
    with Stage(nc, name) as st:
        ps = [st.ps(f"acc{i}", [P, BANK]) for i in range(8)]
        product_done = st.sem("product_done")
        stored = (st.sem("stored_v"), st.sem("stored_a"))
        block = st.block()

        @block.sync
        def _(sp):
            w.load_stage(sp, name)

        @block.tensor
        def _(pe):
            for b in range(b0, b1):
                _, widths, ks = w.blocks[b]
                pe.wait_ge(w.split_done, b + 1)
                high, low = w.view(w.high[b % w.splits], b), w.view(w.low[b % w.splits], b)
                for t, (t0, rows) in enumerate(pieces):
                    n = group[b] * nt + t
                    if n >= 8 and ks[0] == 0:
                        pe.wait_ge(stored[n % 2], (n - 8) // 2 + 1)
                    at = slice(t0, t0 + rows)
                    split_products(pe, ps[n % 8][0:rows, 0:sum(widths)], [
                        (x(k)[:, at], lo(k)[:, at], high[:, j, :], low[:, j, :]) for j, k in enumerate(ks)],
                        first=(ks[0] == 0), last=(ks[-1] == kc - 1)).then_inc(product_done, 1)

        def evictions(engine, which, b):
            if w.blocks[b][2][-1] == kc - 1:
                for t in range(nt):
                    n = group[b] * nt + t
                    if n % 2 == which:
                        engine.wait_ge(product_done, nt * (b - b0) + t + 1)
                        evict(engine, group[b], t, ps[n % 8]).then_inc(stored[which], 1)

        @block.vector
        def _(dve):
            for b in range(b0, min(b0 + w.splits - 1, b1)):
                w.make_low(dve, b)
            for b in range(b0, b1):
                if b + w.splits - 1 < b1:
                    w.make_low(dve, b + w.splits - 1)
                evictions(dve, 0, b)

        @block.scalar
        def _(act):
            for b in range(b0, min(b0 + w.splits - 1, b1)):
                w.make_high(act, b, b0, product_done, None)
            for b in range(b0, b1):
                if b + w.splits - 1 < b1:
                    w.make_high(act, b + w.splits - 1, b0, product_done, lambda b: nt * (b - b0 + 1))
                evictions(act, 1, b)


def copy_on(engine, nc, out, in_, scale=None):
    if engine is nc.vector or engine.engine == nc.vector.engine:
        if scale is None:
            return engine.tensor_copy(out, in_)
        return engine.tensor_scalar(out, in_, scale, None, ALU.mult)
    if scale is None:
        return engine.copy(out, in_)
    return engine.activation(out, in_, ACT.Copy, scale=scale)


def norm(nc, name, x, T, gain, c, out=None, split=None, kc=KD, width=D, shift=None, residual=None, half=1.0,
         scratch=None):
    with Stage(nc, name) as st:
        rs = st.sb("rstd", [P, T])
        if scratch is None:
            squares = st.sb("squares", [P, kc, T])
        sq = scratch or (lambda k: squares[:, k, :])
        ps = st.ps("sum", [P, -(-T // BANK) * BANK])
        squared, summed, rooted = st.sem("squared"), st.sem("summed"), st.sem("rooted")
        scaled, high_done, own = st.sem("scaled"), st.sem("high_done"), st.sem("own")
        block = st.block()

        def low_part(engine, k):
            engine.wait_ge(high_done, k + 1)
            high = split[0](k).bitcast(F32)
            if shift is None:
                engine.tensor_tensor(split[1](k), sq(k), high, ALU.subtract)
            else:
                engine.scalar_tensor_tensor(out=split[1](k), in0=sq(k), scalar=shift(k), in1=high,
                                            op0=ALU.add, op1=ALU.subtract)

        @block.scalar
        def _(act):
            for k in range(kc):
                act.activation(sq(k), x(k), ACT.Square, scale=float(width) ** -0.5).then_inc(squared, 1)
            act.wait_ge(summed, 1)
            act.activation(rs[:], ps[:, 0:T], ACT.Sqrt, bias=c["eps"]).then_inc(rooted, 1)
            if split is not None:
                for k in range(kc):
                    act.wait_ge(scaled, k + 1)
                    if shift is None:
                        act.copy(split[0](k), sq(k)).then_inc(high_done, 1)
                    else:
                        act.activation(split[0](k), sq(k), ACT.Identity, bias=shift(k)).then_inc(high_done, 1)

        @block.tensor
        def _(pe):
            for t0, tn in spans(T, BANK):
                for k in range(kc):
                    if t0 == 0:
                        pe.wait_ge(squared, k + 1)
                    ins = pe.matmul(ps[:, t0:t0 + tn], c["ones"], sq(k)[:, t0:t0 + tn],
                                    start=(k == 0), stop=(k == kc - 1))
            ins.then_inc(summed, 1)

        @block.vector
        def _(dve):
            chain = Chain(dve, own)
            dve.wait_ge(rooted, 1)
            chain.link(dve.reciprocal(rs[:], rs[:]))
            for k in range(kc):
                dst = sq(k) if out is None else out(k)
                ins = dve.scalar_tensor_tensor(out=dst, in0=x(k), scalar=gain(k), in1=rs[:],
                                               op0=ALU.mult, op1=ALU.mult)
                ins.then_inc(scaled, 1)
            if residual is not None:
                for k in range(kc):
                    dve.wait_ge(scaled, k + 1)
                    dve.scalar_tensor_tensor(out=residual(k), in0=sq(k), scalar=half, in1=residual(k),
                                             op0=ALU.mult, op1=ALU.add)
            for k in range(0, kc if split is not None else 0, 1 if shift is not None else 2):
                low_part(dve, k)

        if split is not None and shift is None:
            @block.gpsimd
            def _(pool):
                for k in range(1, kc, 2):
                    low_part(pool, k)
def adaln(nc, w, cond, layers, ident):
    with ExitStack() as keep:
        rows = keep.enter_context(nc.sbuf_tensor("adaln_rows", [2, len(layers) * 3 * D], F32))
        high, low = (keep.enter_context(nc.sbuf_tensor("adaln_cond_" + n, [P, KD, 2], F32R)) for n in ("high", "low"))
        with Stage(nc, "adaln_silu") as st:
            silu = st.sb("silu", [P, KD, 2])
            silu_done, high_done = st.sem("silu_done"), st.sem("high_done")
            block = st.block()

            @block.scalar
            def _(act):
                act.activation(silu[:], cond, ACT.Silu).then_inc(silu_done, 1)
                act.wait_ge(silu_done, 1)
                act.copy(high[:], silu[:]).then_inc(high_done, 1)

            @block.vector
            def _(dve):
                dve.wait_ge(high_done, 1)
                dve.tensor_tensor(low[:], silu[:], high[:].bitcast(F32), ALU.subtract)

        linear_tokens(nc, "adaln", w, lambda k: high[:, k, :], lambda k: low[:, k, :], 2,
                      lambda e, g, t, ps: copy_on(e, nc, rows[:, BANK * g:BANK * g + BANK], ps[0:2, :]))
        with Stage(nc, "adaln_turn") as st:
            ps = st.ps("m", [P, len(layers), 24, 2])
            turned, own = st.sem("turned"), st.sem("own")
            block = st.block()

            @block.tensor
            def _(pe):
                for i in range(len(layers)):
                    for n in range(24):
                        at = 3 * D * i + P * n
                        ins = pe.transpose(ps[:, i, n, :], rows[:, at:at + P], ident[0:2, 0:2])
                ins.then_inc(turned, 1)

            @block.vector
            def _(dve):
                chain = Chain(dve, own)
                dve.wait_ge(turned, 1)
                for i, (bias, gain, mod, gs) in enumerate(layers):
                    for j in range(2):
                        chain.link(dve.tensor_tensor(mod[:, :, j], ps[:, i, :, j], bias, ALU.add))
                        chain.link(dve.tensor_scalar(gs[:, :, j], mod[:, KD:2 * KD, j], 1.0, None, ALU.add))
                        chain.link(dve.tensor_tensor(gs[:, :, j], gs[:, :, j], gain, ALU.mult))


def head_norm(nc, name, c, chunks, gains, pick, spread, rope=None, outs=None, scaled=False, eps=None):
    n, T, rows = len(chunks), chunks[0].shape[1], spread.shape[0]
    per = 2 if rows == 16 else 1
    outs = outs or chunks
    with Stage(nc, name) as st:
        sq = [st.sb(f"sq{i}", [P, T]) for i in range(2)]
        spread_sb, rs = st.sb("spread", [rows, n * P]), st.sb("rs", [rows, T])
        width = -(-T // BANK) * BANK
        sums = st.ps("sums", [rows, width])
        ps = [st.ps(f"spread{i}", [P, width]) for i in range(2)]
        if rope is not None:
            turned = [st.ps(f"turned{i}", [P, BANK]) for i in range(2)]
            tmp = [st.sb(f"tmp{i}", [P, S]) for i in range(2)]
            cosine = [st.sb(f"cosine{i}", [P, S]) for i in range(2)]
        landed, squared, summed, rooted, inverted, spread_done = (
            st.sem(x) for x in ("landed", "squared", "summed", "rooted", "inverted", "spread_done"))
        normed, swapped, cosined, done, own = (st.sem(x) for x in ("normed", "swapped", "cosined", "done", "own"))
        block = st.block()

        @block.sync
        def _(sp):
            sp.dma_start(spread_sb[:], spread[:, 0:n * P]).then_inc(landed, 16)

        @block.scalar
        def _(act):
            for i in range(n):
                if i >= 2:
                    act.wait_ge(summed, i - 1)
                act.activation(sq[i % 2][:], chunks[i], ACT.Square,
                               scale=gains[i] if scaled else 1.0).then_inc(squared, 1)
            act.wait_ge(summed, n)
            act.activation(rs[:], sums[:, 0:T], ACT.Sqrt, bias=(c["eps"] if eps is None else eps)[0:rows]
                           ).then_inc(rooted, 1)

        def swap(pe, i):
            pe.wait_ge(normed, i + 1)
            if i >= 2:
                pe.wait_ge(done, i - 1)
            pe.matmul(turned[i % 2][:], rope[2], outs[i][:, 0:S], start=True, stop=True).then_inc(swapped, 1)

        @block.tensor
        def _(pe):
            for i in range(n):
                pe.wait_ge(squared, i + 1)
                for t0, tn in spans(T, BANK):
                    ins = pe.matmul(sums[:, t0:t0 + tn], pick[:, 16 - per * i:16 - per * i + rows],
                                    sq[i % 2][:, t0:t0 + tn], start=(i == 0), stop=(i == n - 1))
                ins.then_inc(summed, 1)
            pe.wait_ge(landed, 16)
            pe.wait_ge(inverted, 1)
            for i in range(n):
                if i >= 2:
                    pe.wait_ge(normed, i - 1)
                for t0, tn in spans(T, BANK):
                    ins = pe.matmul(ps[i % 2][:, t0:t0 + tn], spread_sb[:, i * P:(i + 1) * P], rs[:, t0:t0 + tn],
                                    start=True, stop=True)
                ins.then_inc(spread_done, 1)
                if rope is not None and i >= 1:
                    swap(pe, i - 1)
            if rope is not None:
                swap(pe, n - 1)

        if rope is not None:
            @block.gpsimd
            def _(pool):
                for i in range(n):
                    pool.wait_ge(normed, i + 1)
                    if i >= 2:
                        pool.wait_ge(done, i - 1)
                    pool.tensor_tensor(cosine[i % 2][:], outs[i][:, 0:S], rope[0], ALU.mult).then_inc(cosined, 1)

        @block.vector
        def _(dve):
            chain = Chain(dve, own)

            def turn(i):
                dve.wait_ge(swapped, i + 1)
                chain.link(dve.tensor_tensor(tmp[i % 2][:], turned[i % 2][:], rope[1], ALU.mult))
                dve.wait_ge(cosined, i + 1)
                dve.tensor_tensor(outs[i][:, 0:S], cosine[i % 2][:], tmp[i % 2][:], ALU.add).then_inc(done, 1)

            dve.wait_ge(rooted, 1)
            dve.reciprocal(rs[:], rs[:]).then_inc(inverted, 1)
            for i in range(n):
                dve.wait_ge(spread_done, i + 1)
                dve.scalar_tensor_tensor(out=outs[i], in0=chunks[i], scalar=gains[i], in1=ps[i % 2][:, 0:T],
                                         op0=ALU.mult, op1=ALU.mult).then_inc(normed, 1)
                if rope is not None and i >= 1:
                    turn(i - 1)
            if rope is not None:
                turn(n - 1)


def attention(nc, name, units, ident, ones, bufs=2):
    n_units = len(units)
    with Stage(nc, name) as st:
        lag = bufs - 1
        prob = [st.sb(f"prob{i}", [P, TT if bufs == 2 else S]) for i in range(bufs)]
        prob_t = [st.sb(f"prob_t{i}", [P, 6, P]) for i in range(2)]
        stat = st.sb("stat", [P, lag + 2, 8])
        spread = st.sb("spread", [P, 2, P])
        diag = [st.sb(f"diag{i}", [P, P]) for i in range(2)]
        score = [st.ps(f"score{i}", [P, 1024 if bufs == 2 else BANK]) for i in range(bufs)]
        turned = st.ps("turned", [P, 1024])
        out_ps = [st.ps(f"out{i}", [P, BANK]) for i in range(2)]
        scored, maxed, exped, transposed, copied, inverted, diag_done, weighed, stored, own = (
            st.sem(x) for x in ("scored", "maxed", "exped", "transposed", "copied", "inverted", "diag_done",
                                "weighed", "stored", "own"))
        block = st.block()

        def widths(u):
            return [k.shape[1] for k in u["keys"]]

        def tiles(u):
            return spans(sum(widths(u)), P)

        def rows_of(u):
            return slice(u["at"], u["at"] + u["out"].shape[0])

        @block.gpsimd
        def _(pool):
            for i, u in enumerate(units):
                pool.wait_ge(inverted, i + 1)
                if i >= 2:
                    pool.wait_ge(weighed, i - 1)
                rows = 1.0 if u.get("rows") is None else u["rows"]
                pool.tensor_scalar(diag[i % 2][:], ident, stat[:, i % (lag + 2), 6:7], rows,
                                   ALU.mult, ALU.mult).then_inc(diag_done, 1)

        @block.tensor
        def _(pe):
            def scores(i):
                u = units[i]
                if i >= bufs:
                    pe.wait_ge(exped, i - bufs + 1)
                at = 0
                for k in u["keys"]:
                    ins = pe.matmul(score[i % bufs][:, at:at + k.shape[1]], u["q"], k, start=True, stop=True)
                    at += BANK if at + k.shape[1] < sum(widths(u)) else 0
                ins.then_inc(scored, 1)

            def transposes(i):
                pe.wait_ge(exped, i + 1)
                if i >= 1:
                    pe.wait_ge(copied, i)
                for j, (a, m) in enumerate(tiles(units[i])):
                    ins = pe.transpose(turned[0:m, j * P:(j + 1) * P], prob[i % bufs][:, a:a + m], ident)
                ins.then_inc(transposed, 1)

            def weigh(i):
                pe.wait_ge(copied, i + 1)
                if i >= 2:
                    pe.wait_ge(stored, i - 1)
                u = units[i]
                last = len(tiles(u)) - 1
                r = rows_of(u)
                for j, (a, m) in enumerate(tiles(u)):
                    pe.matmul(out_ps[i % 2][r, 0:P], u["values"][j], prob_t[i % 2][0:m, j, :],
                              start=(j == 0), stop=(j == last))
                pe.wait_ge(diag_done, i + 1)
                pe.matmul(out_ps[i % 2][r, P:2 * P], ones[:, 0:u["out"].shape[0]], diag[i % 2][:],
                          start=True, stop=True).then_inc(weighed, 1)

            for i in range(n_units + lag + 1):
                if i < n_units:
                    scores(i)
                if i >= lag + 1:
                    weigh(i - lag - 1)
                if lag <= i < n_units + lag:
                    transposes(i - lag)

        @block.vector
        def _(dve):
            chain = Chain(dve, own)

            def maxima(i):
                u, s = units[i], stat[:, i % (lag + 2), :]
                dve.wait_ge(scored, i + 1)
                if u["bias"] is None:
                    n = sum(widths(u))
                    dve.tensor_reduce(s[:, 0:1], score[i % bufs][:, 0:n], AX.X, ALU.max, negate=True).then_inc(maxed, 1)
                    return
                if i >= bufs:
                    dve.wait_ge(transposed, i - bufs + 1)
                n = widths(u)[0]
                chain.link(dve.tensor_tensor_reduce(out=prob[i % bufs][:, 0:n], in0=score[i % bufs][:, 0:n], in1=u["bias"],
                                                    scale=1.0, scalar=-3e38, op0=ALU.add, op1=ALU.max,
                                                    accum_out=s[:, 1:2]))
                if len(u["keys"]) == 2:
                    m = widths(u)[1]
                    chain.link(dve.tensor_reduce(s[:, 2:3], score[i % bufs][:, BANK:BANK + m], AX.X, ALU.max))
                    dve.tensor_scalar(s[:, 0:1], s[:, 1:2], s[:, 2:3], -1.0, ALU.max, ALU.mult).then_inc(maxed, 1)
                else:
                    dve.tensor_scalar(s[:, 0:1], s[:, 1:2], -1.0, None, ALU.mult).then_inc(maxed, 1)

            def invert(i):
                u, s = units[i], stat[:, i % (lag + 2), :]
                dve.wait_ge(exped, i + 1)
                total = s[:, 3:4]
                if u["bias"] is not None and len(u["keys"]) == 2:
                    chain.link(dve.tensor_tensor(s[:, 5:6], s[:, 3:4], s[:, 4:5], ALU.add))
                    total = s[:, 5:6]
                dve.reciprocal(s[:, 6:7], total).then_inc(inverted, 1)

            def store(i):
                u, r = units[i], rows_of(units[i])
                dve.wait_ge(weighed, i + 1)
                chain.link(dve.tensor_copy(spread[r, i % 2, :], out_ps[i % 2][r, P:2 * P]))
                dve.tensor_tensor(u["out"], out_ps[i % 2][r, 0:P], spread[r, i % 2, :], ALU.mult).then_inc(stored, 1)

            for i in range(n_units + lag + 1):
                if i < n_units:
                    if i >= lag + 2:
                        dve.wait_ge(stored, i - lag - 1)
                    maxima(i)
                if lag <= i < n_units + lag:
                    invert(i - lag)
                if i >= lag + 1:
                    store(i - lag - 1)

        @block.scalar
        def _(act):
            def exponentials(i):
                u, s = units[i], stat[:, i % (lag + 2), :]
                act.wait_ge(maxed, i + 1)
                if u["bias"] is None:
                    if i >= bufs:
                        act.wait_ge(transposed, i - bufs + 1)
                    n = sum(widths(u))
                    act.activation(prob[i % bufs][:, 0:n], score[i % bufs][:, 0:n], ACT.Exp, bias=s[:, 0:1],
                                   accum_out=s[:, 3:4]).then_inc(exped, 1)
                    return
                n = widths(u)[0]
                ins = act.activation(prob[i % bufs][:, 0:n], prob[i % bufs][:, 0:n], ACT.Exp, bias=s[:, 0:1],
                                     accum_out=s[:, 3:4])
                if len(u["keys"]) == 2:
                    m = widths(u)[1]
                    ins = act.activation(prob[i % bufs][:, n:n + m], score[i % bufs][:, BANK:BANK + m], ACT.Exp,
                                         bias=s[:, 0:1], accum_out=s[:, 4:5])
                ins.then_inc(exped, 1)

            def copies(i):
                act.wait_ge(transposed, i + 1)
                if i >= 2:
                    act.wait_ge(weighed, i - 1)
                ts = tiles(units[i])
                full = len([m for _, m in ts if m == P])
                if full:
                    ins = act.copy(prob_t[i % 2][:, 0:full, :].rearrange("p j q -> p (j q)"), turned[:, 0:full * P])
                if full < len(ts):
                    m = ts[-1][1]
                    ins = act.copy(prob_t[i % 2][0:m, full, :], turned[0:m, full * P:(full + 1) * P])
                ins.then_inc(copied, 1)

            for i in range(n_units + lag):
                if i < n_units:
                    exponentials(i)
                if i >= lag:
                    copies(i - lag)


def to_features(nc, name, jobs, ident):
    n = len(jobs)
    with Stage(nc, name) as st:
        ps = [st.ps(f"turned{i}", [P, 1024]) for i in range(3)]
        turned, stored = st.sem("turned"), st.sem("stored")
        block = st.block()

        @block.tensor
        def _(pe):
            for i, (pieces, _, _) in enumerate(jobs):
                if i >= 3:
                    pe.wait_ge(stored, i - 2)
                for j, piece in enumerate(pieces):
                    ins = pe.transpose(ps[i % 3][:, j * P:(j + 1) * P], piece, ident)
                ins.then_inc(turned, 1)

        @block.vector
        def _(dve):
            for i, (pieces, factor, out) in enumerate(jobs):
                dve.wait_ge(turned, i + 1)
                src = ps[i % 3][:, 0:len(pieces) * P]
                if factor is None:
                    dve.tensor_copy(out, src).then_inc(stored, 1)
                else:
                    dve.tensor_tensor(out, src, factor, ALU.mult).then_inc(stored, 1)


def in_place(nc, name, parts, func):
    with Stage(nc, name) as st:
        block = st.block()

        @block.scalar
        def _(act):
            for part in parts:
                out, src = part if isinstance(part, tuple) else (part, part)
                act.activation(out, src, func)


NA_HEADS, NA_ROWS, NA_COLS, NA_TILES = 8, 15, 31, 14
NA_WIDE = 127


def na_bias_rows(nc, rpb, padded, ahead, pad_dram):
    zero(nc, "na_pad", [padded])
    with Stage(nc, "na_rows") as st:
        landed = st.sem("landed")
        block = st.block()

        @block.sync
        def _(sp):
            sp.dma_start(padded[:, 48:79], rpb.rearrange("h r c -> (h r) c")).then_inc(landed, 16)
            sp.wait_ge(landed, 16)
    ahead.start(pad_dram.rearrange("c r w -> r c w"),
                padded.rearrange("r (a w) -> r a w", a=1).broadcast_to([NA_HEADS * NA_ROWS, 64, NA_WIDE]))


def na_bias_tables(nc, ahead, pad_dram):
    table = ahead.sb("table", [P, NA_HEADS, NA_TILES, 64])
    ahead.wait(nc.sync)
    for h in range(NA_HEADS):
        for half in range(2):
            src = bass.AP(tensor=pad_dram.tensor, offset=(h * NA_ROWS + 1 - half) * NA_WIDE + 63,
                          ap=[[NA_HEADS * NA_ROWS * NA_WIDE - 1, 64], [NA_WIDE, NA_TILES], [1, 64]])
            ahead.start(table[64 * half:64 * half + 64, h], src)
    return table


def na_bias_mask(nc, ahead, table, mask):
    with Stage(nc, "attn_bias_mask") as st:
        block = st.block()

        def add(engine, heads):
            ahead.wait(engine)
            for h in heads:
                engine.tensor_tensor(table[:, h], table[:, h],
                                     mask.rearrange("p (a c) -> p a c", a=1).broadcast_to([P, NA_TILES, 64]), ALU.add)

        @block.vector
        def _(dve):
            add(dve, range(0, 5))

        @block.gpsimd
        def _(pool):
            add(pool, range(5, NA_HEADS))


def pair_blocks(wv, at, i0, kc=KD):
    def load(k0, i, s):
        c = P * (i - i0) + 64 * s
        return (lambda buf: buf[:, :, c:c + 64], wv[:, k0:k0 + 4, at + 256 * s + 64 * i:at + 256 * s + 64 * i + 64])

    return [([load(k0, i, s) for i in (i0, i0 + 1) for s in range(2)], [P, P], list(range(k0, k0 + 4)))
            for k0 in (0, 4)]


def attn_weights(d):
    W = d["attn_w_in"]
    wv = W.rearrange("(k p) n -> p k n", p=P)
    return {"attn_in": weight_blocks(W, 0, 1024) + weight_blocks(W, 1536, 512) + pair_blocks(wv, 2048, 0)
            + pair_blocks(wv, 2048, 2) + weight_blocks(W, 2816, 512) + weight_blocks(W, 2560, 128),
            "attn_v": weight_blocks(W, 1024, 512, width=512) + weight_blocks(W, 2688, 128),
            "attn_out": weight_blocks(d["attn_w_out"], 0, D)}


def attn_layer(nc, d, w, c, x, ctx, mod, gs):
    with ExitStack() as keep:
        def sb(name, shape):
            return keep.enter_context(nc.sbuf_tensor("attn_" + name, shape, F32))

        qa, ka, ga, qb, gb = (sb(n, [P, 4, TT]) for n in ("qa", "ka", "ga", "qb", "gb"))
        kb = sb("kb", [P, TT])
        va, vb = sb("va", [P, 6, 512]), sb("vb", [P, 6, P])
        right = keep.enter_context(ExitStack())
        bias = Ahead(nc, right, "na_bias")
        na_bias_rows(nc, d["na_rpb"], va[0:NA_HEADS * NA_ROWS, 0, 0:NA_WIDE], bias, d["s_rpb"])
        roped = keep.enter_context(ExitStack())
        rope = roped.enter_context(nc.sbuf_tensor("attn_rope", [P, 2, S], F32))
        tables = Ahead(nc, roped, "rope")
        for i, n in enumerate(("c_cos", "c_sin")):
            tables.start(rope[:, i, :], d[n])
        with ExitStack() as inner:
            h = [inner.enter_context(nc.sbuf_tensor("attn_h_" + part, [P, KD, TT], F32R)) for part in ("high", "low")]
            norm(nc, "attn_norm_x", lambda k: x[:, k, :], S, lambda k: gs[:, k, 0:1], c,
                 split=[lambda k, t=t: t[:, k, 0:S] for t in h], shift=lambda k: mod[:, k, 0:1],
                 scratch=lambda k: (qa, ka)[k // 4][:, k % 4, 0:S])
            norm(nc, "attn_norm_ctx", lambda k: ctx[:, k, :], LC, lambda k: gs[:, k, 1:2], c,
                 split=[lambda k, t=t: t[:, k, S:TT] for t in h], shift=lambda k: mod[:, k, 1:2],
                 scratch=lambda k: (qa, ka)[k // 4][:, k % 4, 0:LC])
            h = [lambda k, t=t: t[:, k, :] for t in h]
            outs = [(t[:, i, :], 0.125 if t is qa else None) for t in (qa, ka, ga, qb, gb) for i in range(4)]
            outs.append((kb[:], None))
            bias.wait(nc.sync)
            linear(nc, "attn_in", w, *h, TT, lambda e, n, ps: copy_on(e, nc, outs[n][0], ps[:, 0:TT], outs[n][1]))
            linear_tokens(nc, "attn_v", w, *h, TT,
                          lambda e, g, t, ps: copy_on(e, nc, vb[:, t, :] if g else va[:, t, :],
                                                      ps[:, 0:P] if g else ps[:, 0:512]))
        tables.arrive()
        table = na_bias_tables(nc, bias, d["s_rpb"])
        head_norm(nc, "attn_head_norm", c, [qb[:, i, :] for i in range(4)] + [kb[:]],
                  [c["q_gain"]] * 4 + [c["k_gain"]], c["pick_mean64"], d["c_spread2"], (rope[:, 0, :], rope[:, 1, :], c["swap"]))
        roped.close()
        with ExitStack() as inner:
            ob = inner.enter_context(nc.sbuf_tensor("attn_ob", [P, 4, TT], F32))
            na_bias_mask(nc, bias, table, c["window"])
            units = []
            for t in range(6):
                q_at = slice(t * P, (t + 1) * P)
                for h in range(8):
                    a, b = 64 * (h % 2), 64 * (h // 4)
                    first = 4 if t >= 4 else 0
                    local = [] if t >= 4 else [ka[a:a + 64, h // 2, 0:S]]
                    units.append(dict(
                        q=qa[a:a + 64, h // 2, q_at], keys=local + [ka[a:a + 64, h // 2, S:TT]],
                        bias=None if t >= 4 else
                        table[:, h, 6 - 2 * t:14 - 2 * t, :].rearrange("p r c -> p (r c)"),
                        values=[va[:, j, 64 * h:64 * h + 64] for j in range(first, 6)],
                        at=a, out=qa[a:a + 64, h // 2, q_at]))
                    grouped = [] if t >= 4 else [kb[b:b + 64, 0:S]]
                    units.append(dict(
                        q=qb[b:b + 64, h % 4, q_at], keys=grouped + [kb[b:b + 64, S:TT]], bias=None,
                        values=[vb[:, j, b:b + 64] for j in range(first, 6)],
                        at=a, out=ob[a:a + 64, h // 2, q_at]))
            attention(nc, "attn", units, c["ident"], c["ones"])
            right.close()
            with Stage(nc, "attn_gated") as st:
                opened = st.sem("opened")
                block = st.block()

                @block.scalar
                def _(act):
                    for g in (ga, gb):
                        for i in range(4):
                            act.activation(g[:, i, :], g[:, i, :], ACT.Silu).then_inc(opened, 1)

                @block.vector
                def _(dve):
                    for n, (o, g, y) in enumerate(((qa, ga, qa), (ob, gb, qb))):
                        for i in range(4):
                            dve.wait_ge(opened, 4 * n + i + 1)
                            dve.tensor_tensor(y[:, i, :], o[:, i, :], g[:, i, :], ALU.mult)
        gated_out(nc, "attn_out", w, lambda k: (qa, qb)[k // 4][:, k % 4, :], x, ctx, mod)


def gated_out(nc, name, w, y, x, ctx, mod):
    T = TT if ctx is not None else S
    with ExitStack() as keep:
        y2 = [keep.enter_context(nc.sbuf_tensor(f"{name}_y_{part}", [P, KD, T], F32R)) for part in ("high", "low")]

        def evict(dve, n, ps):
            ins = dve.scalar_tensor_tensor(out=x[:, n, :], in0=ps[:, 0:S], scalar=mod[:, 16 + n, 0:1],
                                           in1=x[:, n, :], op0=ALU.mult, op1=ALU.add)
            if ctx is not None:
                ins = dve.scalar_tensor_tensor(out=ctx[:, n, :], in0=ps[:, S:TT], scalar=mod[:, 16 + n, 1:2],
                                               in1=ctx[:, n, :], op0=ALU.mult, op1=ALU.add)
            return ins

        linear(nc, name, w, *(lambda k, t=t: t[:, k, :] for t in y2), T, evict, engines="v", raw=y)
CH = 64
PAIRS = 4
PADDED = TT + 4


def rwkv_features(nc, name, d, c, v, us, kk, bonus, ends):
    with Stage(nc, name) as st:
        up = st.sb("up", [P, 4, 512])
        restart = st.sb("restart", [P, TT])
        not_ka = st.sb("not_ka", [P, 4])
        gate_ps = [st.ps(f"gate{i}", [P, 1024]) for i in range(4)]
        sw, sa = ([st.sb(f"{x}{i}", [P, TT]) for i in range(2)] for x in ("sw", "sa"))
        lsum, before, upto, kd = ([st.sb(f"{x}{i}", [P, TT]) for i in range(2)]
                                  for x in ("lsum", "before", "upto", "kd"))
        out = [[st.sb(f"out{j}_{i}", [P, TT]) for j in range(4)] for i in range(2)]
        (cleared, landed, tanhed, gates_done, sigmoids, summed_log,
         exps, features, own, keyed, pool_own, bonus_done) = (st.sem(x) for x in (
             "cleared", "landed", "tanhed", "gates_done", "sigmoids",
             "summed_log", "exps", "features", "own", "keyed", "pool_own", "bonus_done"))
        saved = [st.sem(f"saved{i}") for i in range(2)]
        block = st.block()
        lora = us[12]
        rate = float(np.exp(-0.5))

        @block.gpsimd
        def _(pool):
            pool.memset(up[:], 0.0).then_inc(cleared, 1)
            pool.memset(restart[:], 1.0).then_inc(cleared, 1)
            pool.wait_ge(cleared, 2)
            pool.memset(restart[:].rearrange("p (c t) -> p c t", t=CH)[:, :, 0:1], 0.0).then_inc(cleared, 1)
            def then(ins):
                pool_steps[0] += 1
                ins.then_inc(pool_own, 1)
                pool.wait_ge(pool_own, pool_steps[0])

            pool_steps = [0]
            then(pool.tensor_scalar(not_ka[:], v("rwkv_k_a"), -1.0, 1.0, ALU.mult, ALU.add))
            for n in range(8):
                dr, i = n // 4, n % 4
                a, k = sa[n % 2], kd[n % 2]
                pool.wait_ge(sigmoids, 2 * (n + 1))
                if n >= 2:
                    pool.wait_ge(features, n - 1)
                    pool.wait_ge(bonus_done, n - 1)
                then(pool.tensor_scalar(k[:], a[:], v("rwkv_k_a", i, 1), not_ka[:, i:i + 1], ALU.mult, ALU.add))
                pool.tensor_tensor(k[:], k[:], us[4 + i], ALU.mult).then_inc(keyed, 1)
                pool.wait_ge(keyed, n + 1)
                if dr == 0:
                    pool.tensor_copy(bonus[:, i, :], k[:, 0:S]).then_inc(bonus_done, 1)
                else:
                    pool.wait_ge(bonus_done, n)
                    then(pool.tensor_tensor(bonus[:, i, :], bonus[:, i, :], k[:, 0:S], ALU.add))
                    then(pool.tensor_scalar(bonus[:, i, :], bonus[:, i, :], v("r_k", i, 1), 0.5, ALU.mult, ALU.mult))
                    pool.tensor_tensor(bonus[:, i, :], bonus[:, i, :], us[i][:, 0:S], ALU.mult).then_inc(bonus_done, 1)

        @block.sync
        def _(sp):
            sp.wait_ge(cleared, 1)
            for i, w in enumerate((d["rwkv_w_up"][0], d["rwkv_w_up"][1], d["rwkv_a_up"][0], d["rwkv_a_up"][1])):
                sp.dma_start(up[32 * i:32 * i + 32, i, :], w).then_inc(landed, 16)
            for n in range(8):
                sp.wait_ge(features, n + 1)
                for j in range(4):
                    sp.dma_start(d["s_feat"][n // 4, j, (n % 4) * P:(n % 4) * P + P, :],
                                 out[n % 2][j][:]).then_inc(saved[n % 2], 16)
            for s in saved:
                sp.wait_ge(s, 16 * 16)

        @block.tensor
        def _(pe):
            pe.wait_ge(landed, 64)
            pe.wait_ge(tanhed, 1)
            for n in range(8):
                dr, i = n // 4, n % 4
                if n >= 2:
                    pe.wait_ge(sigmoids, 2 * (n - 1))
                for g in range(2):
                    for t0, tn in spans(TT, BANK):
                        ins = pe.matmul(gate_ps[2 * (n % 2) + g][:, t0:t0 + tn], up[:, 2 * g + dr, i * P:(i + 1) * P],
                                        lora[:, t0:t0 + tn], start=True, stop=True)
                ins.then_inc(gates_done, 1)

        @block.scalar
        def _(act):
            act.activation(lora[0:64, :], lora[0:64, :], ACT.Tanh).then_inc(tanhed, 1)
            for n in range(8):
                dr, i = n // 4, n % 4
                act.wait_ge(gates_done, n + 1)
                if n >= 2:
                    act.wait_ge(features, n - 1)
                act.activation(sw[n % 2][:], gate_ps[2 * (n % 2)][:, 0:TT], ACT.Sigmoid,
                               bias=v("w0", 4 * dr + i, 1)).then_inc(sigmoids, 1)
                act.activation(sa[n % 2][:], gate_ps[2 * (n % 2) + 1][:, 0:TT], ACT.Sigmoid,
                               bias=v("a0", 4 * dr + i, 1)).then_inc(sigmoids, 1)
                act.wait_ge(summed_log, n + 1)
                act.activation(upto[n % 2][:], lsum[n % 2][:], ACT.Exp, scale=-rate)
                act.activation(before[n % 2][:], before[n % 2][:], ACT.Exp, scale=-rate)
                act.activation(lsum[n % 2][:], lsum[n % 2][:], ACT.Exp, scale=rate).then_inc(exps, 1)

        @block.vector
        def _(dve):
            chain = Chain(dve, own)
            dve.wait_ge(cleared, 3)

            def sums(n):
                ls, w, bf = lsum[n % 2], sw[n % 2], before[n % 2]
                dve.wait_ge(sigmoids, 2 * (n + 1))
                chain.link(dve.tensor_tensor_scan(ls[:], restart[:], w[:], 0.0, ALU.mult, ALU.add))
                if n < 4:
                    dve.tensor_tensor(bf[:], ls[:], w[:], ALU.subtract).then_inc(summed_log, 1)
                else:
                    chunks = ls[:].rearrange("p (c t) -> p c t", t=CH)
                    chain.link(dve.tensor_tensor(bf[:].rearrange("p (c t) -> p c t", t=CH),
                                                 chunks[:, :, CH - 1:CH].broadcast_to([P, TT // CH, CH]), chunks,
                                                 ALU.subtract))
                    dve.tensor_tensor(ls[:], bf[:], w[:], ALU.add).then_inc(summed_log, 1)

            sums(0)
            for n in range(8):
                dr, i, p = n // 4, n % 4, n % 2
                a, o = sa[p], out[p]
                if n + 1 < 8:
                    sums(n + 1)
                dve.wait_ge(keyed, n + 1)
                chain.link(dve.tensor_tensor(a[:], a[:], kk[:, i, :], ALU.mult))
                if n >= 2:
                    dve.wait_ge(saved[p], 64 * (n // 2))
                dve.wait_ge(exps, n + 1)
                dve.tensor_tensor(o[0][:], kk[:, i, :], before[p][:], ALU.mult)
                dve.tensor_tensor(o[1][:], us[i], upto[p][:], ALU.mult)
                dve.tensor_tensor(o[2][:], a[:], lsum[p][:], ALU.mult)
                at = CH - 1 if dr == 0 else 0
                dve.tensor_copy(ends[:, dr, i, :], upto[p][:].rearrange("p (c t) -> p c t", t=CH)[:, :, at])
                dve.tensor_tensor(o[3][:], kd[p][:], lsum[p][:], ALU.mult).then_inc(features, 1)


HEADS_T = 8
TURN, GRAM, FLIP, POW2, POW4, POW8, TDIAG, OFF, Z1, Z2, Z3, LAY = range(12)
DVE_STEPS = (GRAM, FLIP, POW4, POW8, TDIAG, OFF, Z1, Z2, Z3)
ACT_STEPS = (TURN, FLIP, POW2, POW4, POW8, OFF, LAY)


def upto_step(steps, step, i, per=HEADS_T):
    return per * steps.index(step) + i + 1


def last_step(steps, step):
    return max(s for s in steps if s < step) if any(s < step for s in steps) else None


def rwkv_group(nc, name, c, feat, feat_landed, state, value, ends, y, dr, tile):
    lat = tile < 4
    strict, incl = (c["strict_fwd"], c["incl_fwd"]) if dr == 0 else (c["strict_rev"], c["incl_rev"])
    with Stage(nc, name) as st:
        tok = st.sb("tok", [P, PAIRS, 3, P])
        mask = st.sb("mask", [P, 2, P])
        off16 = st.sb("off16", [P, P])
        gram = st.sb("gram", [P, HEADS_T, 4, P])
        dn, en = st.sb("diag", [P, HEADS_T, P]), st.sb("off", [P, HEADS_T, P])
        dt, m = st.sb("diag_t", [P, HEADS_T, P]), st.sb("inv_t", [P, HEADS_T, P])
        p2, p4 = st.sb("pow2", [P, HEADS_T, 2, P]), st.sb("pow4", [P, HEADS_T, 2, P])
        p8, ft = st.sb("pow8", [P, HEADS_T, P]), st.sb("off_t", [P, HEADS_T, P])
        xs = st.sb("rhs", [P, 2, HEADS_T, CH])
        y1, z = (st.sb(n, [P, HEADS_T, 2, CH]) for n in ("y1", "z"))
        wt = st.sb("w_t", [P, PAIRS, P])
        san = st.sb("minus_sa", [P, PAIRS, P])
        ps = [st.ps(f"ps{i}", [P, BANK]) for i in range(8)]
        banks = 8
        (made, pe_done, dve_done, act_done, pool_done, scan_pe, scan_dve, own) = (
            st.sem(x) for x in ("made", "pe_done", "dve_done", "act_done", "pool_done", "scan_pe",
                                "scan_dve", "own"))
        block = st.block()
        halves = (0, 1) if dr == 0 else (1, 0)
        at = tile * P

        @block.tensor
        def _(pe):
            def order(step, i):
                n = step * HEADS_T + i
                for steps, sem in ((DVE_STEPS, dve_done), (ACT_STEPS, act_done)):
                    s = last_step(steps, step)
                    if s is not None:
                        pe.wait_ge(sem, upto_step(steps, s, i))
                return ps[n % banks]

            pe.wait_ge(*feat_landed)
            for i in range(HEADS_T):
                b = order(TURN, i)
                pair = i // 2
                srcs = (0, 2) if i % 2 == 0 else (3,)
                for j, s in enumerate(srcs):
                    ins = pe.transpose(b[:, j * P:(j + 1) * P], feat[:, s, pair, :], c["ident"])
                ins.then_inc(pe_done, 1)
            for i in range(HEADS_T):
                b = order(GRAM, i)
                pair, r = i // 2, slice(CH * (i % 2), CH * (i % 2) + CH)
                for j in range(2):
                    ins = pe.matmul(b[:, 2 * j * P:(2 * j + 2) * P], feat[r, 2 + j, pair, :],
                                    feat[r, 0:2, pair, :], start=True, stop=True)
                ins.then_inc(pe_done, 1)
            for i in range(HEADS_T):
                b = order(FLIP, i)
                pe.transpose(b[:, 0:P], gram[:, i, 0, :], c["ident"])
                pe.matmul(b[:, P:P + CH], gram[:, i, 2, :], value[:, tile, CH * i:CH * i + CH],
                          start=True, stop=True).then_inc(pe_done, 1)
            for i in range(HEADS_T):
                b = order(POW2, i)
                pe.wait_ge(pool_done, i + 1)
                pe.matmul(b[:, 0:P], dt[:, i, :], dn[:, i, :], start=True, stop=True)
                pe.matmul(b[:, P:2 * P], dn[:, i, :], dt[:, i, :], start=True, stop=True).then_inc(pe_done, 1)
            for i in range(HEADS_T):
                b = order(POW4, i)
                pe.matmul(b[:, 0:P], p2[:, i, 1, :], p2[:, i, 0, :], start=True, stop=True)
                pe.matmul(b[:, P:2 * P], p2[:, i, 0, :], p2[:, i, 1, :], start=True, stop=True)
                pe.matmul(b[:, 2 * P:3 * P], p2[:, i, 0, :], m[:, i, :], start=True, stop=True).then_inc(pe_done, 1)
            for i in range(HEADS_T):
                b = order(POW8, i)
                pe.matmul(b[:, 0:P], p4[:, i, 1, :], p4[:, i, 0, :], start=True, stop=True)
                pe.matmul(b[:, P:2 * P], p4[:, i, 0, :], m[:, i, :], start=True, stop=True).then_inc(pe_done, 1)
            for i in range(HEADS_T):
                b = order(TDIAG, i)
                pe.matmul(b[:, 0:P], p8[:, i, :], m[:, i, :], start=True, stop=True).then_inc(pe_done, 1)
            for i in range(HEADS_T):
                b = order(OFF, i)
                pe.matmul(b[:, 0:P], en[:, i, :], m[:, i, :], start=True, stop=True)
                pe.matmul(b[:, P:2 * P], m[:, i, :], xs[:, :, i, :],
                          start=True, stop=True).then_inc(pe_done, 1)
            for step in (Z1, Z2, Z3):
                for i in range(HEADS_T):
                    b = order(step, i)
                    src = y1 if step == Z1 else z
                    pe.matmul(b[:, 0:P], ft[:, i, :], src[:, i].rearrange("p a b -> p (a b)"),
                              start=True, stop=True).then_inc(pe_done, 1)
            for i in range(PAIRS):
                b = order(LAY, 2 * i + 1)
                pe.transpose(b[:, 0:P], xs[:, 1, 2 * i:2 * i + 2, :].rearrange("p a b -> p (a b)"),
                             c["ident"]).then_inc(pe_done, 1)
            pe.wait_ge(act_done, upto_step(ACT_STEPS, LAY, PAIRS - 1))
            pe.wait_ge(dve_done, upto_step(DVE_STEPS, Z3, HEADS_T - 1))
            for k, hf in enumerate(halves):
                r = slice(CH * hf, CH * hf + CH)
                if k:
                    pe.wait_ge(scan_dve, 2)
                for i in range(PAIRS):
                    ins = pe.matmul(ps[0][r, i * P:(i + 1) * P], wt[:, i, r], state[:, i, :], start=True, stop=True)
                ins.then_inc(scan_pe, 1)
                if lat:
                    for i in range(PAIRS):
                        pe.matmul(ps[2 + hf][:, i * CH:(i + 1) * CH], state[:, i, :], feat[:, 1, i, r],
                                  start=True, stop=True)
                for i in range(PAIRS):
                    pe.matmul(ps[1][:, i * P:(i + 1) * P], tok[r, i, 2, :], value[r, tile, i * P:(i + 1) * P],
                              start=True, stop=False)
                    pe.wait_ge(scan_dve, 2 * k + 1)
                    ins = pe.matmul(ps[1][:, i * P:(i + 1) * P], tok[r, i, 1, :], san[r, i, :], start=False, stop=True)
                ins.then_inc(scan_pe, 1)
            if lat:
                for i in range(HEADS_T):
                    r = slice(CH * (i % 2), CH * (i % 2) + CH)
                    cols = slice((i // 2) * P, (i // 2) * P + P)
                    pe.matmul(ps[4 + i % 2][r, cols], value[:, tile, CH * i:CH * i + CH], gram[:, i, 3, :],
                              start=True, stop=False)
                    ins = pe.matmul(ps[4 + i % 2][r, cols], san[:, i // 2, r], gram[:, i, 1, :],
                                    start=False, stop=True)
                ins.then_inc(scan_pe, 1)

        @block.gpsimd
        def _(pool):
            for j, mk in enumerate((strict, incl)):
                pool.tensor_copy(mask[:, j, :], mk)
            pool.tensor_scalar(off16[:], c["same16"], -1.0, 1.0, ALU.mult, ALU.add).then_inc(made, 1)
            pool.wait_ge(made, 1)
            for i in range(HEADS_T):
                pool.wait_ge(dve_done, upto_step(DVE_STEPS, GRAM, i))
                pool.wait_ge(act_done, upto_step(ACT_STEPS, TURN, i - i % 2 + 1))
                pool.tensor_tensor(dt[:, i, :], gram[:, i, 0, :], c["same16"], ALU.mult).then_inc(made, 1)
                pool.tensor_scalar(xs[:, 1, i, :], tok[:, i // 2, 0, CH * (i % 2):CH * (i % 2) + CH], -1.0, None,
                                   ALU.mult)
                pool.wait_ge(made, i + 2)
                pool.tensor_tensor(m[:, i, :], c["ident"], dt[:, i, :], ALU.subtract).then_inc(pool_done, 1)

        @block.vector
        def _(dve):
            def ready(step, i):
                dve.wait_ge(pe_done, step * HEADS_T + i + 1)
                return ps[(step * HEADS_T + i) % banks]

            dve.wait_ge(made, 1)
            for i in range(HEADS_T):
                b = ready(GRAM, i)
                dve.tensor_tensor(gram[:, i].rearrange("p (a b) t -> p a b t", a=2),
                                  b[:].rearrange("p (a b t) -> p a b t", a=2, b=2),
                                  bass.AP(tensor=mask[:].tensor, offset=mask[:].offset,
                                          ap=[list(mask[:].ap[0]), [0, 2], [P, 2], [1, P]]),
                                  ALU.mult).then_inc(dve_done, 1)
            for i in range(HEADS_T):
                b = ready(FLIP, i)
                dve.tensor_tensor(dn[:, i, :], b[:, 0:P], c["same16"], ALU.mult)
                dve.tensor_tensor(en[:, i, :], b[:, 0:P], off16[:], ALU.mult).then_inc(dve_done, 1)
            for step, col in ((POW4, 2), (POW8, 1), (TDIAG, 0)):
                for i in range(HEADS_T):
                    b = ready(step, i)
                    dve.tensor_tensor(m[:, i, :], m[:, i, :], b[:, col * P:(col + 1) * P], ALU.add).then_inc(dve_done, 1)
            for i in range(HEADS_T):
                b = ready(OFF, i)
                dve.tensor_copy(y1[:, i].rearrange("p a b -> p (a b)"), b[:, P:2 * P]).then_inc(dve_done, 1)
            for step in (Z1, Z2, Z3):
                for i in range(HEADS_T):
                    b = ready(step, i)
                    dst = xs[:, :, i, :] if step == Z3 else z[:, i]
                    dve.tensor_tensor(dst, y1[:, i], b[:, 0:P].rearrange("p (a b) -> p a b", a=2),
                                      ALU.subtract).then_inc(dve_done, 1)
            dve.wait_ge(dve_done, upto_step(DVE_STEPS, Z3, HEADS_T - 1))
            chain = Chain(dve, own)
            for k, hf in enumerate(halves):
                r = slice(CH * hf, CH * hf + CH)
                n_chunk = 2 * tile + hf
                dve.wait_ge(scan_pe, 2 * k + 1)
                dve.tensor_tensor(san[r].rearrange("p i (h j) -> p i h j", h=2),
                                  xs[r, 0].rearrange("p (i h) j -> p i h j", h=2),
                                  ps[0][r, :].rearrange("p (i h j) -> p i h j", h=2, j=CH), ALU.add).then_inc(scan_dve, 1)
                dve.wait_ge(scan_pe, 2 * k + 2)
                def end(i):
                    return ends[:, dr, i, n_chunk:n_chunk + 1]

                def new(i):
                    return y1[:, i].rearrange("p a b -> p (a b)")

                for i in range(PAIRS):
                    ins = dve.scalar_tensor_tensor(out=new(i), in0=ps[1][:, i * P:(i + 1) * P], scalar=end(i),
                                                   in1=c["heads2"], op0=ALU.mult, op1=ALU.mult)
                chain.link(ins)
                for i in range(PAIRS):
                    ins = dve.scalar_tensor_tensor(out=state[:, i, :], in0=state[:, i, :], scalar=end(i), in1=new(i),
                                                   op0=ALU.mult, op1=ALU.add)
                ins.then_inc(scan_dve, 1)
            if lat:
                dve.wait_ge(scan_pe, 5)
                yt = y[:, :, at:at + P]
                for hf in range(2):
                    a = yt[:, :, CH * hf:CH * hf + CH]
                    chain.link(dve.tensor_tensor(a, a, ps[2 + hf][:, 0:PAIRS * CH].rearrange("p (i t) -> p i t", t=CH),
                                                 ALU.add))
                for h in range(2):
                    r = slice(CH * h, CH * h + CH)
                    chain.link(dve.tensor_tensor(yt[r], yt[r], ps[4 + h][r, :].rearrange("p (i t) -> p i t", t=P),
                                                 ALU.add))

        @block.scalar
        def _(act):
            def ready(step, i):
                act.wait_ge(pe_done, step * HEADS_T + i + 1)
                if step in DVE_STEPS:
                    act.wait_ge(dve_done, upto_step(DVE_STEPS, step, i))
                return ps[(step * HEADS_T + i) % banks]

            for i in range(HEADS_T):
                b = ready(TURN, i)
                if i % 2 == 0:
                    act.copy(tok[:, i // 2, 0:2, :].rearrange("p a b -> p (a b)"), b[:, 0:2 * P]).then_inc(act_done, 1)
                else:
                    act.copy(tok[:, i // 2, 2, :], b[:, 0:P]).then_inc(act_done, 1)
            for i in range(HEADS_T):
                b = ready(FLIP, i)
                act.mul(xs[:, 0, i, :], b[:, P:P + CH], -1.0).then_inc(act_done, 1)
            for i in range(HEADS_T):
                b = ready(POW2, i)
                act.copy(p2[:, i].rearrange("p a b -> p (a b)"), b[:, 0:2 * P]).then_inc(act_done, 1)
            for i in range(HEADS_T):
                b = ready(POW4, i)
                act.copy(p4[:, i].rearrange("p a b -> p (a b)"), b[:, 0:2 * P]).then_inc(act_done, 1)
            for i in range(HEADS_T):
                b = ready(POW8, i)
                act.copy(p8[:, i, :], b[:, 0:P]).then_inc(act_done, 1)
            for i in range(HEADS_T):
                b = ready(OFF, i)
                act.copy(ft[:, i, :], b[:, 0:P]).then_inc(act_done, 1)
            for i in range(PAIRS):
                act.wait_ge(pe_done, LAY * HEADS_T + i + 1)
                act.copy(wt[:, i, :], ps[2 * i + 1][:, 0:P]).then_inc(act_done, 1)


def group_norm_out(nc, name, c, v, y, bonus, value, gate, out):
    with Stage(nc, name) as st:
        mean_ps, var_ps, bonus_ps = (st.ps(x, [P, BANK]) for x in ("mean", "var", "bonus"))
        sq, rs, t = (st.sb(x, [P, S]) for x in ("sq", "rs", "t"))
        summed, centred, squared, varied, rooted, done, own = (
            st.sem(x) for x in ("summed", "centred", "squared", "varied", "rooted", "done", "own"))
        block = st.block()

        @block.tensor
        def _(pe):
            for i in range(4):
                if i:
                    pe.wait_ge(done, i)
                pe.matmul(mean_ps[:], c["group64"], y[:, i, :], start=True, stop=True)
                pe.matmul(bonus_ps[:], c["heads2"], bonus[:, i, :], start=True, stop=True).then_inc(summed, 1)
                pe.wait_ge(squared, i + 1)
                pe.matmul(var_ps[:], c["group64"], sq[:], start=True, stop=True).then_inc(varied, 1)

        @block.scalar
        def _(act):
            for i in range(4):
                act.wait_ge(centred, i + 1)
                act.activation(sq[:], y[:, i, :], ACT.Square).then_inc(squared, 1)
                act.activation(gate[:, i, :], gate[:, i, :], ACT.Silu)
                act.wait_ge(varied, i + 1)
                if i:
                    act.wait_ge(done, i)
                act.activation(rs[:], var_ps[:], ACT.Sqrt, bias=c["eps_gn"]).then_inc(rooted, 1)

        @block.vector
        def _(dve):
            chain = Chain(dve, own)
            for i in range(4):
                dve.wait_ge(summed, i + 1)
                dve.tensor_tensor(y[:, i, :], y[:, i, :], mean_ps[:], ALU.subtract).then_inc(centred, 1)
                chain.link(dve.tensor_tensor(t[:], bonus_ps[:], value[:, i, :], ALU.mult))
                dve.wait_ge(rooted, i + 1)
                chain.link(dve.reciprocal(rs[:], rs[:]))
                chain.link(dve.scalar_tensor_tensor(out=rs[:], in0=y[:, i, :], scalar=v("rwkv_gn_w", i, 1), in1=rs[:],
                                                    op0=ALU.mult, op1=ALU.mult))
                chain.link(dve.scalar_tensor_tensor(out=rs[:], in0=rs[:], scalar=v("rwkv_gn_b", i, 1), in1=t[:],
                                                    op0=ALU.add, op1=ALU.add))
                dve.tensor_tensor(out[:, i, :], rs[:], gate[:, i, :], ALU.mult).then_inc(done, 1)
                dve.wait_ge(done, i + 1)


def zero(nc, name, parts):
    with Stage(nc, name) as st:
        block = st.block()

        @block.vector
        def _(dve):
            for part in parts:
                dve.memset(part, 0.0)


def rwkv_input(nc, w, v, h, us, scratch):
    mu = v("mu")
    flat = scratch.rearrange("p k t -> p (k t)")
    padded = flat[:, 0:2 * PADDED].rearrange("p (i t) -> p i t", i=2)
    total = flat[:, 2 * PADDED:2 * PADDED + TT]
    zero(nc, "rwkv_pad", [padded])

    def evict(act, n, ps):
        act.copy(padded[:, n % 2, 1:S + 1], ps[:, 0:S])
        return act.copy(padded[:, n % 2, S + 3:S + 3 + LC], ps[:, S:TT])

    def shift(dve, chain, n):
        u = padded[:, n % 2, :]
        for a, b, m in ((0, 1, S), (S, S + 3, LC)):
            t = total[:, a:a + m]
            chain.link(dve.tensor_tensor(t, u[:, b - 1:b - 1 + m], u[:, b + 1:b + 1 + m], ALU.add))
            chain.link(dve.scalar_tensor_tensor(out=t, in0=t, scalar=0.5, in1=u[:, b:b + m],
                                                op0=ALU.mult, op1=ALU.subtract))
            ins = dve.scalar_tensor_tensor(out=us[:, n, a:a + m], in0=t, scalar=mu[:, n:n + 1],
                                           in1=u[:, b:b + m], op0=ALU.mult, op1=ALU.add)
        return ins

    linear(nc, "rwkv_in", w, *h, TT, evict, engines="a", after=(shift, 13))


def rwkv_scan(nc, d, c, vt, ends, y):
    with nc.sbuf_tensor("rwkv_state", [P, 2, PAIRS, P], F32) as state:
        with Stage(nc, "rwkv_zero") as st:
            block = st.block()

            @block.vector
            def _(dve):
                dve.memset(state[:], 0.0)
                dve.memset(y[:], 0.0)
        with ExitStack() as right:
            feats = [right.enter_context(nc.sbuf_tensor(f"rwkv_feat{i}", [P, 4, PAIRS, P], F32, side="right"))
                     for i in range(2)]
            landed = [right.enter_context(nc.semaphore(f"rwkv_feat_landed{i}")) for i in range(2)]
            groups = [(dr, ((4, 5, 0, 1, 2, 3), (5, 4, 3, 2, 1, 0))[dr][step]) for step in range(6) for dr in range(2)]

            def start(n):
                dr, tile = groups[n]
                for j in range(4):
                    nc.sync.dma_start(feats[n % 2][:, j], d["s_feat"][dr, j].rearrange("(i p) t -> p i t", p=P)
                                      [:, :, tile * P:tile * P + P]).then_inc(landed[n % 2], 16)

            start(0)
            for n, (dr, tile) in enumerate(groups):
                if n + 1 < len(groups):
                    start(n + 1)
                rwkv_group(nc, f"rwkv{n}", c, feats[n % 2], (landed[n % 2], 64 * (n // 2 + 1)), state[:, dr], vt,
                           ends, y, dr, tile)


def in_sbuf_copy(nc, name, out, in_):
    with Stage(nc, name) as st:
        block = st.block()

        @block.vector
        def _(dve):
            dve.tensor_copy(out, in_)
def products(nc, name, jobs, engines=2, slots=6):
    with Stage(nc, name) as st:
        ps = [st.ps(f"acc{i}", [P, BANK]) for i in range(slots)]
        product_done, out_v, out_a = st.sem("product_done"), st.sem("out_v"), st.sem("out_a")
        block = st.block()

        @block.tensor
        def _(pe):
            for n, (rows, cols, terms, _) in enumerate(jobs):
                if n >= slots:
                    before = n - slots
                    if engines == 1:
                        pe.wait_ge(out_v, before + 1)
                    else:
                        pe.wait_ge((out_v, out_a)[before % 2], before // 2 + 1)
                for j, (lhs, rhs) in enumerate(terms):
                    ins = pe.matmul(ps[n % slots][0:rows, 0:cols], lhs, rhs, start=(j == 0), stop=(j == len(terms) - 1))
                ins.then_inc(product_done, 1)

        @block.vector
        def _(dve):
            for n in range(0, len(jobs), engines):
                dve.wait_ge(product_done, n + 1)
                jobs[n][3](dve, ps[n % slots][0:jobs[n][0], 0:jobs[n][1]]).then_inc(out_v, 1)

        if engines == 2:
            @block.scalar
            def _(act):
                for n in range(1, len(jobs), 2):
                    act.wait_ge(product_done, n + 1)
                    jobs[n][3](act, ps[n % slots][0:jobs[n][0], 0:jobs[n][1]]).then_inc(out_a, 1)


def copy_to(nc, out, scale=None):
    return lambda e, ps: copy_on(e, nc, out, ps, scale)


def filter_loads(nc, d, keep, inner):
    late, early = Ahead(nc, keep, "dft"), Ahead(nc, inner, "filt")
    t = {"dft": late.sb("table", [P, 2, 4, 512])}
    for name, shape in (("w3", [65, 2048]), ("decay", [P, 4, 512]), ("w1", [33, 64]), ("w2", [64, 64]),
                        ("feats", [33, S])):
        t[name] = early.sb(name, shape)
    for dst, src in ((t["w1"][:], d["hy_w1"]), (t["w2"][:], d["hy_w2"]), (t["feats"][:], d["c_feats"]),
                     (t["w3"][0:64, :], d["hy_w3"]), (t["w3"][64:65, :], d["hy_b3"]),
                     (t["decay"][:], d["c_decay"].rearrange("(a p) n -> p a n", p=P))):
        early.start(dst, src)
    for j in range(2):
        late.start(t["dft"][:, j], d["c_dft"][j].rearrange("(a p) n -> p a n", p=P))
    return early, late, t


def hyena_filters(nc, c, v, spectrum, root, loads, loaded, begin_next):
    early, late, tables = loads
    dft, w1, w2, feats, w3, decay = (tables[n] for n in ("dft", "w1", "w2", "feats", "w3", "decay"))
    two_pi = float(2 * np.pi)
    with ExitStack() as keep:
        def sb(name, shape, stack=keep):
            return stack.enter_context(nc.sbuf_tensor("filt_" + name, shape, F32))

        ab = sb("sum_difference", [P, 2, 2, 4, 512])
        with ExitStack() as inner:
            hid = sb("hid", [65, S], inner)
            taps = sb("taps", [P, 4, 2, 2, 512], inner)
            early.arrive()
            with Stage(nc, "filt_hidden") as st:
                arg, turns = st.sb("arg", [64, S]), st.sb("turns", [64, S])
                hid1 = st.sb("hid1", [64, S])
                ps = st.ps("hid", [64, BANK])
                summed, reduced, sined, own = (st.sem(x) for x in ("summed", "reduced", "sined", "own"))
                block = st.block()

                @block.gpsimd
                def _(pool):
                    pool.memset(hid[64:65, :], 1.0)

                @block.tensor
                def _(pe):
                    pe.matmul(ps[:], w1[:], feats[:], start=True, stop=True).then_inc(summed, 1)
                    pe.wait_ge(sined, 1)
                    pe.matmul(ps[:], w2[:], hid1[:], start=True, stop=True).then_inc(summed, 1)

                @block.vector
                def _(dve):
                    chain = Chain(dve, own)
                    for n, b in enumerate(("hy_b1", "hy_b2")):
                        dve.wait_ge(summed, n + 1)
                        chain.link(dve.tensor_scalar(arg[:], ps[:], v(b)[0:64, :], None, ALU.add))
                        chain.link(dve.tensor_scalar(turns[:], arg[:], 1.0 / two_pi, 12582912.0, ALU.mult, ALU.add))
                        chain.link(dve.tensor_scalar(turns[:], turns[:], -12582912.0, None, ALU.add))
                        chain.link(dve.scalar_tensor_tensor(out=arg[:], in0=turns[:], scalar=-6.28125, in1=arg[:],
                                                            op0=ALU.mult, op1=ALU.add))
                        chain.link(dve.scalar_tensor_tensor(out=arg[:], in0=turns[:], scalar=-(two_pi - 6.28125),
                                                            in1=arg[:], op0=ALU.mult, op1=ALU.add))
                        dve.tensor_scalar(arg[:], arg[:], 3.1415925, -3.1415925, ALU.min, ALU.max).then_inc(reduced, 1)
                        dve.wait_ge(sined, n + 1)

                @block.scalar
                def _(act):
                    for n, out in enumerate((hid1[:], hid[0:64, :])):
                        act.wait_ge(reduced, n + 1)
                        act.activation(out, arg[:], ACT.Sin).then_inc(sined, 1)

            def windowed(t, j):
                return lambda e, ps: e.tensor_tensor(taps[:, t, j // 2, j % 2, :], ps, decay[:, t, :], ALU.mult)

            products(nc, "filt_taps", [(P, 512, [(hid[:, t * P:(t + 1) * P], w3[:, 512 * j:512 * j + 512])],
                                        windowed(t, j)) for t in range(4) for j in range(4)], engines=1)
            with Stage(nc, "filt_sum") as st:
                block = st.block()

                @block.vector
                def _(dve):
                    for o in range(2):
                        dve.tensor_tensor(ab[:, o, 0], taps[:, :, 0, o, :], taps[:, :, 1, o, :], ALU.add)

                @block.gpsimd
                def _(pool):
                    for o in range(2):
                        pool.tensor_tensor(ab[:, o, 1], taps[:, :, 0, o, :], taps[:, :, 1, o, :], ALU.subtract)
        loaded.close()
        begin_next()
        late.arrive()
        with ExitStack() as inner:
            sq = sb("sq", [P, 2, 2, 4, 512], inner)
            with Stage(nc, "filt_sq") as st:
                squared, own = st.sem("squared"), st.sem("own")
                block = st.block()

                @block.scalar
                def _(act):
                    for o in range(2):
                        for j in range(2):
                            act.activation(sq[:, o, j, 0], ab[:, o, j, 0], ACT.Square, scale=(c["sum_root"], c["diff_root"])[j])
                            act.activation(sq[:, o, j, 1:4], ab[:, o, j, 1:4], ACT.Square,
                                           scale=c["half_root"]).then_inc(squared, 1)

                @block.vector
                def _(dve):
                    chain = Chain(dve, own)
                    for o in range(2):
                        dve.wait_ge(squared, 2 * o + 2)
                        chain.link(dve.tensor_tensor(sq[:, o, 0], sq[:, o, 0], sq[:, o, 1], ALU.add))
                        chain.link(dve.tensor_tensor(sq[:, o, 0, 0:2], sq[:, o, 0, 0:2], sq[:, o, 0, 2:4], ALU.add))
                        chain.link(dve.tensor_tensor(sq[:, o, 0, 0], sq[:, o, 0, 0], sq[:, o, 0, 1], ALU.add))

            products(nc, "filt_norm", [
                (P, 1, [(sq[:, o, 0, 0, i * P:(i + 1) * P], c["ones"][:, 0:1])],
                 copy_to(nc, root[:, 4 * o + i:4 * o + i + 1])) for o in range(2) for i in range(4)])
        with Stage(nc, "filt_root") as st:
            rooted = st.sem("rooted")
            block = st.block()

            @block.scalar
            def _(act):
                act.activation(root[:], root[:], ACT.Sqrt).then_inc(rooted, 1)

            @block.vector
            def _(dve):
                dve.wait_ge(rooted, 1)
                dve.reciprocal(root[:], root[:])

        products(nc, "filt_spectrum", [
            (P, 512, [(dft[:, j, t, w * P:(w + 1) * P], ab[:, o, j, t, :]) for t in range(4)],
             copy_to(nc, spectrum[:, o, j, w, :])) for o in range(2) for j in range(2) for w in range(4)])


def hyena_input(nc, d, w, v, h, parts, gate):
    with ExitStack() as keep:
        padded = keep.enter_context(nc.sbuf_tensor("hyin_padded", [P, 2, S + 2], F32))
        zero(nc, "hy_pad", [padded[:]])

        def evict(act, n, ps):
            if n < 12:
                return act.copy(padded[:, n % 2, 1:S + 1], ps[:, 0:S])
            return act.activation(gate[:, n - 12, :], ps[:, 0:S], ACT.Silu)

        def convolve(dve, chain, n):
            u = parts[n // 4][:, n % 4, :]
            chain.link(dve.tensor_scalar(u, padded[:, n % 2, 0:S], v("hy_short", n, 1), None, ALU.mult))
            for tap in (1, 2):
                ins = dve.scalar_tensor_tensor(out=u, in0=padded[:, n % 2, tap:tap + S],
                                               scalar=v("hy_short", 12 * tap + n, 1), in1=u,
                                               op0=ALU.mult, op1=ALU.add)
                if tap == 1:
                    chain.link(ins)
            return ins

        saved = keep.enter_context(nc.semaphore("hyin_saved"))

        def save(queue, followed, stored):
            out = d["s_hy"].rearrange("(i p) t -> p i t", p=P)
            for i, part in enumerate((*parts, gate)):
                if i < 3:
                    queue.wait_ge(followed, 4 * (i + 1))
                else:
                    queue.wait_ge(stored["a"], 16)
                queue.dma_start(out[:, 4 * i:4 * i + 4], part).then_inc(saved, 16)
            queue.wait_ge(saved, 64)

        linear(nc, "hy_in", w, *h, S, evict, engines="a", after=(convolve, 12), save=save)


def hyena_branch(nc, d, c, v, out, loads, loaded):
    with ExitStack() as keep:
        def sb(name, shape, stack=keep):
            return stack.enter_context(nc.sbuf_tensor("hy_" + name, shape, F32))

        spectrum = sb("spectrum", [P, 2, 2, 4, 512])
        root = sb("root", [P, 8])
        branch = Ahead(nc, keep, "hyena")
        dft, idft, inputs = loads[2]["dft"], [], []

        def begin():
            idft.append(branch.sb("idft", [P, 2, 4, 512]))
            inputs.append(branch.sb("inputs", [P, 16, S]))
            for j in range(2):
                branch.start(idft[0][:, j], d["c_idft"][j].rearrange("(a p) n -> p a n", p=P))
            branch.start(inputs[0][:], d["s_hy"].rearrange("(i p) t -> p i t", p=P))

        hyena_filters(nc, c, v, spectrum, root, loads, loaded, begin)
        branch.arrive()
        idft, u, gate = idft[0], inputs[0][:, 0:12, :], inputs[0][:, 12:16, :]
        z = u[:, 0:4, :]
        zt = sb("z_tokens", [P, 4, 512])
        zw, yw = sb("z_spectrum", [P, 2, 4, 512]), sb("y_spectrum", [P, 2, 4, 512])
        tmp = sb("tmp", [P, 2, 4, 512])
        for o in range(2):
            to_features(nc, f"hy_turn{o}", [([z[:, i, t * P:(t + 1) * P] for i in range(4)], None, zt[:, t, :])
                                            for t in range(4)], c["ident"])
            products(nc, f"hy_dft{o}", [
                (P, 512, [(dft[:, j, t, w * P:(w + 1) * P], zt[:, t, :]) for t in range(4)],
                 copy_to(nc, zw[:, j, w, :])) for j in range(2) for w in range(4)])
            with Stage(nc, f"hy_mult{o}") as st:
                own, crossed = st.sem("own"), st.sem("crossed")
                block = st.block()

                @block.vector
                def _(dve):
                    chain = Chain(dve, own)
                    dve.tensor_tensor(yw[:, 0], zw[:, 0], spectrum[:, o, 0], ALU.mult)
                    chain.link(dve.tensor_tensor(tmp[:, 0], zw[:, 1], spectrum[:, o, 1], ALU.mult))
                    dve.tensor_tensor(yw[:, 0], yw[:, 0], tmp[:, 0], ALU.subtract)
                    dve.wait_ge(crossed, 2)
                    dve.tensor_tensor(yw[:, 1], yw[:, 1], tmp[:, 1], ALU.add)

                @block.gpsimd
                def _(pool):
                    pool.tensor_tensor(yw[:, 1], zw[:, 0], spectrum[:, o, 1], ALU.mult).then_inc(crossed, 1)
                    pool.tensor_tensor(tmp[:, 1], zw[:, 1], spectrum[:, o, 0], ALU.mult).then_inc(crossed, 1)
            products(nc, f"hy_idft{o}", [
                (P, 512, [(yw[:, j, w, i * P:(i + 1) * P], idft[:, j, w, :]) for j in range(2) for w in range(4)],
                 copy_to(nc, tmp[:, 0, i, :], root[:, 4 * o + i:4 * o + i + 1])) for i in range(4)])
            with Stage(nc, f"hy_gate{o}") as st:
                own = st.sem("own")
                block = st.block()

                @block.vector
                def _(dve):
                    chain = Chain(dve, own)
                    for i in range(4):
                        chain.link(dve.scalar_tensor_tensor(out=tmp[:, 1, i, :], in0=z[:, i, :],
                                                            scalar=v("hy_skip", 4 * o + i, 1), in1=tmp[:, 0, i, :],
                                                            op0=ALU.mult, op1=ALU.add))
                        chain.link(dve.tensor_tensor(z[:, i, :], tmp[:, 1, i, :], u[:, 4 + 4 * o + i, :], ALU.mult))
                        if o == 1:
                            dve.tensor_tensor(out[:, i, :], z[:, i, :], gate[:, i, :], ALU.mult)
FF = 2816
FFK = FF // P


def ffn_weights(d, n):
    gate, up = d[f"ffn{n}_w_gate_2"], d[f"ffn{n}_w_up_2"]
    return {f"ffn{n}_in": [b for a in range(0, FF, 256) for W in (gate, up) for b in weight_blocks(W, a, 256)],
            f"ffn{n}_down": weight_blocks(d[f"ffn{n}_w_down_2"], 0, D, kc=FFK)}


def ffn(nc, name, d, w, c, v, x, n):
    with ExitStack() as keep:
        def sb(what, shape, dtype=F32, stack=keep):
            return stack.enter_context(nc.sbuf_tensor(f"{name}_{what}", shape, dtype))

        out = sb("out", [P, KD, S])
        with ExitStack() as inner:
            mid = [sb("mid_" + p, [P, FFK, S], F32R, inner) for p in ("high", "low")]
            with ExitStack() as first:
                h = [sb("h_" + p, [P, KD, S], F32R, first) for p in ("high", "low")]
                silu = sb("silu", [P, 4, S], stack=first)
                own = first.enter_context(nc.semaphore(f"{name}_own"))
                norm(nc, name + "_pre", lambda k: x[:, k, :], S, lambda k: v(f"ffn{n}_pre_norm_2", k, 1), c,
                     split=[lambda k, t=t: t[:, k, :] for t in h], scratch=lambda k: out[:, k, :])
                chain = Chain(nc.vector, own)

                def before(engine, t, stored):
                    if t % 4 < 2:
                        if t >= 8:
                            engine.wait_ge(stored["v"], 2 * (t // 4 - 1))
                    else:
                        engine.wait_ge(stored["a"], 2 * (t // 4) + t % 4 - 1)

                def evict(engine, t, ps):
                    s = silu[:, 2 * (t // 4 % 2) + t % 2, :]
                    if t % 4 < 2:
                        return engine.activation(s, ps[:], ACT.Silu)
                    m = 2 * (t // 4) + t % 2
                    chain.link(engine.tensor_tensor(s, s, ps[:], ALU.mult))
                    chain.link(engine.tensor_copy(mid[0][:, m, :], s))
                    return engine.tensor_tensor(mid[1][:, m, :], s, mid[0][:, m, :].bitcast(F32), ALU.subtract)

                linear(nc, name + "_in", w, *(lambda k, t=t: t[:, k, :] for t in h), S, evict,
                       engines="aavv", before=before)
            linear(nc, name + "_down", w, *(lambda k, t=t: t[:, k, :] for t in mid), S,
                   lambda e, m, ps: copy_on(e, nc, out[:, m, :], ps[:, 0:S]), kc=FFK)
        norm(nc, name + "_post", lambda k: out[:, k, :], S, lambda k: v(f"ffn{n}_post_norm_2", k, 1), c,
             residual=lambda k: x[:, k, :], half=0.5)


REL_WIDE = 2 * S


def rel_bias_lines(nc, d, ahead):
    bucket, bias = ahead.sb("bucket", [32, REL_WIDE]), ahead.sb("bias", [32, 8])
    causal, line = ahead.sb("causal", [8, REL_WIDE]), ahead.sb("line", [8, REL_WIDE])
    for dst, src in ((bucket[:], d["c_bucket"]), (bias[:], d["rel_bias_2"]), (causal[:], d["c_causal"])):
        ahead.start(dst, src)
    with Stage(nc, "rel_bias") as st:
        ps = st.ps("spread_line", [8, REL_WIDE])
        spread = st.sem("spread")
        block = st.block()

        @block.tensor
        def _(pe):
            ahead.wait(pe)
            for a in range(2):
                ins = pe.matmul(ps[:, a * BANK:(a + 1) * BANK], bias[:], bucket[:, a * BANK:(a + 1) * BANK],
                                start=True, stop=True)
            ins.then_inc(spread, 1)

        @block.vector
        def _(dve):
            ahead.wait(dve)
            dve.wait_ge(spread, 1)
            dve.tensor_tensor(line[:], ps[:], causal[:], ALU.add)
    ahead.start(d["s_rel"], line[:].rearrange("h (a m) -> h a m", a=1).broadcast_to([8, P, REL_WIDE]))


def rel_bias_table(nc, d, ahead):
    table = ahead.sb("table", [P, 8, 896])
    ahead.wait(nc.sync)
    ahead.start(table[:], bass.AP(tensor=d["s_rel"].tensor, offset=P - 1,
                                  ap=[[REL_WIDE - 1, P], [P * REL_WIDE, 8], [1, 896]]))
    return table


N_CMP = 31


def compress(nc, w, both, pos, w2, ident, keys, values, meanwhile):
    with ExitStack() as keep:
        def sb(name, shape, dtype=F32):
            return keep.enter_context(nc.sbuf_tensor("cmp_" + name, shape, dtype))

        n = 2 * N_CMP
        high, low = sb("high", [P, 2, 16, n], F32R), sb("low", [P, 2, 16, n], F32R)
        hid = sb("hid", [n, 2, 256])
        with Stage(nc, "cmp_blocks") as st:
            swapped = st.sb("swapped", [P, 2, S])
            blocks = st.sb("blocks", [P, 2, 16, n])
            moved, added, high_done = st.sem("moved"), st.sem("added"), st.sem("high_done")
            block = st.block()

            @block.sync
            def _(sp):
                sp.dma_start(swapped[0:64], both[64:128]).then_inc(moved, 16)
                sp.dma_start(swapped[64:128], both[0:64]).then_inc(moved, 16)

            @block.vector
            def _(dve):
                for moves in (False, True):
                    if moves:
                        dve.wait_ge(moved, 32)
                    for j in range(2):
                        for odd in range(2):
                            g, r = (1 - odd if moves else odd), slice(64 * odd, 64 * odd + 64)
                            kv = (swapped if moves else both)[r, j, :]
                            src = bass.AP(tensor=kv.tensor, offset=kv.offset + odd,
                                          ap=[list(kv.ap[0]), [2, 16], [16, N_CMP]])
                            at = pos[j][r, odd:32:2].rearrange("p (t a) -> p t a", a=1).broadcast_to([64, 16, N_CMP])
                            ins = dve.tensor_tensor(blocks[r, j, :, N_CMP * g:N_CMP * g + N_CMP], src, at, ALU.add)
                ins.then_inc(added, 1)
                dve.wait_ge(high_done, 1)
                dve.tensor_tensor(low[:], blocks[:], high[:].bitcast(F32), ALU.subtract)

            @block.scalar
            def _(act):
                act.wait_ge(added, 1)
                act.copy(high[:], blocks[:]).then_inc(high_done, 1)

        meanwhile()
        for j, name in enumerate(("cmp_k", "cmp_v")):
            linear_tokens(nc, name, w, *(lambda k, t=t: t[:, j, k, :] for t in (high, low)), n,
                          lambda e, g, t, ps: copy_on(e, nc, hid[:, j, :], ps[0:n, 0:256]), kc=16)
        with Stage(nc, "cmp_out") as st:
            w2_sb = st.sb("w2", [P, 2, 2, 64])
            hid_t = st.sb("hid_t", [P, 2, 2, n])
            turned = st.ps("turned", [P, 2, 2, n])
            out_ps = [st.ps(f"out{i}", [P, BANK]) for i in range(3)]
            landed, silu_done, turn_done, copied, out_done = (st.sem(x) for x in (
                "landed", "silu_done", "turn_done", "copied", "out_done"))
            block = st.block()

            @block.sync
            def _(sp):
                for j in range(2):
                    sp.dma_start(w2_sb[:, j], w2[j].rearrange("(a p) n -> p a n", p=P)).then_inc(landed, 16)

            @block.scalar
            def _(act):
                act.activation(hid[:], hid[:], ACT.Silu).then_inc(silu_done, 1)

            @block.tensor
            def _(pe):
                pe.wait_ge(silu_done, 1)
                for j in range(2):
                    for a in range(2):
                        ins = pe.transpose(turned[:, j, a, :], hid[:, j, a * P:(a + 1) * P], ident[0:n, 0:n])
                ins.then_inc(turn_done, 1)
                pe.wait_ge(landed, 32)
                pe.wait_ge(copied, 1)
                for g in range(2):
                    cols = slice(N_CMP * g, N_CMP * g + N_CMP)
                    for a in range(2):
                        pe.matmul(out_ps[g][64 * g:64 * g + 64, 0:N_CMP], w2_sb[:, 0, a, :], hid_t[:, 0, a, cols],
                                  start=(a == 0), stop=(a == 1))
                    for a in range(2):
                        ins = pe.matmul(out_ps[2][0:N_CMP, 64 * g:64 * g + 64], hid_t[:, 1, a, cols], w2_sb[:, 1, a, :],
                                        start=(a == 0), stop=(a == 1))
                ins.then_inc(out_done, 1)

            @block.vector
            def _(dve):
                dve.wait_ge(turn_done, 1)
                dve.tensor_copy(hid_t[:], turned[:]).then_inc(copied, 1)
                dve.wait_ge(out_done, 1)
                for g in range(2):
                    r = slice(64 * g, 64 * g + 64)
                    dve.tensor_copy(keys[r, :], out_ps[g][r, 0:N_CMP])
                dve.tensor_copy(values[:], out_ps[2][0:N_CMP, 0:P])


def solve(nc, name, c, n_mat, rhs, out, n, width):
    steps = ("flip", "pow2", "pow4", "pow8", "tdiag", "off", "z1", "z2", "z3")
    with Stage(nc, name) as st:
        off16 = st.sb("off16", [P, P])
        dn, en, dt, m = (st.sb(x, [P, n, P]) for x in ("diag", "off", "diag_t", "inv_t"))
        p2, p4 = st.sb("pow2", [P, n, 2, P]), st.sb("pow4", [P, n, 2, P])
        p8, ft = st.sb("pow8", [P, n, P]), st.sb("off_t", [P, n, P])
        y1, z = st.sb("y1", [P, n, width]), st.sb("z", [P, n, width])
        ps = [st.ps(f"ps{i}", [P, BANK]) for i in range(8)]
        made, split = st.sem("made"), st.sem("split")
        pe_done, dve_done, act_done, pool_done = (st.sem(x) for x in ("pe_done", "dve_done", "act_done", "pool_done"))
        block = st.block()

        dve_steps = ("flip", "pow4", "pow8", "tdiag", "off", "z1", "z2", "z3")
        act_steps = ("pow2", "pow4", "pow8", "off")

        def counted(of, step, i):
            return n * of.index(step) + i + 1

        @block.tensor
        def _(pe):
            def order(step, i):
                earlier = steps[:steps.index(step)]
                for of, sem in ((dve_steps, dve_done), (act_steps, act_done)):
                    before = [s for s in earlier if s in of]
                    if before:
                        pe.wait_ge(sem, counted(of, before[-1], i))
                return ps[i % 8]

            for i in range(n):
                pe.transpose(order("flip", i)[:, 0:P], n_mat[:, i, :], c["ident"]).then_inc(pe_done, 1)
            for i in range(n):
                b = order("pow2", i)
                pe.wait_ge(pool_done, i + 1)
                pe.matmul(b[:, 0:P], dt[:, i, :], dn[:, i, :], start=True, stop=True)
                pe.matmul(b[:, P:2 * P], dn[:, i, :], dt[:, i, :], start=True, stop=True).then_inc(pe_done, 1)
            for i in range(n):
                b = order("pow4", i)
                pe.matmul(b[:, 0:P], p2[:, i, 1, :], p2[:, i, 0, :], start=True, stop=True)
                pe.matmul(b[:, P:2 * P], p2[:, i, 0, :], p2[:, i, 1, :], start=True, stop=True)
                pe.matmul(b[:, 2 * P:3 * P], p2[:, i, 0, :], m[:, i, :], start=True, stop=True).then_inc(pe_done, 1)
            for i in range(n):
                b = order("pow8", i)
                pe.matmul(b[:, 0:P], p4[:, i, 1, :], p4[:, i, 0, :], start=True, stop=True)
                pe.matmul(b[:, P:2 * P], p4[:, i, 0, :], m[:, i, :], start=True, stop=True).then_inc(pe_done, 1)
            for i in range(n):
                pe.matmul(order("tdiag", i)[:, 0:P], p8[:, i, :], m[:, i, :], start=True, stop=True).then_inc(pe_done, 1)
            for i in range(n):
                b = order("off", i)
                pe.matmul(b[:, 0:P], en[:, i, :], m[:, i, :], start=True, stop=True)
                pe.matmul(b[:, P:P + width], m[:, i, :], rhs[:, i, :], start=True, stop=True).then_inc(pe_done, 1)
            for step, src in (("z1", y1), ("z2", z), ("z3", z)):
                for i in range(n):
                    pe.matmul(order(step, i)[:, 0:width], ft[:, i, :], src[:, i, :],
                              start=True, stop=True).then_inc(pe_done, 1)

        @block.gpsimd
        def _(pool):
            pool.tensor_scalar(off16[:], c["same16"], -1.0, 1.0, ALU.mult, ALU.add).then_inc(made, 1)
            pool.wait_ge(made, 1)
            for i in range(n):
                pool.tensor_tensor(dn[:, i, :], n_mat[:, i, :], c["same16"], ALU.mult)
                pool.tensor_tensor(en[:, i, :], n_mat[:, i, :], off16[:], ALU.mult)
                pool.wait_ge(dve_done, i + 1)
                pool.tensor_tensor(m[:, i, :], c["ident"], dt[:, i, :], ALU.subtract).then_inc(pool_done, 1)

        @block.vector
        def _(dve):
            def ready(step, i):
                dve.wait_ge(pe_done, counted(steps, step, i))
                return ps[i % 8]

            for i in range(n):
                dve.tensor_tensor(dt[:, i, :], ready("flip", i)[:, 0:P], c["same16"], ALU.mult).then_inc(dve_done, 1)
            for step, col in (("pow4", 2), ("pow8", 1), ("tdiag", 0)):
                for i in range(n):
                    b = ready(step, i)
                    dve.tensor_tensor(m[:, i, :], m[:, i, :], b[:, col * P:(col + 1) * P], ALU.add).then_inc(dve_done, 1)
            for i in range(n):
                dve.tensor_copy(y1[:, i, :], ready("off", i)[:, P:P + width]).then_inc(dve_done, 1)
            for step in ("z1", "z2", "z3"):
                for i in range(n):
                    dve.tensor_tensor((out if step == "z3" else z)[:, i, :], y1[:, i, :],
                                      ready(step, i)[:, 0:width], ALU.subtract).then_inc(dve_done, 1)

        @block.scalar
        def _(act):
            for step, dst, cols in (("pow2", p2, 2 * P), ("pow4", p4, 2 * P), ("pow8", p8, P), ("off", ft, P)):
                for i in range(n):
                    act.wait_ge(pe_done, counted(steps, step, i))
                    if step in dve_steps:
                        act.wait_ge(dve_done, counted(dve_steps, step, i))
                    o = dst[:, i] if cols == P else dst[:, i].rearrange("p a b -> p (a b)")
                    act.copy(o, ps[i % 8][:, 0:cols]).then_inc(act_done, 1)


def delta_branch(nc, d, c, v, qkv, ab, out, spare):
    with ExitStack() as keep:
        def sb(name, shape, stack=keep):
            return stack.enter_context(nc.sbuf_tensor("dn_" + name, shape, F32))

        q, k, val = qkv[:, 0:4], qkv[:, 4:8], qkv[:, 8:12]
        head_norm(nc, "dn_l2", c, [qkv[:, i, :] for i in range(8)], [c["root128"]] * 4 + [c["ones"][:, 0:1]] * 4,
                  c["pick_sum128"], d["c_spread1"])
        g, beta, sp_tmp = sb("g", [P, 4, 4]), sb("beta", [P, 4, 4]), sb("softplus", [P, 4, 4])
        gc, left, eg = sb("gc", [P, 4, 4]), sb("left", [P, 4, 4]), sb("exp_gc", [P, 4, 4])
        ktok, vtok = spare, out
        to_features(nc, "dn_turn", [([src[:, i, t * P:(t + 1) * P] for i in range(4)], None, dst[:, t, :])
                                    for src, dst in ((k, ktok), (val, vtok)) for t in range(4)], c["ident"])
        with Stage(nc, "dn_gates") as st:
            a_log, dt_bias = st.sb("a_log", [P, 4]), st.sb("dt_bias", [P, 4])
            x, neg, e = st.sb("x", [P, 4, 4]), st.sb("neg", [P, 4, 4]), st.sb("e", [P, 4, 4])
            ps = [st.ps(f"sum{i}", [P, BANK]) for i in range(2)]
            landed, exped, prepared, logged, decays, summed, own = (
                st.sem(n) for n in ("landed", "exped", "prepared", "logged", "decays", "summed", "own"))
            block = st.block()

            @block.sync
            def _(sp):
                for dst, src in ((a_log, d["dn_a_log_2"]), (dt_bias, d["dn_dt_bias_2"])):
                    sp.dma_start(dst[:], bass.AP(tensor=src.tensor, offset=src.offset, ap=[[0, P], [1, 4]])
                                 ).then_inc(landed, 16)

            @block.scalar
            def _(act):
                act.wait_ge(landed, 32)
                act.activation(a_log[:], a_log[:], ACT.Exp).then_inc(exped, 1)
                act.activation(beta[:], ab[:, :, 4:8], ACT.Sigmoid).then_inc(exped, 1)
                act.wait_ge(prepared, 1)
                act.activation(e[:], neg[:], ACT.Exp).then_inc(logged, 1)
                act.wait_ge(prepared, 2)
                act.activation(e[:], e[:], ACT.Ln).then_inc(logged, 1)
                act.wait_ge(decays, 2)
                act.activation(left[:], left[:], ACT.Exp)
                act.activation(eg[:], gc[:], ACT.Exp)

            @block.vector
            def _(dve):
                chain = Chain(dve, own)

                def tiles(t):
                    return t[:].rearrange("p (a h) -> p a h", a=1).broadcast_to([P, 4, 4])

                dve.wait_ge(landed, 32)
                dve.wait_ge(exped, 2)
                chain.link(dve.tensor_tensor(x[:], ab[:, :, 0:4], tiles(dt_bias), ALU.add))
                chain.link(dve.tensor_scalar(neg[:], x[:], -1.0, None, ALU.mult))
                dve.tensor_tensor(neg[:], neg[:], x[:], ALU.min).then_inc(prepared, 1)
                dve.wait_ge(logged, 1)
                dve.tensor_scalar(e[:], e[:], 1.0, None, ALU.add).then_inc(prepared, 1)
                dve.wait_ge(logged, 2)
                chain.link(dve.scalar_tensor_tensor(out=g[:], in0=x[:], scalar=0.0, in1=e[:], op0=ALU.max, op1=ALU.add))
                chain.link(dve.tensor_tensor(g[:], g[:], tiles(a_log), ALU.mult))
                dve.tensor_scalar(g[:], g[:], -1.0, None, ALU.mult).then_inc(decays, 1)
                dve.wait_ge(summed, 1)
                chain.link(dve.tensor_copy(gc[:].rearrange("p a h -> p (a h)"), ps[0][:, 0:16]))
                dve.tensor_tensor(left[:].rearrange("p a h -> p (a h)"), ps[1][:, 0:16],
                                  gc[:].rearrange("p a h -> p (a h)"), ALU.subtract).then_inc(decays, 1)

            @block.tensor
            def _(pe):
                pe.wait_ge(decays, 1)
                gf = g[:].rearrange("p a h -> p (a h)")
                pe.matmul(ps[0][:, 0:16], c["incl_fwd"], gf, start=True, stop=True)
                pe.matmul(ps[1][:, 0:16], c["heads2"], gf, start=True, stop=True).then_inc(summed, 1)

        n_all = 16
        nmat, aqk = sb("n", [P, n_all, P]), sb("aqk_t", [P, n_all, P])
        rhs = sb("rhs", [P, n_all, 256])
        sol = rhs
        ends = sb("ends", [P, n_all, 2])
        with Stage(nc, "dn_matrices") as st:
            gb = [st.sb(f"g_spread{i}", [P, P]) for i in range(2)]
            arg = [st.sb(f"arg{i}", [P, 2, P]) for i in range(2)]
            row = [st.sb(f"row{i}", [P, P]) for i in range(2)]
            eb = st.sb("exp_beta", [P, 4, 4])
            ps_r = [st.ps(f"row_ps{i}", [P, BANK]) for i in range(2)]
            ps_k = [st.ps(f"gram{i}", [P, BANK]) for i in range(2)]
            spread, rowed, grammed, args, exped, rowed_exp, masked, own = (
                st.sem(n) for n in ("spread", "rowed", "grammed", "args", "exped", "rowed_exp", "masked", "own"))
            block = st.block()

            @block.gpsimd
            def _(pool):
                for i in range(n_all):
                    if i >= 2:
                        pool.wait_ge(rowed, i - 1)
                    pool.tensor_scalar(gb[i % 2][:], c["ones"], g[:, i // 4, i % 4:i % 4 + 1], None,
                                       ALU.mult).then_inc(spread, 1)

            @block.tensor
            def _(pe):
                for i in range(n_all):
                    t, h = i // 4, i % 4
                    at = slice(t * P, (t + 1) * P)
                    pe.wait_ge(spread, i + 1)
                    if i >= 2:
                        pe.wait_ge(exped, i - 1)
                        pe.wait_ge(masked, i - 1)
                    pe.matmul(ps_r[i % 2][:, 0:P], gb[i % 2][:], c["incl_fwd"], start=True, stop=True).then_inc(rowed, 1)
                    pe.matmul(ps_k[i % 2][:, 0:P], k[:, h, at], k[:, h, at], start=True, stop=True)
                    pe.matmul(ps_k[i % 2][:, P:2 * P], k[:, h, at], q[:, h, at], start=True, stop=True).then_inc(grammed, 1)

            @block.scalar
            def _(act):
                for i in range(n_all):
                    act.wait_ge(args, i + 1)
                    act.activation(row[i % 2][:], ps_r[i % 2][:, 0:P], ACT.Exp)
                    act.activation(arg[i % 2][:], arg[i % 2][:], ACT.Exp).then_inc(exped, 1)

            @block.vector
            def _(dve):
                chain = Chain(dve, own)
                chain.link(dve.tensor_tensor(eb[:], eg[:], beta[:], ALU.mult))
                chain.link(dve.tensor_scalar(eb[:], eb[:], -1.0, None, ALU.mult))
                for i in range(n_all):
                    t, h = i // 4, i % 4
                    at, hs = slice(t * P, (t + 1) * P), slice(h * P, (h + 1) * P)
                    dve.wait_ge(rowed, i + 1)
                    chain.link(dve.tensor_scalar(arg[i % 2][:, 0, :], ps_r[i % 2][:, 0:P], gc[:, t, h:h + 1], 0.0,
                                                 ALU.subtract, ALU.min))
                    chain.link(dve.tensor_scalar(arg[i % 2][:, 1, :], ps_r[i % 2][:, 0:P], gc[:, t, h:h + 1], 0.0,
                                                 ALU.subtract, ALU.max))
                    dve.tensor_scalar(arg[i % 2][:, 1, :], arg[i % 2][:, 1, :], -1.0, None, ALU.mult).then_inc(args, 1)
                    dve.tensor_scalar(rhs[:, i, 0:P], vtok[:, t, hs], beta[:, t, h:h + 1], None, ALU.mult)
                    dve.tensor_scalar(rhs[:, i, P:2 * P], ktok[:, t, hs], eb[:, t, h:h + 1], None, ALU.mult)
                    dve.wait_ge(exped, i + 1)
                    dve.wait_ge(grammed, i + 1)
                    chain.link(dve.tensor_tensor(arg[i % 2][:, 0, :], arg[i % 2][:, 0, :], c["incl_fwd"], ALU.mult))
                    chain.link(dve.tensor_tensor(arg[i % 2][:, 1, :], arg[i % 2][:, 1, :], c["strict_rev"], ALU.mult))
                    chain.link(dve.tensor_copy(ends[:, i, 0:1], row[i % 2][:, 63:64]))
                    chain.link(dve.tensor_copy(ends[:, i, 1:2], row[i % 2][:, 127:128]))
                    dve.tensor_tensor(aqk[:, i, :], ps_k[i % 2][:, P:2 * P], arg[i % 2][:, 0, :], ALU.mult)
                    dve.scalar_tensor_tensor(out=nmat[:, i, :], in0=ps_k[i % 2][:, 0:P], scalar=beta[:, t, h:h + 1],
                                             in1=arg[i % 2][:, 1, :], op0=ALU.mult, op1=ALU.mult).then_inc(masked, 1)
                    dve.wait_ge(masked, i + 1)
                    chain.link(dve.tensor_tensor(q[:, h, at], q[:, h, at], row[i % 2][:], ALU.mult))
                    chain.link(dve.tensor_scalar(ktok[:, t, hs], ktok[:, t, hs], left[:, t, h:h + 1], None, ALU.mult))
        for b in range(4):
            s = slice(4 * b, 4 * b + 4)
            solve(nc, f"dn_solve{b}", c, nmat[:, s], rhs[:, s], sol[:, s], 4, 256)
        turned = sb("w_t", [P, n_all, P])
        to_features(nc, "dn_w", [([sol[:, i + j, P:2 * P] for j in range(4)], None,
                                  turned[:, i:i + 4, :].rearrange("p a b -> p (a b)")) for i in range(0, n_all, 4)],
                    c["ident"])
        with Stage(nc, "dn_scan") as st:
            state, vnew = st.sb("state", [P, 4, P]), st.sb("v_new", [P, 4, P])
            ps_w, ps_s = st.ps("w_state", [P, BANK]), st.ps("new_state", [P, BANK])
            ps_o, ps_a = [st.ps(f"q_state{i}", [P, BANK]) for i in range(2)], [st.ps(f"qk_v{i}", [P, BANK]) for i in range(2)]
            cleared, pe_done, dve_done, tile_out, own = (st.sem(n) for n in ("cleared", "pe_done", "dve_done", "tile_out", "own"))
            block = st.block()

            @block.tensor
            def _(pe):
                pe.wait_ge(cleared, 1)
                for n in range(8):
                    t, hf = n // 2, n % 2
                    r = slice(CH * hf, CH * hf + CH)
                    at = slice(n * CH, n * CH + CH)
                    if n:
                        pe.wait_ge(dve_done, 2 * n)
                    if hf == 0 and t >= 2:
                        pe.wait_ge(tile_out, t - 1)
                    for h in range(4):
                        ins = pe.matmul(ps_w[r, h * P:(h + 1) * P], turned[:, 4 * t + h, r], state[:, h, :],
                                        start=True, stop=True)
                    ins.then_inc(pe_done, 1)
                    for h in range(4):
                        pe.matmul(ps_o[t % 2][:, h * P + CH * hf:h * P + CH * hf + CH], state[:, h, :], q[:, h, at],
                                  start=True, stop=True)
                    pe.wait_ge(dve_done, 2 * n + 1)
                    for h in range(4):
                        ins = pe.matmul(ps_s[:, h * P:(h + 1) * P], ktok[r, t, h * P:(h + 1) * P], vnew[r, h, :],
                                        start=True, stop=True)
                    ins.then_inc(pe_done, 1)
                    if hf == 1:
                        for h in range(4):
                            ins = pe.matmul(ps_a[t % 2][:, h * P:(h + 1) * P], vnew[:, h, :], aqk[:, 4 * t + h, :],
                                            start=True, stop=True)
                        ins.then_inc(pe_done, 1)

            @block.vector
            def _(dve):
                chain = Chain(dve, own)
                dve.memset(state[:], 0.0).then_inc(cleared, 1)
                dve.wait_ge(cleared, 1)
                for n in range(8):
                    t, hf = n // 2, n % 2
                    r = slice(CH * hf, CH * hf + CH)
                    done = 2 * n + n // 2
                    dve.wait_ge(pe_done, done + 1)
                    dve.tensor_tensor(vnew[r], sol[r, 4 * t:4 * t + 4, 0:P],
                                      ps_w[r, :].rearrange("p (h j) -> p h j", j=P), ALU.add).then_inc(dve_done, 1)
                    dve.wait_ge(pe_done, done + 2)
                    for h in range(4):
                        ins = dve.scalar_tensor_tensor(out=state[:, h, :], in0=state[:, h, :],
                                                       scalar=ends[:, 4 * t + h, hf:hf + 1],
                                                       in1=ps_s[:, h * P:(h + 1) * P], op0=ALU.mult, op1=ALU.add)
                    ins.then_inc(dve_done, 1)
                    if hf == 1:
                        dve.wait_ge(pe_done, done + 3)
                        o = out[:, :, t * P:(t + 1) * P]
                        chain.link(dve.tensor_copy(o, ps_o[t % 2][:].rearrange("p (h t) -> p h t", t=P)))
                        dve.tensor_tensor(o, o, ps_a[t % 2][:].rearrange("p (h t) -> p h t", t=P),
                                          ALU.add).then_inc(tile_out, 1)
                    dve.wait_ge(dve_done, 2 * n + 2)


def rows_to_tokens(nc, name, rows, out, ident):
    m = rows.shape[0]
    with Stage(nc, name) as st:
        ps = st.ps("turned", [P, 4, m])
        turned = st.sem("turned")
        block = st.block()

        @block.tensor
        def _(pe):
            for t in range(4):
                ins = pe.transpose(ps[:, t, :], rows[:, t * P:(t + 1) * P], ident[0:m, 0:m])
            ins.then_inc(turned, 1)

        @block.vector
        def _(dve):
            dve.wait_ge(turned, 1)
            dve.tensor_copy(out[:], ps[:])


Q0, KV0, G0, DN0, AB0, Z0, MQ0 = 0, 512, 1280, 1304, 2840, 2848, 3360


def mixer_weights(d):
    W, kv = d["w_in_2"], d["w_mem_kv_2"]
    wv = W.rearrange("(k p) n -> p k n", p=P)
    v_blocks = [([(lambda buf, i=i: buf[:, :, P * i:P * i + P],
                   wv[:, k0:k0 + 4, KV0 + 384 + 256 * i:KV0 + 512 + 256 * i]) for i in range(2)],
                 [P, P], list(range(k0, k0 + 4))) for k0 in (0, 4)]
    return {"nsa_in": pair_blocks(wv, Q0, 0) + pair_blocks(wv, Q0, 2) + weight_blocks(W, KV0, 256)
            + weight_blocks(W, KV0 + 256, 128) + weight_blocks(W, KV0 + 512, 128) + weight_blocks(W, G0, 24),
            "nsa_v": v_blocks,
            "cmp_k": weight_blocks(d["cmp_k_w1_2"], 0, 256, kc=16), "cmp_v": weight_blocks(d["cmp_v_w1_2"], 0, 256, kc=16),
            "dn_in": weight_blocks(W, DN0, 1536) + weight_blocks(W, Z0, 512) + weight_blocks(W, AB0, 8),
            "mem_q": weight_blocks(W, MQ0, 512), "mem_k": weight_blocks(kv, 0, 512),
            "mem_v": weight_blocks(kv, 512, 512, width=512),
            "merge_gates": weight_blocks(d["w_branch_gate_2"], 0, 3 * D),
            **{f"merge{b}": weight_blocks(d[n], 0, D, kc=4)
               for b, n in enumerate(("w_branch_nsa_2", "w_branch_dn_2", "w_branch_mem_2"))},
            "mix_out": weight_blocks(d["w_out_2"], 0, D)}


def mixer(nc, d, w, c, v, x):
    with ExitStack() as keep:
        def sb(name, shape, stack=keep, dtype=F32):
            return stack.enter_context(nc.sbuf_tensor("mix_" + name, shape, dtype))

        def pair(name, shape, stack):
            return [sb(f"{name}_{part}", shape, stack, F32R) for part in ("high", "low")]

        def parts(tiles):
            return [lambda k, t=t: t[:, k, :] for t in tiles]

        u2 = pair("u", [P, KD, S], keep)
        u = parts(u2)
        branch = [sb(f"branch{i}", [P, 4, S]) for i in range(3)]
        norm(nc, "mix_pre", lambda k: x[:, k, :], S, lambda k: v("mix_pre_norm_2", k, 1), c, split=u)

        with ExitStack() as inner:
            relative = Ahead(nc, inner, "relative")
            rel_bias_lines(nc, d, relative)
            q = sb("q", [P, 4, S], inner)
            ks = sb("keys", [P, 4, S], inner)
            vs = sb("values", [P, 4, 256], inner)
            gates, gate_rows = sb("gates", [P, 4, 24], inner), sb("gate_rows", [24, S], inner)
            outs = ([(q[:, i, :], 0.125) for i in range(4)] + [(ks[:, i, :], None) for i in range(4)]
                    + [(gate_rows[:], None)])
            linear(nc, "nsa_in", w, *u, S,
                   lambda e, n, ps: copy_on(e, nc, outs[n][0], ps[0:outs[n][0].shape[0], 0:S], outs[n][1]))

            linear_tokens(nc, "nsa_v", w, *u, S, lambda e, b, t, ps: copy_on(e, nc, vs[:, t, :], ps[:, 0:256]))
            rows_to_tokens(nc, "nsa_gate_turn", gate_rows[:], gates, c["ident"])
            kc, vc = sb("k_cmp", [P, N_CMP], inner), sb("v_cmp", [N_CMP, P], inner)
            tables = []
            compress(nc, w, ks[:, 0:2, :], (v("cmp_pos_k"), v("cmp_pos_v")), (d["cmp_k_w2_2"], d["cmp_v_w2_2"]),
                     c["ident"], kc, vc, lambda: tables.append(rel_bias_table(nc, d, relative)))
            table = tables[0]
            with Stage(nc, "nsa_gates") as st:
                opened = st.sem("opened")
                block = st.block()

                @block.scalar
                def _(act):
                    act.activation(gates[:], gates[:], ACT.Sigmoid).then_inc(opened, 1)

                @block.vector
                def _(dve):
                    dve.wait_ge(opened, 1)
                    dve.tensor_scalar(gates[:, 0, 0:8], gates[:, 0, 0:8], c["has_block"], None, ALU.mult)

            o = [branch[0]] + [sb(f"o{i}", [P, 4, 512], inner) for i in range(2)]
            relative.arrive()
            units = []
            for t in range(4):
                for h in range(8):
                    b = 64 * (h // 4)
                    y0 = 384 - P * t
                    a, q_at = 64 * (h % 2), slice(t * P, (t + 1) * P)
                    common = dict(at=a, q=q[b:b + 64, h % 4, t * P:(t + 1) * P])
                    ends = y0 + 31 + 16 * (N_CMP - 1) + 1
                    units.append(dict(common, keys=[kc[b:b + 64, :]], bias=table[:, h, y0 + 31:ends:16],
                                      values=[vc[:, b:b + 64]], out=o[0][a:a + 64, h // 2, q_at],
                                      rows=gates[:, t, h:h + 1]))
                    for n in range(2):
                        units.append(dict(common, keys=[ks[b:b + 64, 2 + n, 0:(t + 1) * P]],
                                          bias=table[:, h, y0:y0 + (t + 1) * P],
                                          values=[vs[:, j, P * n + b:P * n + b + 64] for j in range(t + 1)],
                                          out=o[1 + n][a:a + 64, h // 2, q_at],
                                          rows=gates[:, t, 8 * (n + 1) + h:8 * (n + 1) + h + 1]))
            attention(nc, "nsa", units, c["ident"], c["ones"], bufs=3)
            with Stage(nc, "nsa_sum") as st:
                own = st.sem("own")
                block = st.block()

                @block.vector
                def _(dve):
                    chain = Chain(dve, own)
                    chain.link(dve.tensor_tensor(o[1][:], o[1][:], o[0][:], ALU.add))
                    dve.tensor_tensor(branch[0][:], o[2][:], o[1][:], ALU.add)

        right = keep.enter_context(ExitStack())
        mem_ahead = Ahead(nc, right, "memory")
        with ExitStack() as inner:
            zg = sb("dn_z", [P, 4, S], inner)
            qkv, ab = sb("qkv", [P, 12, S], inner), sb("ab", [P, 4, 8], inner)
            ab_rows = sb("ab_rows", [8, S], inner)
            with nc.sbuf_tensor("dn_padded", [P, 2, S + 3], F32) as padded:
                zero(nc, "dn_pad", [padded[:]])

                def evict(act, n, ps):
                    if n < 12:
                        return act.copy(padded[:, n % 2, 3:3 + S], ps[:, 0:S])
                    if n < 16:
                        return act.activation(zg[:, n - 12, :], ps[:, 0:S], ACT.Silu)
                    return act.copy(ab_rows[:], ps[0:8, 0:S])

                def convolve(dve, chain, n):
                    o = qkv[:, n, :]
                    chain.link(dve.tensor_scalar(o, padded[:, n % 2, 0:S], v("dn_conv", n, 1), None, ALU.mult))
                    for tap in (1, 2, 3):
                        ins = dve.scalar_tensor_tensor(out=o, in0=padded[:, n % 2, tap:tap + S],
                                                       scalar=v("dn_conv", 12 * tap + n, 1), in1=o,
                                                       op0=ALU.mult, op1=ALU.add)
                        if tap < 3:
                            chain.link(ins)
                    return ins

                linear(nc, "dn_in", w, *u, S, evict, engines="a", after=(convolve, 12))
            in_place(nc, "dn_conv_silu", [qkv[:, i, :] for i in range(12)], ACT.Silu)
            rows_to_tokens(nc, "dn_ab_turn", ab_rows[:], ab, c["ident"])
            delta_branch(nc, d, c, v, qkv, ab, branch[1], branch[2])
            mem = mem_ahead.sb("mem", [P, KD, 256])
            mem_ahead.start(mem[:], d["mem"].rearrange("(k p) t -> p k t", p=P))
            head_norm(nc, "dn_out_norm", c, [branch[1][:, i, :] for i in range(4)], [v("dn_out_norm")] * 4,
                      c["pick_mean128"], d["c_spread1"])
            with Stage(nc, "dn_gated") as st:
                block = st.block()

                @block.vector
                def _(dve):
                    dve.tensor_tensor(branch[1][:], branch[1][:], zg[:], ALU.mult)

        with ExitStack() as inner:
            mq, mk = sb("mem_q", [P, 4, S], inner), sb("mem_k", [P, 4, 256], inner)
            mv = sb("mem_v", [P, 2, 512], inner)
            mem_n2 = pair("mem_n", [P, KD, 256], inner)
            mem_n = parts(mem_n2)
            mem_ahead.arrive()
            norm(nc, "mem_norm", lambda k: mem[:, k, :], 256,
                 lambda k: v("mem_norm_2", k, 1), c, split=mem_n)
            linear(nc, "mem_q", w, *u, S,
                   lambda e, n, ps: copy_on(e, nc, mq[:, n, :], ps[:, 0:S], 128.0 ** -0.5))
            linear(nc, "mem_k", w, *mem_n, 256,
                   lambda e, n, ps: copy_on(e, nc, mk[:, n, :], ps[:, 0:256]))
            linear_tokens(nc, "mem_v", w, *mem_n, 256,
                          lambda e, b, t, ps: copy_on(e, nc, mv[:, t, :], ps[:]))
            attention(nc, "mem", [dict(q=mq[:, h, t * P:(t + 1) * P], keys=[mk[:, h, :]], bias=None,
                                       values=[mv[:, j, h * P:(h + 1) * P] for j in range(2)],
                                       at=0, out=branch[2][:, h, t * P:(t + 1) * P])
                                  for t in range(4) for h in range(4)], c["ident"], c["ones"], bufs=3)

        right.close()

        with ExitStack() as inner:
            gate = sb("branch_gates", [P, 24, S], inner)
            linear(nc, "merge_gates", w, *u, S,
                   lambda e, n, ps: e.activation(gate[:, n, :], ps[:, 0:S], ACT.Sigmoid), engines="a")
            merged = inner.enter_context(nc.semaphore("merged"))
            chain = Chain(nc.vector, merged)

            def merge(dve, b, n, ps):
                g = gate[:, 8 * b + n, :]
                ins = dve.tensor_tensor(g, g, ps[:, 0:S], ALU.mult)
                if b:
                    chain.link(ins)
                    ins = dve.tensor_tensor(gate[:, n, :], gate[:, n, :], g, ALU.add)
                return ins

            branch2 = parts(pair("branch_now", [P, 4, S], inner))
            for b in range(3):
                linear(nc, f"merge{b}", w, *branch2, S,
                       lambda e, n, ps: merge(e, b, n, ps), kc=4, engines="v", raw=lambda k: branch[b][:, k, :])
            linear(nc, "mix_out", w, *u, S,
                   lambda e, n, ps: copy_on(e, nc, gate[:, 8 + n, :], ps[:, 0:S]),
                   raw=lambda k: gate[:, k, :])
            norm(nc, "mix_post", lambda k: gate[:, 8 + k, :], S,
                 lambda k: v("mix_post_norm_2", k, 1), c, residual=lambda k: x[:, k, :])


def constants():
    out = {}
    ident = np.eye(P, dtype=np.float32)
    ones = np.ones((P, P), np.float32)
    group64 = np.kron(np.eye(2), np.ones((64, 64)) / 64).astype(np.float32)
    swap = np.zeros((P, P), np.float32)
    for f in range(P):
        if f % 32 < 16:
            swap[f + 16, f] = -1.0
        else:
            swap[f - 16, f] = 1.0
    t = np.arange(S)
    pos = np.stack([t // 64, t % 64], 0).astype(np.float32)
    inv = (np.float32(10000.0) ** (-np.arange(16, dtype=np.float32) / np.float32(16))).astype(np.float32)
    f = np.arange(P) % 64
    ang = (pos[f // 32] * inv[f % 16][:, None]).astype(np.float32)
    out["cos"], out["sin"] = np.cos(ang).astype(np.float32), np.sin(ang).astype(np.float32)
    col = np.arange(64)
    start = np.clip(col - 8, 0, 48)
    window = np.where((col[None] >= start[:, None]) & (col[None] < start[:, None] + 16), 0.0, NEG)
    window = np.concatenate([window, window], 0).astype(np.float32)
    small = {"ident": ident, "ones": ones, "group64": group64, "swap": swap, "window": window}
    s_i, t_i = np.arange(P)[:, None], np.arange(P)[None, :]
    same64, same16 = s_i // 64 == t_i // 64, s_i // 16 == t_i // 16
    for name, before in (("fwd", s_i < t_i), ("rev", s_i > t_i)):
        small[f"strict_{name}"] = (before & same64).astype(np.float32)
        small[f"incl_{name}"] = ((before | (s_i == t_i)) & same64).astype(np.float32)
    small["same16"] = same16.astype(np.float32)
    small["heads2"] = np.kron(np.eye(2), np.ones((64, 64))).astype(np.float32)
    has = (np.arange(P) >= 31).astype(np.float32)[:, None]
    small["has_block"] = has
    small["group128"] = np.full((P, P), 1 / 128, np.float32)
    small["root128"] = np.full((P, 1), 128.0 ** -0.5, np.float32)
    first = (np.arange(P) == 0)[:, None]
    small["half_root"] = np.full((P, 1), 0.5 ** 0.5, np.float32)
    small["sum_root"] = np.where(first, 1.0, 0.5 ** 0.5).astype(np.float32)
    small["diff_root"] = np.where(first, 0.0, 0.5 ** 0.5).astype(np.float32)
    for name, eps in (("eps", 1e-6), ("eps12", 1e-12), ("eps_gn", 64e-5)):
        small[name] = np.full((P, 1), eps, np.float32)
    col = np.arange(32)[None]
    for name, heads, value in (("mean64", 2, 1 / 64), ("sum64", 2, 1.0), ("mean128", 1, 1 / 128), ("sum128", 1, 1.0)):
        small["pick_" + name] = np.where(col == 16 + np.arange(P)[:, None] * heads // P, value, 0.0).astype(np.float32)
    for heads in (1, 2):
        at = np.arange(8 * P)[None]
        out[f"spread{heads}"] = (np.arange(8 * heads)[:, None] == at * heads // P).astype(np.float32)
    del small["group128"]
    out["small"] = np.concatenate(list(small.values()), 1)
    where, at = {}, 0
    for k, v in small.items():
        where[k] = (at, v.shape[1])
        at += v.shape[1]
    w = 2 * np.pi * (np.arange(S)[None, :] + 0.5) / (2 * S) * np.arange(S)[:, None]
    out["dft"] = np.stack([np.cos(w), np.sin(w)]).astype(np.float32)
    out["idft"] = (np.stack([np.cos(w).T, np.sin(w).T]) / S).astype(np.float32)
    ti = np.arange(S, dtype=np.float32)
    tt = ti / np.float32(S - 1)
    bands = np.linspace(1e-4, 15, 16, dtype=np.float32)
    ang = (np.float32(2.0 * np.pi) * bands[None, :] * ti[:, None] / np.float32(S)).astype(np.float32)
    out["feats"] = np.concatenate([tt[:, None], np.cos(ang), -np.sin(ang)], -1).T.astype(np.float32).copy()
    deltas = np.linspace(np.log(1e-2) / 0.3, np.log(1e-2) / 1.5, S, dtype=np.float32)
    out["decay"] = np.exp(-tt[:, None] * np.abs(deltas)).astype(np.float32)
    m = np.arange(2 * S)
    dist = (S - 1) - m
    dd = np.maximum(dist, 0)
    logb = 16 + (np.log(np.maximum(dd, 1).astype(np.float32) / 16) / np.log(128 / 16) * 16).astype(np.int32)
    bucket = np.where(dd < 16, dd, np.minimum(logb, 31))
    out["bucket"] = (np.arange(32)[:, None] == bucket[None]).astype(np.float32)
    out["causal"] = np.broadcast_to(np.where(dist >= 0, 0.0, NEG), (8, 2 * S)).astype(np.float32).copy()
    return out, where


def columns(v):
    return np.asarray(v).reshape(-1, P).T


def vectors(i):
    v = {
        "cond": np.stack([columns(i["c"][0]), columns(i["c_ctx"])], 2).reshape(P, -1),
        "attn_ada_b": columns(i["attn_ada_b"][0]), "rec_ada_b": columns(i["rec_ada_b"][0]),
        "q_gain": np.tile(i["gqa_q_gain"][0], 2)[:, None], "k_gain": np.tile(i["gqa_k_gain"][0], 2)[:, None],
        "mu": columns(i["rwkv_mu"][0]),
        "w0": columns(i["rwkv_w0"][0].reshape(-1)), "a0": columns(i["rwkv_a0"][0].reshape(-1)),
        "hy_short": columns(i["hy_short"][0].reshape(-1)), "hy_skip": columns(i["hy_skip"][0].reshape(-1)),
        "hy_b1": np.tile(i["hy_b1"][0], 2)[:, None], "hy_b2": np.tile(i["hy_b2"][0], 2)[:, None],
        "r_k": columns(i["rwkv_r_k"][0].reshape(-1)),
        "dn_conv": columns(i["dn_conv_w_2"][0].reshape(-1)),
        "dn_out_norm": columns(i["dn_out_norm_2"][0]),
        "cmp_pos_k": np.tile(i["cmp_pos_k_2"][0].T, (2, 1)), "cmp_pos_v": np.tile(i["cmp_pos_v_2"][0].T, (2, 1)),
    }
    for name in ("attn_norm", "rec_norm", "rwkv_k_k", "rwkv_k_a", "rwkv_gn_w", "rwkv_gn_b", "ffn1_pre_norm_2",
                 "ffn1_post_norm_2", "mix_pre_norm_2", "mem_norm_2", "mix_post_norm_2", "ffn2_pre_norm_2",
                 "ffn2_post_norm_2"):
        v[name] = columns(i[name][0])
    v["final_norm"] = columns(i["final_norm"])
    where, at = {}, 0
    for k, a in v.items():
        where[k] = (at, a.shape[1])
        at += a.shape[1]
    return np.ascontiguousarray(np.concatenate(list(v.values()), 1)), where
class Columns:

    def __init__(self, tile, where):
        self.tile, self.where = tile, where

    def __call__(self, name, first=0, count=None):
        at, n = self.where[name]
        n = n - first if count is None else count
        return self.tile[:, at + first:at + first + n]


def rec_weights(d):
    W = d["rec_w_in"]
    return {"rec_gate": weight_blocks(W, 1664, 512), "hy_in": weight_blocks(W, 2176, 2048),
            "rwkv_in": weight_blocks(W, 0, 1664)}


def rec_layer(nc, d, w, streams, c, v, x, ctx, mod, gs):
    with ExitStack() as keep:
        def sb(name, shape, stack=keep):
            return stack.enter_context(nc.sbuf_tensor("rec_" + name, shape, F32))

        y = sb("y", [P, KD, S])
        filters, loaded = keep.enter_context(ExitStack()), keep.enter_context(ExitStack())
        with ExitStack() as mid:
            gate, ends = sb("gate", [P, 4, S], mid), sb("ends", [P, 2, 4, TT // CH], mid)
            v_feat, bonus = sb("v_features", [P, 4, S], mid), sb("bonus", [P, 4, S], mid)
            with ExitStack() as shifted:
                us = sb("shifted", [P, 13, TT], shifted)
                with ExitStack() as inner:
                    h = [inner.enter_context(nc.sbuf_tensor("rec_h_" + part, [P, KD, TT], F32R))
                         for part in ("high", "low")]
                    norm(nc, "rec_norm_x", lambda k: x[:, k, :], S, lambda k: gs[:, k, 0:1], c,
                         split=[lambda k, t=t: t[:, k, 0:S] for t in h], shift=lambda k: mod[:, k, 0:1], scratch=lambda k: y[:, k, :])
                    norm(nc, "rec_norm_ctx", lambda k: ctx[:, k, :], LC, lambda k: gs[:, k, 1:2], c,
                         split=[lambda k, t=t: t[:, k, S:TT] for t in h], shift=lambda k: mod[:, k, 1:2], scratch=lambda k: y[:, k, 0:LC])
                    h = [lambda k, t=t: t[:, k, :] for t in h]
                    linear(nc, "rec_gate", w, *h, S, lambda e, n, ps: copy_on(e, nc, gate[:, n, :], ps[:, 0:S]))
                    hyena_input(nc, d, w, v, h, [y[:, 0:4], y[:, 4:8], bonus[:]], v_feat[:])
                    rwkv_input(nc, w, v, h, us, y[:])
                    streams.close()
                tokens = mid.enter_context(ExitStack())
                vt = tokens.enter_context(nc.sbuf_tensor("rec_v_tokens", [P, 6, 512], F32, side="right"))
                to_features(nc, "rwkv_vt", [([us[:, 8 + i, t * P:(t + 1) * P] for i in range(4)], None, vt[:, t, :])
                                            for t in range(6)], c["ident"])
                in_sbuf_copy(nc, "rwkv_v", v_feat[:], us[:, 8:12, 0:S])
                kk = sb("kk", [P, 4, TT], shifted)
                head_norm(nc, "rwkv_kk", c, [us[:, 4 + i, :] for i in range(4)],
                          [v("rwkv_k_k", i, 1) for i in range(4)], c["pick_sum64"], d["c_spread2"],
                          outs=[kk[:, i, :] for i in range(4)], scaled=True, eps=c["eps12"])
                rwkv_features(nc, "rwkv_feat", d, c, v, [us[:, i, :] for i in range(13)], kk, bonus, ends)
            scanned = sb("scanned", [P, 4, S], mid)
            rwkv_scan(nc, d, c, vt, ends, scanned)
            tokens.close()
            loads = filter_loads(nc, d, filters, loaded)
            group_norm_out(nc, "rwkv_out", c, v, scanned, bonus, v_feat, gate, y[:, 0:4, :])
        hyena_branch(nc, d, c, v, y[:, 4:8, :], loads, loaded)
        filters.close()
        out_weights = WeightStream(nc, keep, "rec_out", {"rec_out": weight_blocks(d["rec_w_out"], 0, D)})
        gated_out(nc, "rec_out", out_weights, lambda k: y[:, k, :], x, None, mod)


def program(nc, d, vec_at, const_at):
    Stage.used = 0
    for name, shape in (("s_rpb", [64, 8 * 15, 127]), ("s_feat", [2, 4, 512, TT]), ("s_rel", [8, P, 2 * S]),
                        ("s_hy", [4 * 512, S])):
        d[name] = nc.dram_tensor(name, shape, F32, kind="Internal").ap()
    with ExitStack() as keep:
        def sb(name, shape, stack=keep):
            return stack.enter_context(nc.sbuf_tensor(name, shape, F32))

        out_stored = keep.enter_context(nc.semaphore("out_stored"))
        x = sb("x", [P, KD, S])
        vec, const = sb("vectors", list(d["vec"].shape)), sb("constants", list(d["c_small"].shape))
        v, constant = Columns(vec, vec_at), Columns(const, const_at)
        c = {n: constant(n) for n in const_at}
        with ExitStack() as first:
            ctx = sb("ctx", [P, KD, LC], first)
            mods = [(sb(f"mod{i}", [P, 24, 2], first), sb(f"gain_scale{i}", [P, KD, 2], first)) for i in range(2)]
            q_gain = sb("q_gain", [P, 1], first)
            streams = first.enter_context(ExitStack())
            w = WeightStream(nc, streams, "first_w", {
                "adaln": [b for n in ("attn", "rec") for b in weight_blocks(d[n + "_ada_w"], 0, 3 * D, width=512)],
                **attn_weights(d), **rec_weights(d)})
            load(nc, "vectors", [(vec[:], d["vec"]), (const[:], d["c_small"])])
            w.start()
            inputs = Ahead(nc, first, "inputs")
            for dst, n in ((x, "x"), (ctx, "ctx")):
                inputs.start(dst[:], d[n].rearrange("(k p) t -> p k t", p=P))
            cond = v("cond").rearrange("p (k j) -> p k j", j=2)
            adaln(nc, w, cond, [(v(n + "_ada_b"), v(n + "_norm"), *mods[i]) for i, n in enumerate(("attn", "rec"))],
                  c["ident"])
            with Stage(nc, "gains") as st:
                block = st.block()

                @block.vector
                def _(dve):
                    dve.tensor_scalar(q_gain[:], v("q_gain"), 0.125, None, ALU.mult)
            c["q_gain"], c["k_gain"] = q_gain[:], v("k_gain")
            inputs.arrive()
            attn_layer(nc, d, w, c, x, ctx, *mods[0])
            rec_layer(nc, d, w, streams, c, v, x, ctx, *mods[1])
            norm(nc, "final_norm", lambda k: x[:, k, :], S, lambda k: v("final_norm", k, 1), c,
                 out=lambda k: x[:, k, :])
        with ExitStack() as streams:
            w = WeightStream(nc, streams, "second_w", {**ffn_weights(d, 1), **mixer_weights(d), **ffn_weights(d, 2)}, splits=2)
            w.start()
            ffn(nc, "ffn1", d, w, c, v, x, 1)
            mixer(nc, d, w, c, v, x)
            ffn(nc, "ffn2", d, w, c, v, x, 2)
        with Stage(nc, "store_out") as st:
            block = st.block()

            @block.sync
            def _(sp):
                sp.dma_start(d["out"].rearrange("(k p) t -> p k t", p=P), x[:]).then_inc(out_stored, 16)
                sp.wait_ge(out_stored, 16)


_WEIGHTS = ["attn_ada_w", "attn_w_in", "na_rpb", "attn_w_out", "rec_ada_w", "rec_w_in", "rwkv_w_up", "rwkv_a_up",
            "hy_w1", "hy_w2", "hy_w3", "rec_w_out", "ffn1_w_gate_2", "ffn1_w_up_2", "ffn1_w_down_2", "w_in_2",
            "cmp_k_w1_2", "cmp_k_w2_2", "cmp_v_w1_2", "cmp_v_w2_2", "dn_a_log_2", "dn_dt_bias_2", "w_mem_kv_2",
            "w_branch_nsa_2", "w_branch_dn_2", "w_branch_mem_2", "w_branch_gate_2", "w_out_2", "ffn2_w_gate_2",
            "ffn2_w_up_2", "ffn2_w_down_2"]


def kernel(**inputs):
    import concourse.bacc as _bacc
    from concourse.bass_utils import run_bass_kernel_spmd as _run

    i = {name: np.asarray(a) for name, a in inputs.items()}
    consts, const_at = constants()
    vec, vec_at = vectors(i)
    arrays = {name: i[name][0] for name in _WEIGHTS}
    arrays["rel_bias_2"], arrays["hy_b3"] = i["rel_bias_2"], i["hy_b3"]
    arrays["x"], arrays["ctx"], arrays["mem"] = i["x"][0].T, i["ctx"][0].T, i["mem_2"][0].T
    arrays["vec"] = vec
    arrays.update({"c_" + name: a for name, a in consts.items()})
    nc = _bacc.Bacc("TRN2", target_bir_lowering=False, num_devices=1)
    sent, d = {}, {}
    for name, a in arrays.items():
        sent[f"in_{name}"] = np.ascontiguousarray(a)
        d[name] = nc.dram_tensor(f"in_{name}", a.shape, F32, kind="ExternalInput").ap()
    d["out"] = nc.dram_tensor("out_0", [D, S], F32, kind="ExternalOutput").ap()
    program(nc, d, vec_at, const_at)
    r = _run(nc, [sent], core_ids=[0])
    return np.ascontiguousarray(r.results[0]["out_0"].T)[None]
```
